# Optimizing a Trainium2 kernel written in Bass

```python
import math
import jax, jax.numpy as jnp
from jax import lax
import numpy as np
import jax
import jax.numpy as jnp

D_MODEL = 1024
BATCH = 1
SEQ = 1024
DEPTH = 1

CONV_CH = D_MODEL // 2
CONV_WIDTH = 31
DA_HEADS = 4
DA_HEAD_DIM = 64
DA_V_DIM = 2 * DA_HEAD_DIM
ATTN_W = DA_HEADS * DA_V_DIM
N_BRANCH = 2
COL_CONV = 2 * CONV_CH
COL_Q = DA_HEADS * 2 * DA_HEAD_DIM
COL_K = DA_HEADS * 2 * DA_HEAD_DIM
COL_V = ATTN_W
COL_GATE = N_BRANCH * D_MODEL
IN_COLS = COL_CONV + COL_Q + COL_K + COL_V + COL_GATE
N_GROUPS = 4
EXPERTS_PER_GROUP = 8
N_EXPERTS = N_GROUPS * EXPERTS_PER_GROUP
TOP_K_IN_GROUP = 2
D_EXPERT = D_MODEL // 2

Q_BLOCK = 128
ROW_BLOCK = 128
EPS = 1e-6


def rms_norm(x, g):
    xf = x.astype(jnp.float32)
    y = xf * lax.rsqrt(jnp.mean(xf * xf, axis=-1, keepdims=True) + EPS)
    return (y * g.astype(jnp.float32)).astype(x.dtype)

def layer_norm(x, g, b):
    xf = x.astype(jnp.float32)
    mu = jnp.mean(xf, axis=-1, keepdims=True)
    var = jnp.mean(jnp.square(xf - mu), axis=-1, keepdims=True)
    y = (xf - mu) * lax.rsqrt(var + EPS)
    return (y * g.astype(jnp.float32) + b.astype(jnp.float32)).astype(x.dtype)

def conformer_conv(u, dw_w, dw_b, ln_g, ln_b):
    a, gate = jnp.split(u, 2, axis=-1)
    y = a * jax.nn.sigmoid(gate)
    y = lax.conv_general_dilated(
        y, dw_w[:, None, :].astype(y.dtype), window_strides=(1,),
        padding=[(CONV_WIDTH - 1, 0)],
        dimension_numbers=("NWC", "WIO", "NWC"),
        feature_group_count=CONV_CH) + dw_b
    y = layer_norm(y, ln_g, ln_b)
    return jax.nn.silu(y)

def diff_attention(q, k, v, lam, subln_g, lam_init):
    B, S = q.shape[0], q.shape[1]
    nb = S // Q_BLOCK
    scale = DA_HEAD_DIM ** -0.5
    qb = q.reshape(B, nb, Q_BLOCK, DA_HEADS, 2, DA_HEAD_DIM).transpose(1, 0, 2, 3, 4, 5)
    key_pos = jnp.arange(S)

    def block(args):
        qi, bi = args
        s = jnp.einsum("bqhcd,bkhcd->bhcqk", qi, k,
                       preferred_element_type=jnp.float32) * scale
        q_pos = bi * Q_BLOCK + jnp.arange(Q_BLOCK)
        mask = key_pos[None, :] <= q_pos[:, None]
        s = jnp.where(mask, s, -jnp.inf)
        p = jax.nn.softmax(s, axis=-1)
        a = (p[:, :, 0] - lam * p[:, :, 1]).astype(v.dtype)
        return jnp.einsum("bhqk,bkhe->bqhe", a, v)

    o = lax.map(block, (qb, jnp.arange(nb)))
    o = o.transpose(1, 0, 2, 3, 4).reshape(B, S, DA_HEADS, DA_V_DIM)
    o = rms_norm(o, subln_g) * (1.0 - lam_init)
    return o.reshape(B, S, ATTN_W)

def hierarchical_moe(h, w_rg, b_rg, w_re, b_re, w_g, w_u, w_d):
    B, S, D = h.shape
    T = B * S
    hf = h.reshape(T, D)
    g_logits = jnp.matmul(hf, w_rg, preferred_element_type=jnp.float32) + b_rg.astype(jnp.float32)
    g_prob = jax.nn.softmax(g_logits, axis=-1)
    g_sel = jnp.argmax(g_logits, axis=-1)
    g_w = jnp.take_along_axis(g_prob, g_sel[:, None], axis=1)
    e_logits = (jnp.matmul(hf, w_re, preferred_element_type=jnp.float32)
                + b_re.astype(jnp.float32)).reshape(T, N_GROUPS, EXPERTS_PER_GROUP)
    e_logits = jnp.take_along_axis(e_logits, g_sel[:, None, None], axis=1)[:, 0]
    e_prob = jax.nn.softmax(e_logits, axis=-1)
    top_p, top_i = lax.top_k(e_prob, TOP_K_IN_GROUP)
    wts = top_p / jnp.sum(top_p, axis=-1, keepdims=True) * g_w
    eidx = g_sel[:, None] * EXPERTS_PER_GROUP + top_i

    A = T * TOP_K_IN_GROUP
    e_flat = eidx.reshape(A).astype(jnp.int32)
    tok_flat = jnp.repeat(jnp.arange(T, dtype=jnp.int32), TOP_K_IN_GROUP)
    w_flat = wts.reshape(A).astype(h.dtype)
    order = jnp.argsort(e_flat, stable=True)
    e_s, tok_s, w_s = e_flat[order], tok_flat[order], w_flat[order]
    counts = jnp.zeros((N_EXPERTS,), jnp.int32).at[e_flat].add(1)
    padded = (counts + ROW_BLOCK - 1) // ROW_BLOCK * ROW_BLOCK
    start = jnp.cumsum(counts) - counts
    pad_end = jnp.cumsum(padded)
    pstart = pad_end - padded
    dest = pstart[e_s] + jnp.arange(A, dtype=jnp.int32) - start[e_s]
    n_rows = A + N_EXPERTS * ROW_BLOCK
    n_blk = n_rows // ROW_BLOCK
    row_tok = jnp.zeros((n_rows,), jnp.int32).at[dest].set(tok_s)
    row_w = jnp.zeros((n_rows,), h.dtype).at[dest].set(w_s)
    blk_exp = jnp.clip(jnp.searchsorted(pad_end, jnp.arange(n_blk, dtype=jnp.int32) * ROW_BLOCK,
                                        side="right"), 0, N_EXPERTS - 1)

    def expert_block(args):
        toks, wb, e = args
        xb = hf[toks]
        hid = jax.nn.silu(jnp.matmul(xb, w_g[e])) * jnp.matmul(xb, w_u[e])
        return jnp.matmul(hid, w_d[e]) * wb[:, None]

    yb = lax.map(expert_block, (row_tok.reshape(n_blk, ROW_BLOCK),
                                row_w.reshape(n_blk, ROW_BLOCK), blk_exp))
    y = jnp.zeros_like(hf).at[row_tok].add(yb.reshape(n_rows, D))
    return y.reshape(B, S, D)

def first_inputs(seed: int = 0) -> dict:
    key = jax.random.key(seed)
    ks = jax.random.split(key, 26)
    f32 = jnp.float32

    def nrm(k, shape, scale):
        return jax.random.normal(k, shape, f32) * scale

    L, D, C = DEPTH, D_MODEL, CONV_CH
    return {
        "x": nrm(ks[0], (BATCH, SEQ, D), 1.0),
        "attn_norm_g": 1.0 + nrm(ks[1], (L, D), 0.05),
        "w_in": nrm(ks[2], (L, D, IN_COLS), D ** -0.5),
        "conv_dw_w": nrm(ks[3], (L, CONV_WIDTH, C), CONV_WIDTH ** -0.5),
        "conv_dw_b": nrm(ks[4], (L, C), 0.02),
        "conv_ln_g": 1.0 + nrm(ks[5], (L, C), 0.05),
        "conv_ln_b": nrm(ks[6], (L, C), 0.02),
        "w_conv_out": nrm(ks[7], (L, C, D), C ** -0.5),
        "q_norm_g": 1.0 + nrm(ks[8], (L, DA_HEAD_DIM), 0.05),
        "k_norm_g": 1.0 + nrm(ks[9], (L, DA_HEAD_DIM), 0.05),
        "lambda_q1": nrm(ks[10], (L, DA_HEAD_DIM), 0.1),
        "lambda_k1": nrm(ks[11], (L, DA_HEAD_DIM), 0.1),
        "lambda_q2": nrm(ks[12], (L, DA_HEAD_DIM), 0.1),
        "lambda_k2": nrm(ks[13], (L, DA_HEAD_DIM), 0.1),
        "subln_g": 1.0 + nrm(ks[14], (L, DA_V_DIM), 0.05),
        "w_attn_out": nrm(ks[15], (L, ATTN_W, D), ATTN_W ** -0.5),
        "w_out": nrm(ks[16], (L, D, D), D ** -0.5),
        "ffn_norm_g": 1.0 + nrm(ks[17], (L, D), 0.05),
        "w_router_group": nrm(ks[18], (L, D, N_GROUPS), D ** -0.5),
        "b_router_group": nrm(ks[19], (L, N_GROUPS), 0.01),
        "w_router_expert": nrm(ks[20], (L, D, N_EXPERTS), D ** -0.5),
        "b_router_expert": nrm(ks[21], (L, N_EXPERTS), 0.01),
        "w_gate_e": nrm(ks[22], (L, N_EXPERTS, D, D_EXPERT), D ** -0.5),
        "w_up_e": nrm(ks[23], (L, N_EXPERTS, D, D_EXPERT), D ** -0.5),
        "w_down_e": nrm(ks[24], (L, N_EXPERTS, D_EXPERT, D), D_EXPERT ** -0.5),
    }

def first_block(x, attn_norm_g, w_in, conv_dw_w, conv_dw_b, conv_ln_g, conv_ln_b, w_conv_out,
              q_norm_g, k_norm_g, lambda_q1, lambda_k1, lambda_q2, lambda_k2, subln_g,
              w_attn_out, w_out, ffn_norm_g, w_router_group, b_router_group,
              w_router_expert, b_router_expert, w_gate_e, w_up_e, w_down_e):
    B, S, D = x.shape
    for l in range(DEPTH):
        lam_init = 0.8 - 0.6 * math.exp(-0.3 * l)
        h = rms_norm(x, attn_norm_g[l])
        proj = jnp.matmul(h, w_in[l])
        o0 = COL_CONV
        o1 = o0 + COL_Q
        o2 = o1 + COL_K
        o3 = o2 + COL_V
        u_conv = proj[..., :o0]
        q = proj[..., o0:o1].reshape(B, S, DA_HEADS, 2, DA_HEAD_DIM)
        k = proj[..., o1:o2].reshape(B, S, DA_HEADS, 2, DA_HEAD_DIM)
        v = proj[..., o2:o3].reshape(B, S, DA_HEADS, DA_V_DIM)
        gates = jax.nn.sigmoid(proj[..., o3:]).reshape(B, S, N_BRANCH, D)

        conv_out = conformer_conv(u_conv, conv_dw_w[l], conv_dw_b[l], conv_ln_g[l], conv_ln_b[l])

        q = rms_norm(q, q_norm_g[l])
        k = rms_norm(k, k_norm_g[l])
        lam = (jnp.exp(jnp.sum(lambda_q1[l].astype(jnp.float32) * lambda_k1[l].astype(jnp.float32)))
               - jnp.exp(jnp.sum(lambda_q2[l].astype(jnp.float32) * lambda_k2[l].astype(jnp.float32)))
               + lam_init)
        attn_out = diff_attention(q, k, v, lam, subln_g[l], lam_init)

        merged = (gates[:, :, 0] * jnp.matmul(conv_out, w_conv_out[l])
                  + gates[:, :, 1] * jnp.matmul(attn_out, w_attn_out[l]))
        x = x + jnp.matmul(merged, w_out[l])
        h2 = rms_norm(x, ffn_norm_g[l])
        x = x + hierarchical_moe(h2, w_router_group[l], b_router_group[l], w_router_expert[l],
                                 b_router_expert[l], w_gate_e[l], w_up_e[l], w_down_e[l])
    return x


HEAD_DIM = 64
RWKV_HEADS = 4
RWKV_N = 64
RWKV_W = RWKV_HEADS * RWKV_N
RWKV_DECAY_RANK = 64
RWKV_AAA_RANK = 64
RWKV_GATE_RANK = 128
RWKV_LN_EPS = 64e-5
MLSTM_HEADS = 4
MLSTM_DV = 64
MLSTM_DK = 32
MLSTM_W = MLSTM_HEADS * MLSTM_DV
MLSTM_CONV = 4
MLSTM_CHUNK = 64
GATE_SOFTCAP = 15.0
SWA_Q_HEADS = 4
SWA_KV_HEADS = 2
SWA_WINDOW = 128
SWA_W = SWA_Q_HEADS * HEAD_DIM
SWA_KV_W = SWA_KV_HEADS * HEAD_DIM
FOX_HEADS = 4
FOX_W = FOX_HEADS * HEAD_DIM
ATTN_BLOCK = 128
REL_BUCKETS = 32
REL_MAX_DIST = 128
D_FF = 2816
FFN_CONV = 3
NORM_EPS = 1e-6

RWKV_SPLITS = (RWKV_W, RWKV_W, RWKV_W, RWKV_DECAY_RANK, RWKV_AAA_RANK, RWKV_GATE_RANK)
MLSTM_SPLITS = (2 * MLSTM_HEADS * MLSTM_DK, MLSTM_W, MLSTM_W, MLSTM_HEADS, MLSTM_HEADS)
SWA_SPLITS = (SWA_W, SWA_KV_W, SWA_KV_W)
FOX_SPLITS = (FOX_W, FOX_W, FOX_W, FOX_HEADS)
GROUP_SPLITS = (sum(RWKV_SPLITS), sum(MLSTM_SPLITS), sum(SWA_SPLITS), sum(FOX_SPLITS))
N_IN = sum(GROUP_SPLITS)
D_MIX = RWKV_W + MLSTM_W + SWA_W + FOX_W


def _split(z, sizes):
    idx = np.cumsum(sizes)[:-1].tolist()
    return jnp.split(z, idx, axis=-1)

def _rmsnorm(x, g):
    xf = x.astype(jnp.float32)
    return xf * lax.rsqrt(jnp.mean(xf * xf, axis=-1, keepdims=True) + NORM_EPS) * g.astype(jnp.float32)

def _token_shift(u):
    return jnp.pad(u, ((0, 0), (1, 0), (0, 0)))[:, :-1]

def _causal_dwconv(u, w, b):
    k = w.shape[0]
    y = lax.conv_general_dilated(u, w[:, None, :].astype(u.dtype), window_strides=(1,),
                                 padding=[(k - 1, 0)], dimension_numbers=('NWC', 'WIO', 'NWC'),
                                 feature_group_count=u.shape[-1])
    return y + b.astype(u.dtype)

def _t5_bucket(dist):
    max_exact = REL_BUCKETS // 2
    d = np.maximum(dist, 1).astype(np.float32)
    large = max_exact + (np.log(d / max_exact) / math.log(REL_MAX_DIST / max_exact)
                         * (REL_BUCKETS - max_exact)).astype(np.int32)
    large = np.minimum(large, REL_BUCKETS - 1)
    return np.where(dist < max_exact, dist, large).astype(np.int32)

def _rwkv7(z, mu, w0, w_up, a0, a_up, g_up, k_k, k_a, r_k, ln_w, ln_b):
    z = z.astype(jnp.float32)
    z = z + mu * (_token_shift(z) - z)
    r, k, v, wd, ad, gd = _split(z, RWKV_SPLITS)
    bsz, t = r.shape[0], r.shape[1]
    log_decay = -jnp.exp(-jax.nn.softplus(-(w0 + jnp.tanh(wd) @ w_up)) - 0.5)
    decay = jnp.exp(log_decay)
    a = jax.nn.sigmoid(a0 + ad @ a_up)
    g = jax.nn.sigmoid(gd) @ g_up
    heads = lambda u: u.reshape(bsz, t, RWKV_HEADS, RWKV_N)
    kk = heads(k * k_k)
    kk = kk / jnp.maximum(jnp.sqrt(jnp.sum(kk * kk, axis=-1, keepdims=True)), 1e-12)
    k = k * (1.0 + (a - 1.0) * k_a)
    r, k, v, decay, a = heads(r), heads(k), heads(v), heads(decay), heads(a)

    def step(s, inp):
        r_t, w_t, k_t, v_t, kk_t, a_t = inp
        sa = jnp.einsum('bhvk,bhk->bhv', s, -kk_t)
        s = (s * w_t[:, :, None, :] + sa[..., None] * (kk_t * a_t)[:, :, None, :]
             + v_t[..., None] * k_t[:, :, None, :])
        return s, jnp.einsum('bhvk,bhk->bhv', s, r_t)

    xs = tuple(jnp.moveaxis(u, 1, 0) for u in (r, decay, k, v, kk, a))
    s0 = jnp.zeros((bsz, RWKV_HEADS, RWKV_N, RWKV_N), jnp.float32)
    _, y = lax.scan(step, s0, xs)
    y = jnp.moveaxis(y, 0, 1)
    mean = jnp.mean(y, axis=-1, keepdims=True)
    var = jnp.mean(jnp.square(y - mean), axis=-1, keepdims=True)
    y = ((y - mean) * lax.rsqrt(var + RWKV_LN_EPS)).reshape(bsz, t, RWKV_W) * ln_w + ln_b
    bonus = jnp.sum(r * k * r_k, axis=-1, keepdims=True) * v
    return (y + bonus.reshape(bsz, t, RWKV_W)) * g

def _mlstm(z, conv_w, conv_b, b_i, b_f, norm_g):
    z = z.astype(jnp.float32)
    qk, v, o, i_pre, f_pre = _split(z, MLSTM_SPLITS)
    qk = jax.nn.silu(_causal_dwconv(qk, conv_w, conv_b))
    q, k = jnp.split(qk, 2, axis=-1)
    cap = lambda u: GATE_SOFTCAP * jnp.tanh(u / GATE_SOFTCAP)
    li = cap(i_pre + b_i)
    lf = jax.nn.log_sigmoid(cap(f_pre + b_f))
    bsz, t = z.shape[0], z.shape[1]
    nc, L = t // MLSTM_CHUNK, MLSTM_CHUNK

    def chunks(u, d):
        return u.reshape(bsz, nc, L, MLSTM_HEADS, d).transpose(1, 0, 3, 2, 4)

    def gchunks(u):
        return u.reshape(bsz, nc, L, MLSTM_HEADS).transpose(1, 0, 3, 2)

    causal = np.tril(np.ones((L, L), dtype=bool))

    def step(carry, inp):
        c_st, n_st, m_st = carry
        qc, kc, vc, lic, lfc = inp
        b = jnp.cumsum(lfc, axis=-1)
        dmat = jnp.where(causal, b[..., :, None] - b[..., None, :] + lic[..., None, :], -jnp.inf)
        m_inter = b + m_st[..., None]
        m_t = jnp.maximum(m_inter, jnp.max(dmat, axis=-1))
        inter = jnp.exp(m_inter - m_t)
        s = jnp.einsum('bhtk,bhsk->bhts', qc, kc) * jnp.exp(dmat - m_t[..., None])
        num = jnp.einsum('bhts,bhsv->bhtv', s, vc) + inter[..., None] * jnp.einsum('bhvk,bhtk->bhtv', c_st, qc)
        den = jnp.sum(s, axis=-1) + inter * jnp.einsum('bhk,bhtk->bht', n_st, qc)
        h = num / jnp.maximum(jnp.abs(den), jnp.exp(-m_t))[..., None]
        b_last = b[..., -1]
        gexp = b_last[..., None] - b + lic
        m_new = jnp.maximum(b_last + m_st, jnp.max(gexp, axis=-1))
        wts = jnp.exp(gexp - m_new[..., None])
        dec = jnp.exp(b_last + m_st - m_new)
        c_new = dec[..., None, None] * c_st + jnp.einsum('bhs,bhsv,bhsk->bhvk', wts, vc, kc)
        n_new = dec[..., None] * n_st + jnp.einsum('bhs,bhsk->bhk', wts, kc)
        return (c_new, n_new, m_new), h

    xs = (chunks(q * MLSTM_DK ** -0.5, MLSTM_DK), chunks(k, MLSTM_DK), chunks(v, MLSTM_DV), gchunks(li), gchunks(lf))
    init = (jnp.zeros((bsz, MLSTM_HEADS, MLSTM_DV, MLSTM_DK), jnp.float32),
            jnp.zeros((bsz, MLSTM_HEADS, MLSTM_DK), jnp.float32),
            jnp.zeros((bsz, MLSTM_HEADS), jnp.float32))
    _, h = lax.scan(step, init, xs)
    h = h.transpose(1, 0, 3, 2, 4).reshape(bsz, t, MLSTM_HEADS, MLSTM_DV)
    h = h * lax.rsqrt(jnp.mean(h * h, axis=-1, keepdims=True) + NORM_EPS)
    return h.reshape(bsz, t, MLSTM_W) * norm_g * jax.nn.sigmoid(o)

def _swa(z, sinks, rel_bias):
    z = z.astype(jnp.float32)
    q, k, v = _split(z, SWA_SPLITS)
    bsz, t = z.shape[0], z.shape[1]
    nb, blk, grp = t // ATTN_BLOCK, ATTN_BLOCK, SWA_Q_HEADS // SWA_KV_HEADS
    qb = q.reshape(bsz, nb, blk, SWA_KV_HEADS, grp, HEAD_DIM)

    def kv_band(u):
        ub = u.reshape(bsz, nb, blk, SWA_KV_HEADS, HEAD_DIM)
        prev = jnp.pad(ub, ((0, 0), (1, 0), (0, 0), (0, 0), (0, 0)))[:, :-1]
        return jnp.concatenate([prev, ub], axis=2)

    kw, vw = kv_band(k), kv_band(v)
    logits = jnp.einsum('bnqhgd,bnkhd->bnhgqk', qb, kw) * HEAD_DIM ** -0.5
    tq = np.arange(blk)[:, None]
    sk = np.arange(2 * blk)[None, :]
    dist = tq + blk - sk
    in_window = (dist >= 0) & (dist < SWA_WINDOW)
    key_pos = np.arange(nb)[:, None, None] * blk - blk + sk[None]
    mask = in_window[None] & (key_pos >= 0)
    bias = rel_bias[_t5_bucket(np.clip(dist, 0, SWA_WINDOW - 1))].astype(jnp.float32)
    bias = jnp.transpose(bias, (2, 0, 1)).reshape(SWA_KV_HEADS, grp, blk, 2 * blk)
    logits = jnp.where(mask[None, :, None, None], logits + bias, -jnp.inf)
    sink = sinks.astype(jnp.float32).reshape(SWA_KV_HEADS, grp)[None, None, :, :, None, None]
    m = jnp.maximum(jnp.max(logits, axis=-1, keepdims=True), sink)
    p = jnp.exp(logits - m)
    denom = jnp.sum(p, axis=-1, keepdims=True) + jnp.exp(sink - m)
    out = jnp.einsum('bnhgqk,bnkhd->bnqhgd', p / denom, vw)
    return out.reshape(bsz, t, SWA_W)

def _fox(z, b_f):
    z = z.astype(jnp.float32)
    q, k, v, f_pre = _split(z, FOX_SPLITS)
    bsz, t = z.shape[0], z.shape[1]
    nb, blk = t // ATTN_BLOCK, ATTN_BLOCK
    k = k.reshape(bsz, t, FOX_HEADS, HEAD_DIM)
    v = v.reshape(bsz, t, FOX_HEADS, HEAD_DIM)
    c = jnp.cumsum(jax.nn.log_sigmoid(f_pre + b_f), axis=1)
    c_keys = c.transpose(0, 2, 1)
    qb = (q * HEAD_DIM ** -0.5).reshape(bsz, nb, blk, FOX_HEADS, HEAD_DIM).transpose(1, 0, 2, 3, 4)
    cqb = c.reshape(bsz, nb, blk, FOX_HEADS).transpose(1, 0, 3, 2)
    qpos = jnp.arange(t).reshape(nb, blk)
    kpos = jnp.arange(t)

    def block(args):
        qi, cqi, pi = args
        s = jnp.einsum('bqhd,bkhd->bhqk', qi, k) + cqi[..., :, None] - c_keys[:, :, None, :]
        s = jnp.where(kpos[None, :] <= pi[:, None], s, -jnp.inf)
        return jnp.einsum('bhqk,bkhd->bqhd', jax.nn.softmax(s, axis=-1), v)

    out = lax.map(block, (qb, cqb, qpos))
    return out.transpose(1, 0, 2, 3, 4).reshape(bsz, t, FOX_W)

def second_inputs(seed: int = 0) -> dict:
    key = jax.random.key(seed)
    ks = iter(jax.random.split(key, 40))
    L = DEPTH
    nrm = lambda shape, scale: jax.random.normal(next(ks), shape, jnp.float32) * scale
    uni = lambda shape, lo, hi: jax.random.uniform(next(ks), shape, jnp.float32, lo, hi)
    gain = lambda shape: 1.0 + nrm(shape, 0.05)
    return {
        'x': nrm((BATCH, SEQ, D_MODEL), 1.0),
        'w_in': nrm((L, D_MODEL, N_IN), D_MODEL ** -0.5),
        'w_out': nrm((L, D_MIX, D_MODEL), D_MIX ** -0.5),
        'norm_mix_pre': gain((L, D_MODEL)),
        'norm_mix_post': gain((L, D_MODEL)),
        'norm_ffn_pre': gain((L, D_MODEL)),
        'norm_ffn_post': gain((L, D_MODEL)),
        'rwkv_mu': uni((L, GROUP_SPLITS[0]), 0.0, 1.0),
        'rwkv_w0': uni((L, RWKV_W), -6.0, 1.0),
        'rwkv_w_up': nrm((L, RWKV_DECAY_RANK, RWKV_W), 0.5 * RWKV_DECAY_RANK ** -0.5),
        'rwkv_a0': nrm((L, RWKV_W), 0.5),
        'rwkv_a_up': nrm((L, RWKV_AAA_RANK, RWKV_W), 0.5 * RWKV_AAA_RANK ** -0.5),
        'rwkv_g_up': nrm((L, RWKV_GATE_RANK, RWKV_W), RWKV_GATE_RANK ** -0.5),
        'rwkv_k_k': 0.85 + nrm((L, RWKV_W), 0.05),
        'rwkv_k_a': gain((L, RWKV_W)),
        'rwkv_r_k': nrm((L, RWKV_HEADS, RWKV_N), 0.1),
        'rwkv_ln_w': gain((L, RWKV_W)),
        'rwkv_ln_b': nrm((L, RWKV_W), 0.02),
        'mlstm_conv_w': nrm((L, MLSTM_CONV, 2 * MLSTM_HEADS * MLSTM_DK), MLSTM_CONV ** -0.5),
        'mlstm_conv_b': nrm((L, 2 * MLSTM_HEADS * MLSTM_DK), 0.02),
        'mlstm_b_i': nrm((L, MLSTM_HEADS), 0.5),
        'mlstm_b_f': uni((L, MLSTM_HEADS), 3.0, 6.0),
        'mlstm_norm': gain((L, MLSTM_W)),
        'swa_sinks': nrm((L, SWA_Q_HEADS), 0.5),
        'fox_b_f': uni((L, FOX_HEADS), 2.0, 4.0),
        'rel_bias': nrm((REL_BUCKETS, SWA_Q_HEADS), 0.5),
        'ffn_w_up': nrm((L, D_MODEL, 2 * D_FF), D_MODEL ** -0.5),
        'ffn_conv_w': nrm((L, FFN_CONV, D_FF), FFN_CONV ** -0.5),
        'ffn_conv_b': nrm((L, D_FF), 0.02),
        'ffn_w_down': nrm((L, D_FF, D_MODEL), D_FF ** -0.5),
    }

def second_block(x, w_in, w_out, norm_mix_pre, norm_mix_post, norm_ffn_pre, norm_ffn_post,
              rwkv_mu, rwkv_w0, rwkv_w_up, rwkv_a0, rwkv_a_up, rwkv_g_up, rwkv_k_k, rwkv_k_a,
              rwkv_r_k, rwkv_ln_w, rwkv_ln_b, mlstm_conv_w, mlstm_conv_b, mlstm_b_i, mlstm_b_f,
              mlstm_norm, swa_sinks, fox_b_f, rel_bias, ffn_w_up, ffn_conv_w, ffn_conv_b, ffn_w_down):
    dt = x.dtype
    for l in range(DEPTH):
        h = _rmsnorm(x, norm_mix_pre[l]).astype(dt)
        z = h @ w_in[l]
        z_a, z_b, z_c, z_d = _split(z, GROUP_SPLITS)
        y_a = _rwkv7(z_a, rwkv_mu[l], rwkv_w0[l], rwkv_w_up[l], rwkv_a0[l], rwkv_a_up[l], rwkv_g_up[l],
                     rwkv_k_k[l], rwkv_k_a[l], rwkv_r_k[l], rwkv_ln_w[l], rwkv_ln_b[l])
        y_b = _mlstm(z_b, mlstm_conv_w[l], mlstm_conv_b[l], mlstm_b_i[l], mlstm_b_f[l], mlstm_norm[l])
        y_c = _swa(z_c, swa_sinks[l], rel_bias)
        y_d = _fox(z_d, fox_b_f[l])
        y = jnp.concatenate([y_a, y_b, y_c, y_d], axis=-1).astype(dt)
        x = x + _rmsnorm(y @ w_out[l], norm_mix_post[l]).astype(dt)
        h = _rmsnorm(x, norm_ffn_pre[l]).astype(dt)
        gate, up = jnp.split(h @ ffn_w_up[l], 2, axis=-1)
        gate = _causal_dwconv(gate, ffn_conv_w[l], ffn_conv_b[l])
        f = jax.nn.gelu(gate, approximate=True) * up
        x = x + _rmsnorm(f @ ffn_w_down[l], norm_ffn_post[l]).astype(dt)
    return x


def setup_inputs(seed=0):
    out = dict(first_inputs(seed))
    for name, value in second_inputs(seed + 1).items():
        if name != "x":
            out[name + "_2"] = value
    return out


def reference(
    x, attn_norm_g, w_in, conv_dw_w, conv_dw_b, conv_ln_g, conv_ln_b, w_conv_out, q_norm_g,
    k_norm_g, lambda_q1, lambda_k1, lambda_q2, lambda_k2, subln_g, w_attn_out, w_out,
    ffn_norm_g, w_router_group, b_router_group, w_router_expert, b_router_expert, w_gate_e,
    w_up_e, w_down_e, w_in_2, w_out_2, norm_mix_pre_2, norm_mix_post_2, norm_ffn_pre_2,
    norm_ffn_post_2, rwkv_mu_2, rwkv_w0_2, rwkv_w_up_2, rwkv_a0_2, rwkv_a_up_2, rwkv_g_up_2,
    rwkv_k_k_2, rwkv_k_a_2, rwkv_r_k_2, rwkv_ln_w_2, rwkv_ln_b_2, mlstm_conv_w_2,
    mlstm_conv_b_2, mlstm_b_i_2, mlstm_b_f_2, mlstm_norm_2, swa_sinks_2, fox_b_f_2, rel_bias_2,
    ffn_w_up_2, ffn_conv_w_2, ffn_conv_b_2, ffn_w_down_2,
):
    x = first_block(
        x, attn_norm_g, w_in, conv_dw_w, conv_dw_b, conv_ln_g, conv_ln_b, w_conv_out, q_norm_g,
        k_norm_g, lambda_q1, lambda_k1, lambda_q2, lambda_k2, subln_g, w_attn_out, w_out,
        ffn_norm_g, w_router_group, b_router_group, w_router_expert, b_router_expert, w_gate_e,
        w_up_e, w_down_e,
    )
    return second_block(
        x, w_in_2, w_out_2, norm_mix_pre_2, norm_mix_post_2, norm_ffn_pre_2, norm_ffn_post_2,
        rwkv_mu_2, rwkv_w0_2, rwkv_w_up_2, rwkv_a0_2, rwkv_a_up_2, rwkv_g_up_2, rwkv_k_k_2,
        rwkv_k_a_2, rwkv_r_k_2, rwkv_ln_w_2, rwkv_ln_b_2, mlstm_conv_w_2, mlstm_conv_b_2,
        mlstm_b_i_2, mlstm_b_f_2, mlstm_norm_2, swa_sinks_2, fox_b_f_2, rel_bias_2, ffn_w_up_2,
        ffn_conv_w_2, ffn_conv_b_2, ffn_w_down_2,
    )


_drawn_inputs = setup_inputs


def setup_inputs(seed=0):
    import zlib

    import numpy as np

    out = dict(_drawn_inputs(seed))
    spreads = {}
    factors = {'lambda_q1': 3.038,
     'b_router_group': 3.118,
     'b_router_expert': 3.335,
     'rwkv_w_up_2': 4.029,
     'rwkv_ln_b_2': 6.377,
     'mlstm_conv_b_2': 4.361,
     'mlstm_b_i_2': 8.0,
     'swa_sinks_2': 42.885,
     'ffn_conv_b_2': 5.223}
    for name, (base, spread) in spreads.items():
        noise = np.random.default_rng([zlib.crc32(name.encode()), seed]).standard_normal(out[name].shape)
        drawn = base * np.exp(spread * noise) if base else spread * noise
        out[name] = jnp.asarray(drawn.astype(out[name].dtype))
    for name, factor in factors.items():
        out[name] = (out[name] * factor).astype(out[name].dtype)
    return out
```

```python
import math
from contextlib import ExitStack

import numpy as np

import concourse.bass as bass
from concourse import mybir

F32 = mybir.dt.float32
I32 = mybir.dt.int32
U32 = mybir.dt.uint32
ACT = mybir.ActivationFunctionType
ALU = mybir.AluOpType
AX = mybir.AxisListType.X

P = 128
S = 1024
D = 1024
NT = S // P
KT = D // P
HALF = 512
EPS = 1e-6
NEG = -1e30

CONV_CH, TAPS = 512, 31
CT = CONV_CH // P
HEADS, HD, VD = 4, 64, 128
LAM_INIT = 0.8 - 0.6 * math.exp(0.0)
GROUPS, EPG = 4, 8
EXPERTS = GROUPS * EPG
DE = 512
FT = DE // P
ROWS = 2 * S + EXPERTS * P
BLOCKS = ROWS // P
COL_QKV, COL_GATE = 1024, 2560

RW = 256
CHUNK = 32
ML0, SW0, FX0, N_IN = 1024, 1800, 2312, 3084
WINDOW = 128
DFF = 2816
FFT = DFF // P


def shape_constants():
    p, j = np.arange(P)[:, None], np.arange(P)[None, :]
    same = (p // CHUNK) == (j // CHUNK)
    parts = {
        "ident": p == j,
        "flip": p == P - 1 - j,
        "ones": np.ones((P, P)),
        "pair": (p // 64) == (j // 64),
        "before": p < j,
        "causal": np.where(j <= p, 0.0, NEG),
        "chunk_below": same & (j < p),
        "chunk_above": same & (p < j),
        "chunk_upto": same & (p <= j),
        "block_start": np.broadcast_to(np.arange(BLOCKS) * P, (P, BLOCKS)),
        "rank4": np.broadcast_to(np.arange(GROUPS, 0, -1), (P, GROUPS)),
        "rank8": np.broadcast_to(np.arange(EPG, 0, -1), (P, EPG)),
        "token": np.arange(NT)[None, :] * P + p,
    }
    dist = 255 - np.arange(3 * P)
    d = np.maximum(np.clip(dist, 0, WINDOW - 1), 1).astype(np.float32)
    large = 16 + (np.log(d / 16) / math.log(128 / 16) * 16).astype(np.int32)
    bucket = np.where(np.clip(dist, 0, WINDOW - 1) < 16, np.clip(dist, 0, WINDOW - 1), np.minimum(large, 31))
    inside = (dist >= 0) & (dist < WINDOW)
    onehot = np.zeros((P, 3 * P))
    onehot[:32] = (np.arange(32)[:, None] == bucket[None, :]) & inside[None, :]
    parts["bucket"] = onehot
    parts["outside"] = np.broadcast_to(np.where(inside, 0.0, NEG), (P, 3 * P))
    at, off = {}, 0
    for name, a in parts.items():
        at[name] = (off, off + a.shape[1])
        off += a.shape[1]
    table = np.concatenate([np.broadcast_to(a, (P, a.shape[1])).astype(np.float32) for a in parts.values()], 1)
    return np.ascontiguousarray(table), at


CONST_COLS = shape_constants()[1]

VECTORS = [
    ("conv_dw_w", TAPS * CT),
    ("attn_norm_g", KT), ("ffn_norm_g", KT), ("norm_mix_pre_2", KT), ("norm_ffn_pre_2", KT),
    ("conv_dw_b", CT), ("conv_ln_g", CT), ("conv_ln_b", CT), ("subln_g", 1), ("q_norm_g", 1), ("k_norm_g", 1),
    ("rwkv_mu_2", 8), ("rwkv_w0_2", 2), ("rwkv_a0_2", 2), ("rwkv_k_k_2", 2), ("rwkv_k_a_2", 2), ("rwkv_r_k_2", 2),
    ("rwkv_ln_w_2", 2), ("rwkv_ln_b_2", 2), ("mlstm_conv_w_2", 8), ("mlstm_conv_b_2", 2), ("mlstm_norm_2", 2),
    ("ffn_conv_w_2", 3 * FFT), ("ffn_conv_b_2", FFT),
]


def vector_places():
    places, tile, row = {}, 0, 0
    for name, n in VECTORS:
        if row + n > P:
            tile, row = tile + 1, 0
        places[name] = (tile, row, n)
        row += n
    return places, tile + 1


class Kernel:

    def __init__(self, nc, A, out, ctx):
        self.nc, self.A, self.out, self.ctx = nc, A, out, ctx
        self.ps = ctx.enter_context(nc.psum_tensor("banks", [P, 8, HALF], F32))
        self.sems = []

    def sem(self, name):
        self.sems.append(self.nc.alloc_semaphore(name))
        return self.sems[-1]

    def recycle(self):
        self.nc.clear_and_free_semaphores(self.sems)
        self.nc.all_engine_barrier()
        self.sems = []

    def sb(self, scope, name, shape, dt=F32):
        return scope.enter_context(self.nc.sbuf_tensor(name, shape, dt))

    def dram(self, name, shape, dt=F32):
        return self.nc.dram_tensor(name, shape, dt).ap()

    def const(self, name):
        a, b = CONST_COLS[name]
        return self.consts[:, a:b]

    def vec(self, name, j=0, n=1):
        tile, row, _ = self.vplaces[name]
        return self.vectors[:, tile * P + row + j:tile * P + row + j + n]


def rows_of(ap):
    return ap.rearrange("o (r p) -> (o r) p", p=P)


def load_vectors(K):
    nc, A = K.nc, K.A
    K.consts = K.sb(K.ctx, "consts", [P, A["shape_consts"].shape[1]])
    K.vplaces, tiles = vector_places()
    K.vectors = K.sb(K.ctx, "vectors", [P, tiles * P])
    K.lam = K.sb(K.ctx, "minus_lambda", [P, 1])
    K.qk_gain = K.sb(K.ctx, "qk_gain", [P, 2 * HEADS])
    K.head_gain = K.sb(K.ctx, "head_gain", [P, HEADS])
    zeroed, landed, const_landed = K.sem("rows_zeroed"), K.sem("rows_landed"), K.sem("const_landed")
    turned, lam_landed, lam_dot, lam_exp = K.sem("rows_turned"), K.sem("lam_landed"), K.sem("lam_dot"), K.sem("lam_exp")
    loads = 0
    with ExitStack() as scope, nc.Block() as block:
        rows = K.sb(scope, "vector_rows", [P, tiles, P])
        lam4 = K.sb(scope, "lam_vectors", [P, 4, HD])
        prod = K.sb(scope, "lam_products", [P, 2, HD])
        dots = K.sb(scope, "lam_dots", [P, 2])
        exps = K.sb(scope, "lam_exps", [P, 2])
        sources = []
        for name, n in VECTORS:
            tile, row, _ = K.vplaces[name]
            src = A[name]
            if name in ("q_norm_g", "k_norm_g"):
                sources += [(rows[row:row + 1, tile, 0:HD], src), (rows[row:row + 1, tile, HD:P], src)]
            elif len(src.shape) == 3 and name != "rwkv_r_k_2":
                sources.append((rows[row:row + n, tile, :], src.rearrange("o w (r p) -> (o w r) p", p=P)))
            elif name == "rwkv_r_k_2":
                sources.append((rows[row:row + n, tile, :], src.rearrange("o (r g) n -> (o r) (g n)", g=2)))
            else:
                sources.append((rows[row:row + n, tile, :], rows_of(src)))

        @block.sync
        def _(sp):
            sp.dma_start(K.consts[:], A["shape_consts"]).then_inc(const_landed, 16)
            for j, name in enumerate(("lambda_q1", "lambda_q2", "lambda_k1", "lambda_k2")):
                sp.dma_start(lam4[:, j, :], A[name].to_broadcast([P, HD])).then_inc(lam_landed, 16)
            sp.wait_ge(zeroed, 1)
            for dst, src in sources:
                sp.dma_start(dst, src).then_inc(landed, 16)

        @block.tensor
        def _(pe):
            pe.wait_ge(const_landed, 16)
            pe.wait_ge(landed, 16 * len(sources))
            for t in range(tiles):
                mm = nc.tensor.transpose(K.ps[:, 0, t * P:(t + 1) * P], rows[:, t, :], K.const("ident"))
            mm.then_inc(turned, 1)

        @block.vector
        def _(dve):
            nc.vector.memset(rows[:], 0.0).then_inc(zeroed, 1)
            dve.wait_ge(lam_landed, 64)
            nc.vector.tensor_tensor(prod[:], lam4[:, 0:2, :], lam4[:, 2:4, :], ALU.mult)
            dve.drain()
            nc.vector.tensor_reduce(dots[:], prod[:], AX, ALU.add).then_inc(lam_dot, 1)
            dve.wait_ge(lam_exp, 1)
            nc.vector.tensor_scalar(K.lam[:], exps[:, 1:2], exps[:, 0:1], -LAM_INIT, ALU.subtract, ALU.add)
            dve.wait_ge(turned, 1)
            nc.vector.tensor_copy(K.vectors[:], K.ps[:, 0, 0:tiles * P])
            dve.drain()
            for h in range(HEADS):
                nc.vector.tensor_copy(K.qk_gain[:, h:h + 1], K.vec("q_norm_g"))
                nc.vector.tensor_copy(K.qk_gain[:, HEADS + h:HEADS + h + 1], K.vec("k_norm_g"))
                nc.vector.tensor_scalar(K.head_gain[:, h:h + 1], K.vec("subln_g"), 1.0 - LAM_INIT, None, ALU.mult)

        @block.scalar
        def _(act):
            act.wait_ge(lam_dot, 1)
            nc.scalar.activation(exps[:], dots[:], ACT.Exp).then_inc(lam_exp, 1)


def norm_and_turn(K, tag, x, gain, hT, src=None, keep=None):
    nc = K.nc
    landed = [K.sem(f"{tag}_x_landed{h}") for h in range(2)]
    squared, meaned, rooted = K.sem(f"{tag}_squared"), K.sem(f"{tag}_meaned"), K.sem(f"{tag}_rooted")
    scaled, turned, kept = K.sem(f"{tag}_scaled"), K.sem(f"{tag}_turned"), K.sem(f"{tag}_kept")
    with ExitStack() as scope, nc.Block() as block:
        junk = K.sb(scope, f"{tag}_junk", [P, D])
        ss = K.sb(scope, f"{tag}_ss", [P, NT])
        rstd = K.sb(scope, f"{tag}_rstd", [P, NT])
        xn = K.sb(scope, f"{tag}_xn", [P, 2, D])

        if src is not None:
            @block.sync
            def _(sp):
                for h in range(2):
                    sp.dma_start(x[:, 4 * h:4 * h + 4, :],
                                 src.rearrange("(t p) d -> p t d", p=P)[:, 4 * h:4 * h + 4, :]).then_inc(landed[h], 16)

        if keep is not None:
            x_kept = K.sem(f"{tag}_x_kept")

            @block.sync
            def _(sp):
                sp.dma_start(keep.rearrange("(t p) d -> p t d", p=P), x[:]).then_inc(x_kept, 16)
                sp.wait_ge(x_kept, 16)

        @block.scalar
        def _(act):
            if src is not None:
                for h in range(2):
                    act.wait_ge(landed[h], 16)
            with act.Fori(0, NT) as t:
                nc.scalar.activation(junk[:], x[:, t, :], ACT.Square, accum_out=ss[:, bass.ds(t, 1)])
                act.drain()
            act.sem_inc(squared, 1)
            act.wait_ge(meaned, 1)
            nc.scalar.activation(rstd[:], ss[:], ACT.Sqrt).then_inc(rooted, 1)

        @block.vector
        def _(dve):
            dve.sem_inc(kept, 2)
            dve.wait_ge(squared, 1)
            nc.vector.tensor_scalar(ss[:], ss[:], 1.0 / D, EPS, ALU.mult, ALU.add).then_inc(meaned, 1)
            dve.wait_ge(rooted, 1)
            nc.vector.reciprocal(rstd[:], rstd[:])
            dve.drain()
            with dve.Fori(0, NT // 2) as i:
                for b in range(2):
                    dve.wait_ge(turned, i * 2 + (b + 1))
                    nc.vector.tensor_scalar(xn[:, b, :], x[:, i * 2 + b, :], rstd[:, bass.ds(i * 2 + b, 1)], None,
                                            ALU.mult).then_inc(scaled, 1)
                for b in range(2):
                    dve.wait_ge(turned, i * 2 + (b + 3))
                    nc.vector.tensor_tensor(
                        hT[:, :, bass.ds((i * 2 + b) * P, P)],
                        K.ps[:, 2 * b:2 * b + 2, :].rearrange("p c (k n) -> p (c k) n", n=P),
                        gain.unsqueeze(2).to_broadcast([P, KT, P]), ALU.mult).then_inc(kept, 1)

        @block.tensor
        def _(pe):
            pe.sem_inc(turned, 2)
            with pe.Fori(0, NT // 2) as i:
                for b in range(2):
                    pe.wait_ge(scaled, i * 2 + (b + 1))
                    pe.wait_ge(kept, i * 2 + (b + 1))
                    for k in range(KT):
                        mm = nc.tensor.transpose(K.ps[:, 2 * b + k // 4, (k % 4) * P:(k % 4 + 1) * P],
                                                 xn[:, b, k * P:(k + 1) * P], K.const("ident"))
                    mm.then_inc(turned, 1)


def project_and_convolve(K, hT, conv, qkv):
    nc, A = K.nc, K.A
    w = A["w_in"].rearrange("o (k p) n -> p (o k) n", p=P)
    landed = [K.sem(f"p_slab_landed{b}") for b in range(2)]
    done, emptied = K.sem("p_bank_done"), K.sem("p_bank_emptied")
    gated, kept = K.sem("p_gated"), K.sem("p_qkv_kept")
    PAD = TAPS - 1
    with ExitStack() as scope, nc.Block() as block:
        slab = K.sb(scope, "p_slab", [P, 2, KT, HALF])
        gate = K.sb(scope, "p_gate", [P, 2, HALF])
        y = K.sb(scope, "p_y", [P, CT, PAD + S])

        @block.sync
        def _(sp):
            for b in range(2):
                sp.dma_start(slab[:, b], w[:, :, b * HALF:(b + 1) * HALF]).then_inc(landed[b], 16)
            for s in range(3):
                sp.wait_ge(done, 16 if s < 2 else 16 + NT)
                sp.dma_start(slab[:, s % 2], w[:, :, COL_QKV + s * HALF:COL_QKV + (s + 1) * HALF]) \
                    .then_inc(landed[s % 2], 16)

        @block.tensor
        def _(pe):
            for b in range(2):
                pe.wait_ge(landed[b], 16)
            n = 0
            for c in range(CT):
                for h in range(2):
                    for b in range(2):
                        if n >= 8:
                            pe.wait_ge(emptied, n - 6 - b)
                        for k in range(KT):
                            mm = nc.tensor.matmul(K.ps[:, n % 8, :], slab[:, b, k, c * P:(c + 1) * P],
                                                  hT[:, k, h * HALF:(h + 1) * HALF], start=(k == 0), stop=(k == KT - 1))
                        mm.then_inc(done, 1)
                        n += 1
            for s in range(3):
                pe.wait_ge(landed[s % 2], 16 * (s // 2 + 2))
                for t in range(NT):
                    if s == 0:
                        pe.wait_ge(emptied, n - 6 - n % 2)
                    else:
                        pe.wait_ge(kept, n - 23)
                    for k in range(KT):
                        mm = nc.tensor.matmul(K.ps[:, n % 8, :], hT[:, k, t * P:(t + 1) * P], slab[:, s % 2, k, :],
                                              start=(k == 0), stop=(k == KT - 1))
                    mm.then_inc(done, 1)
                    n += 1

        @block.scalar
        def _(act):
            for c in range(CT):
                for h in range(2):
                    n = 2 * (2 * c + h)
                    if n >= 4:
                        act.wait_ge(emptied, n - 2)
                    act.wait_ge(done, n + 2)
                    nc.scalar.activation(gate[:, h, :], K.ps[:, (n + 1) % 8, :], ACT.Sigmoid).then_inc(gated, 1)
            for s in range(3):
                with act.Fori(0, NT) as t:
                    act.wait_ge(done, t + (17 + NT * s))
                    nc.scalar.activation(qkv[:, t, s * HALF:(s + 1) * HALF],
                                         K.ps[:, bass.ds(t, 1), :].rearrange("p o n -> p (o n)"), ACT.Copy) \
                        .then_inc(kept, 1)

        @block.vector
        def _(dve):
            nc.vector.memset(y[:, :, 0:PAD], 0.0)
            for c in range(CT):
                for h in range(2):
                    n = 2 * (2 * c + h)
                    dve.wait_ge(gated, n // 2 + 1)
                    nc.vector.tensor_tensor(y[:, c, PAD + h * HALF:PAD + (h + 1) * HALF], K.ps[:, n % 8, :],
                                            gate[:, h, :], ALU.mult).then_inc(emptied, 2)
            dve.drain()
            taps = K.vec("conv_dw_w", 0, TAPS * CT).rearrange("p (w c) -> p c w", c=CT)
            bias = K.vec("conv_dw_b", 0, CT)
            with dve.Fori(0, CT) as c:
                out = conv[:, bass.ds(c, 1), :].rearrange("p o n -> p (o n)")
                col = lambda j: taps[:, bass.ds(c, 1), j:j + 1].rearrange("p o n -> p (o n)")
                row = lambda j: y[:, bass.ds(c, 1), j:j + S].rearrange("p o n -> p (o n)")
                nc.vector.tensor_scalar(out, row(0), col(0), bias[:, bass.ds(c, 1)], ALU.mult, ALU.add)
                for j in range(1, TAPS):
                    dve.drain()
                    nc.vector.scalar_tensor_tensor(out, row(j), col(j), out, ALU.mult, ALU.add)
                dve.drain()


def conv_norm(K, conv):
    nc = K.nc
    summed, centred, squared, varied, rooted, ready = (K.sem(f"cn_{n}") for n in
        ("summed", "centred", "squared", "varied", "rooted", "ready"))
    whitened = K.sem("cn_whitened")
    with ExitStack() as scope, nc.Block() as block:
        sq = K.sb(scope, "cn_sq", [P, CT, S])
        rstd = K.sb(scope, "cn_rstd", [P, S])

        def halves(bank):
            return K.ps[:, bank:bank + 2, :].rearrange("p b n -> p (b n)")

        @block.tensor
        def _(pe):
            for h in range(2):
                for c in range(CT):
                    mm = nc.tensor.matmul(K.ps[:, h, :], K.const("ones"), conv[:, c, h * HALF:(h + 1) * HALF],
                                          start=(c == 0), stop=(c == CT - 1))
            mm.then_inc(summed, 1)
            for h in range(2):
                for c in range(CT):
                    pe.wait_ge(squared, c + 1)
                    mm = nc.tensor.matmul(K.ps[:, 2 + h, :], K.const("ones"), sq[:, c, h * HALF:(h + 1) * HALF],
                                          start=(c == 0), stop=(c == CT - 1))
            mm.then_inc(varied, 1)

        @block.vector
        def _(dve):
            dve.wait_ge(summed, 1)
            for c in range(CT):
                nc.vector.scalar_tensor_tensor(conv[:, c, :], halves(0), -1.0 / CONV_CH, conv[:, c, :],
                                               ALU.mult, ALU.add).then_inc(centred, 1)
            dve.wait_ge(varied, 1)
            nc.vector.tensor_scalar(rstd[:], halves(2), 1.0 / CONV_CH, EPS, ALU.mult, ALU.add).then_inc(ready, 1)
            dve.wait_ge(rooted, 1)
            nc.vector.reciprocal(rstd[:], rstd[:])
            dve.drain()
            for c in range(CT):
                nc.vector.tensor_tensor(conv[:, c, :], conv[:, c, :], rstd[:], ALU.mult).then_inc(whitened, 1)

        @block.scalar
        def _(act):
            for c in range(CT):
                act.wait_ge(centred, c + 1)
                nc.scalar.activation(sq[:, c, :], conv[:, c, :], ACT.Square).then_inc(squared, 1)
            act.wait_ge(ready, 1)
            nc.scalar.activation(rstd[:], rstd[:], ACT.Sqrt).then_inc(rooted, 1)
            for c in range(CT):
                act.wait_ge(whitened, c + 1)
                nc.scalar.activation(conv[:, c, :], conv[:, c, :], ACT.Silu,
                                     scale=K.vec("conv_ln_g", c), bias=K.vec("conv_ln_b", c))


def group_norm_and_turn(K, tag, src, groups, gain, dst, gate=None):
    nc = K.nc
    width = src.shape[2]
    size, tiles = width // groups, width // P
    squared, summed, meaned, rooted, scaled, turned, kept = (K.sem(f"{tag}_{n}") for n in
        ("squared", "summed", "meaned", "rooted", "scaled", "turned", "kept"))
    with ExitStack() as scope, nc.Block() as block:
        sq = K.sb(scope, f"{tag}_sq", [P, 2, width])
        ss = K.sb(scope, f"{tag}_ss", [P, NT, groups])
        rstd = K.sb(scope, f"{tag}_rstd", [P, NT, groups])
        xn = K.sb(scope, f"{tag}_xn", [P, 2, width])

        @block.scalar
        def _(act):
            with act.Fori(0, NT // 2) as i:
                for b in range(2):
                    act.wait_ge(summed, i * 2 + (b + 1))
                    nc.scalar.activation(sq[:, b, :], src[:, i * 2 + b, :], ACT.Square).then_inc(squared, 1)
            act.wait_ge(meaned, 1)
            nc.scalar.activation(rstd[:], ss[:], ACT.Sqrt).then_inc(rooted, 1)

        @block.vector
        def _(dve):
            dve.sem_inc(kept, 2)
            dve.sem_inc(summed, 2)
            with dve.Fori(0, NT // 2) as i:
                for b in range(2):
                    dve.wait_ge(squared, i * 2 + (b + 1))
                    nc.vector.tensor_reduce(ss[:, i * 2 + b, :], sq[:, b, :].rearrange("p (g n) -> p g n", g=groups),
                                            AX, ALU.add).then_inc(summed, 1)
            dve.drain()
            nc.vector.tensor_scalar(ss[:], ss[:], 1.0 / size, EPS, ALU.mult, ALU.add).then_inc(meaned, 1)
            dve.wait_ge(rooted, 1)
            nc.vector.reciprocal(rstd[:], rstd[:])
            dve.drain()
            with dve.Fori(0, NT // 2) as i:
                for b in range(2):
                    dve.wait_ge(turned, i * 2 + (b + 1))
                    nc.vector.tensor_tensor(
                        xn[:, b, :].rearrange("p (g n) -> p g n", g=groups),
                        src[:, bass.ds(i * 2 + b, 1), :].rearrange("p o (g n) -> p (o g) n", g=groups),
                        rstd[:, bass.ds(i * 2 + b, 1), :].rearrange("p o g -> p (o g)").unsqueeze(2)
                        .to_broadcast([P, groups, size]), ALU.mult).then_inc(scaled, 1)
                for b in range(2):
                    dve.wait_ge(turned, i * 2 + (b + 3))
                    nc.vector.tensor_tensor(
                        dst[:, :, bass.ds((i * 2 + b) * P, P)],
                        K.ps[:, 2 * b:2 * b + 2, :].rearrange("p c (k n) -> p (c k) n", n=P)[:, 0:tiles, :],
                        gain.unsqueeze(2).to_broadcast([P, tiles, P]), ALU.mult).then_inc(kept, 1)
            if gate is not None:
                dve.drain()
                nc.vector.tensor_tensor(dst, dst, gate, ALU.mult)

        @block.tensor
        def _(pe):
            pe.sem_inc(turned, 2)
            with pe.Fori(0, NT // 2) as i:
                for b in range(2):
                    pe.wait_ge(scaled, i * 2 + (b + 1))
                    pe.wait_ge(kept, i * 2 + (b + 1))
                    for k in range(tiles):
                        mm = nc.tensor.transpose(K.ps[:, 2 * b + k // 4, (k % 4) * P:(k % 4 + 1) * P],
                                                 xn[:, b, k * P:(k + 1) * P], K.const("ident"))
                    mm.then_inc(turned, 1)


def diff_attention(K, qkT, qkv, o):
    nc = K.nc
    SCALE = HD ** -0.5
    UNITS = 2 * NT
    copied, scored, peaked, exped, mixed, turned, turned_kept, weighed, stored = (K.sem(f"da_{n}") for n in
        ("copied", "scored", "peaked", "exped", "mixed", "turned", "turned_kept", "weighed", "stored"))
    with ExitStack() as scope, nc.Block() as block:
        qh = K.sb(scope, "da_q", [P, S])
        kh = K.sb(scope, "da_k", [P, S])
        p = K.sb(scope, "da_p", [P, 2, 2, S])
        a = K.sb(scope, "da_a", [P, 2, S])
        aT = K.sb(scope, "da_aT", [P, 2, S])
        peak = K.sb(scope, "da_peak", [P, 2, 2])
        low = K.sb(scope, "da_low", [P, 2, 2])
        mass = K.sb(scope, "da_mass", [P, 2, 2])
        part = K.sb(scope, "da_part", [P, 2, 2])

        def score_bank(i, c, n):
            return K.ps[:, 2 * c:2 * c + 2, :].rearrange("p b n -> p (b n)")[:, 0:n]

        turn_bank = K.ps[:, 4:6, :].rearrange("p b n -> p (b n)")

        @block.gpsimd
        def _(pool):
            with pool.Fori(0, HEADS) as h:
                pool.wait_ge(weighed, h * NT + 1)
                nc.gpsimd.tensor_copy(qh[:], qkT[:, h, :]).then_inc(copied, 1)
                nc.gpsimd.tensor_copy(kh[:], qkT[:, h + HEADS, :]).then_inc(copied, 1)

        @block.tensor
        def _(pe):
            pe.sem_inc(weighed, 1)
            with pe.Fori(0, HEADS) as h:
                pe.wait_ge(copied, h * 2 + 2)

                def scores(i):
                    n = (i + 1) * P
                    for c in range(2):
                        pe.wait_ge(exped, h * UNITS + (2 * (i - 1) + c + 3))
                        rows = slice(c * HD, (c + 1) * HD)
                        for b in range(0, n, HALF):
                            m = min(HALF, n - b)
                            last = b + m == n
                            mm = nc.tensor.matmul(score_bank(i, c, n)[:, b:b + m], qh[rows, i * P:(i + 1) * P],
                                                  kh[rows, b:b + m], start=True, stop=not last)
                        mm = nc.tensor.matmul(score_bank(i, c, n)[:, n - P:n], K.const("ident"), K.const("causal"),
                                              start=False, stop=True)
                        mm.then_inc(scored, 1)

                def values(i):
                    pe.wait_ge(mixed, h * NT + (i + 1))
                    pe.wait_ge(turned_kept, h * NT + (i + 1))
                    for j in range(i + 1):
                        mm = nc.tensor.transpose(turn_bank[:, j * P:(j + 1) * P], a[:, i % 2, j * P:(j + 1) * P],
                                                 K.const("ident"))
                    mm.then_inc(turned, 1)
                    pe.wait_ge(turned_kept, h * NT + (i + 2))
                    pe.wait_ge(stored, h * NT + (i + 1))
                    for j in range(i + 1):
                        mm = nc.tensor.matmul(K.ps[:, 6 + i % 2, 0:VD], aT[:, i % 2, j * P:(j + 1) * P],
                                              qkv[:, j, bass.ds(h * VD + 2 * HALF, VD)],
                                              start=(j == 0), stop=(j == i))
                    mm.then_inc(weighed, 1)

                scores(0)
                for i in range(NT):
                    if i + 1 < NT:
                        scores(i + 1)
                    values(i)

        @block.vector
        def _(dve):
            with dve.Fori(0, HEADS) as h:
                def peaks(i):
                    n = (i + 1) * P
                    for c in range(2):
                        dve.wait_ge(scored, h * UNITS + (2 * i + c + 1))
                        nc.vector.tensor_reduce(peak[:, i % 2, c:c + 1], score_bank(i, c, n), AX, ALU.max)
                        dve.drain()
                        nc.vector.tensor_scalar(low[:, i % 2, c:c + 1], peak[:, i % 2, c:c + 1], -SCALE, None,
                                                ALU.mult).then_inc(peaked, 1)

                def mix(i):
                    n = (i + 1) * P
                    dve.wait_ge(exped, h * UNITS + (2 * i + 4))
                    nc.vector.reciprocal(part[:, i % 2, :], mass[:, i % 2, :])
                    dve.drain()
                    nc.vector.tensor_scalar(part[:, i % 2, 1:2], part[:, i % 2, 1:2], K.lam[:], None, ALU.mult)
                    nc.vector.tensor_scalar(p[:, i % 2, 0, 0:n], p[:, i % 2, 0, 0:n], part[:, i % 2, 0:1], None, ALU.mult)
                    dve.drain()
                    nc.vector.scalar_tensor_tensor(a[:, i % 2, 0:n], p[:, i % 2, 1, 0:n], part[:, i % 2, 1:2],
                                                   p[:, i % 2, 0, 0:n], ALU.mult, ALU.add).then_inc(mixed, 1)

                peaks(0)
                for i in range(NT):
                    if i + 1 < NT:
                        peaks(i + 1)
                    mix(i)

        @block.scalar
        def _(act):
            act.sem_inc(exped, 2)
            act.sem_inc(turned_kept, 1)
            act.sem_inc(stored, 2)
            with act.Fori(0, HEADS) as h:
                def exps(i):
                    n = (i + 1) * P
                    for c in range(2):
                        act.wait_ge(peaked, h * UNITS + (2 * i + c + 1))
                        nc.scalar.activation(p[:, i % 2, c, 0:n], score_bank(i, c, n), ACT.Exp, scale=SCALE,
                                             bias=low[:, i % 2, c:c + 1], accum_out=mass[:, i % 2, c:c + 1]) \
                            .then_inc(exped, 1)

                def keep(i):
                    n = (i + 1) * P
                    act.wait_ge(turned, h * NT + (i + 1))
                    nc.scalar.activation(aT[:, i % 2, 0:n], turn_bank[:, 0:n], ACT.Copy).then_inc(turned_kept, 1)
                    act.wait_ge(weighed, h * NT + (i + 2))
                    nc.scalar.activation(o[:, i, bass.ds(h * VD, VD)], K.ps[:, 6 + i % 2, 0:VD], ACT.Copy) \
                        .then_inc(stored, 1)

                exps(0)
                for i in range(NT):
                    if i + 1 < NT:
                        exps(i + 1)
                    keep(i)


def merge_branches(K, hT, conv, oT, merged):
    nc, A = K.nc, K.A
    W = 2 * P
    chunks = D // W
    sources = [A["w_in"][:, :, COL_GATE:COL_GATE + D], A["w_in"][:, :, COL_GATE + D:COL_GATE + 2 * D],
               A["w_conv_out"], A["w_attn_out"]]
    depth = [KT, KT, CT, HEADS]
    first = [0, KT, 2 * KT, 2 * KT + CT]
    moving = [hT, hT, conv, oT]
    landed = [K.sem(f"m_landed{b}") for b in range(2)]
    projected, opened, merged_sem = (K.sem(f"m_{n}") for n in ("projected", "opened", "merged"))
    with ExitStack() as scope, nc.Block() as block:
        w = K.sb(scope, "m_w", [P, 2, sum(depth), W])
        gates = K.sb(scope, "m_gates", [P, 2, 2, HALF])
        branch = K.sb(scope, "m_branch", [P, 2, 2, HALF])

        @block.sync
        def _(sp):
            for j in range(chunks):
                if j >= 2:
                    sp.wait_ge(projected, 4 * (j - 1))
                for src, k0, kn in zip(sources, first, depth):
                    sp.dma_start(w[:, j % 2, k0:k0 + kn, :],
                                 src[:, :, j * W:(j + 1) * W].rearrange("o (k p) n -> p (o k) n", p=P)) \
                        .then_inc(landed[j % 2], 16)

        @block.tensor
        def _(pe):
            with pe.Fori(0, chunks // 2) as i:
                for b in range(2):
                    pe.wait_ge(landed[b], i * 64 + 64)
                    for c in range(2):
                        for h in range(2):
                            pe.wait_ge(merged_sem, i * 8 + (4 * b + 2 * c + h + 1))
                            for j in range(4):
                                for k in range(depth[j]):
                                    mm = nc.tensor.matmul(K.ps[:, 4 * h + j, :], w[:, b, first[j] + k, c * P:(c + 1) * P],
                                                          moving[j][:, k, h * HALF:(h + 1) * HALF],
                                                          start=(k == 0), stop=(k == depth[j] - 1))
                            mm.then_inc(projected, 1)

        @block.scalar
        def _(act):
            with act.Fori(0, 2 * chunks) as c:
                for h in range(2):
                    act.wait_ge(merged_sem, c * 2 + (h + 1))
                    act.wait_ge(projected, c * 2 + (h + 1))
                    nc.scalar.activation(gates[:, h], K.ps[:, 4 * h:4 * h + 2, :], ACT.Sigmoid).then_inc(opened, 1)

        @block.vector
        def _(dve):
            dve.sem_inc(merged_sem, 2)
            with dve.Fori(0, 2 * chunks) as c:
                for h in range(2):
                    dve.wait_ge(opened, c * 2 + (h + 1))
                    nc.vector.tensor_tensor(branch[:, h], gates[:, h], K.ps[:, 4 * h + 2:4 * h + 4, :], ALU.mult)
                    dve.drain()
                    nc.vector.tensor_tensor(merged[:, c, h * HALF:(h + 1) * HALF], branch[:, h, 0, :], branch[:, h, 1, :],
                                            ALU.add).then_inc(merged_sem, 1)


def project_and_add(K, tag, srcT, weight, x, src):
    nc = K.nc
    landed, x_landed, projected, added = (K.sem(f"{tag}_{n}") for n in ("landed", "x_landed", "projected", "added"))
    with ExitStack() as scope, nc.Block() as block:
        w = K.sb(scope, f"{tag}_w", [P, KT, D])

        @block.sync
        def _(sp):
            sp.dma_start(w[:], weight.rearrange("o (k p) n -> p (o k) n", p=P)).then_inc(landed, 16)
            sp.dma_start(x[:], src.rearrange("(t p) d -> p t d", p=P)).then_inc(x_landed, 16)

        @block.tensor
        def _(pe):
            pe.wait_ge(landed, 16)
            for s in range(2):
                for t in range(NT):
                    if s:
                        pe.wait_ge(added, t + 1)
                    for k in range(KT):
                        mm = nc.tensor.matmul(K.ps[:, t, :], srcT[:, k, t * P:(t + 1) * P],
                                              w[:, k, s * HALF:(s + 1) * HALF], start=(k == 0), stop=(k == KT - 1))
                    mm.then_inc(projected, 1)

        @block.vector
        def _(dve):
            dve.wait_ge(x_landed, 16)
            for s in range(2):
                with dve.Fori(0, NT) as t:
                    dve.wait_ge(projected, t + (1 + NT * s))
                    nc.vector.tensor_tensor(x[:, t, s * HALF:(s + 1) * HALF], x[:, t, s * HALF:(s + 1) * HALF],
                                            K.ps[:, t, :], ALU.add).then_inc(added, 1)


def norm_and_route(K, x, rows, logits):
    nc, A = K.nc, K.A
    NL = GROUPS + EXPERTS
    squared, meaned, rooted, scaled, turned, kept, routed, biased = (K.sem(f"r_{n}") for n in
        ("squared", "meaned", "rooted", "scaled", "turned", "kept", "routed", "biased"))
    landed = K.sem("r_landed")
    stored = [K.sem(f"r_stored{b}") for b in range(2)]
    with ExitStack() as scope, nc.Block() as block:
        gain = K.sb(scope, "r_gain", [P, D])
        wr = K.sb(scope, "r_w", [P, KT, NL])
        bias = K.sb(scope, "r_bias", [P, NL])
        junk = K.sb(scope, "r_junk", [P, D])
        ss = K.sb(scope, "r_ss", [P, NT])
        h2 = K.sb(scope, "r_h2", [P, 2, D])
        h2T = K.sb(scope, "r_h2T", [P, 2, KT, P])

        @block.sync
        def _(sp):
            sp.dma_start(gain[:], A["ffn_norm_g"].to_broadcast([P, D])).then_inc(landed, 16)
            sp.dma_start(wr[:, :, 0:GROUPS], A["w_router_group"].rearrange("o (k p) n -> p (o k) n", p=P)).then_inc(landed, 16)
            sp.dma_start(wr[:, :, GROUPS:NL], A["w_router_expert"].rearrange("o (k p) n -> p (o k) n", p=P)).then_inc(landed, 16)
            sp.dma_start(bias[:, 0:GROUPS], A["b_router_group"].to_broadcast([P, GROUPS])).then_inc(landed, 16)
            sp.dma_start(bias[:, GROUPS:NL], A["b_router_expert"].to_broadcast([P, EXPERTS])).then_inc(landed, 16)
            for t in range(NT):
                sp.wait_ge(scaled, t + 1)
                sp.dma_start(rows[t * P:(t + 1) * P, :], h2[:, t % 2, :]).then_inc(stored[t % 2], 16)
            for b in range(2):
                sp.wait_ge(stored[b], 16 * (NT // 2 + 1))

        @block.scalar
        def _(act):
            with act.Fori(0, NT) as t:
                nc.scalar.activation(junk[:], x[:, t, :], ACT.Square, accum_out=ss[:, bass.ds(t, 1)])
                act.drain()
            act.sem_inc(squared, 1)
            act.wait_ge(meaned, 1)
            nc.scalar.activation(ss[:], ss[:], ACT.Sqrt).then_inc(rooted, 1)
            with act.Fori(0, NT // 2) as i:
                for b in range(2):
                    act.wait_ge(turned, i * 2 + (b + 3))
                    act.wait_ge(routed, i * 2 + (b + 1))
                    nc.scalar.activation(h2T[:, b], K.ps[:, 2 * b:2 * b + 2, :].rearrange("p c (k n) -> p (c k) n", n=P),
                                         ACT.Copy).then_inc(kept, 1)

        @block.vector
        def _(dve):
            dve.sem_inc(stored[0], 16)
            dve.sem_inc(stored[1], 16)
            dve.sem_inc(biased, 2)
            dve.wait_ge(squared, 1)
            nc.vector.tensor_scalar(ss[:], ss[:], 1.0 / D, EPS, ALU.mult, ALU.add).then_inc(meaned, 1)
            dve.wait_ge(rooted, 1)
            nc.vector.reciprocal(ss[:], ss[:])
            dve.drain()
            dve.wait_ge(landed, 80)
            with dve.Fori(0, NT // 2) as i:
                for b in range(2):
                    dve.wait_ge(turned, i * 2 + (b + 1))
                    dve.wait_ge(stored[b], i * 16 + 16)
                    nc.vector.scalar_tensor_tensor(h2[:, b, :], x[:, i * 2 + b, :], ss[:, bass.ds(i * 2 + b, 1)], gain[:],
                                                   ALU.mult, ALU.mult).then_inc(scaled, 1)
                for b in range(2):
                    dve.wait_ge(routed, i * 2 + (b + 3))
                    nc.vector.tensor_tensor(logits[:, i * 2 + b, :], K.ps[:, 4 + b, 0:NL], bias[:], ALU.add) \
                        .then_inc(biased, 1)

        @block.tensor
        def _(pe):
            pe.sem_inc(turned, 2)
            pe.sem_inc(routed, 2)
            pe.wait_ge(landed, 80)
            with pe.Fori(0, NT // 2) as i:
                for b in range(2):
                    pe.wait_ge(scaled, i * 2 + (b + 1))
                    pe.wait_ge(biased, i * 2 + (b + 1))
                    for k in range(KT):
                        mm = nc.tensor.transpose(K.ps[:, 2 * b + k // 4, (k % 4) * P:(k % 4 + 1) * P],
                                                 h2[:, b, k * P:(k + 1) * P], K.const("ident"))
                    mm.then_inc(turned, 1)
                for b in range(2):
                    pe.wait_ge(kept, i * 2 + (b + 1))
                    for k in range(KT):
                        mm = nc.tensor.matmul(K.ps[:, 4 + b, 0:NL], h2T[:, b, k, :], wr[:, k, :],
                                              start=(k == 0), stop=(k == KT - 1))
                    mm.then_inc(routed, 1)


def choose_experts(K, logits, weights, dest, expert_of_block, table):
    nc = K.nc
    exped, peaked, chosen, counted, placed, zeroed, cleared, scattered = (K.sem(f"c_{n}") for n in
        ("exped", "peaked", "chosen", "counted", "placed", "zeroed", "cleared", "scattered"))
    with ExitStack() as scope, nc.Block() as block:
        sb = lambda name, shape, dt=F32: K.sb(scope, f"c_{name}", shape, dt)
        gpeak, gexp, gmass = sb("gpeak", [P, NT]), sb("gexp", [P, NT, GROUPS]), sb("gmass", [P, NT])
        ghot, g_pick = sb("ghot", [P, NT, GROUPS]), sb("g_pick", [P, NT])
        mine, part = sb("mine", [P, NT, EPG]), sb("part", [P, NT, EPG])
        top = sb("top", [P, 2, NT])
        hot = sb("hot", [P, 2, NT, EPG])
        hot32 = sb("hot32", [P, 2, NT, EXPERTS])
        both = sb("both", [P, NT, EXPERTS])
        gap, share = sb("gap", [P, NT]), sb("share", [P, NT])
        count_i, padded = sb("count_i", [P, EXPERTS], I32), sb("padded", [P, EXPERTS])
        ends, begins, ones = sb("ends", [P, EXPERTS]), sb("begins", [P, EXPERTS]), sb("ones", [P, EXPERTS])
        place, dest_f = sb("place", [P, NT, EXPERTS]), sb("dest_f", [P, NT, 2])
        behind, owner = sb("behind", [P, BLOCKS, EXPERTS]), sb("owner", [P, BLOCKS])
        tokens, zeros = sb("tokens", [P, NT], I32), sb("zeros", [P, BLOCKS], I32)

        def wide(ap, n):
            return ap.unsqueeze(2).to_broadcast([P, ap.shape[1], n])

        def rows(ap):
            return ap.unsqueeze(1).to_broadcast([P, NT, ap.shape[1]])

        @block.vector
        def _(dve):
            tt, ts = nc.vector.tensor_tensor, nc.vector.tensor_scalar

            def first_of(equal, rank, pick, out):
                tt(equal, equal, rows(rank), ALU.mult)
                dve.drain()
                nc.vector.tensor_reduce(pick, equal, AX, ALU.max)
                dve.drain()
                tt(out, rows(rank), wide(pick, rank.shape[1]), ALU.is_equal)
                dve.drain()

            nc.vector.memset(zeros[:], 0).then_inc(zeroed, 1)
            nc.vector.memset(ones[:], 1.0)
            nc.vector.tensor_copy(tokens[:], K.const("token"))
            g = logits[:, :, 0:GROUPS]
            nc.vector.tensor_reduce(gpeak[:], g, AX, ALU.max)
            dve.drain()
            tt(gexp[:], g, wide(gpeak[:], GROUPS), ALU.subtract).then_inc(peaked, 1)
            tt(ghot[:], g, wide(gpeak[:], GROUPS), ALU.is_equal)
            dve.drain()
            first_of(ghot[:], K.const("rank4"), g_pick[:], ghot[:])
            for j in range(GROUPS):
                e = logits[:, :, GROUPS + j * EPG:GROUPS + (j + 1) * EPG]
                tt(part[:] if j else mine[:], e, wide(ghot[:, :, j], EPG), ALU.mult)
                dve.drain()
                if j:
                    tt(mine[:], mine[:], part[:], ALU.add)
                    dve.drain()
            for c in range(2):
                nc.vector.tensor_reduce(top[:, c, :], mine[:], AX, ALU.max)
                dve.drain()
                tt(part[:], mine[:], wide(top[:, c, :], EPG), ALU.is_equal)
                dve.drain()
                first_of(part[:], K.const("rank8"), g_pick[:], hot[:, c])
                if c == 0:
                    nc.vector.scalar_tensor_tensor(mine[:], hot[:, 0], 4 * NEG, mine[:], ALU.mult, ALU.add)
                    dve.drain()
            for c in range(2):
                for j in range(GROUPS):
                    tt(hot32[:, c, :, j * EPG:(j + 1) * EPG], hot[:, c], wide(ghot[:, :, j], EPG), ALU.mult)
            dve.drain()
            tt(both[:], hot32[:, 0], hot32[:, 1], ALU.add).then_inc(chosen, 1)
            tt(gap[:], top[:, 1, :], top[:, 0, :], ALU.subtract).then_inc(peaked, 1)
            dve.wait_ge(exped, 2)
            nc.vector.tensor_reduce(gmass[:], gexp[:], AX, ALU.add)
            ts(share[:], gap[:], 1.0, None, ALU.add)
            dve.drain()
            tt(share[:], share[:], gmass[:], ALU.mult)
            dve.drain()
            nc.vector.reciprocal(share[:], share[:])
            dve.drain()
            nc.vector.tensor_copy(weights[:, :, 0], share[:])
            tt(weights[:, :, 1], share[:], gap[:], ALU.mult)
            dve.wait_ge(counted, 1)
            ts(count_i[:], K.ps[:, 0, NT * EXPERTS:(NT + 1) * EXPERTS], float(P - 1), None, ALU.add)
            dve.drain()
            ts(count_i[:], count_i[:], 7, 7, ALU.logical_shift_right, ALU.logical_shift_left)
            dve.drain()
            nc.vector.tensor_copy(padded[:], count_i[:])
            dve.drain()
            nc.vector.tensor_tensor_scan(ends[:], ones[:], padded[:], 0.0, ALU.mult, ALU.add)
            dve.drain()
            tt(begins[:], ends[:], padded[:], ALU.subtract)
            dve.drain()
            tt(place[:], K.ps[:, 0, 0:NT * EXPERTS].rearrange("p (t e) -> p t e", e=EXPERTS), rows(begins[:]), ALU.add)
            dve.drain()
            for c in range(2):
                tt(both[:], place[:], hot32[:, c], ALU.mult)
                dve.drain()
                nc.vector.tensor_reduce(dest_f[:, :, c], both[:], AX, ALU.add)
                dve.drain()
            nc.vector.tensor_copy(dest[:], dest_f[:].rearrange("p t c -> p (t c)")).then_inc(placed, 1)
            tt(behind[:], ends[:].unsqueeze(1).to_broadcast([P, BLOCKS, EXPERTS]), wide(K.const("block_start"), EXPERTS),
               ALU.is_le)
            dve.drain()
            nc.vector.tensor_reduce(owner[:], behind[:], AX, ALU.add)
            dve.drain()
            ts(expert_of_block[:], owner[:], float(EXPERTS - 1), None, ALU.min)

        @block.scalar
        def _(act):
            act.wait_ge(peaked, 1)
            nc.scalar.activation(gexp[:], gexp[:], ACT.Exp).then_inc(exped, 1)
            act.wait_ge(peaked, 2)
            nc.scalar.activation(gap[:], gap[:], ACT.Exp).then_inc(exped, 1)

        @block.tensor
        def _(pe):
            pe.wait_ge(chosen, 1)
            nc.tensor.matmul(K.ps[:, 0, 0:NT * EXPERTS], K.const("before"), both[:].rearrange("p t e -> p (t e)"),
                             start=True, stop=False, skip_group_check=True)
            for j in range(NT):
                mm = nc.tensor.matmul(K.ps[:, 0, (j + 1) * EXPERTS:(NT + 1) * EXPERTS].rearrange("p (t e) -> p t e", e=EXPERTS),
                                      K.const("ones"), both[:, j, :].unsqueeze(1).to_broadcast([P, NT - j, EXPERTS]),
                                      start=False, stop=(j == NT - 1), skip_group_check=True)
            mm.then_inc(counted, 1)

        @block.gpsimd
        def _(pool):
            pool.wait_ge(zeroed, 1)
            pool.dma_start(table.rearrange("(p b) o -> p (b o)", p=P), zeros[:]).then_inc(cleared, 16)
            pool.wait_ge(cleared, 16)
            pool.wait_ge(placed, 1)
            for t in range(NT):
                for c in range(2):
                    pool.indirect_dma_start(table, bass.IndirectOffsetOnAxis(ap=dest[:, 2 * t + c:2 * t + c + 1], axis=0),
                                            tokens[:, t:t + 1], None).then_inc(scattered, 16)
            pool.wait_ge(scattered, 16 * 2 * NT)


def run_experts(K, rows, table, expert_of_block, results):
    nc, A = K.nc, K.A
    gathered = [K.sem(f"e_gathered{b}") for b in range(2)]
    g_landed, u_landed, d_landed = ([K.sem(f"e_{n}_landed{b}") for b in range(2)] for n in "gud")
    stored = [K.sem(f"e_stored{b}") for b in range(2)]
    padded, fetching = K.sem("e_padded"), K.sem("e_fetching")
    listed, picked, turned, x_kept, opened, silued, gated, mid_turned, mid_kept, closed, y_kept = (K.sem(f"e_{n}") for n in
        ("listed", "picked", "turned", "x_kept", "opened", "silued", "gated", "mid_turned", "mid_kept", "closed", "y_kept"))
    with ExitStack() as scope, nc.Block() as block:
        index = K.sb(scope, "e_index", [P, BLOCKS + 1], I32)
        pick = K.sb(scope, "e_pick", [P, 2, 1], I32)
        xb = K.sb(scope, "e_x", [P, 2, D])
        xT = K.sb(scope, "e_xT", [P, 2, KT, P])
        wg = K.sb(scope, "e_wg", [P, 2, KT, DE])
        wu = K.sb(scope, "e_wu", [P, 2, KT, DE])
        wd = K.sb(scope, "e_wd", [P, 2, FT, D])
        sg = K.sb(scope, "e_sg", [P, DE])
        mid = K.sb(scope, "e_mid", [P, DE])
        midT = K.sb(scope, "e_midT", [P, FT, P])
        y = K.sb(scope, "e_y", [P, 2, D])
        x_banks = K.ps[:, 0:2, :].rearrange("p c (k n) -> p (c k) n", n=P)
        g_bank, u_bank, mid_bank = K.ps[:, 2, :], K.ps[:, 3, :], K.ps[:, 4, :]
        y_banks = K.ps[:, 6:8, :].rearrange("p c n -> p (c n)")

        @block.gpsimd
        def _(pool):
            pool.wait_ge(listed, 16)
            pool.wait_ge(padded, 1)

            def gather(n, b):
                pool.wait_ge(turned, n + 1)
                nc.gpsimd.tensor_copy(pick[:, b, :], index[:, bass.ds(n, 1)]).then_inc(picked, 1)
                pool.wait_ge(picked, n + 1)
                pool.sem_inc(fetching, 1)
                pool.indirect_dma_start(xb[:, b, :], None, rows, bass.IndirectOffsetOnAxis(ap=pick[:, b, :], axis=0)) \
                    .then_inc(gathered[b], 16)

            gather(0, 0)
            with pool.Fori(0, BLOCKS // 2) as i:
                for b in range(2):
                    gather(i * 2 + (b + 1), 1 - b)

        @block.sync
        def _(sp):
            with sp.Fori(0, BLOCKS // 2) as i:
                for b in range(2):
                    e = sp.value_load(expert_of_block[0:1, bass.ds(i * 2 + b, 1)], min_val=0, max_val=EXPERTS - 1)
                    sp.wait_ge(opened, i * 2 + (b + 1))
                    sp.dma_start(wg[:, b], A["w_gate_e"][0][bass.ds(e, 1)].rearrange("e (k p) n -> p (e k) n", p=P)) \
                        .then_inc(g_landed[b], 16)
                    sp.dma_start(wu[:, b], A["w_up_e"][0][bass.ds(e, 1)].rearrange("e (k p) n -> p (e k) n", p=P)) \
                        .then_inc(u_landed[b], 16)
                    sp.wait_ge(closed, i * 2 + (b + 1))
                    sp.dma_start(wd[:, b], A["w_down_e"][0][bass.ds(e, 1)].rearrange("e (k p) n -> p (e k) n", p=P)) \
                        .then_inc(d_landed[b], 16)

        @block.tensor
        def _(pe):
            pe.sem_inc(turned, 2)
            pe.sem_inc(opened, 2)
            pe.sem_inc(closed, 2)

            def turn_x(b):
                for k in range(KT):
                    mm = nc.tensor.transpose(x_banks[:, k, :], xb[:, b, k * P:(k + 1) * P], K.const("ident"))
                mm.then_inc(turned, 1)

            pe.wait_ge(gathered[0], 16)
            turn_x(0)
            with pe.Fori(0, BLOCKS // 2) as i:
                for b in range(2):
                    n = i * 2 + b
                    pe.wait_ge(x_kept, n + 1)
                    pe.wait_ge(gated, n + 1)
                    for w, bank, landed in ((wg, g_bank, g_landed), (wu, u_bank, u_landed)):
                        pe.wait_ge(landed[b], i * 16 + 16)
                        for k in range(KT):
                            mm = nc.tensor.matmul(bank, xT[:, b, k, :], w[:, b, k, :], start=(k == 0), stop=(k == KT - 1))
                    mm.then_inc(opened, 1)
                    pe.wait_ge(gathered[1 - b], i * 16 + 16 * (b + 1))
                    turn_x(1 - b)
                    pe.wait_ge(gated, n + 2)
                    pe.wait_ge(mid_kept, n + 1)
                    for k in range(FT):
                        mm = nc.tensor.transpose(mid_bank[:, k * P:(k + 1) * P], mid[:, k * P:(k + 1) * P], K.const("ident"))
                    mm.then_inc(mid_turned, 1)
                    pe.wait_ge(mid_kept, n + 2)
                    pe.wait_ge(y_kept, n + 1)
                    pe.wait_ge(d_landed[b], i * 16 + 16)
                    for h in range(2):
                        for k in range(FT):
                            mm = nc.tensor.matmul(K.ps[:, 6 + h, :], midT[:, k, :], wd[:, b, k, h * HALF:(h + 1) * HALF],
                                                  start=(k == 0), stop=(k == FT - 1))
                    mm.then_inc(closed, 1)

        @block.scalar
        def _(act):
            act.dma_start(index[:, 0:BLOCKS], table.rearrange("(b p) o -> p (b o)", p=P),
                          allow_slow_non_contiguous=True).then_inc(listed, 16)

            def keep_x(n, b):
                act.wait_ge(turned, n + 3)
                nc.scalar.activation(xT[:, b], x_banks, ACT.Copy).then_inc(x_kept, 1)

            keep_x(0, 0)
            with act.Fori(0, BLOCKS // 2) as i:
                for b in range(2):
                    n = i * 2 + b
                    act.wait_ge(opened, n + 3)
                    nc.scalar.activation(sg[:], g_bank, ACT.Silu).then_inc(silued, 1)
                    keep_x(n + 1, 1 - b)
                    act.wait_ge(y_kept, n + 2)
                    act.dma_start(results[bass.ds(n * P, P), :], y[:, b, :]).then_inc(stored[b], 16)
            for b in range(2):
                act.wait_ge(stored[b], 16 * (BLOCKS // 2 + 1))

        @block.vector
        def _(dve):
            nc.vector.memset(index[:, BLOCKS:BLOCKS + 1], 0).then_inc(padded, 1)
            dve.sem_inc(gated, 1)
            dve.sem_inc(mid_kept, 1)
            dve.sem_inc(y_kept, 1)
            dve.sem_inc(stored[0], 16)
            dve.sem_inc(stored[1], 16)
            with dve.Fori(0, BLOCKS // 2) as i:
                for b in range(2):
                    n = i * 2 + b
                    dve.wait_ge(silued, n + 1)
                    nc.vector.tensor_tensor(mid[:], sg[:], u_bank, ALU.mult).then_inc(gated, 1)
                    dve.wait_ge(mid_turned, n + 1)
                    nc.vector.tensor_copy(midT[:].rearrange("p k n -> p (k n)"), mid_bank).then_inc(mid_kept, 1)
                    dve.wait_ge(closed, n + 3)
                    dve.wait_ge(stored[b], i * 16 + 16)
                    nc.vector.tensor_copy(y[:, b, :], y_banks).then_inc(y_kept, 1)


def combine_experts(K, x, weights, dest, results):
    nc = K.nc
    gathered = [K.sem(f"a_gathered{t}") for t in range(NT // 2)]
    with ExitStack() as scope, nc.Block() as block:
        y = K.sb(scope, "a_y", [P, NT, 2, D])

        @block.gpsimd
        def _(pool):
            for t in range(NT):
                for c in range(2):
                    pool.indirect_dma_start(y[:, t, c, :], None, results,
                                            bass.IndirectOffsetOnAxis(ap=dest[:, 2 * t + c:2 * t + c + 1], axis=0)) \
                        .then_inc(gathered[t // 2], 16)

        @block.vector
        def _(dve):
            for t in range(NT):
                dve.wait_ge(gathered[t // 2], 64)
                for c in range(2):
                    nc.vector.scalar_tensor_tensor(x[:, t, :], y[:, t, c, :], weights[:, t, c:c + 1], x[:, t, :],
                                                   ALU.mult, ALU.add)
                    dve.drain()


def project_mixers(K, hT, slabs):
    nc = K.nc
    w_in = K.A["w_in_2"].rearrange("o (k p) n -> p (o k) n", p=P)
    landed = [K.sem(f"z_landed{b}") for b in range(2)]
    projected, kept = K.sem("z_projected"), K.sem("z_kept")
    widest = max(sum(n for _, n in pieces) for pieces, _ in slabs)
    done, counts = [], 0
    for _, jobs in slabs:
        counts += sum(2 if j[0] == "T" else NT for j in jobs)
        done.append(counts)
    with ExitStack() as scope, nc.Block() as block:
        w = K.sb(scope, "z_w", [P, 2, KT, widest])

        @block.sync
        def _(sp):
            for s, (pieces, _) in enumerate(slabs):
                if s >= 2:
                    sp.wait_ge(projected, done[s - 2])
                at = 0
                for c, n in pieces:
                    sp.dma_start(w[:, s % 2, :, at:at + n], w_in[:, :, c:c + n]).then_inc(landed[s % 2], 16)
                    at += n

        @block.tensor
        def _(pe):
            n, loads = 0, [0, 0]
            for s, (pieces, jobs) in enumerate(slabs):
                loads[s % 2] += 16 * len(pieces)
                pe.wait_ge(landed[s % 2], loads[s % 2])
                for kind, col, m, *_ in jobs:
                    for part in range(2 if kind == "T" else NT):
                        if n >= 8:
                            pe.wait_ge(kept, n - 7)
                        for k in range(KT):
                            if kind == "T":
                                mm = nc.tensor.matmul(K.ps[0:m, n % 8, :], w[:, s % 2, k, col:col + m],
                                                      hT[:, k, part * HALF:(part + 1) * HALF],
                                                      start=(k == 0), stop=(k == KT - 1))
                            else:
                                mm = nc.tensor.matmul(K.ps[:, n % 8, 0:m], hT[:, k, part * P:(part + 1) * P],
                                                      w[:, s % 2, k, col:col + m], start=(k == 0), stop=(k == KT - 1))
                        mm.then_inc(projected, 1)
                        n += 1

        @block.scalar
        def _(act):
            n = 0
            for _, jobs in slabs:
                for kind, col, m, dst, *how in jobs:
                    scale, func = how or (1.0, ACT.Copy)
                    for part in range(2 if kind == "T" else NT):
                        act.wait_ge(projected, n + 1)
                        bank = K.ps[0:m, n % 8, :] if kind == "T" else K.ps[:, n % 8, 0:m]
                        nc.scalar.activation(dst(part), bank, func, scale=scale).then_inc(kept, 1)
                        n += 1


def turn(K, tag, src, dst):
    nc = K.nc
    tiles = src.shape[2] // P
    turned, kept, staged = K.sem(f"{tag}_turned"), K.sem(f"{tag}_kept"), K.sem(f"{tag}_staged")
    with ExitStack() as scope, nc.Block() as block:
        stage = K.sb(scope, f"{tag}_stage", [P, 2, src.shape[2]])

        @block.vector
        def _(dve):
            with dve.Fori(0, NT // 2) as i:
                for b in range(2):
                    dve.wait_ge(turned, i * 2 + (b + 1))
                    nc.vector.tensor_copy(stage[:, b, :], src[:, i * 2 + b, :]).then_inc(staged, 1)

        @block.tensor
        def _(pe):
            pe.sem_inc(turned, 2)
            with pe.Fori(0, NT // 2) as i:
                for b in range(2):
                    pe.wait_ge(staged, i * 2 + (b + 1))
                    pe.wait_ge(kept, i * 2 + (b + 1))
                    for k in range(tiles):
                        mm = nc.tensor.transpose(K.ps[:, b, k * P:(k + 1) * P], stage[:, b, k * P:(k + 1) * P],
                                                 K.const("ident"))
                    mm.then_inc(turned, 1)

        @block.scalar
        def _(act):
            act.sem_inc(kept, 2)
            with act.Fori(0, NT // 2) as i:
                for b in range(2):
                    act.wait_ge(turned, i * 2 + (b + 3))
                    nc.scalar.activation(dst[:, :, bass.ds((i * 2 + b) * P, P)],
                                         K.ps[:, b, 0:tiles * P].rearrange("p (k n) -> p k n", n=P), ACT.Copy) \
                        .then_inc(kept, 1)


def project_norm_add(K, tag, srcT, depth, weight, gain_row, x, src=None, out=None, y=None):
    nc = K.nc
    PART = 2 if depth > KT else depth
    parts = depth // PART
    landed = [K.sem(f"{tag}_landed{b}") for b in range(2)]
    gain_landed, x_landed, stored = K.sem(f"{tag}_gain_landed"), K.sem(f"{tag}_x_landed"), K.sem(f"{tag}_stored")
    projected, chunked, kept, squared, meaned, rooted, added = (K.sem(f"{tag}_{n}") for n in
        ("projected", "chunked", "kept", "squared", "meaned", "rooted", "added"))
    with ExitStack() as scope, nc.Block() as block:
        w = K.sb(scope, f"{tag}_w", [P, 2, PART, HALF])
        gain = K.sb(scope, f"{tag}_gain", [P, D])
        if y is None:
            y = K.sb(scope, f"{tag}_y", [P, NT, D])
        junk = K.sb(scope, f"{tag}_junk", [P, D])
        ss = K.sb(scope, f"{tag}_ss", [P, NT])

        @block.sync
        def _(sp):
            for s in range(2):
                for c in range(parts):
                    n = s * parts + c
                    if n >= 2:
                        sp.wait_ge(chunked, n - 1)
                    sp.dma_start(w[:, n % 2], weight[:, c * PART * P:(c + 1) * PART * P, s * HALF:(s + 1) * HALF]
                                 .rearrange("o (k p) n -> p (o k) n", p=P)).then_inc(landed[n % 2], 16)
            sp.dma_start(gain[:], gain_row.to_broadcast([P, D])).then_inc(gain_landed, 16)
            if src is not None:
                sp.dma_start(x[:], src.rearrange("(t p) d -> p t d", p=P)).then_inc(x_landed, 16)
            if out is not None:
                for t in range(NT):
                    sp.wait_ge(added, t + 1)
                    sp.dma_start(out[t * P:(t + 1) * P, :], x[:, t, :]).then_inc(stored, 16)
                sp.wait_ge(stored, 16 * NT)

        @block.tensor
        def _(pe):
            for s in range(2):
                for c in range(parts):
                    n = s * parts + c
                    pe.wait_ge(landed[n % 2], 16 * (n // 2 + 1))
                    for t in range(NT):
                        if s and c == 0:
                            pe.wait_ge(kept, t + 1)
                        for k in range(PART):
                            mm = nc.tensor.matmul(K.ps[:, t, :], srcT[:, c * PART + k, t * P:(t + 1) * P], w[:, n % 2, k, :],
                                                  start=(c == 0 and k == 0), stop=(c == parts - 1 and k == PART - 1))
                        if t == NT - 1:
                            mm.then_inc(chunked, 1)
                        elif c == parts - 1:
                            mm.then_inc(projected, 1)

        @block.scalar
        def _(act):
            for s in range(2):
                for t in range(NT):
                    if t == NT - 1:
                        act.wait_ge(chunked, (s + 1) * parts)
                    else:
                        act.wait_ge(projected, s * (NT - 1) + t + 1)
                    nc.scalar.activation(y[:, t, s * HALF:(s + 1) * HALF], K.ps[:, t, :], ACT.Copy).then_inc(kept, 1)
            act.drain()
            with act.Fori(0, NT) as t:
                nc.scalar.activation(junk[:], y[:, t, :], ACT.Square, accum_out=ss[:, bass.ds(t, 1)])
                act.drain()
            act.sem_inc(squared, 1)
            act.wait_ge(meaned, 1)
            nc.scalar.activation(ss[:], ss[:], ACT.Sqrt).then_inc(rooted, 1)

        @block.vector
        def _(dve):
            dve.wait_ge(squared, 1)
            nc.vector.tensor_scalar(ss[:], ss[:], 1.0 / D, EPS, ALU.mult, ALU.add).then_inc(meaned, 1)
            dve.wait_ge(rooted, 1)
            nc.vector.reciprocal(ss[:], ss[:])
            dve.drain()
            dve.wait_ge(gain_landed, 16)
            if src is not None:
                dve.wait_ge(x_landed, 16)
            with dve.Fori(0, NT) as t:
                nc.vector.scalar_tensor_tensor(y[:, t, :], y[:, t, :], ss[:, bass.ds(t, 1)], gain[:], ALU.mult, ALU.mult)
                dve.drain()
                nc.vector.tensor_tensor(x[:, t, :], x[:, t, :], y[:, t, :], ALU.add).then_inc(added, 1)


def ffn_up(K, hT, f):
    nc, A = K.nc, K.A
    w_up = A["ffn_w_up_2"].rearrange("o (k p) n -> p (o k) n", p=P)
    landed = [K.sem(f"u_landed{b}") for b in range(2)]
    projected, kept, filtered, gelued, done = (K.sem(f"u_{n}") for n in ("projected", "kept", "filtered", "gelued", "done"))
    with ExitStack() as scope, nc.Block() as block:
        w = K.sb(scope, "u_w", [P, 2, 2, KT, P])
        g = K.sb(scope, "u_g", [P, 2, 2 + S])
        c = K.sb(scope, "u_c", [P, 2, S])
        taps = K.vec("ffn_conv_w_2", 0, 3 * FFT).rearrange("p (w j) -> p w j", j=FFT)
        bias = K.vec("ffn_conv_b_2", 0, FFT)

        def banks(b, up):
            return K.ps[:, 4 * b + 2 * up:4 * b + 2 * up + 2, :].rearrange("p c n -> p (c n)")

        @block.sync
        def _(sp):
            def load(j, b):
                for up in range(2):
                    sp.dma_start(w[:, b, up], w_up[:, :, bass.ds(up * DFF + j * P, P)]).then_inc(landed[b], 16)
            load(0, 0)
            load(1, 1)
            with sp.Fori(0, FFT // 2 - 1) as i:
                for b in range(2):
                    off = [sp.snap((i * 2 + (b + 2)) * P + up * DFF) for up in range(2)]
                    sp.wait_ge(projected, i * 2 + (b + 1))
                    for up in range(2):
                        sp.dma_start(w[:, b, up], w_up[:, :, bass.ds(off[up], P)]).then_inc(landed[b], 16)

        @block.tensor
        def _(pe):
            with pe.Fori(0, FFT // 2) as i:
                for b in range(2):
                    pe.wait_ge(landed[b], i * 32 + 32)
                    pe.wait_ge(done, i * 2 + (b + 1))
                    for up in range(2):
                        for h in range(2):
                            for k in range(KT):
                                mm = nc.tensor.matmul(K.ps[:, 4 * b + 2 * up + h, :], w[:, b, up, k, :],
                                                      hT[:, k, h * HALF:(h + 1) * HALF], start=(k == 0), stop=(k == KT - 1))
                    mm.then_inc(projected, 1)

        @block.scalar
        def _(act):
            with act.Fori(0, FFT // 2) as i:
                for b in range(2):
                    act.wait_ge(projected, i * 2 + (b + 1))
                    act.wait_ge(done, i * 2 + (b + 1))
                    nc.scalar.activation(g[:, b, 2:2 + S], banks(b, 0), ACT.Copy).then_inc(kept, 1)
                    act.wait_ge(filtered, i * 2 + (b + 1))
                    nc.scalar.activation(c[:, b, :], c[:, b, :], ACT.Gelu_apprx_tanh).then_inc(gelued, 1)

        @block.vector
        def _(dve):
            nc.vector.memset(g[:, :, 0:2], 0.0).then_inc(done, 2)
            with dve.Fori(0, FFT // 2) as i:
                for b in range(2):
                    j = i * 2 + b
                    tap = lambda v: taps[:, v, bass.ds(j, 1)]
                    dve.wait_ge(kept, j + 1)
                    nc.vector.tensor_scalar(c[:, b, :], g[:, b, 0:S], tap(0), bias[:, bass.ds(j, 1)], ALU.mult, ALU.add)
                    dve.drain()
                    nc.vector.scalar_tensor_tensor(c[:, b, :], g[:, b, 1:1 + S], tap(1), c[:, b, :], ALU.mult, ALU.add)
                    dve.drain()
                    nc.vector.scalar_tensor_tensor(c[:, b, :], g[:, b, 2:2 + S], tap(2), c[:, b, :], ALU.mult, ALU.add) \
                        .then_inc(filtered, 1)
                    dve.wait_ge(gelued, j + 1)
                    nc.vector.tensor_tensor(f[:, j, :], c[:, b, :], banks(b, 1), ALU.mult).then_inc(done, 1)


def prepare_mixers(K, Z, R):
    nc, A = K.nc, K.A
    CAP, DK = 15.0, 32
    filtered, silued, q_ready, saved = (K.sem(f"q_{n}") for n in ("filtered", "silued", "q_ready", "saved"))
    landed, biased, capped, decayed, logged, summed, turned, rows_saved, spread, revealed, spread_kept = (K.sem(f"q_{n}") for n in
        ("landed", "biased", "capped", "decayed", "logged", "summed", "turned", "rows_saved", "spread", "revealed", "spread_kept"))
    with ExitStack() as scope, nc.Block() as block:
        sb = lambda name, shape: K.sb(scope, f"q_{name}", shape)
        mqk = sb("mqk", [P, 2, S])
        bias = sb("bias", [4, 3])
        bias15 = sb("bias15", [4, 2])
        t = sb("t", [4, 2, S])
        x = sb("x", [4, S])
        u = sb("u", [4, 2, S])
        least = sb("least", [4, S])
        total = sb("total", [4, 2, S])
        keys = sb("keys", [4, 2, S])
        rel = sb("rel", [32, 4])
        band = sb("band", [4, 3 * P])
        raw, gates = Z["mlstm"], Z["gates"]

        @block.sync
        def _(sp):
            for j, name in enumerate(("mlstm_b_i_2", "mlstm_b_f_2", "fox_b_f_2")):
                sp.dma_start(bias[:, j:j + 1], A[name].rearrange("o h -> h o")).then_inc(landed, 16)
            sp.dma_start(rel[:], A["rel_bias_2"]).then_inc(landed, 16)
            for name in ("fox_q", "fox_k", "swa_q"):
                sp.dma_start(R[name].rearrange("(j p) t -> p j t", p=P), Z[name][:]).then_inc(saved, 16)
            for r in range(2):
                sp.dma_start(R["swa_k"].rearrange("(g r p) t -> g r p t", g=2, r=2)[:, r],
                             Z["swa_k"][:, 0, :]).then_inc(saved, 16)
            sp.wait_ge(q_ready, 1)
            sp.dma_start(R["mlstm_q"], mqk[:, 0, :]).then_inc(saved, 16)
            sp.dma_start(R["mlstm_k"], mqk[:, 1, :]).then_inc(saved, 16)
            sp.wait_ge(spread_kept, 1)
            sp.dma_start(R["band"], band[:]).then_inc(revealed, 16)
            sp.wait_ge(revealed, 16)
            tile = bass.AP(R["band"].tensor, 0, [[1, P], [3 * P, 4], [1, 2 * P]])
            sp.dma_start(K.window_bias[:], tile).then_inc(saved, 16)
            sp.wait_ge(summed, 1)
            sp.dma_start(R["mlstm_decay"], keys[:, 0, :]).then_inc(saved, 16)
            sp.dma_start(R["fox_decay"], keys[:, 1, :]).then_inc(saved, 16)
            sp.dma_start(K.sinks[:], A["swa_sinks_2"].to_broadcast([P, 4])).then_inc(saved, 16)
            sp.wait_ge(saved, 16 * 11)

        @block.tensor
        def _(pe):
            pe.wait_ge(landed, 64)
            nc.tensor.matmul(K.ps[0:4, 0, 0:3 * P], rel[:], K.const("bucket")[0:32, :], start=True, stop=True).then_inc(spread, 1)
            pe.wait_ge(summed, 1)
            for i in range(NT):
                mm = nc.tensor.transpose(K.ps[:, 1, 4 * i:4 * i + 4], total[:, 0, i * P:(i + 1) * P], K.const("ident")[0:4, 0:4])
            mm.then_inc(turned, 1)

        @block.vector
        def _(dve):
            ts, tt, stt = nc.vector.tensor_scalar, nc.vector.tensor_tensor, nc.vector.scalar_tensor_tensor
            dve.wait_ge(landed, 64)
            ts(bias15[:], bias[:, 0:2], 1.0 / CAP, None, ALU.mult).then_inc(biased, 1)
            ts(x[:], gates[:, 2, :], bias[:, 2:3], None, ALU.add)
            dve.drain()
            ts(least[:], x[:], 0.0, None, ALU.min)
            stt(u[:, 1, :], x[:], -1.0, x[:], ALU.mult, ALU.max).then_inc(biased, 1)
            for c in range(2):
                out = mqk[:, c, :]
                ts(out, raw[:, c, 0:S], K.vec("mlstm_conv_w_2", c), None, ALU.mult)
                for w in range(1, 4):
                    dve.drain()
                    last = stt(out, raw[:, c, w:w + S], K.vec("mlstm_conv_w_2", 2 * w + c), out, ALU.mult, ALU.add)
                last.then_inc(filtered, 1)
            dve.wait_ge(spread, 1)
            tt(band[:], K.ps[0:4, 0, 0:3 * P], K.const("outside")[0:4, :], ALU.add).then_inc(spread_kept, 1)
            dve.wait_ge(silued, 2)
            ts(mqk[:, 0, :], mqk[:, 0, :], DK ** -0.5, None, ALU.mult).then_inc(q_ready, 1)
            dve.wait_ge(logged, 1)
            ts(u[:, 0, :], u[:, 0, :], -1.0, None, ALU.mult)
            tt(u[:, 1, :], least[:], u[:, 1, :], ALU.subtract)
            dve.drain()
            for c in range(2):
                nc.vector.tensor_tensor_scan(total[:, c, :], K.const("ones")[0:4, 0:1].to_broadcast([4, S]), u[:, c, :], 0.0, ALU.mult, ALU.add)
            dve.drain()
            stt(keys[:, 0, :], t[:, 0, :], CAP, total[:, 0, :], ALU.mult, ALU.subtract)
            ts(keys[:, 1, :], total[:, 1, :], -1.0, None, ALU.mult)
            dve.drain()
            dve.sem_inc(summed, 1)
            dve.wait_ge(turned, 1)
            nc.vector.tensor_copy(K.mlstm_rise[:], K.ps[:, 1, 0:4 * NT])

        @block.scalar
        def _(act):
            act.wait_ge(biased, 2)
            for c in range(2):
                nc.scalar.activation(t[:, c, :], gates[:, c, :], ACT.Tanh, scale=1.0 / CAP, bias=bias15[:, c:c + 1])
            act.drain()
            nc.scalar.activation(u[:, 0, :], t[:, 1, :], ACT.Exp, scale=-CAP)
            nc.scalar.activation(u[:, 1, :], u[:, 1, :], ACT.Exp, scale=-1.0)
            act.drain()
            nc.scalar.activation(u[:], u[:], ACT.Ln, bias=1.0).then_inc(logged, 1)
            for c in range(2):
                act.wait_ge(filtered, c + 1)
                nc.scalar.activation(mqk[:, c, :], mqk[:, c, :], ACT.Silu, bias=K.vec("mlstm_conv_b_2", c)).then_inc(silued, 1)


def attend(K, tag, kind, dk, q_rows, k_rows, decay_rows, v, v_col, o, o_col):
    nc = K.nc
    soft = kind != "mlstm"
    DV = 64
    loaded, scored, peaked, exped, mixed, rated, turned, turned_kept, weighed, stored = (K.sem(f"{tag}_{n}") for n in
        ("loaded", "scored", "peaked", "exped", "mixed", "rated", "turned", "turned_kept", "weighed", "stored"))
    begun = K.sem(f"{tag}_begun")
    first = (lambda i: max(i - 1, 0)) if kind == "swa" else (lambda i: 0)
    with ExitStack() as scope, nc.Block() as block:
        qh = K.sb(scope, f"{tag}_q", [dk, S])
        kh = K.sb(scope, f"{tag}_k", [dk, S])
        decay = K.sb(scope, f"{tag}_decay", [1, S])
        p = K.sb(scope, f"{tag}_p", [P, 2, S])
        w = None if soft else K.sb(scope, f"{tag}_w", [P, 2, S])
        pT = K.sb(scope, f"{tag}_pT", [P, 2, S])
        low = K.sb(scope, f"{tag}_low", [P, 2])
        mass = K.sb(scope, f"{tag}_mass", [P, 2])
        drop = K.sb(scope, f"{tag}_drop", [P, 2])
        share = K.sb(scope, f"{tag}_share", [P, 2])

        def banks(b, n):
            return K.ps[:, b:b + 2, :].rearrange("p b n -> p (b n)")[:, 0:n]

        def width(i):
            return (i + 1 - first(i)) * P

        turn_bank = banks(4, 2 * HALF)

        @block.sync
        def _(sp):
            with sp.Fori(0, 4) as h:
                row, line = sp.snap(h * dk), sp.snap(h)
                sp.wait_ge(weighed, h * NT + 1)
                sp.dma_start(qh[:], q_rows[bass.ds(row, dk), :]).then_inc(loaded, 16)
                sp.dma_start(kh[:], k_rows[bass.ds(row, dk), :]).then_inc(loaded, 16)
                if decay_rows is not None:
                    sp.dma_start(decay[:], decay_rows[bass.ds(line, 1), :]).then_inc(loaded, 16)

        @block.tensor
        def _(pe):
            pe.sem_inc(weighed, 1)
            pe.sem_inc(turned, 2)
            loads = 32 if decay_rows is None else 48
            with pe.Fori(0, 4) as h:
                pe.wait_ge(loaded, h * loads + loads)

                def scores(i):
                    n, b0 = width(i), 2 * (i % 2) if soft else 0
                    u = h * NT + i
                    if soft:
                        pe.wait_ge(exped, u + 1)
                    else:
                        pe.wait_ge(mixed, u + 1)
                    for b in range(0, n, HALF):
                        m = min(HALF, n - b)
                        keys = slice(first(i) * P + b, first(i) * P + b + m)
                        mm = nc.tensor.matmul(banks(b0, n)[:, b:b + m], qh[:, i * P:(i + 1) * P], kh[:, keys],
                                              start=True, stop=(not soft))
                        if kind != "swa":
                            mm = nc.tensor.matmul(banks(b0 if soft else 2, n)[:, b:b + m], K.const("ones")[0:1, :], decay[:, keys],
                                                  start=not soft, stop=(b + m < n))
                    if kind == "swa":
                        mm = nc.tensor.matmul(banks(b0, n), K.const("flip"), K.window_bias[:, h, 2 * P - n:2 * P],
                                              start=False, stop=True)
                    else:
                        mm = nc.tensor.matmul(banks(b0 if soft else 2, n)[:, n - P:n], K.const("ident"), K.const("causal"),
                                              start=False, stop=True)
                    mm.then_inc(scored, 1)

                def values(i):
                    u, tiles = h * NT + i, width(i) // P
                    if soft:
                        pe.wait_ge(exped, u + 3)
                    else:
                        pe.wait_ge(mixed, u + 2)
                    pe.wait_ge(turned_kept, u + 1)
                    for j in range(tiles):
                        mm = nc.tensor.transpose(turn_bank[:, j * P:(j + 1) * P], p[:, i % 2, j * P:(j + 1) * P], K.const("ident"))
                    mm.then_inc(turned, 1)
                    pe.wait_ge(turned_kept, u + 2)
                    pe.wait_ge(stored, u + 1)
                    for j in range(tiles):
                        mm = nc.tensor.matmul(K.ps[:, 6 + i % 2, 0:DV], pT[:, i % 2, j * P:(j + 1) * P],
                                              v[:, first(i) + j, bass.ds(h * DV + v_col, DV)],
                                              start=(j == 0), stop=(j == tiles - 1))
                    mm.then_inc(weighed, 1)

                scores(0)
                for i in range(NT):
                    if i + 1 < NT:
                        scores(i + 1)
                    values(i)

        @block.vector
        def _(dve):
            if not soft:
                dve.sem_inc(mixed, 1)
            with dve.Fori(0, 4) as h:
                def peaks(i):
                    s = i % 2
                    dve.wait_ge(scored, h * NT + (i + 1))
                    nc.vector.tensor_reduce(low[:, s:s + 1], banks(2 * s, width(i)), AX, ALU.max)
                    dve.drain()
                    if kind == "swa":
                        nc.vector.tensor_scalar(low[:, s:s + 1], low[:, s:s + 1], K.sinks[:, bass.ds(h, 1)], -1.0,
                                                ALU.max, ALU.mult).then_inc(peaked, 1)
                    else:
                        nc.vector.tensor_scalar(low[:, s:s + 1], low[:, s:s + 1], -1.0, None, ALU.mult).then_inc(peaked, 1)

                def rate(i):
                    s, u = i % 2, h * NT + i
                    if soft:
                        dve.wait_ge(exped, u + 3)
                        if kind == "swa":
                            nc.vector.tensor_tensor(mass[:, s:s + 1], mass[:, s:s + 1], drop[:, s:s + 1], ALU.add)
                            dve.drain()
                    else:
                        n = width(i)
                        dve.wait_ge(exped, u + 1)
                        dve.wait_ge(turned, u + 1)
                        nc.vector.scalar_tensor_tensor(p[:, s, 0:n], w[:, s, 0:n], 1.0, banks(0, n), ALU.mult, ALU.mult,
                                                       accum_out=mass[:, s:s + 1]).then_inc(mixed, 1)
                        dve.drain()
                        nc.vector.scalar_tensor_tensor(share[:, s:s + 1], mass[:, s:s + 1], -1.0, mass[:, s:s + 1],
                                                       ALU.mult, ALU.max)
                        dve.drain()
                        nc.vector.tensor_scalar(mass[:, s:s + 1], share[:, s:s + 1], 1.0, None, ALU.max)
                        dve.drain()
                    nc.vector.reciprocal(share[:, s:s + 1], mass[:, s:s + 1]).then_inc(rated, 1)

                if soft:
                    peaks(0)
                for i in range(NT):
                    if soft and i + 1 < NT:
                        peaks(i + 1)
                    rate(i)

        @block.scalar
        def _(act):
            if soft:
                act.sem_inc(exped, 2)
            act.sem_inc(turned_kept, 1)
            act.sem_inc(stored, 2)
            with act.Fori(0, 4) as h:
                def exps(i):
                    s, n, u = i % 2, width(i), h * NT + i
                    if soft:
                        act.wait_ge(peaked, u + 1)
                        act.wait_ge(turned, u + 1)
                        if kind == "swa":
                            act.sem_inc(begun, 1)
                            nc.scalar.activation(drop[:, s:s + 1], K.sinks[:, bass.ds(h, 1)], ACT.Exp, bias=low[:, s:s + 1])
                        nc.scalar.activation(p[:, s, 0:n], banks(2 * s, n), ACT.Exp, bias=low[:, s:s + 1],
                                             accum_out=mass[:, s:s + 1]).then_inc(exped, 1)
                    else:
                        act.wait_ge(scored, u + 1)
                        act.sem_inc(begun, 1)
                        nc.scalar.activation(w[:, s, 0:n], banks(2, n), ACT.Exp,
                                             bias=K.mlstm_rise[:, bass.ds(h + 4 * i, 1)]).then_inc(exped, 1)

                def keep(i):
                    s, n, u = i % 2, width(i), h * NT + i
                    act.wait_ge(turned, u + 3)
                    nc.scalar.activation(pT[:, s, 0:n], turn_bank[:, 0:n], ACT.Copy).then_inc(turned_kept, 1)
                    act.wait_ge(rated, u + 1)
                    act.wait_ge(weighed, u + 2)
                    act.sem_inc(begun, 1)
                    nc.scalar.activation(o[:, i, bass.ds(h * DV + o_col, DV)], K.ps[:, 6 + s, 0:DV], ACT.Copy,
                                         scale=share[:, s:s + 1]).then_inc(stored, 1)

                exps(0)
                for i in range(NT):
                    if i + 1 < NT:
                        exps(i + 1)
                    keep(i)


def mixer_slabs(Z):
    def tile(name, j, lead=0):
        return lambda h: Z[name][:, j, lead + h * HALF:lead + (h + 1) * HALF]

    def gate(j):
        return lambda h: Z["gates"][:, j, h * HALF:(h + 1) * HALF]

    def rows(c, n):
        return lambda t: Z["values"][:, t, c:c + n]

    SCALE = HD ** -0.5
    ml_v, ml_o, ml_i, ml_f = ML0 + RW, ML0 + 2 * RW, ML0 + 3 * RW, ML0 + 3 * RW + 4
    sw_k, sw_v = SW0 + RW, SW0 + RW + P
    fx_k, fx_v, fx_f = FX0 + RW, FX0 + 2 * RW, FX0 + 3 * RW
    return [
        ([(0, HALF)], [("T", j * P, P, tile("rwkv", j, 1)) for j in range(4)]),
        ([(HALF, HALF)], [("T", j * P, P, tile("rwkv", 4 + j, 1)) for j in range(4)]),
        ([(ML0, RW), (ml_o, RW)], [("T", j * P, P, tile("mlstm", j, 3)) for j in range(2)]
         + [("T", RW + j * P, P, tile("mlstm_o", j), 1.0, ACT.Sigmoid) for j in range(2)]),
        ([(FX0, 2 * RW)], [("T", j * P, P, tile("fox_q", j), SCALE, ACT.Copy) for j in range(2)]
         + [("T", RW + j * P, P, tile("fox_k", j)) for j in range(2)]),
        ([(SW0, RW + P), (ml_i, 8), (fx_f, 4)], [("T", j * P, P, tile("swa_q", j), SCALE, ACT.Copy) for j in range(2)]
         + [("T", RW, P, tile("swa_k", 0))] + [("T", RW + P + 4 * j, 4, gate(j)) for j in range(3)]),
        ([(ml_v, RW), (fx_v, RW)], [("N", 0, 2 * RW, rows(0, 2 * RW))]),
        ([(sw_v + 64 * (h // 2), 64) for h in range(4)], [("N", 0, RW, rows(2 * RW, RW))]),
    ]


def rwkv_gates(K, z, zm, W):
    nc, A = K.nc, K.A
    loaded, mixed, squashed, projected, gated, squares, rooted, summed, cumulated, exped = (K.sem(f"rg_{n}") for n in
        ("loaded", "mixed", "squashed", "projected", "gated", "squares", "rooted", "summed", "cumulated", "exped"))
    spare = [z[:, 2 * j:2 * j + 2, 1:S + 1] for j in range(4)]
    lw, c, a, tmp = spare
    r, k, v = zm[:, 0:2, :], zm[:, 2:4, :], zm[:, 4:6, :]
    kk, b = W["kk"], W["b"]

    def banks(n):
        return K.ps[:, n:n + 4, :].rearrange("p (j h) n -> p j (h n)", j=2)

    with ExitStack() as scope, nc.Block() as block:
        up = K.sb(scope, "rg_up", [P, RW])
        g_up = K.sb(scope, "rg_g_up", [P, RW])
        within = K.sb(scope, "rg_within", [P, S])

        @block.sync
        def _(sp):
            sp.dma_start(up[0:64, :], A["rwkv_w_up_2"].rearrange("o k n -> (o k) n")).then_inc(loaded, 16)
            sp.dma_start(up[64:P, :], A["rwkv_a_up_2"].rearrange("o k n -> (o k) n")).then_inc(loaded, 16)
            sp.dma_start(g_up[:], A["rwkv_g_up_2"].rearrange("o k n -> (o k) n")).then_inc(loaded, 16)

        @block.tensor
        def _(pe):
            pe.wait_ge(loaded, 48)
            pe.wait_ge(squashed, 2)
            for base, rows in ((0, slice(0, 64)), (4, slice(64, P))):
                for j in range(2):
                    for h in range(2):
                        mm = nc.tensor.matmul(K.ps[:, base + 2 * j + h, :], up[rows, j * P:(j + 1) * P],
                                              zm[rows, 6, h * HALF:(h + 1) * HALF], start=True, stop=True)
                mm.then_inc(projected, 1)
            pe.wait_ge(gated, 2)
            for j in range(2):
                for h in range(2):
                    mm = nc.tensor.matmul(K.ps[:, 2 * j + h, :], g_up[:, j * P:(j + 1) * P],
                                          zm[:, 7, h * HALF:(h + 1) * HALF], start=True, stop=True)
            mm.then_inc(projected, 1)
            for n, (base, free) in enumerate(((4, 4), (0, 6))):
                pe.wait_ge(squares, n + 1)
                pe.wait_ge(gated, free)
                for j in range(2):
                    for h in range(2):
                        mm = nc.tensor.matmul(K.ps[:, base + 2 * j + h, :], K.const("pair"),
                                              tmp[:, j, h * HALF:(h + 1) * HALF], start=True, stop=True)
                mm.then_inc(summed, 1)

        @block.vector
        def _(dve):
            ts, tt, stt = nc.vector.tensor_scalar, nc.vector.tensor_tensor, nc.vector.scalar_tensor_tensor
            for tiles in (range(6, 8), range(6)):
                span = slice(tiles.start, tiles.stop)
                tt(zm[:, span, :], z[:, span, 0:S], z[:, span, 1:S + 1], ALU.subtract)
                dve.drain()
                for j in tiles:
                    stt(zm[:, j, :], zm[:, j, :], K.vec("rwkv_mu_2", j), z[:, j, 1:S + 1], ALU.mult, ALU.add).then_inc(mixed, 1)
            dve.drain()
            for j in range(2):
                ts(kk[:, j, :], k[:, j, :], K.vec("rwkv_k_k_2", j), None, ALU.mult)
            nc.vector.memset(within[:], 1.0)
            dve.drain()
            nc.vector.memset(within[:].rearrange("p (c n) -> p c n", n=CHUNK)[:, :, 0:1], 0.0)
            tt(tmp, kk[:], kk[:], ALU.mult).then_inc(squares, 1)
            dve.wait_ge(gated, 2)
            ts(lw, lw, -math.exp(-0.5), None, ALU.mult)
            dve.drain()
            for j in range(2):
                nc.vector.tensor_tensor_scan(c[:, j, :], within[:], lw[:, j, :], 0.0, ALU.mult, ALU.add)
            dve.drain()
            tt(lw, c, lw, ALU.subtract).then_inc(cumulated, 1)
            dve.wait_ge(rooted, 1)
            ts(tmp, tmp, 1e-12, None, ALU.max)
            dve.drain()
            nc.vector.reciprocal(tmp, tmp)
            dve.drain()
            tt(kk[:], kk[:], tmp, ALU.mult)
            dve.drain()
            dve.wait_ge(gated, 4)
            for j in range(2):
                ts(tmp[:, j, :], a[:, j, :], -1.0, K.vec("rwkv_k_a_2", j), ALU.add, ALU.mult)
            dve.drain()
            stt(k, tmp, 1.0, k, ALU.add, ALU.mult)
            dve.drain()
            for j in range(2):
                bonus = stt(tmp[:, j, :], r[:, j, :], K.vec("rwkv_r_k_2", j), k[:, j, :], ALU.mult, ALU.mult)
            bonus.then_inc(squares, 1)
            tt(a, kk[:], a, ALU.mult)
            dve.wait_ge(summed, 2)
            tt(W["bonus"][:], banks(0), v, ALU.mult)
            dve.wait_ge(exped, 3)
            dve.drain()
            tt(b[:], a, tmp, ALU.mult)
            tt(kk[:], kk[:], lw, ALU.mult)
            tt(k, k, tmp, ALU.mult)
            tt(r, r, c, ALU.mult)
            for half in range(2):
                nc.vector.tensor_copy(W["whole"][:].rearrange("p (j e) n -> p e j n", e=2)[:, half],
                                      c[64 * half:64 * half + 64, :, CHUNK - 1::CHUNK])

        @block.scalar
        def _(act):
            act.wait_ge(mixed, 2)
            nc.scalar.activation(zm[0:64, 6, :], zm[0:64, 6, :], ACT.Tanh).then_inc(squashed, 1)
            nc.scalar.activation(zm[:, 7, :], zm[:, 7, :], ACT.Sigmoid).then_inc(squashed, 1)
            act.wait_ge(mixed, 8)
            for n, (out, name) in enumerate(((lw, "rwkv_w0_2"), (a, "rwkv_a0_2"))):
                act.wait_ge(projected, n + 1)
                for j in range(2):
                    nc.scalar.activation(out[:, j, :], banks(4 * n)[:, j, :], ACT.Sigmoid, bias=K.vec(name, j)).then_inc(gated, 1)
            act.wait_ge(projected, 3)
            for j in range(2):
                nc.scalar.activation(W["g"][:, j, :], banks(0)[:, j, :], ACT.Copy).then_inc(gated, 1)
            act.wait_ge(summed, 1)
            nc.scalar.activation(tmp, banks(4), ACT.Sqrt).then_inc(rooted, 1)
            act.wait_ge(cumulated, 1)
            nc.scalar.activation(lw, lw, ACT.Exp).then_inc(exped, 1)
            act.wait_ge(summed, 2)
            nc.scalar.activation(tmp, c, ACT.Exp, scale=-1.0).then_inc(exped, 1)
            act.drain()
            nc.scalar.activation(c, c, ACT.Exp).then_inc(exped, 1)


def rwkv_solve(K, W, solve, scratch):
    nc = K.nc
    H = 4
    staged, shifted, scored, kept, cut, m_saved, m_loaded, solved, t_saved, cleared, t_loaded = (K.sem(f"rm_{n}") for n in
        ("staged", "shifted", "scored", "kept", "cut", "m_saved", "m_loaded", "solved", "t_saved", "cleared", "t_loaded"))
    with ExitStack() as scope, nc.Block() as block:
        ks = K.sb(scope, "rm_kk", [64, 2, H, P])
        bs = K.sb(scope, "rm_b", [64, 2, H, P])
        masked = K.sb(scope, "rm_masked", [P, H, P])
        minus = K.sb(scope, "rm_minus", [P, NT, H, CHUNK])
        rows = K.sb(scope, "rm_rows", [P, CHUNK, CHUNK])
        prod = K.sb(scope, "rm_prod", [P, CHUNK, CHUNK])
        inv = K.sb(scope, "rm_inv", [P, CHUNK, CHUNK])

        @block.gpsimd
        def _(pool):
            with pool.Fori(0, NT // 2) as i:
                for x in range(2):
                    pool.wait_ge(scored, i * 2 + (x + 1))
                    for dst, src in ((ks, W["kk"]), (bs, W["b"])):
                        nc.gpsimd.tensor_copy(dst[:, x, 0::2, :], src[0:64, :, bass.ds((i * 2 + x) * P, P)]).then_inc(staged, 1)

        @block.tensor
        def _(pe):
            pe.sem_inc(scored, 2)
            with pe.Fori(0, NT // 2) as i:
                for x in range(2):
                    pe.wait_ge(staged, i * 4 + 2 * (x + 1))
                    pe.wait_ge(shifted, i * 4 + 2 * (x + 1))
                    pe.wait_ge(kept, i * 2 + (x + 1))
                    for h in range(H):
                        mm = nc.tensor.matmul(K.ps[:, x, h * P:(h + 1) * P], ks[:, x, h, :], bs[:, x, h, :], start=True, stop=True)
                    mm.then_inc(scored, 1)

        @block.vector
        def _(dve):
            dve.sem_inc(kept, 2)
            nc.vector.memset(solve[:], 0.0).then_inc(cleared, 1)
            below = K.const("chunk_below").unsqueeze(1).to_broadcast([P, H, P])
            with dve.Fori(0, NT // 2) as i:
                for x in range(2):
                    dve.wait_ge(scored, i * 2 + (x + 1))
                    for dst, src in ((ks, W["kk"]), (bs, W["b"])):
                        nc.vector.tensor_copy(dst[:, x, 1::2, :], src[64:P, :, bass.ds((i * 2 + x) * P, P)]).then_inc(shifted, 1)
                for x in range(2):
                    dve.wait_ge(scored, i * 2 + (x + 3))
                    nc.vector.scalar_tensor_tensor(masked[:], K.ps[:, x, :].rearrange("p (h n) -> p h n", h=H), -1.0, below,
                                                   ALU.mult, ALU.mult).then_inc(kept, 1)
                    dve.drain()
                    nc.vector.tensor_reduce(minus[:, i * 2 + x], masked[:].rearrange("p h (c s) -> p h s c", s=CHUNK), AX, ALU.add)
                    dve.drain()
            dve.sem_inc(cut, 1)
            nc.vector.memset(inv[:], 0.0)
            dve.drain()
            nc.vector.memset(inv[:].rearrange("p u t -> p (u t)")[:, 0::CHUNK + 1], 1.0)
            dve.wait_ge(m_loaded, 16)
            for t in range(1, CHUNK):
                dve.drain()
                nc.vector.tensor_tensor(prod[:, 0:t, 0:t], rows[:, t, 0:t].unsqueeze(1).to_broadcast([P, t, t]),
                                        inv[:, 0:t, 0:t], ALU.mult)
                dve.drain()
                nc.vector.tensor_reduce(inv[:, 0:t, t], prod[:, 0:t, 0:t], AX, ALU.add)
            dve.drain()
            dve.sem_inc(solved, 1)

        @block.sync
        def _(sp):
            def pieces(ap):
                return ap.rearrange("(i c h) t s -> i c t h s", i=NT, h=H)

            sp.wait_ge(cut, 1)
            for i in range(NT):
                for q in range(4):
                    sp.dma_start(pieces(scratch["minus"])[i, q], minus[q * CHUNK:(q + 1) * CHUNK, i]).then_inc(m_saved, 16)
            sp.wait_ge(m_saved, 16 * 4 * NT)
            sp.dma_start(rows[:], scratch["minus"]).then_inc(m_loaded, 16)
            sp.wait_ge(solved, 1)
            sp.dma_start(scratch["inverse"], inv[:]).then_inc(t_saved, 16)
            sp.wait_ge(cleared, 1)
            sp.wait_ge(t_saved, 16)
            for i in range(NT):
                for q in range(4):
                    sp.dma_start(solve[q * CHUNK:(q + 1) * CHUNK, H * i:H * i + H, q * CHUNK:(q + 1) * CHUNK],
                                 pieces(scratch["inverse"])[i, q]).then_inc(t_loaded, 16)
            sp.wait_ge(t_loaded, 16 * 4 * NT)


def rwkv_chunks(K, zm, W, solve, y):
    nc = K.nc
    H, N = 4, 64
    (staged, shifted, turned, tokens_kept, scored, masked, crossed, x_kept, solved, uw_kept, moved, queried, h_kept, g_kept, q_kept,
     stepped, s_kept, y_ready, y_kept, tiles_begun, steps_begun, summed, own_kept) = (K.sem(f"rs_{n}") for n in
        ("staged", "shifted", "turned", "tokens_kept", "scored", "masked", "crossed", "x_kept", "solved", "uw_kept", "moved", "queried",
         "h_kept", "g_kept", "q_kept", "stepped", "s_kept", "y_ready", "y_kept", "tiles_begun", "steps_begun",
         "summed", "own_kept"))
    with ExitStack() as scope, nc.Block() as block:
        sb = lambda name, shape: K.sb(scope, f"rs_{name}", shape)
        feat = sb("feat", [N, 5, H, P])
        inv = sb("inv", [P, H, P])
        bk = sb("bk", [P, 2, H, N])
        vt = sb("vt", [P, H, N])
        xk = sb("xk", [P, H, 2 * N])
        uw = sb("uw", [P, H, 2 * N])
        m2, n1, n2 = sb("m2", [P, H, P]), sb("n1", [P, H, P]), sb("n2", [P, H, P])
        grow = sb("grow", [N, 4, H, N])
        add = sb("add", [N, 4, H, N])
        q = sb("q", [N, H, P])
        own = sb("own", [N, H, P])
        state = sb("state", [N, 2, H, N])
        sources = (W["b"], zm[:, 2:4, :], zm[:, 4:6, :], W["kk"], zm[:, 0:2, :])
        COPIES = len(sources)

        def heads(bank, n):
            return K.ps[:, bank, 0:H * n].rearrange("p (h n) -> p h n", h=H)

        def chunk_rows(g):
            return slice(g * CHUNK, (g + 1) * CHUNK)

        @block.gpsimd
        def _(pool):
            with pool.Fori(0, NT) as i:
                pool.wait_ge(y_ready, i + 1)
                for s, src in enumerate(sources):
                    nc.gpsimd.tensor_copy(feat[:, s, 0::2, :], src[0:64, :, bass.ds(i * P, P)]).then_inc(staged, 1)
                nc.gpsimd.tensor_copy(inv[:], solve[:, bass.ds(i * H, H), :]).then_inc(staged, 1)

        @block.tensor
        def _(pe):
            mm = nc.tensor.matmul
            pe.sem_inc(y_ready, 1)
            b, k, v, kk, r = (feat[:, s] for s in range(5))
            with pe.Fori(0, NT) as i:
                pe.wait_ge(staged, i * (COPIES + 1) + (COPIES + 1))
                pe.wait_ge(shifted, i * COPIES + COPIES)
                pe.sem_inc(tiles_begun, 1)
                for n, src in enumerate((b, k, v, kk)):
                    for h in range(H):
                        last = nc.tensor.transpose(K.ps[:, n // 2, (n % 2) * RW + h * N:(n % 2) * RW + (h + 1) * N],
                                                   src[:, h, :], K.const("ident")[0:N, 0:N])
                last.then_inc(turned, 1)
                for n, (left, right) in enumerate(((k, kk), (b, r), (k, r))):
                    for h in range(H):
                        last = mm(heads(2 + n, P)[:, h], left[:, h, :], right[:, h, :], start=True, stop=True)
                    last.then_inc(scored, 1)
                pe.wait_ge(masked, i * 3 + 1)
                pe.wait_ge(tokens_kept, i * 3 + 3)
                pe.wait_ge(y_kept, i * 2 + 2)
                for h in range(H):
                    last = mm(heads(5, N)[:, h], m2[:, h, :], vt[:, h, :], start=True, stop=True)
                last.then_inc(crossed, 1)
                pe.wait_ge(x_kept, i + 1)
                for h in range(H):
                    last = mm(heads(6, 2 * N)[:, h], inv[:, h, :], xk[:, h, :], start=True, stop=True)
                last.then_inc(solved, 1)
                pe.wait_ge(masked, i * 3 + 3)
                pe.wait_ge(uw_kept, i + 1)
                for h in range(H):
                    last = mm(heads(4, P)[0:N, h], uw[:, h, N:2 * N], n1[:, h, :], start=True, stop=True)
                last.then_inc(queried, 1)
                for g in range(4):
                    for h in range(H):
                        last = mm(heads(g, N)[0:N, h], uw[chunk_rows(g), h, N:2 * N], bk[chunk_rows(g), 0, h, :], start=True, stop=True)
                for g in range(4):
                    for h in range(H):
                        out = K.ps[0:N, g, RW + h * N:RW + (h + 1) * N]
                        mm(out, bk[chunk_rows(g), 0, h, :], uw[chunk_rows(g), h, 0:N], start=True, stop=False)
                        last = mm(out, bk[chunk_rows(g), 1, h, :], vt[chunk_rows(g), h, :], start=False, stop=True)
                last.then_inc(moved, 1)
                for h in range(H):
                    mm(heads(5, P)[0:N, h], vt[:, h, :], n2[:, h, :], start=True, stop=False)
                    last = mm(heads(5, P)[0:N, h], uw[:, h, 0:N], n1[:, h, :], start=False, stop=True)
                last.then_inc(summed, 1)
                pe.wait_ge(q_kept, i + 1)
                pe.wait_ge(g_kept, i + 1)
                pe.wait_ge(h_kept, i + 1)
                for g in range(4):
                    pe.wait_ge(s_kept, i * 4 + (g + 1))
                    pe.sem_inc(steps_begun, 1)
                    for h in range(H):
                        mm(heads(7, N)[0:N, h], grow[:, g, h, :], state[:, g % 2, h, :], start=True, stop=False)
                        last = mm(heads(7, N)[0:N, h], K.const("ident")[0:N, 0:N], add[:, g, h, :], start=False, stop=True)
                    last.then_inc(stepped, 1)
                    for h in range(H):
                        last = mm(heads(6, P)[0:N, h, chunk_rows(g)], state[:, g % 2, h, :], q[:, h, chunk_rows(g)],
                                  start=True, stop=True)
                last.then_inc(y_ready, 1)

        @block.scalar
        def _(act):
            with act.Fori(0, NT) as i:
                act.wait_ge(turned, i + 1)
                nc.scalar.activation(bk[:], K.ps[:, 0, :].rearrange("p (s h n) -> p s h n", s=2, h=H), ACT.Copy).then_inc(tokens_kept, 1)
                nc.scalar.activation(vt[:], K.ps[:, 1, 0:RW].rearrange("p (h n) -> p h n", h=H), ACT.Copy).then_inc(tokens_kept, 1)
                nc.scalar.activation(xk[:, :, N:2 * N], K.ps[:, 1, RW:2 * RW].rearrange("p (h n) -> p h n", h=H),
                                     ACT.Copy).then_inc(tokens_kept, 1)
                act.wait_ge(crossed, i + 1)
                nc.scalar.activation(xk[:, :, 0:N], heads(5, N), ACT.Copy).then_inc(x_kept, 1)
                act.wait_ge(solved, i + 1)
                nc.scalar.activation(uw[:], heads(6, 2 * N), ACT.Copy, scale=-1.0).then_inc(uw_kept, 1)
                act.wait_ge(summed, i + 1)
                nc.scalar.activation(own[:], heads(5, P)[0:N], ACT.Copy).then_inc(own_kept, 1)

        @block.vector
        def _(dve):
            tt = nc.vector.tensor_tensor
            dve.sem_inc(y_kept, 2)
            nc.vector.memset(state[:, 0], 0.0).then_inc(s_kept, 1)
            above = K.const("chunk_above").unsqueeze(1).to_broadcast([P, H, P])
            upto = K.const("chunk_upto").unsqueeze(1).to_broadcast([P, H, P])
            with dve.Fori(0, NT) as i:
                dve.wait_ge(y_ready, i + 1)
                for s, src in enumerate(sources):
                    nc.vector.tensor_copy(feat[:, s, 1::2, :], src[64:P, :, bass.ds(i * P, P)]).then_inc(shifted, 1)
                for n, (dst, mask) in enumerate(((m2, above), (n1, upto), (n2, upto))):
                    dve.wait_ge(scored, i * 3 + (n + 1))
                    tt(dst[:], heads(2 + n, P), mask, ALU.mult).then_inc(masked, 1)
                dve.wait_ge(queried, i + 1)
                tt(q[:], heads(4, P)[0:N], feat[:, 4], ALU.add).then_inc(q_kept, 1)
                dve.wait_ge(moved, i + 1)
                tt(grow[:], K.ps[0:N, 0:4, 0:RW].rearrange("p g (h n) -> p g h n", h=H),
                   K.const("ident")[0:N, 0:N].unsqueeze(1).unsqueeze(1).to_broadcast([N, 4, H, N]), ALU.add).then_inc(g_kept, 1)
                nc.vector.tensor_copy(add[:], K.ps[0:N, 0:4, RW:2 * RW].rearrange("p g (h n) -> p g h n", h=H)).then_inc(h_kept, 1)
                for g in range(4):
                    dve.wait_ge(stepped, i * 4 + (g + 1))
                    tt(state[:, (g + 1) % 2], heads(7, N)[0:N],
                       W["whole"][:, :, bass.ds(i * 4 + g, 1)].to_broadcast([N, H, N]), ALU.mult).then_inc(s_kept, 1)
                dve.wait_ge(own_kept, i + 1)
                dve.wait_ge(y_ready, i + 2)
                for half in range(2):
                    tt(y[64 * half:64 * half + 64, :, bass.ds(i * P, P)], own[:, half::2, :], heads(6, P)[0:N, half::2],
                       ALU.add).then_inc(y_kept, 1)


def rwkv_finish(K, y, W, out):
    nc = K.nc
    eps = 64e-5
    summed, centred, squared, meaned, rooted = (K.sem(f"rf_{n}") for n in ("summed", "centred", "squared", "meaned", "rooted"))
    with ExitStack() as scope, nc.Block() as block:
        sq = K.sb(scope, "rf_sq", [P, 2, S])
        var = K.sb(scope, "rf_var", [P, 2, S])

        def banks(n):
            return K.ps[:, n:n + 4, :].rearrange("p (j h) n -> p j (h n)", j=2)

        @block.tensor
        def _(pe):
            for n, src in enumerate((y, sq)):
                if n:
                    pe.wait_ge(squared, 1)
                for j in range(2):
                    for h in range(2):
                        mm = nc.tensor.matmul(K.ps[:, 4 * n + 2 * j + h, :], K.const("pair"), src[:, j, h * HALF:(h + 1) * HALF],
                                              start=True, stop=True)
                mm.then_inc(summed, 1)

        @block.vector
        def _(dve):
            stt = nc.vector.scalar_tensor_tensor
            dve.wait_ge(summed, 1)
            stt(y[:], banks(0), -1.0 / 64, y[:], ALU.mult, ALU.add).then_inc(centred, 1)
            dve.wait_ge(summed, 2)
            nc.vector.tensor_scalar(var[:], banks(4), 1.0 / 64, eps, ALU.mult, ALU.add).then_inc(meaned, 1)
            dve.wait_ge(rooted, 1)
            nc.vector.reciprocal(var[:], var[:])
            dve.drain()
            nc.vector.tensor_tensor(y[:], y[:], var[:], ALU.mult)
            dve.drain()
            for j in range(2):
                nc.vector.tensor_scalar(y[:, j, :], y[:, j, :], K.vec("rwkv_ln_w_2", j), K.vec("rwkv_ln_b_2", j), ALU.mult, ALU.add)
            dve.drain()
            nc.vector.tensor_tensor(y[:], y[:], W["bonus"][:], ALU.add)
            dve.drain()
            nc.vector.tensor_tensor(out, y[:], W["g"][:], ALU.mult)

        @block.scalar
        def _(act):
            act.wait_ge(centred, 1)
            nc.scalar.activation(sq[:], y[:], ACT.Square).then_inc(squared, 1)
            act.wait_ge(meaned, 1)
            nc.scalar.activation(var[:], var[:], ACT.Sqrt).then_inc(rooted, 1)


def rwkv(K, z, yT):
    scratch = {n: K.dram(f"rwkv_{n}", (P, CHUNK, CHUNK)) for n in ("minus", "inverse")}
    with ExitStack() as scope:
        wide = lambda name: K.sb(scope, f"rwkv_{name}", [P, 2, S])
        W = {name: wide(name) for name in ("kk", "b", "g", "bonus")}
        W["whole"] = K.sb(scope, "rwkv_whole", [64, 4, S // CHUNK])
        zm = K.sb(scope, "rwkv_zm", [P, 8, S])
        solve = K.sb(scope, "rwkv_solve", [P, 4 * NT, P])
        rwkv_gates(K, z, zm, W)
        rwkv_solve(K, W, solve, scratch)
        y = zm[:, 6:8, :]
        rwkv_chunks(K, zm, W, solve, y)
        rwkv_finish(K, y, W, yT[:, 0:2, :])


def first_block(K, hT, x):
    x_dram = K.A["x"].rearrange("o s d -> (o s) d")
    rows, results = K.dram("expert_rows", (S, D)), K.dram("expert_results", (ROWS, D))
    table = K.dram("expert_table", (ROWS, 1), I32)
    norm_and_turn(K, "n1", x, K.vec("attn_norm_g", 0, KT), hT, src=x_dram)
    with ExitStack() as scope:
        conv = K.sb(scope, "conv", [P, CT, S])
        oT = K.sb(scope, "oT", [P, HEADS, S])
        with ExitStack() as inner:
            qkv = K.sb(inner, "qkv", [P, NT, 3 * HALF])
            project_and_convolve(K, hT, conv, qkv)
            conv_norm(K, conv)
            qkT = x
            group_norm_and_turn(K, "qk", qkv[:, :, 0:2 * HALF], 4 * HEADS, K.qk_gain[:], qkT[:])
            o = qkv[:, :, 0:HALF]
            diff_attention(K, qkT, qkv, o)
            group_norm_and_turn(K, "on", o, HEADS, K.head_gain[:], oT[:])
        merged = K.sb(scope, "merged", [P, KT, S])
        merge_branches(K, hT, conv, oT, merged)
        project_and_add(K, "wo", merged, K.A["w_out"], x, x_dram)
    with ExitStack() as scope:
        logits = K.sb(scope, "logits", [P, NT, GROUPS + EXPERTS])
        weights = K.sb(scope, "weights", [P, NT, 2])
        dest = K.sb(scope, "dest", [P, 2 * NT], I32)
        expert_of_block = K.sb(scope, "expert_of_block", [P, BLOCKS], I32)
        norm_and_route(K, x, rows, logits)
        choose_experts(K, logits, weights, dest, expert_of_block, table)
        run_experts(K, rows, table, expert_of_block, results)
        combine_experts(K, x, weights, dest, results)


def mixers(K, hT, z):
    nc = K.nc
    heads = {"fox_q": RW, "fox_k": RW, "swa_q": RW, "swa_k": RW, "mlstm_q": P, "mlstm_k": P, "mlstm_decay": 4, "fox_decay": 4}
    R = {name: K.dram(name, (n, S)) for name, n in heads.items()}
    R["band"] = K.dram("window_band", (4, 3 * P))
    with ExitStack() as scope:
        sb = lambda name, shape: K.sb(scope, name, shape)
        K.window_bias, K.sinks = sb("window_bias", [P, 4, 2 * P]), sb("sinks", [P, 4])
        K.mlstm_rise = sb("mlstm_rise", [P, 4 * NT])
        Z = {"rwkv": z, "mlstm_o": sb("mlstm_o", [P, 2, S]), "values": sb("values", [P, NT, 3 * RW])}
        with ExitStack() as inner:
            for name, tiles in (("fox_q", 2), ("fox_k", 2), ("swa_q", 2), ("swa_k", 1)):
                Z[name] = K.sb(inner, f"z_{name}", [P, tiles, S])
            Z["mlstm"] = K.sb(inner, "z_mlstm", [P, 2, 3 + S])
            Z["gates"] = K.sb(inner, "z_gates", [4, 3, S])
            with nc.Block() as block:

                @block.vector
                def _(dve):
                    nc.vector.memset(z[:, :, 0:1], 0.0)
                    nc.vector.memset(Z["mlstm"][:, :, 0:3], 0.0)

            project_mixers(K, hT, mixer_slabs(Z))
            prepare_mixers(K, Z, R)
        o = sb("o_soft", [P, NT, 2 * RW])
        o_mlstm = sb("o_mlstm", [P, NT, RW])
        values = Z["values"]
        attend(K, "fx", "fox", HD, R["fox_q"], R["fox_k"], R["fox_decay"], values, RW, o, RW)
        attend(K, "sw", "swa", HD, R["swa_q"], R["swa_k"], None, values, 2 * RW, o, 0)
        attend(K, "ml", "mlstm", 32, R["mlstm_q"], R["mlstm_k"], R["mlstm_decay"], values, 0, o_mlstm, 0)
        turn(K, "tm", o, hT[:, 4:8, :])
        group_norm_and_turn(K, "mn", o_mlstm[:], 4, K.vec("mlstm_norm_2", 0, 2), hT[:, 2:4, :], gate=Z["mlstm_o"][:])
    K.recycle()
    rwkv(K, z, hT)


def build(nc, A, out):
    with ExitStack() as ctx:
        K = Kernel(nc, A, out, ctx)
        load_vectors(K)
        x_kept = K.dram("x_kept", (S, D))
        hT = K.sb(ctx, "hT", [P, KT, S])
        with ExitStack() as scope:
            x = K.sb(scope, "x_first", [P, NT, D])
            first_block(K, hT, x)
            K.recycle()
            norm_and_turn(K, "n3", x, K.vec("norm_mix_pre_2", 0, KT), hT, keep=x_kept)
        with ExitStack() as scope:
            z = K.sb(scope, "z_rwkv", [P, 8, 1 + S])
            mixers(K, hT, z)
        with ExitStack() as scope:
            x = K.sb(scope, "x_second", [P, NT, D])
            project_norm_add(K, "o2", hT, KT, A["w_out_2"], A["norm_mix_post_2"], x, src=x_kept)
            f = K.sb(scope, "f", [P, FFT, S])
            norm_and_turn(K, "n4", x, K.vec("norm_ffn_pre_2", 0, KT), hT)
            ffn_up(K, hT, f)
            project_norm_add(K, "fd", f, FFT, A["ffn_w_down_2"], A["norm_ffn_post_2"], x, out=out, y=hT)


_INS = ["x", "attn_norm_g", "w_in", "conv_dw_w", "conv_dw_b", "conv_ln_g", "conv_ln_b", "w_conv_out", "q_norm_g", "k_norm_g",
        "lambda_q1", "lambda_k1", "lambda_q2", "lambda_k2", "subln_g", "w_attn_out", "w_out", "ffn_norm_g", "w_router_group",
        "b_router_group", "w_router_expert", "b_router_expert", "w_gate_e", "w_up_e", "w_down_e", "w_in_2", "w_out_2",
        "norm_mix_pre_2", "norm_mix_post_2", "norm_ffn_pre_2", "norm_ffn_post_2", "rwkv_mu_2", "rwkv_w0_2", "rwkv_w_up_2",
        "rwkv_a0_2", "rwkv_a_up_2", "rwkv_g_up_2", "rwkv_k_k_2", "rwkv_k_a_2", "rwkv_r_k_2", "rwkv_ln_w_2", "rwkv_ln_b_2",
        "mlstm_conv_w_2", "mlstm_conv_b_2", "mlstm_b_i_2", "mlstm_b_f_2", "mlstm_norm_2", "swa_sinks_2", "fox_b_f_2", "rel_bias_2",
        "ffn_w_up_2", "ffn_conv_w_2", "ffn_conv_b_2", "ffn_w_down_2"]


def kernel(**inputs):
    import concourse.bacc as bacc
    from concourse.bass_utils import run_bass_kernel_spmd

    nc = bacc.Bacc("TRN2", target_bir_lowering=False, num_devices=1)
    arrays, A = {}, {}
    given = {name: np.ascontiguousarray(inputs[name]) for name in _INS}
    given["shape_consts"] = shape_constants()[0]
    for name, a in given.items():
        arrays[f"in_{name}_dram"] = a
        A[name] = nc.dram_tensor(f"in_{name}_dram", a.shape, mybir.dt.from_np(a.dtype), kind="ExternalInput").ap()
    out = nc.dram_tensor("out_0_dram", (1, S, D), F32, kind="ExternalOutput").ap()
    build(nc, A, out.rearrange("o s d -> (o s) d"))
    r = run_bass_kernel_spmd(nc, [arrays], core_ids=[0])
    return r.results[0]["out_0_dram"]
```

```python
import math
from contextlib import ExitStack

import numpy as np

import concourse.bass as bass
from concourse import mybir

F32 = mybir.dt.float32
F32R = mybir.dt.float32r
I32 = mybir.dt.int32
U32 = mybir.dt.uint32
ACT = mybir.ActivationFunctionType
ALU = mybir.AluOpType
AX = mybir.AxisListType.X

P = 128
S = 1024
D = 1024
NT = S // P
KT = D // P
HALF = 512
EPS = 1e-6
NEG = -1e30

CONV_CH, TAPS = 512, 31
CT = CONV_CH // P
HEADS, HD, VD = 4, 64, 128
LAM_INIT = 0.8 - 0.6 * math.exp(0.0)
GROUPS, EPG = 4, 8
EXPERTS = GROUPS * EPG
DE = 512
FT = DE // P
ROWS = 2 * S + EXPERTS * P
BLOCKS = ROWS // P
COL_QKV, COL_GATE = 1024, 2560

RW = 256
CHUNK = 32
ML0, SW0, FX0, N_IN = 1024, 1800, 2312, 3084
WINDOW = 128
DFF = 2816
FFT = DFF // P


def shape_constants():
    p, j = np.arange(P)[:, None], np.arange(P)[None, :]
    same = (p // CHUNK) == (j // CHUNK)
    parts = {
        "ident": p == j,
        "flip": p == P - 1 - j,
        "ones": np.ones((P, P)),
        "pair": (p // 64) == (j // 64),
        "before": p < j,
        "causal": np.where(j <= p, 0.0, NEG),
        "causal_t": np.where(p <= j, 0.0, NEG),
        "chunk_below": same & (j < p),
        "chunk_above": same & (p < j),
        "chunk_upto": same & (p <= j),
        "block_start": np.broadcast_to(np.arange(BLOCKS) * P, (P, BLOCKS)),
        "rank4": np.broadcast_to(np.arange(GROUPS, 0, -1), (P, GROUPS)),
        "rank8": np.broadcast_to(np.arange(EPG, 0, -1), (P, EPG)),
        "token": np.arange(NT)[None, :] * P + p,
    }
    dist = 255 - np.arange(3 * P)
    d = np.maximum(np.clip(dist, 0, WINDOW - 1), 1).astype(np.float32)
    large = 16 + (np.log(d / 16) / math.log(128 / 16) * 16).astype(np.int32)
    bucket = np.where(np.clip(dist, 0, WINDOW - 1) < 16, np.clip(dist, 0, WINDOW - 1), np.minimum(large, 31))
    inside = (dist >= 0) & (dist < WINDOW)
    onehot = np.zeros((P, 3 * P))
    onehot[:32] = (np.arange(32)[:, None] == bucket[None, :]) & inside[None, :]
    parts["bucket"] = onehot
    parts["outside"] = np.broadcast_to(np.where(inside, 0.0, NEG), (P, 3 * P))
    for_mixers = ("flip", "pair", "chunk_below", "chunk_above", "chunk_upto", "bucket", "outside")
    tables, places = {}, {}
    for table, names in (("shape_consts", [n for n in parts if n not in for_mixers]), ("mixer_consts", for_mixers)):
        off = 0
        for name in names:
            places[name] = (table, off, off + parts[name].shape[1])
            off += parts[name].shape[1]
        tables[table] = np.ascontiguousarray(
            np.concatenate([np.broadcast_to(parts[n], (P, parts[n].shape[1])).astype(np.float32) for n in names], 1))
    return tables, places


CONST_PLACES = shape_constants()[1]

VECTORS = [
    ("conv_dw_w", TAPS * CT),
    ("attn_norm_g", KT), ("ffn_norm_g", KT), ("norm_mix_pre_2", KT), ("norm_ffn_pre_2", KT),
    ("conv_dw_b", CT), ("conv_ln_g", CT), ("conv_ln_b", CT), ("subln_g", 1), ("q_norm_g", 1), ("k_norm_g", 1),
    ("rwkv_mu_2", 8), ("rwkv_w0_2", 2), ("rwkv_a0_2", 2), ("rwkv_k_k_2", 2), ("rwkv_k_a_2", 2), ("rwkv_r_k_2", 2),
    ("rwkv_ln_w_2", 2), ("rwkv_ln_b_2", 2), ("mlstm_conv_w_2", 8), ("mlstm_conv_b_2", 2), ("mlstm_norm_2", 2),
    ("ffn_conv_w_2", 3 * FFT), ("ffn_conv_b_2", FFT),
]


def vector_places():
    places, tile, row = {}, 0, 0
    for name, n in VECTORS:
        if row + n > P:
            tile, row = tile + 1, 0
        places[name] = (tile, row, n)
        row += n
    return places, tile + 1


class Kernel:

    def __init__(self, nc, A, out, ctx):
        self.nc, self.A, self.out, self.ctx = nc, A, out, ctx
        self.ps = ctx.enter_context(nc.psum_tensor("banks", [P, 8, HALF], F32))
        self.sems = []
        self.tables = {}

    def sem(self, name):
        self.sems.append(self.nc.alloc_semaphore(name))
        return self.sems[-1]

    def recycle(self):
        self.nc.clear_and_free_semaphores(self.sems)
        self.nc.all_engine_barrier()
        self.sems = []

    def sb(self, scope, name, shape, dt=F32, side=None):
        return scope.enter_context(self.nc.sbuf_tensor(name, shape, dt, side=side))

    def dram(self, name, shape, dt=F32):
        return self.nc.dram_tensor(name, shape, dt).ap()

    def const(self, name):
        table, a, b = CONST_PLACES[name]
        return self.tables[table][:, a:b]

    def vec(self, name, j=0, n=1):
        tile, row, _ = self.vplaces[name]
        return self.vectors[:, tile * P + row + j:tile * P + row + j + n]


def rows_of(ap):
    return ap.rearrange("o (r p) -> (o r) p", p=P)


def load_vectors(K):
    nc, A = K.nc, K.A
    K.tables["shape_consts"] = K.sb(K.ctx, "consts", [P, A["shape_consts"].shape[1]])
    K.vplaces, tiles = vector_places()
    K.vectors = K.sb(K.ctx, "vectors", [P, tiles * P])
    K.lam = K.sb(K.ctx, "minus_lambda", [P, 1])
    K.qk_gain = K.sb(K.ctx, "qk_gain", [P, 2 * HEADS])
    K.head_gain = K.sb(K.ctx, "head_gain", [P, HEADS])
    K.ident_r, K.causal_r, K.causal_t_r = (K.sb(K.ctx, f"{name}_r", [P, P], F32R) for name in ("ident", "causal", "causal_t"))
    zeroed, landed, const_landed = K.sem("rows_zeroed"), K.sem("rows_landed"), K.sem("const_landed")
    turned, lam_landed, lam_dot, lam_exp = K.sem("rows_turned"), K.sem("lam_landed"), K.sem("lam_dot"), K.sem("lam_exp")
    loads = 0
    with ExitStack() as scope, nc.Block() as block:
        rows = K.sb(scope, "vector_rows", [P, tiles, P])
        lam4 = K.sb(scope, "lam_vectors", [P, 4, HD])
        prod = K.sb(scope, "lam_products", [P, 2, HD])
        dots = K.sb(scope, "lam_dots", [P, 2])
        exps = K.sb(scope, "lam_exps", [P, 2])
        sources = []
        for name, n in VECTORS:
            tile, row, _ = K.vplaces[name]
            src = A[name]
            if name in ("q_norm_g", "k_norm_g"):
                sources += [(rows[row:row + 1, tile, 0:HD], src), (rows[row:row + 1, tile, HD:P], src)]
            elif len(src.shape) == 3 and name != "rwkv_r_k_2":
                sources.append((rows[row:row + n, tile, :], src.rearrange("o w (r p) -> (o w r) p", p=P)))
            elif name == "rwkv_r_k_2":
                sources.append((rows[row:row + n, tile, :], src.rearrange("o (r g) n -> (o r) (g n)", g=2)))
            else:
                sources.append((rows[row:row + n, tile, :], rows_of(src)))

        @block.sync
        def _(sp):
            sp.dma_start(K.tables["shape_consts"][:], A["shape_consts"]).then_inc(const_landed, 16)
            for j, name in enumerate(("lambda_q1", "lambda_q2", "lambda_k1", "lambda_k2")):
                sp.dma_start(lam4[:, j, :], A[name].to_broadcast([P, HD])).then_inc(lam_landed, 16)
            sp.wait_ge(zeroed, 1)
            for dst, src in sources:
                sp.dma_start(dst, src).then_inc(landed, 16)

        @block.tensor
        def _(pe):
            pe.wait_ge(const_landed, 16)
            pe.wait_ge(landed, 16 * len(sources))
            for t in range(tiles):
                mm = nc.tensor.transpose(K.ps[:, 0, t * P:(t + 1) * P], rows[:, t, :], K.const("ident"))
            mm.then_inc(turned, 1)

        @block.vector
        def _(dve):
            nc.vector.memset(rows[:], 0.0).then_inc(zeroed, 1)
            dve.wait_ge(lam_landed, 64)
            nc.vector.tensor_tensor(prod[:], lam4[:, 0:2, :], lam4[:, 2:4, :], ALU.mult)
            dve.drain()
            nc.vector.tensor_reduce(dots[:], prod[:], AX, ALU.add).then_inc(lam_dot, 1)
            dve.wait_ge(lam_exp, 1)
            nc.vector.tensor_scalar(K.lam[:], exps[:, 1:2], exps[:, 0:1], -LAM_INIT, ALU.subtract, ALU.add)
            dve.wait_ge(turned, 1)
            nc.vector.tensor_copy(K.vectors[:], K.ps[:, 0, 0:tiles * P])
            dve.drain()
            for h in range(HEADS):
                nc.vector.tensor_copy(K.qk_gain[:, h:h + 1], K.vec("q_norm_g"))
                nc.vector.tensor_copy(K.qk_gain[:, HEADS + h:HEADS + h + 1], K.vec("k_norm_g"))
                nc.vector.tensor_scalar(K.head_gain[:, h:h + 1], K.vec("subln_g"), 1.0 - LAM_INIT, None, ALU.mult)

        @block.scalar
        def _(act):
            act.wait_ge(const_landed, 16)
            for dst, name in ((K.ident_r, "ident"), (K.causal_r, "causal"), (K.causal_t_r, "causal_t")):
                nc.scalar.activation(dst[:], K.const(name), ACT.Copy)
            act.wait_ge(lam_dot, 1)
            nc.scalar.activation(exps[:], dots[:], ACT.Exp).then_inc(lam_exp, 1)


def norm_and_turn(K, tag, x, gain, hi, lo, room, src=None, keep=None):
    nc = K.nc
    landed = [K.sem(f"{tag}_x_landed{h}") for h in range(2)]
    squared, meaned, rooted, rated, begun = (K.sem(f"{tag}_{n}") for n in ("squared", "meaned", "rooted", "rated", "begun"))
    scaled, turned, gained, rounded = (K.sem(f"{tag}_{n}") for n in ("scaled", "turned", "gained", "rounded"))
    with ExitStack() as scope, nc.Block() as block:
        junk = K.sb(scope, f"{tag}_junk", [P, D])
        ss = K.sb(scope, f"{tag}_ss", [P, NT])
        rstd = K.sb(scope, f"{tag}_rstd", [P, NT])
        xn = K.sb(scope, f"{tag}_xn", [P, 2, D])
        whole = room.rearrange("p (b k n) -> p b k n", b=2, k=KT)

        if src is not None:
            @block.sync
            def _(sp):
                for h in range(2):
                    sp.dma_start(x[:, 4 * h:4 * h + 4, :],
                                 src.rearrange("(t p) d -> p t d", p=P)[:, 4 * h:4 * h + 4, :]).then_inc(landed[h], 16)

        if keep is not None:
            x_kept = K.sem(f"{tag}_x_kept")

            @block.sync
            def _(sp):
                sp.dma_start(keep.rearrange("(t p) d -> p t d", p=P), x[:]).then_inc(x_kept, 16)
                sp.wait_ge(x_kept, 16)

        @block.scalar
        def _(act):
            if src is not None:
                for h in range(2):
                    act.wait_ge(landed[h], 16)
            with act.Fori(0, NT) as t:
                nc.scalar.activation(junk[:], x[:, t, :], ACT.Square, accum_out=ss[:, bass.ds(t, 1)])
                act.drain()
            act.sem_inc(squared, 1)
            act.wait_ge(meaned, 1)
            nc.scalar.activation(rstd[:], ss[:], ACT.Sqrt).then_inc(rooted, 1)
            act.wait_ge(rated, 1)

            def scale(t, b):
                act.wait_ge(turned, t + 1)
                act.sem_inc(begun, 1)
                nc.scalar.activation(xn[:, b, :], x[:, t, :], ACT.Copy, scale=rstd[:, bass.ds(t, 1)]).then_inc(scaled, 1)

            def round_off(t, b):
                act.wait_ge(gained, t + 3)
                act.sem_inc(begun, 1)
                nc.scalar.activation(hi[:, :, bass.ds(t * P, P)], whole[:, b], ACT.Copy).then_inc(rounded, 1)

            for b in range(2):
                scale(b, b)
            with act.Fori(0, NT // 2 - 1) as i:
                for b in range(2):
                    round_off(i * 2 + b, b)
                    scale(i * 2 + (b + 2), b)
            for b in range(2):
                round_off(NT - 2 + b, b)

        @block.vector
        def _(dve):
            def times_gain(t, b):
                dve.wait_ge(turned, t + 3)
                nc.vector.tensor_tensor(whole[:, b], K.ps[:, 2 * b:2 * b + 2, :].rearrange("p c (k n) -> p (c k) n", n=P),
                                        gain.unsqueeze(2).to_broadcast([P, KT, P]), ALU.mult).then_inc(gained, 1)

            def rest(t, b):
                tokens = bass.ds(t * P, P)
                dve.wait_ge(rounded, t + 1)
                nc.vector.tensor_tensor(lo[:, :, tokens], whole[:, b], hi[:, :, tokens].bitcast(F32), ALU.subtract)
                dve.drain()

            dve.sem_inc(gained, 2)
            dve.wait_ge(squared, 1)
            nc.vector.tensor_scalar(ss[:], ss[:], 1.0 / D, EPS, ALU.mult, ALU.add).then_inc(meaned, 1)
            dve.wait_ge(rooted, 1)
            nc.vector.reciprocal(rstd[:], rstd[:]).then_inc(rated, 1)
            times_gain(0, 0)
            with dve.Fori(0, NT // 2 - 1) as i:
                for b in range(2):
                    times_gain(i * 2 + (b + 1), 1 - b)
                    rest(i * 2 + b, b)
            times_gain(NT - 1, 1)
            for b in range(2):
                rest(NT - 2 + b, b)

        @block.tensor
        def _(pe):
            pe.sem_inc(turned, 2)
            with pe.Fori(0, NT // 2) as i:
                for b in range(2):
                    pe.wait_ge(scaled, i * 2 + (b + 1))
                    pe.wait_ge(gained, i * 2 + (b + 1))
                    for k in range(KT):
                        mm = nc.tensor.transpose(K.ps[:, 2 * b + k // 4, (k % 4) * P:(k % 4 + 1) * P],
                                                 xn[:, b, k * P:(k + 1) * P], K.const("ident"))
                    mm.then_inc(turned, 1)


def project_columns(K, tag, weight, h_hi, h_lo, units, slabs, gates=None, vector=None):
    nc = K.nc
    U, C = len(units), KT * len(slabs)
    w_in = weight.rearrange("o (k p) n -> p (o k) n", p=P)
    widths = [max(at + n for _, n, at in pieces) for pieces, _ in slabs]
    landed = [K.sem(f"{tag}_landed{b}") for b in range(2)]
    rounded, split, projected, chunked, kept, gates_kept = (K.sem(f"{tag}_{n}") for n in
        ("rounded", "split", "projected", "chunked", "kept", "gates_kept"))
    with ExitStack() as scope, nc.Block() as block:
        w = K.sb(scope, f"{tag}_w", [P, 2, KT * P])
        w_hi = K.sb(scope, f"{tag}_w_hi", [P, 2, KT * P], F32R)
        w_lo = K.sb(scope, f"{tag}_w_lo", [P, 2, KT * P], F32R)
        sizes = [KT * P] * U + [m for m in widths for _ in range(KT)]
        pieces_of = [pieces for pieces, *_ in units] + [pieces for pieces, _ in slabs for _ in range(KT)]

        @block.sync
        def _(sp):
            for n, pieces in enumerate(pieces_of):
                if n >= 2:
                    sp.wait_ge(split, n - 1)
                for col, m, at in pieces:
                    if n < U:
                        sp.dma_start(w[:, n % 2].rearrange("p (k n) -> p k n", k=KT)[:, :, at:at + m], w_in[:, :, col:col + m],
                                     allow_slow_non_contiguous=True).then_inc(landed[n % 2], 16)
                    else:
                        sp.dma_start(w[:, n % 2, at:at + m], w_in[:, (n - U) % KT, col:col + m]).then_inc(landed[n % 2], 16)

        @block.tensor
        def _(pe):
            mm = nc.tensor.matmul
            with pe.Fori(0, U // 2) as i:
                for b in range(2):
                    pe.wait_ge(split, i * 2 + (b + 1))
                    for h in range(2):
                        pe.wait_ge(kept, i * 4 + (2 * b + h + 1))
                        bank, tokens = K.ps[:, 2 * b + h, :], slice(h * HALF, (h + 1) * HALF)
                        for k in range(KT):
                            cols = slice(k * P, (k + 1) * P)
                            mm(bank, w_hi[:, b, cols], h_hi[:, k, tokens], start=(k == 0), stop=False)
                            mm(bank, w_hi[:, b, cols], h_lo[:, k, tokens], start=False, stop=False)
                            last = mm(bank, w_lo[:, b, cols], h_hi[:, k, tokens], start=False, stop=(k == KT - 1))
                        last.then_inc(projected, 1)
            done = 2 * U + 4 - (2 if gates else 0)
            if gates:
                pe.wait_ge(gates_kept, 2)
            for s, m in enumerate(widths):
                for k in range(KT):
                    n = U + s * KT + k
                    pe.wait_ge(split, n + 1)
                    for t in range(NT):
                        if k == 0:
                            pe.wait_ge(kept, done if s == 0 else done + (s - 1) * NT + t + 1)
                        bank, tokens, b = K.ps[:, t, 0:m], slice(t * P, (t + 1) * P), n % 2
                        mm(bank, h_hi[:, k, tokens], w_hi[:, b, 0:m], start=(k == 0), stop=False)
                        mm(bank, h_hi[:, k, tokens], w_lo[:, b, 0:m], start=False, stop=False)
                        last = mm(bank, h_lo[:, k, tokens], w_hi[:, b, 0:m], start=False, stop=(k == KT - 1))
                        if t == NT - 1:
                            last.then_inc(chunked, 1)
                        elif k == KT - 1:
                            last.then_inc(projected, 1)

        @block.scalar
        def _(act):
            act.sem_inc(kept, 4)
            loads = [0, 0]

            def fill(n):
                if n >= U + C:
                    return
                loads[n % 2] += 16 * len(pieces_of[n])
                act.wait_ge(landed[n % 2], loads[n % 2])
                nc.scalar.activation(w_hi[:, n % 2, 0:sizes[n]], w[:, n % 2, 0:sizes[n]], ACT.Copy).then_inc(rounded, 1)

            fill(0)
            fill(1)
            for u, (_, out, scale, func, wait) in enumerate(units):
                if wait is not None:
                    act.wait_ge(*wait)
                for h in range(2):
                    act.wait_ge(projected, 2 * u + h + 1)
                    if not (gates and u == U - 1):
                        nc.scalar.activation(out(h), K.ps[:, 2 * (u % 2) + h, :], func, scale=scale).then_inc(kept, 1)
                fill(u + 2)
            for s, (_, out) in enumerate(slabs):
                for k in range(KT):
                    n = s * KT + k
                    if k < KT - 1:
                        act.wait_ge(chunked, n + 1)
                        fill(U + n + 2)
                for t in range(NT):
                    if t < NT - 1:
                        act.wait_ge(projected, 2 * U + s * (NT - 1) + t + 1)
                    else:
                        act.wait_ge(chunked, (s + 1) * KT)
                    nc.scalar.activation(out(t), K.ps[:, t, 0:widths[s]], ACT.Copy).then_inc(kept, 1)
                fill(U + s * KT + KT + 1)

        @block.gpsimd
        def _(pool):
            for n, m in enumerate(sizes):
                pool.wait_ge(rounded, n + 1)
                nc.gpsimd.tensor_tensor(w_lo[:, n % 2, 0:m], w[:, n % 2, 0:m], w_hi[:, n % 2, 0:m].bitcast(F32), ALU.subtract) \
                    .then_inc(split, 1)

        @block.vector
        def _(dve):
            if gates:
                for h in range(2):
                    dve.wait_ge(projected, 2 * (U - 1) + h + 1)
                    for g in range(3):
                        copy = nc.vector.tensor_copy(gates[:, g, h * HALF:(h + 1) * HALF], K.ps[32 * g:32 * g + 4, 2 * ((U - 1) % 2) + h, :])
                    copy.then_inc(gates_kept, 1)
            if vector is not None:
                vector(dve, kept)


def project_and_convolve(K, h_hi, h_lo, conv, qkv, room):
    nc = K.nc
    PAD = TAPS - 1
    gated = K.sem("p_gated")
    y_end = CT * (PAD + S)
    y = room[:, 0:y_end].rearrange("p (c n) -> p c n", c=CT)
    gate = room[:, y_end:y_end + 2 * S].rearrange("p (b n) -> p b n", b=2)

    def tokens(tile, lead=0):
        return lambda h: tile[:, lead + h * HALF:lead + (h + 1) * HALF]

    units = []
    for c in range(CT):
        units.append(([(c * P, P, 0)], tokens(y[:, c, :], PAD), 1.0, ACT.Copy, None))
        units.append(([(CONV_CH + c * P, P, 0)], tokens(gate[:, c % 2, :]), 1.0, ACT.Sigmoid,
                      (gated, c - 1) if c >= 2 else None))
    slabs = [([(COL_QKV + s * HALF, HALF, 0)], lambda t, s=s: qkv[:, t, s * HALF:(s + 1) * HALF]) for s in range(3)]

    def convolve(dve, kept):
        nc.vector.memset(y[:, :, 0:PAD], 0.0)
        for c in range(CT):
            dve.wait_ge(kept, 4 * c + 8)
            nc.vector.tensor_tensor(y[:, c, PAD:PAD + S], y[:, c, PAD:PAD + S], gate[:, c % 2, :], ALU.mult).then_inc(gated, 1)
            dve.drain()
            tap = lambda j: K.vec("conv_dw_w", j * CT + c)
            nc.vector.tensor_scalar(conv[:, c, :], y[:, c, 0:S], tap(0), K.vec("conv_dw_b", c), ALU.mult, ALU.add)
            for j in range(1, TAPS):
                dve.drain()
                nc.vector.scalar_tensor_tensor(conv[:, c, :], y[:, c, j:j + S], tap(j), conv[:, c, :], ALU.mult, ALU.add)
        dve.drain()

    project_columns(K, "p", K.A["w_in"], h_hi, h_lo, units, slabs, vector=convolve)


def conv_norm(K, conv):
    nc = K.nc
    summed, centred, squared, varied, rooted, ready = (K.sem(f"cn_{n}") for n in
        ("summed", "centred", "squared", "varied", "rooted", "ready"))
    whitened = K.sem("cn_whitened")
    with ExitStack() as scope, nc.Block() as block:
        sq = K.sb(scope, "cn_sq", [P, CT, S])
        rstd = K.sb(scope, "cn_rstd", [P, S])

        def halves(bank):
            return K.ps[:, bank:bank + 2, :].rearrange("p b n -> p (b n)")

        @block.tensor
        def _(pe):
            for h in range(2):
                for c in range(CT):
                    mm = nc.tensor.matmul(K.ps[:, h, :], K.const("ones"), conv[:, c, h * HALF:(h + 1) * HALF],
                                          start=(c == 0), stop=(c == CT - 1))
            mm.then_inc(summed, 1)
            for h in range(2):
                for c in range(CT):
                    pe.wait_ge(squared, c + 1)
                    mm = nc.tensor.matmul(K.ps[:, 2 + h, :], K.const("ones"), sq[:, c, h * HALF:(h + 1) * HALF],
                                          start=(c == 0), stop=(c == CT - 1))
            mm.then_inc(varied, 1)

        @block.vector
        def _(dve):
            dve.wait_ge(summed, 1)
            for c in range(CT):
                nc.vector.scalar_tensor_tensor(conv[:, c, :], halves(0), -1.0 / CONV_CH, conv[:, c, :],
                                               ALU.mult, ALU.add).then_inc(centred, 1)
            dve.wait_ge(varied, 1)
            nc.vector.tensor_scalar(rstd[:], halves(2), 1.0 / CONV_CH, EPS, ALU.mult, ALU.add).then_inc(ready, 1)
            dve.wait_ge(rooted, 1)
            nc.vector.reciprocal(rstd[:], rstd[:])
            dve.drain()
            for c in range(CT):
                nc.vector.tensor_tensor(conv[:, c, :], conv[:, c, :], rstd[:], ALU.mult).then_inc(whitened, 1)

        @block.scalar
        def _(act):
            for c in range(CT):
                act.wait_ge(centred, c + 1)
                nc.scalar.activation(sq[:, c, :], conv[:, c, :], ACT.Square).then_inc(squared, 1)
            act.wait_ge(ready, 1)
            nc.scalar.activation(rstd[:], rstd[:], ACT.Sqrt).then_inc(rooted, 1)
            for c in range(CT):
                act.wait_ge(whitened, c + 1)
                nc.scalar.activation(conv[:, c, :], conv[:, c, :], ACT.Silu,
                                     scale=K.vec("conv_ln_g", c), bias=K.vec("conv_ln_b", c))


def group_norm_and_turn(K, tag, src, groups, gain, dst, gate=None):
    nc = K.nc
    width = src.shape[2]
    size, tiles = width // groups, width // P
    squared, summed, meaned, rooted, scaled, turned, kept = (K.sem(f"{tag}_{n}") for n in
        ("squared", "summed", "meaned", "rooted", "scaled", "turned", "kept"))
    with ExitStack() as scope, nc.Block() as block:
        sq = K.sb(scope, f"{tag}_sq", [P, 2, width])
        ss = K.sb(scope, f"{tag}_ss", [P, NT, groups])
        rstd = K.sb(scope, f"{tag}_rstd", [P, NT, groups])
        xn = K.sb(scope, f"{tag}_xn", [P, 2, width])

        @block.scalar
        def _(act):
            with act.Fori(0, NT // 2) as i:
                for b in range(2):
                    act.wait_ge(summed, i * 2 + (b + 1))
                    nc.scalar.activation(sq[:, b, :], src[:, i * 2 + b, :], ACT.Square).then_inc(squared, 1)
            act.wait_ge(meaned, 1)
            nc.scalar.activation(rstd[:], ss[:], ACT.Sqrt).then_inc(rooted, 1)

        @block.vector
        def _(dve):
            dve.sem_inc(kept, 2)
            dve.sem_inc(summed, 2)
            with dve.Fori(0, NT // 2) as i:
                for b in range(2):
                    dve.wait_ge(squared, i * 2 + (b + 1))
                    nc.vector.tensor_reduce(ss[:, i * 2 + b, :], sq[:, b, :].rearrange("p (g n) -> p g n", g=groups),
                                            AX, ALU.add).then_inc(summed, 1)
            dve.drain()
            nc.vector.tensor_scalar(ss[:], ss[:], 1.0 / size, EPS, ALU.mult, ALU.add).then_inc(meaned, 1)
            dve.wait_ge(rooted, 1)
            nc.vector.reciprocal(rstd[:], rstd[:])
            dve.drain()
            with dve.Fori(0, NT // 2) as i:
                for b in range(2):
                    dve.wait_ge(turned, i * 2 + (b + 1))
                    nc.vector.tensor_tensor(
                        xn[:, b, :].rearrange("p (g n) -> p g n", g=groups),
                        src[:, bass.ds(i * 2 + b, 1), :].rearrange("p o (g n) -> p (o g) n", g=groups),
                        rstd[:, bass.ds(i * 2 + b, 1), :].rearrange("p o g -> p (o g)").unsqueeze(2)
                        .to_broadcast([P, groups, size]), ALU.mult).then_inc(scaled, 1)
                for b in range(2):
                    dve.wait_ge(turned, i * 2 + (b + 3))
                    nc.vector.tensor_tensor(
                        dst[:, :, bass.ds((i * 2 + b) * P, P)],
                        K.ps[:, 2 * b:2 * b + 2, :].rearrange("p c (k n) -> p (c k) n", n=P)[:, 0:tiles, :],
                        gain.unsqueeze(2).to_broadcast([P, tiles, P]), ALU.mult).then_inc(kept, 1)
            if gate is not None:
                dve.drain()
                nc.vector.tensor_tensor(dst, dst, gate, ALU.mult)

        @block.tensor
        def _(pe):
            pe.sem_inc(turned, 2)
            with pe.Fori(0, NT // 2) as i:
                for b in range(2):
                    pe.wait_ge(scaled, i * 2 + (b + 1))
                    pe.wait_ge(kept, i * 2 + (b + 1))
                    for k in range(tiles):
                        mm = nc.tensor.transpose(K.ps[:, 2 * b + k // 4, (k % 4) * P:(k % 4 + 1) * P],
                                                 xn[:, b, k * P:(k + 1) * P], K.const("ident"))
                    mm.then_inc(turned, 1)


def part_rows(K, tag, jobs):
    nc = K.nc
    rounded, split = K.sem(f"{tag}_rounded"), K.sem(f"{tag}_split")
    stored = [K.sem(f"{tag}_stored{b}") for b in range(2)]
    with ExitStack() as scope, nc.Block() as block:
        hi = K.sb(scope, f"{tag}_hi", [P, 2, S], F32R)
        lo = K.sb(scope, f"{tag}_lo", [P, 2, S], F32R)

        @block.scalar
        def _(act):
            for n, (src, _, _) in enumerate(jobs):
                if n >= 2:
                    act.wait_ge(stored[n % 2], 32 * (n // 2))
                nc.scalar.activation(hi[0:src.shape[0], n % 2, :], src, ACT.Copy).then_inc(rounded, 1)

        @block.vector
        def _(dve):
            for n, (src, _, _) in enumerate(jobs):
                m = src.shape[0]
                dve.wait_ge(rounded, n + 1)
                nc.vector.tensor_tensor(lo[0:m, n % 2, :], src, hi[0:m, n % 2, :].bitcast(F32), ALU.subtract).then_inc(split, 1)

        @block.sync
        def _(sp):
            for n, (src, to_hi, to_lo) in enumerate(jobs):
                sp.wait_ge(split, n + 1)
                sp.dma_start(to_hi, hi[0:src.shape[0], n % 2, :].bitcast(F32)).then_inc(stored[n % 2], 16)
                sp.dma_start(to_lo, lo[0:src.shape[0], n % 2, :].bitcast(F32)).then_inc(stored[n % 2], 16)
            for b in range(2):
                sp.wait_ge(stored[b], 32 * ((len(jobs) + 1 - b) // 2))


CHUNKS = [(half, j, max(half * HALF, j * P), (half + 1) * HALF - max(half * HALF, j * P))
          for half in range(2) for j in range(4 * (half + 1))]


def soft_attention(K, tag, maps, R, values, v_col, dv, o, o_col, scale, decay, paired, room=None):
    nc = K.nc
    MAX_ROW, EXTRA = 96, 64
    ROWS_2 = MAX_ROW + 1
    seen = EXTRA + (2 if decay else 0)
    loaded = [K.sem(f"{tag}_loaded{b}") for b in range(2)]
    filled, staged, scored, peaked, lowered, m_turned, m_kept, t_scored, exped, weighed, stored, begun, fetching = (K.sem(f"{tag}_{n}") for n in
        ("filled", "staged", "scored", "peaked", "lowered", "m_turned", "m_kept", "t_scored", "exped", "weighed", "stored", "begun", "fetching"))
    loads = 16 * (7 if decay else 6)
    NC = len(CHUNKS)
    with ExitStack() as scope, nc.Block() as block:
        q1 = K.sb(scope, f"{tag}_q1", [P, 2, S], F32R)
        k1 = K.sb(scope, f"{tag}_k1", [P, 2, S], F32R)
        q2 = K.sb(scope, f"{tag}_q2", [P, 2, S], F32R)
        k2 = K.sb(scope, f"{tag}_k2", [P, 2, S], F32R)
        if room is None:
            room = K.sb(scope, f"{tag}_weights", [P, 12 * HALF])[:]
        weights = [room[:, 4 * h * HALF:(4 + 8 * h) * HALF].rearrange("p (j n) -> p j n", n=HALF) for h in range(2)]
        vs = K.sb(scope, f"{tag}_v", [P, 1 if paired else 2, NT, dv + 1])
        peak = K.sb(scope, f"{tag}_peak", [P, 2, NT])
        low = K.sb(scope, f"{tag}_low", [P, 2, NT], F32R)
        share = K.sb(scope, f"{tag}_share", [P, 2])

        def head(i, x):
            return i if paired else i * 2 + x

        def score_bank(t):
            return K.ps[:, 2 * (t % 2):2 * (t % 2) + 2, :].rearrange("p b n -> p (b n)")

        @block.gpsimd
        def _(pool):
            def load(i, x):
                row = pool.snap((i * 2 + x) * HD)
                line = pool.snap(i * 2 + x)
                pool.wait_ge(t_scored, i * (2 * NC) + (NC * x + NC))
                pool.sem_inc(fetching, 1)
                for dst, name in ((q1[0:HD], "q_hi"), (q1[HD:P], "q_lo"), (k1[0:HD], "k_hi"), (k1[HD:P], "k_hi"),
                                  (q2[0:HD], "q_hi"), (k2[0:HD], "k_lo")):
                    pool.dma_start(dst[:, x, :], R[name][bass.ds(row, HD), :]).then_inc(loaded[x], 16)
                if decay:
                    pool.dma_start(k2[EXTRA:EXTRA + 2, x, :], R["decay"][bass.ds(line, 1)].rearrange("o c s -> (o c) s")) \
                        .then_inc(loaded[x], 16)

            pool.wait_ge(filled, 1)
            with pool.Fori(0, maps // 2) as i:
                for x in range(2):
                    load(i, x)
                for x in range(1 if paired else 2):
                    pool.wait_ge(weighed, i * 16 + (16 if paired else 8 * x + 8))
                    nc.gpsimd.tensor_copy(vs[:, x, :, 0:dv], values[:, :, bass.ds(head(i, x) * dv + v_col, dv)]).then_inc(staged, 1)

        @block.tensor
        def _(pe):
            mm = nc.tensor.matmul
            pe.sem_inc(weighed, 16)
            pe.sem_inc(t_scored, 2 * NC)

            def scores(i, x):
                pe.wait_ge(loaded[x], i * loads + loads)
                for t in range(NT):
                    pe.wait_ge(peaked, i * 16 + (8 * x + t + 1))
                    pe.sem_inc(begun, 1)
                    n, queries = (t + 1) * P, slice(t * P, (t + 1) * P)
                    for b in range(0, n, HALF):
                        keys = slice(b, min(b + HALF, n))
                        mm(score_bank(t)[:, keys], q1[:, x, queries], k1[:, x, keys], start=True, stop=False)
                        mm(score_bank(t)[:, keys], q2[0:seen, x, queries], k2[0:seen, x, keys], start=False, stop=(keys.stop < n))
                    mm(score_bank(t)[:, n - P:n], K.ident_r[:], K.causal_r[:], start=False, stop=True).then_inc(scored, 1)

            def maxima(i, x):
                pe.wait_ge(lowered, i * 2 + (x + 1))
                pe.sem_inc(begun, 1)
                for t in range(NT):
                    last = mm(score_bank(0)[0:1, t * P:(t + 1) * P], low[:, x, t:t + 1], K.ident_r[:], start=True, stop=True)
                last.then_inc(m_turned, 1)

            def turned_scores(i, x, half):
                if half == 0:
                    pe.wait_ge(m_kept, i * 2 + (x + 1))
                for c, (part, j, q0, n) in enumerate(CHUNKS):
                    if part != half:
                        continue
                    pe.wait_ge(exped, i * (2 * NC) + (NC * x + c + 1))
                    bank, keys = K.ps[:, 4 + c % 2, 0:n], slice(j * P, (j + 1) * P)
                    crossing = q0 == j * P
                    mm(bank, k1[:, x, keys], q1[:, x, q0:q0 + n], start=True, stop=False)
                    last = mm(bank, k2[0:ROWS_2, x, keys], q2[0:ROWS_2, x, q0:q0 + n], start=False, stop=not crossing)
                    if crossing:
                        last = mm(bank[:, 0:P], K.ident_r[:], K.causal_t_r[:], start=False, stop=True)
                    last.then_inc(t_scored, 1)

            def weigh(i, x, half):
                if half == 0 and not (paired and x):
                    pe.wait_ge(staged, i + 1 if paired else i * 2 + (x + 1))
                for t in range(4 * half, 4 * half + 4):
                    c = CHUNKS.index((half, t, t * P, (half + 1) * HALF - t * P))
                    pe.wait_ge(exped, i * (2 * NC) + (NC * x + c + 3))
                    pe.wait_ge(stored, i * 16 + (8 * x + t + 1))
                    for j in range(t + 1):
                        last = mm(K.ps[:, 6 + t % 2, 0:dv + 1], weights[half][:, j, (t - 4 * half) * P:(t - 4 * half + 1) * P],
                                  vs[:, 0 if paired else x, j, :], start=(j == 0), stop=(j == t))
                    last.then_inc(weighed, 1)

            def step(i, x, more):
                turned_scores(i, x, 0)
                if more:
                    scores(*((i, 1) if x == 0 else (i + 1, 0)))
                weigh(i, x, 0)
                turned_scores(i, x, 1)
                if more:
                    maxima(*((i, 1) if x == 0 else (i + 1, 0)))
                weigh(i, x, 1)

            scores(0, 0)
            maxima(0, 0)
            with pe.Fori(0, maps // 2 - 1) as i:
                for x in range(2):
                    step(i, x, True)
            step(maps // 2 - 1, 0, True)
            step(maps // 2 - 1, 1, False)

        @block.scalar
        def _(act):
            act.sem_inc(exped, 2)
            with act.Fori(0, maps // 2) as i:
                for x in range(2):
                    for c, (half, j, q0, n) in enumerate(CHUNKS):
                        act.wait_ge(t_scored, i * (2 * NC) + (NC * x + c + 2 * NC + 1))
                        nc.scalar.activation(weights[half][:, j, HALF - n:HALF], K.ps[:, 4 + c % 2, 0:n], ACT.Exp, scale=scale) \
                            .then_inc(exped, 1)

        @block.vector
        def _(dve):
            for dst, first, end, value in ((q2, EXTRA, MAX_ROW, 1.0), (k2, EXTRA, MAX_ROW, 0.0), (k2, MAX_ROW, ROWS_2, 1.0)):
                ones = K.const("ones")[first:end, 0:1].unsqueeze(2).to_broadcast([end - first, 2, S])
                nc.vector.tensor_scalar(dst[first:end], ones, value, None, ALU.mult)
            nc.vector.memset(vs[:, :, :, dv:dv + 1], 1.0)
            dve.drain()
            dve.sem_inc(filled, 1)
            dve.sem_inc(peaked, 2)
            dve.sem_inc(stored, 2)

            def peaks(i, x):
                for t in range(NT):
                    dve.wait_ge(scored, i * 16 + (8 * x + t + 1))
                    nc.vector.tensor_reduce(peak[:, x, t:t + 1], score_bank(t)[:, 0:(t + 1) * P], AX, ALU.max).then_inc(peaked, 1)
                dve.drain()
                nc.vector.tensor_scalar(low[:, x, :], peak[:, x, :], -1.0, None, ALU.mult).then_inc(lowered, 1)

            def keep_maxima(i, x):
                dve.wait_ge(m_turned, i * 2 + (x + 1))
                nc.vector.tensor_copy(q2[MAX_ROW:ROWS_2, x, :], score_bank(0)[0:1, :]).then_inc(m_kept, 1)

            def finish(i, x, half):
                for t in range(4 * half, 4 * half + 4):
                    y, part = K.ps[:, 6 + t % 2, 0:dv], share[:, t % 2:t % 2 + 1]
                    place = o[:, t, bass.ds(head(i, x) * dv + o_col, dv)]
                    dve.wait_ge(weighed, i * 16 + (8 * x + t + 17))
                    nc.vector.reciprocal(part, K.ps[:, 6 + t % 2, dv:dv + 1])
                    dve.drain()
                    if paired and x:
                        nc.vector.tensor_scalar(part, part, K.lam[:], None, ALU.mult)
                        dve.drain()
                        nc.vector.scalar_tensor_tensor(place, y, part, place, ALU.mult, ALU.add).then_inc(stored, 1)
                    else:
                        nc.vector.tensor_scalar(place, y, part, None, ALU.mult).then_inc(stored, 1)

            def step(i, x, more):
                ahead = (i, 1) if x == 0 else (i + 1, 0)
                if more:
                    peaks(*ahead)
                finish(i, x, 0)
                if more:
                    keep_maxima(*ahead)
                finish(i, x, 1)

            peaks(0, 0)
            keep_maxima(0, 0)
            with dve.Fori(0, maps // 2 - 1) as i:
                for x in range(2):
                    step(i, x, True)
            step(maps // 2 - 1, 0, True)
            step(maps // 2 - 1, 1, False)
            dve.drain()


def merge_branches(K, h_hi, h_lo, conv, oT, merged):
    nc, A = K.nc, K.A
    w_in = A["w_in"].rearrange("o (k p) n -> p (o k) n", p=P)
    branches = [(A["w_conv_out"].rearrange("o (k p) n -> p (o k) n", p=P), conv, 0, CT),
                (A["w_attn_out"].rearrange("o (k p) n -> p (o k) n", p=P), oT, CT, HEADS)]
    landed = [K.sem(f"m_landed{b}") for b in range(2)]
    b_landed = [K.sem(f"m_b_landed{b}") for b in range(2)]
    rounded, split, projected, gate_done, opened, joined = (K.sem(f"m_{n}") for n in
        ("rounded", "split", "projected", "gate_done", "opened", "joined"))
    tiles = D // P
    with ExitStack() as scope, nc.Block() as block:
        w = K.sb(scope, "m_w", [P, 2, KT, P])
        w_hi = K.sb(scope, "m_w_hi", [P, 2, KT, P], F32R)
        w_lo = K.sb(scope, "m_w_lo", [P, 2, KT, P], F32R)
        wb = K.sb(scope, "m_wb", [P, 2, CT + HEADS, P])
        gates = K.sb(scope, "m_gates", [P, 2, 2, HALF])

        @block.sync
        def _(sp):
            for c in range(tiles):
                for g in range(2):
                    if c:
                        sp.wait_ge(split, 2 * c + g - 1)
                    col = COL_GATE + g * D + c * P
                    sp.dma_start(w[:, g], w_in[:, :, col:col + P]).then_inc(landed[g], 16)
                if c >= 2:
                    sp.wait_ge(projected, 2 * (c - 1))
                for src, _, k0, kn in branches:
                    sp.dma_start(wb[:, c % 2, k0:k0 + kn], src[:, :, c * P:(c + 1) * P]).then_inc(b_landed[c % 2], 16)

        @block.tensor
        def _(pe):
            mm = nc.tensor.matmul
            with pe.Fori(0, tiles // 2) as i:
                for b in range(2):
                    for g in range(2):
                        pe.wait_ge(split, i * 4 + (2 * b + g + 1))
                        for h in range(2):
                            if g == 0:
                                pe.wait_ge(joined, i * 4 + (2 * b + h + 1))
                            bank, tokens = K.ps[:, 4 * h + g, :], slice(h * HALF, (h + 1) * HALF)
                            for k in range(KT):
                                mm(bank, w_hi[:, g, k, :], h_hi[:, k, tokens], start=(k == 0), stop=False)
                                mm(bank, w_hi[:, g, k, :], h_lo[:, k, tokens], start=False, stop=False)
                                last = mm(bank, w_lo[:, g, k, :], h_hi[:, k, tokens], start=False, stop=(k == KT - 1))
                        last.then_inc(gate_done, 1)
                    pe.wait_ge(b_landed[b], i * 32 + 32)
                    for h in range(2):
                        for n, (_, src, k0, kn) in enumerate(branches):
                            for k in range(kn):
                                last = mm(K.ps[:, 4 * h + 2 + n, :], wb[:, b, k0 + k, :], src[:, k, h * HALF:(h + 1) * HALF],
                                          start=(k == 0), stop=(k == kn - 1))
                        last.then_inc(projected, 1)

        @block.scalar
        def _(act):
            def fill(c, g):
                act.wait_ge(landed[g], c * 16 + 16)
                nc.scalar.activation(w_hi[:, g], w[:, g], ACT.Copy).then_inc(rounded, 1)

            def step(c, more):
                for g in range(2):
                    if more:
                        act.wait_ge(gate_done, c * 2 + (g + 1))
                        fill(c + 1, g)
                for h in range(2):
                    act.wait_ge(joined, c * 2 + (h + 1))
                    act.wait_ge(projected, c * 2 + (h + 1))
                    nc.scalar.activation(gates[:, h], K.ps[:, 4 * h:4 * h + 2, :], ACT.Sigmoid).then_inc(opened, 1)

            for g in range(2):
                fill(0, g)
            with act.Fori(0, tiles - 1) as c:
                step(c, True)
            step(tiles - 1, False)

        @block.vector
        def _(dve):
            def fill(n, g):
                dve.wait_ge(rounded, n + 1)
                nc.vector.tensor_tensor(w_lo[:, g], w[:, g], w_hi[:, g].bitcast(F32), ALU.subtract).then_inc(split, 1)

            def step(c, more):
                for g in range(2):
                    if more:
                        fill(c * 2 + (g + 2), g)
                for h in range(2):
                    dve.wait_ge(opened, c * 2 + (h + 1))
                    nc.vector.tensor_tensor(gates[:, h], gates[:, h], K.ps[:, 4 * h + 2:4 * h + 4, :], ALU.mult)
                    dve.drain()
                    nc.vector.tensor_tensor(merged[:, c, h * HALF:(h + 1) * HALF], gates[:, h, 0, :], gates[:, h, 1, :],
                                            ALU.add).then_inc(joined, 1)

            dve.sem_inc(joined, 2)
            for g in range(2):
                fill(g, g)
            with dve.Fori(0, tiles - 1) as c:
                step(c, True)
            step(tiles - 1, False)


def norm_and_route(K, x, rows, logits):
    nc, A = K.nc, K.A
    NL = GROUPS + EXPERTS
    squared, meaned, rooted, scaled, turned, kept, routed, biased = (K.sem(f"r_{n}") for n in
        ("squared", "meaned", "rooted", "scaled", "turned", "kept", "routed", "biased"))
    landed = K.sem("r_landed")
    stored = [K.sem(f"r_stored{b}") for b in range(2)]
    with ExitStack() as scope, nc.Block() as block:
        gain = K.sb(scope, "r_gain", [P, D])
        wr = K.sb(scope, "r_w", [P, KT, NL])
        bias = K.sb(scope, "r_bias", [P, NL])
        junk = K.sb(scope, "r_junk", [P, D])
        ss = K.sb(scope, "r_ss", [P, NT])
        h2 = K.sb(scope, "r_h2", [P, 2, D])
        h2T = K.sb(scope, "r_h2T", [P, 2, KT, P])

        @block.sync
        def _(sp):
            sp.dma_start(gain[:], A["ffn_norm_g"].to_broadcast([P, D])).then_inc(landed, 16)
            sp.dma_start(wr[:, :, 0:GROUPS], A["w_router_group"].rearrange("o (k p) n -> p (o k) n", p=P)).then_inc(landed, 16)
            sp.dma_start(wr[:, :, GROUPS:NL], A["w_router_expert"].rearrange("o (k p) n -> p (o k) n", p=P)).then_inc(landed, 16)
            sp.dma_start(bias[:, 0:GROUPS], A["b_router_group"].to_broadcast([P, GROUPS])).then_inc(landed, 16)
            sp.dma_start(bias[:, GROUPS:NL], A["b_router_expert"].to_broadcast([P, EXPERTS])).then_inc(landed, 16)
            for t in range(NT):
                sp.wait_ge(scaled, t + 1)
                sp.dma_start(rows[t * P:(t + 1) * P, :], h2[:, t % 2, :]).then_inc(stored[t % 2], 16)
            for b in range(2):
                sp.wait_ge(stored[b], 16 * (NT // 2 + 1))

        @block.scalar
        def _(act):
            with act.Fori(0, NT) as t:
                nc.scalar.activation(junk[:], x[:, t, :], ACT.Square, accum_out=ss[:, bass.ds(t, 1)])
                act.drain()
            act.sem_inc(squared, 1)
            act.wait_ge(meaned, 1)
            nc.scalar.activation(ss[:], ss[:], ACT.Sqrt).then_inc(rooted, 1)
            with act.Fori(0, NT // 2) as i:
                for b in range(2):
                    act.wait_ge(turned, i * 2 + (b + 3))
                    act.wait_ge(routed, i * 2 + (b + 1))
                    nc.scalar.activation(h2T[:, b], K.ps[:, 2 * b:2 * b + 2, :].rearrange("p c (k n) -> p (c k) n", n=P),
                                         ACT.Copy).then_inc(kept, 1)

        @block.vector
        def _(dve):
            dve.sem_inc(stored[0], 16)
            dve.sem_inc(stored[1], 16)
            dve.sem_inc(biased, 2)
            dve.wait_ge(squared, 1)
            nc.vector.tensor_scalar(ss[:], ss[:], 1.0 / D, EPS, ALU.mult, ALU.add).then_inc(meaned, 1)
            dve.wait_ge(rooted, 1)
            nc.vector.reciprocal(ss[:], ss[:])
            dve.drain()
            dve.wait_ge(landed, 80)
            with dve.Fori(0, NT // 2) as i:
                for b in range(2):
                    dve.wait_ge(turned, i * 2 + (b + 1))
                    dve.wait_ge(stored[b], i * 16 + 16)
                    nc.vector.scalar_tensor_tensor(h2[:, b, :], x[:, i * 2 + b, :], ss[:, bass.ds(i * 2 + b, 1)], gain[:],
                                                   ALU.mult, ALU.mult).then_inc(scaled, 1)
                for b in range(2):
                    dve.wait_ge(routed, i * 2 + (b + 3))
                    nc.vector.tensor_tensor(logits[:, i * 2 + b, :], K.ps[:, 4 + b, 0:NL], bias[:], ALU.add) \
                        .then_inc(biased, 1)

        @block.tensor
        def _(pe):
            pe.sem_inc(turned, 2)
            pe.sem_inc(routed, 2)
            pe.wait_ge(landed, 80)
            with pe.Fori(0, NT // 2) as i:
                for b in range(2):
                    pe.wait_ge(scaled, i * 2 + (b + 1))
                    pe.wait_ge(biased, i * 2 + (b + 1))
                    for k in range(KT):
                        mm = nc.tensor.transpose(K.ps[:, 2 * b + k // 4, (k % 4) * P:(k % 4 + 1) * P],
                                                 h2[:, b, k * P:(k + 1) * P], K.const("ident"))
                    mm.then_inc(turned, 1)
                for b in range(2):
                    pe.wait_ge(kept, i * 2 + (b + 1))
                    for k in range(KT):
                        mm = nc.tensor.matmul(K.ps[:, 4 + b, 0:NL], h2T[:, b, k, :], wr[:, k, :],
                                              start=(k == 0), stop=(k == KT - 1))
                    mm.then_inc(routed, 1)


class ExpertWeights:

    def __init__(self, K, scope):
        sb = lambda name, shape: K.sb(scope, f"e_{name}", [P, 2, *shape])
        self.K, self.gate, self.up, self.down = K, sb("wg", [KT, DE]), sb("wu", [KT, DE]), sb("wd", [FT, D])
        self.gate_landed, self.up_landed, self.down_landed = (
            [K.sem(f"e_{n}_landed{b}") for b in range(2)] for n in ("gate", "up", "down"))

    def load(self, sp, expert_of_block, n, b, opened=None, closed=None):
        def part(dst, name, landed):
            sp.dma_start(dst[:, b], self.K.A[name][0][bass.ds(e, 1)].rearrange("e (k p) n -> p (e k) n", p=P)).then_inc(landed[b], 16)

        e = sp.value_load(expert_of_block[0:1, bass.ds(n, 1)], min_val=0, max_val=EXPERTS - 1)
        if opened is not None:
            sp.wait_ge(*opened)
        part(self.gate, "w_gate_e", self.gate_landed)
        part(self.up, "w_up_e", self.up_landed)
        if closed is not None:
            sp.wait_ge(*closed)
        part(self.down, "w_down_e", self.down_landed)


def clear_results(K, results, nothing, cleared):
    nc = K.nc
    sure = 2 * S // P
    zeroed = K.sem("e_zeroed")
    with nc.Block() as block:

        @block.vector
        def _(dve):
            nc.vector.memset(nothing[:], 0.0).then_inc(zeroed, 1)

        @block.sync
        def _(sp):
            sp.wait_ge(zeroed, 1)
            width = nothing.shape[1]
            sp.dma_start(results[sure * P:ROWS].rearrange("(p b) (c d) -> p (b c) d", p=P, d=width),
                         nothing[:].unsqueeze(1).to_broadcast([P, (BLOCKS - sure) * D // width, width])).then_inc(cleared, 16)


def choose_experts(K, logits, weights, dest, expert_of_block, pairs, table, experts):
    nc = K.nc
    owned = K.sem("c_owned")
    exped, peaked, chosen, counted, placed, zeroed, cleared, scattered = (K.sem(f"c_{n}") for n in
        ("exped", "peaked", "chosen", "counted", "placed", "zeroed", "cleared", "scattered"))
    with ExitStack() as scope, nc.Block() as block:
        sb = lambda name, shape, dt=F32: K.sb(scope, f"c_{name}", shape, dt)
        gpeak, gexp, gmass = sb("gpeak", [P, NT]), sb("gexp", [P, NT, GROUPS]), sb("gmass", [P, NT])
        ghot, g_pick = sb("ghot", [P, NT, GROUPS]), sb("g_pick", [P, NT])
        mine, part = sb("mine", [P, NT, EPG]), sb("part", [P, NT, EPG])
        top = sb("top", [P, 2, NT])
        hot = sb("hot", [P, 2, NT, EPG])
        hot32 = sb("hot32", [P, 2, NT, EXPERTS])
        both = sb("both", [P, NT, EXPERTS])
        gap, share = sb("gap", [P, NT]), sb("share", [P, NT])
        count_i, padded = sb("count_i", [P, EXPERTS], I32), sb("padded", [P, EXPERTS])
        ends, begins, ones = sb("ends", [P, EXPERTS]), sb("begins", [P, EXPERTS]), sb("ones", [P, EXPERTS])
        place, dest_f = sb("place", [P, NT, EXPERTS]), sb("dest_f", [P, NT, 2])
        behind, owner = sb("behind", [P, BLOCKS, EXPERTS]), sb("owner", [P, BLOCKS])
        tokens, zeros = sb("tokens", [P, NT], I32), sb("zeros", [P, BLOCKS], I32)

        def wide(ap, n):
            return ap.unsqueeze(2).to_broadcast([P, ap.shape[1], n])

        def rows(ap):
            return ap.unsqueeze(1).to_broadcast([P, NT, ap.shape[1]])

        @block.vector
        def _(dve):
            tt, ts = nc.vector.tensor_tensor, nc.vector.tensor_scalar

            def first_of(equal, rank, pick, out):
                tt(equal, equal, rows(rank), ALU.mult)
                dve.drain()
                nc.vector.tensor_reduce(pick, equal, AX, ALU.max)
                dve.drain()
                tt(out, rows(rank), wide(pick, rank.shape[1]), ALU.is_equal)
                dve.drain()

            nc.vector.memset(zeros[:], 0).then_inc(zeroed, 1)
            nc.vector.memset(ones[:], 1.0)
            nc.vector.tensor_copy(tokens[:], K.const("token"))
            g = logits[:, :, 0:GROUPS]
            nc.vector.tensor_reduce(gpeak[:], g, AX, ALU.max)
            dve.drain()
            tt(gexp[:], g, wide(gpeak[:], GROUPS), ALU.subtract).then_inc(peaked, 1)
            tt(ghot[:], g, wide(gpeak[:], GROUPS), ALU.is_equal)
            dve.drain()
            first_of(ghot[:], K.const("rank4"), g_pick[:], ghot[:])
            for j in range(GROUPS):
                e = logits[:, :, GROUPS + j * EPG:GROUPS + (j + 1) * EPG]
                tt(part[:] if j else mine[:], e, wide(ghot[:, :, j], EPG), ALU.mult)
                dve.drain()
                if j:
                    tt(mine[:], mine[:], part[:], ALU.add)
                    dve.drain()
            for c in range(2):
                nc.vector.tensor_reduce(top[:, c, :], mine[:], AX, ALU.max)
                dve.drain()
                tt(part[:], mine[:], wide(top[:, c, :], EPG), ALU.is_equal)
                dve.drain()
                first_of(part[:], K.const("rank8"), g_pick[:], hot[:, c])
                if c == 0:
                    nc.vector.scalar_tensor_tensor(mine[:], hot[:, 0], 4 * NEG, mine[:], ALU.mult, ALU.add)
                    dve.drain()
            for c in range(2):
                for j in range(GROUPS):
                    tt(hot32[:, c, :, j * EPG:(j + 1) * EPG], hot[:, c], wide(ghot[:, :, j], EPG), ALU.mult)
            dve.drain()
            tt(both[:], hot32[:, 0], hot32[:, 1], ALU.add).then_inc(chosen, 1)
            tt(gap[:], top[:, 1, :], top[:, 0, :], ALU.subtract).then_inc(peaked, 1)
            dve.wait_ge(exped, 2)
            nc.vector.tensor_reduce(gmass[:], gexp[:], AX, ALU.add)
            ts(share[:], gap[:], 1.0, None, ALU.add)
            dve.drain()
            tt(share[:], share[:], gmass[:], ALU.mult)
            dve.drain()
            nc.vector.reciprocal(share[:], share[:])
            dve.drain()
            nc.vector.tensor_copy(weights[:, :, 0], share[:])
            tt(weights[:, :, 1], share[:], gap[:], ALU.mult)
            dve.wait_ge(counted, 1)
            ts(count_i[:], K.ps[:, 0, NT * EXPERTS:(NT + 1) * EXPERTS], float(P - 1), None, ALU.add)
            dve.drain()
            ts(count_i[:], count_i[:], 7, 7, ALU.logical_shift_right, ALU.logical_shift_left)
            dve.drain()
            nc.vector.tensor_copy(padded[:], count_i[:])
            dve.drain()
            nc.vector.tensor_tensor_scan(ends[:], ones[:], padded[:], 0.0, ALU.mult, ALU.add)
            dve.drain()
            tt(begins[:], ends[:], padded[:], ALU.subtract)
            dve.drain()
            tt(place[:], K.ps[:, 0, 0:NT * EXPERTS].rearrange("p (t e) -> p t e", e=EXPERTS), rows(begins[:]), ALU.add)
            dve.drain()
            for c in range(2):
                tt(both[:], place[:], hot32[:, c], ALU.mult)
                dve.drain()
                nc.vector.tensor_reduce(dest_f[:, :, c], both[:], AX, ALU.add)
                dve.drain()
            nc.vector.tensor_copy(dest[:], dest_f[:].rearrange("p t c -> p (t c)")).then_inc(placed, 1)
            tt(behind[:], ends[:].unsqueeze(1).to_broadcast([P, BLOCKS, EXPERTS]), wide(K.const("block_start"), EXPERTS),
               ALU.is_le)
            dve.drain()
            nc.vector.tensor_reduce(owner[:], behind[:], AX, ALU.add)
            dve.drain()
            nc.vector.tensor_copy(count_i[:, 0:1], ends[:, EXPERTS - 1:EXPERTS])
            dve.drain()
            ts(pairs[:], count_i[:, 0:1], 2 * P - 1, None, ALU.add)
            dve.drain()
            ts(pairs[:], pairs[:], 8, None, ALU.logical_shift_right)
            ts(expert_of_block[:, 0:BLOCKS], owner[:], float(EXPERTS - 1), None, ALU.min).then_inc(owned, 1)

        @block.sync
        def _(sp):
            sp.wait_ge(owned, 1)
            experts.load(sp, expert_of_block, 0, 0)

        @block.scalar
        def _(act):
            act.wait_ge(peaked, 1)
            nc.scalar.activation(gexp[:], gexp[:], ACT.Exp).then_inc(exped, 1)
            act.wait_ge(peaked, 2)
            nc.scalar.activation(gap[:], gap[:], ACT.Exp).then_inc(exped, 1)

        @block.tensor
        def _(pe):
            pe.wait_ge(chosen, 1)
            nc.tensor.matmul(K.ps[:, 0, 0:NT * EXPERTS], K.const("before"), both[:].rearrange("p t e -> p (t e)"),
                             start=True, stop=False, skip_group_check=True)
            for j in range(NT):
                mm = nc.tensor.matmul(K.ps[:, 0, (j + 1) * EXPERTS:(NT + 1) * EXPERTS].rearrange("p (t e) -> p t e", e=EXPERTS),
                                      K.const("ones"), both[:, j, :].unsqueeze(1).to_broadcast([P, NT - j, EXPERTS]),
                                      start=False, stop=(j == NT - 1), skip_group_check=True)
            mm.then_inc(counted, 1)

        @block.gpsimd
        def _(pool):
            pool.wait_ge(zeroed, 1)
            pool.dma_start(table.rearrange("(p b) o -> p (b o)", p=P), zeros[:]).then_inc(cleared, 16)
            pool.wait_ge(cleared, 16)
            pool.wait_ge(placed, 1)
            for t in range(NT):
                for c in range(2):
                    pool.indirect_dma_start(table, bass.IndirectOffsetOnAxis(ap=dest[:, 2 * t + c:2 * t + c + 1], axis=0),
                                            tokens[:, t:t + 1], None).then_inc(scattered, 16)
            pool.wait_ge(scattered, 16 * 2 * NT)


def run_experts(K, rows, table, expert_of_block, pairs, results, experts, cleared):
    nc, A = K.nc, K.A
    gathered = [K.sem(f"e_gathered{b}") for b in range(2)]
    wg, wu, wd = experts.gate, experts.up, experts.down
    stored = [K.sem(f"e_stored{b}") for b in range(2)]
    padded, fetching, ended, gate_made = (K.sem(f"e_{n}") for n in ("padded", "fetching", "ended", "gate_made"))
    listed, picked, turned, x_kept, opened, silued, gated, mid_turned, mid_kept, closed, y_kept = (K.sem(f"e_{n}") for n in
        ("listed", "picked", "turned", "x_kept", "opened", "silued", "gated", "mid_turned", "mid_kept", "closed", "y_kept"))
    with ExitStack() as scope, nc.Block() as block:
        index = K.sb(scope, "e_index", [P, BLOCKS + 1], I32)
        pick = K.sb(scope, "e_pick", [P, 2, 1], I32)
        xb = K.sb(scope, "e_x", [P, 2, D])
        xT = K.sb(scope, "e_xT", [P, 2, KT, P])
        sg = K.sb(scope, "e_sg", [P, DE])
        mid = K.sb(scope, "e_mid", [P, DE])
        midT = K.sb(scope, "e_midT", [P, FT, P])
        y = K.sb(scope, "e_y", [P, 2, D])
        x_banks = K.ps[:, 0:2, :].rearrange("p c (k n) -> p (c k) n", n=P)
        g_bank, u_bank, mid_bank = K.ps[:, 2, :], K.ps[:, 3, :], K.ps[:, 4, :]
        y_banks = K.ps[:, 6:8, :].rearrange("p c n -> p (c n)")

        @block.gpsimd
        def _(pool):
            pool.wait_ge(listed, 16)
            pool.wait_ge(padded, 1)

            def gather(n, b):
                pool.wait_ge(turned, n + 1)
                nc.gpsimd.tensor_copy(pick[:, b, :], index[:, bass.ds(n, 1)]).then_inc(picked, 1)
                pool.wait_ge(picked, n + 1)
                pool.sem_inc(fetching, 1)
                pool.indirect_dma_start(xb[:, b, :], None, rows, bass.IndirectOffsetOnAxis(ap=pick[:, b, :], axis=0)) \
                    .then_inc(gathered[b], 16)

            gather(0, 0)
            used = pool.value_load(pairs[0:1, 0:1], min_val=1, max_val=BLOCKS // 2)
            with pool.Fori(0, BLOCKS // 2) as i:
                with pool.If(i < used):
                    for b in range(2):
                        gather(i * 2 + (b + 1), 1 - b)

        @block.sync
        def _(sp):
            used = sp.value_load(pairs[0:1, 0:1], min_val=1, max_val=BLOCKS // 2)
            sp.wait_ge(gathered[0], 16)
            with sp.Fori(0, BLOCKS // 2) as i:
                with sp.If(i < used):
                    experts.load(sp, expert_of_block, i * 2 + 1, 1, (opened, i * 2 + 2), (closed, i * 2 + 2))
                with sp.If(i + 1 < used):
                    experts.load(sp, expert_of_block, i * 2 + 2, 0, (opened, i * 2 + 3), (closed, i * 2 + 3))

        @block.tensor
        def _(pe):
            pe.sem_inc(turned, 2)
            pe.sem_inc(opened, 2)
            pe.sem_inc(closed, 2)

            def turn_x(b, half):
                for k in range(half * KT // 2, (half + 1) * KT // 2):
                    mm = nc.tensor.transpose(x_banks[:, k, :], xb[:, b, k * P:(k + 1) * P], K.const("ident"))
                return mm

            pe.wait_ge(gathered[0], 16)
            turn_x(0, 0)
            turn_x(0, 1).then_inc(turned, 1)
            used = pe.value_load(pairs[0:1, 0:1], min_val=1, max_val=BLOCKS // 2)
            with pe.Fori(0, BLOCKS // 2) as i:
                with pe.If(i < used):
                    for b in range(2):
                        n = i * 2 + b
                        pe.wait_ge(x_kept, n + 1)
                        pe.wait_ge(gated, n + 1)
                        for w, bank, landed, made in ((wg, g_bank, experts.gate_landed, gate_made), (wu, u_bank, experts.up_landed, opened)):
                            pe.wait_ge(landed[b], i * 16 + 16)
                            for k in range(KT):
                                mm = nc.tensor.matmul(bank, xT[:, b, k, :], w[:, b, k, :], start=(k == 0), stop=(k == KT - 1))
                            mm.then_inc(made, 1)
                        pe.wait_ge(gathered[1 - b], i * 16 + 16 * (b + 1))
                        turn_x(1 - b, 0)
                        pe.wait_ge(gated, n + 2)
                        pe.wait_ge(mid_kept, n + 1)
                        for k in range(FT):
                            mm = nc.tensor.transpose(mid_bank[:, k * P:(k + 1) * P], mid[:, k * P:(k + 1) * P], K.const("ident"))
                        mm.then_inc(mid_turned, 1)
                        turn_x(1 - b, 1).then_inc(turned, 1)
                        pe.wait_ge(mid_kept, n + 2)
                        pe.wait_ge(y_kept, n + 1)
                        pe.wait_ge(experts.down_landed[b], i * 16 + 16)
                        for h in range(2):
                            for k in range(FT):
                                mm = nc.tensor.matmul(K.ps[:, 6 + h, :], midT[:, k, :], wd[:, b, k, h * HALF:(h + 1) * HALF],
                                                      start=(k == 0), stop=(k == FT - 1))
                        mm.then_inc(closed, 1)

        @block.scalar
        def _(act):
            act.dma_start(index[:, 0:BLOCKS], table.rearrange("(b p) o -> p (b o)", p=P),
                          allow_slow_non_contiguous=True).then_inc(listed, 16)

            def keep_x(n, b):
                act.wait_ge(turned, n + 3)
                nc.scalar.activation(xT[:, b], x_banks, ACT.Copy).then_inc(x_kept, 1)

            keep_x(0, 0)
            act.wait_ge(cleared, 16)
            used = act.value_load(pairs[0:1, 0:1], min_val=1, max_val=BLOCKS // 2)
            with act.Fori(0, BLOCKS // 2) as i:
                with act.If(i < used):
                    for b in range(2):
                        n = i * 2 + b
                        act.wait_ge(gate_made, n + 1)
                        act.wait_ge(gated, n + 1)
                        nc.scalar.activation(sg[:], g_bank, ACT.Silu).then_inc(silued, 1)
                        keep_x(n + 1, 1 - b)
                        act.wait_ge(y_kept, n + 2)
                        act.dma_start(results[bass.ds(n * P, P), :], y[:, b, :]).then_inc(stored[b], 16)
            for b in range(2):
                act.wait_ge(stored[b], used * 16 + 16)
                act.sem_inc(ended, 1)

        @block.vector
        def _(dve):
            nc.vector.memset(index[:, BLOCKS:BLOCKS + 1], 0).then_inc(padded, 1)
            dve.sem_inc(gated, 1)
            dve.sem_inc(mid_kept, 1)
            dve.sem_inc(y_kept, 1)
            dve.sem_inc(stored[0], 16)
            dve.sem_inc(stored[1], 16)
            used = dve.value_load(pairs[0:1, 0:1], min_val=1, max_val=BLOCKS // 2)
            with dve.Fori(0, BLOCKS // 2) as i:
                with dve.If(i < used):
                    for b in range(2):
                        n = i * 2 + b
                        dve.wait_ge(silued, n + 1)
                        dve.wait_ge(opened, n + 3)
                        nc.vector.tensor_tensor(mid[:], sg[:], u_bank, ALU.mult).then_inc(gated, 1)
                        dve.wait_ge(mid_turned, n + 1)
                        nc.vector.tensor_copy(midT[:].rearrange("p k n -> p (k n)"), mid_bank).then_inc(mid_kept, 1)
                        dve.wait_ge(closed, n + 3)
                        dve.wait_ge(stored[b], i * 16 + 16)
                        nc.vector.tensor_copy(y[:, b, :], y_banks).then_inc(y_kept, 1)


def combine_experts(K, x, weights, dest, results):
    nc = K.nc
    gathered = [K.sem(f"a_gathered{t}") for t in range(NT // 2)]
    with ExitStack() as scope, nc.Block() as block:
        y = K.sb(scope, "a_y", [P, NT, 2, D])

        @block.gpsimd
        def _(pool):
            for t in range(NT):
                for c in range(2):
                    pool.indirect_dma_start(y[:, t, c, :], None, results,
                                            bass.IndirectOffsetOnAxis(ap=dest[:, 2 * t + c:2 * t + c + 1], axis=0)) \
                        .then_inc(gathered[t // 2], 16)

        @block.vector
        def _(dve):
            for t in range(NT):
                dve.wait_ge(gathered[t // 2], 64)
                for c in range(2):
                    nc.vector.scalar_tensor_tensor(x[:, t, :], y[:, t, c, :], weights[:, t, c:c + 1], x[:, t, :],
                                                   ALU.mult, ALU.add)
                    dve.drain()


def turn(K, tag, src, dst):
    nc = K.nc
    tiles = src.shape[2] // P
    turned, kept, staged = K.sem(f"{tag}_turned"), K.sem(f"{tag}_kept"), K.sem(f"{tag}_staged")
    with ExitStack() as scope, nc.Block() as block:
        stage = K.sb(scope, f"{tag}_stage", [P, 2, src.shape[2]])

        @block.vector
        def _(dve):
            with dve.Fori(0, NT // 2) as i:
                for b in range(2):
                    dve.wait_ge(turned, i * 2 + (b + 1))
                    nc.vector.tensor_copy(stage[:, b, :], src[:, i * 2 + b, :]).then_inc(staged, 1)

        @block.tensor
        def _(pe):
            pe.sem_inc(turned, 2)
            with pe.Fori(0, NT // 2) as i:
                for b in range(2):
                    pe.wait_ge(staged, i * 2 + (b + 1))
                    pe.wait_ge(kept, i * 2 + (b + 1))
                    for k in range(tiles):
                        mm = nc.tensor.transpose(K.ps[:, b, k * P:(k + 1) * P], stage[:, b, k * P:(k + 1) * P],
                                                 K.const("ident"))
                    mm.then_inc(turned, 1)

        @block.scalar
        def _(act):
            act.sem_inc(kept, 2)
            with act.Fori(0, NT // 2) as i:
                for b in range(2):
                    act.wait_ge(turned, i * 2 + (b + 3))
                    nc.scalar.activation(dst[:, :, bass.ds((i * 2 + b) * P, P)],
                                         K.ps[:, b, 0:tiles * P].rearrange("p (k n) -> p k n", n=P), ACT.Copy) \
                        .then_inc(kept, 1)


def project_and_add(K, tag, srcT, depth, weight, gain_row, x, y, src, out):
    nc = K.nc
    landed = [K.sem(f"{tag}_landed{b}") for b in range(2)]
    gain_landed, x_landed, stored = K.sem(f"{tag}_gain_landed"), K.sem(f"{tag}_x_landed"), K.sem(f"{tag}_stored")
    rounded, split, chunked, projected, squared, kept, meaned, rooted, added = (K.sem(f"{tag}_{n}") for n in
        ("rounded", "split", "chunked", "projected", "squared", "kept", "meaned", "rooted", "added"))
    with ExitStack() as scope, nc.Block() as block:
        w = K.sb(scope, f"{tag}_w", [P, 2, HALF])
        w_hi = K.sb(scope, f"{tag}_w_hi", [P, 2, HALF], F32R)
        w_lo = K.sb(scope, f"{tag}_w_lo", [P, 2, HALF], F32R)
        s_hi = K.sb(scope, f"{tag}_s_hi", [P, 2, S], F32R)
        s_lo = K.sb(scope, f"{tag}_s_lo", [P, 2, S], F32R)
        normed = gain_row is not None
        gain = K.sb(scope, f"{tag}_gain", [P, D]) if normed else None
        junk = K.sb(scope, f"{tag}_junk", [P, HALF]) if normed else None
        ss = K.sb(scope, f"{tag}_ss", [P, 2, NT])
        rstd = K.sb(scope, f"{tag}_rstd", [P, NT])
        pairs = depth // 2

        @block.sync
        def _(sp):
            def load(q, b, s, c):
                row = sp.snap(c * P)
                sp.wait_ge(split, q * 4 + (2 * b + 1))
                sp.dma_start(w[:, b, :], weight[0][bass.ds(row, P), s * HALF:(s + 1) * HALF]).then_inc(landed[b], 16)

            for s in range(2):
                with sp.Fori(0, pairs) as i:
                    for b in range(2):
                        load(i + s * pairs, b, s, i * 2 + b)
                if s == 0 and normed:
                    sp.dma_start(gain[:], gain_row.to_broadcast([P, D])).then_inc(gain_landed, 16)
                if s == 0:
                    sp.dma_start(x[:], src.rearrange("(t p) d -> p t d", p=P)).then_inc(x_landed, 16)
            if out is not None:
                for t in range(NT):
                    sp.wait_ge(added, t + 1)
                    sp.dma_start(out[t * P:(t + 1) * P, :], x[:, t, :]).then_inc(stored, 16)
                sp.wait_ge(stored, 16 * NT)

        @block.tensor
        def _(pe):
            def chunk(q, b, s, first=False, last=False):
                pe.wait_ge(split, q * 4 + (2 * b + 6))
                for t in range(NT):
                    if first and s:
                        pe.wait_ge(kept, t + 1)
                    tokens = slice(t * P, (t + 1) * P)
                    nc.tensor.matmul(K.ps[:, t, :], s_hi[:, b, tokens], w_hi[:, b, :], start=first, stop=False)
                    nc.tensor.matmul(K.ps[:, t, :], s_hi[:, b, tokens], w_lo[:, b, :], start=False, stop=False)
                    mm = nc.tensor.matmul(K.ps[:, t, :], s_lo[:, b, tokens], w_hi[:, b, :], start=False, stop=last)
                    if t == NT - 1:
                        mm.then_inc(chunked, 1)
                    elif last:
                        mm.then_inc(projected, 1)

            pe.sem_inc(chunked, 2)
            for s in range(2):
                chunk(s * pairs, 0, s, first=True)
                chunk(s * pairs, 1, s)
                with pe.Fori(1 + s * pairs, pairs - 1 + s * pairs) as q:
                    for b in range(2):
                        chunk(q, b, s)
                chunk(pairs - 1 + s * pairs, 0, s)
                chunk(pairs - 1 + s * pairs, 1, s, last=True)

        @block.scalar
        def _(act):
            def fill(q, b, c):
                act.wait_ge(landed[b], q * 16 + 16)
                act.wait_ge(chunked, q * 2 + (b + 1))
                nc.scalar.activation(w_hi[:, b, :], w[:, b, :], ACT.Copy).then_inc(rounded, 1)
                nc.scalar.activation(s_hi[:, b, :], srcT[:, c, :], ACT.Copy).then_inc(rounded, 1)

            def squares(s):
                for t in range(NT):
                    if t == NT - 1:
                        act.wait_ge(chunked, (s + 1) * depth + 2)
                    else:
                        act.wait_ge(projected, s * (NT - 1) + t + 1)
                    act.drain()
                    nc.scalar.activation(junk[:], K.ps[:, t, :], ACT.Square, accum_out=ss[:, s, t:t + 1]).then_inc(squared, 1)

            with act.Fori(0, pairs) as i:
                for b in range(2):
                    fill(i, b, i * 2 + b)
            fill(pairs, 0, 0)
            if normed:
                squares(0)
            fill(pairs, 1, 1)
            with act.Fori(1, pairs) as i:
                for b in range(2):
                    fill(i + pairs, b, i * 2 + b)
            if normed:
                squares(1)
                act.wait_ge(meaned, 1)
                nc.scalar.activation(rstd[:], rstd[:], ACT.Sqrt).then_inc(rooted, 1)

        @block.vector
        def _(dve):
            def fill(q, b, c):
                dve.wait_ge(rounded, q * 4 + (2 * b + 1))
                nc.vector.tensor_tensor(w_lo[:, b, :], w[:, b, :], w_hi[:, b, :].bitcast(F32), ALU.subtract).then_inc(split, 1)
                dve.wait_ge(rounded, q * 4 + (2 * b + 2))
                nc.vector.tensor_tensor(s_lo[:, b, :], srcT[:, c, :], s_hi[:, b, :].bitcast(F32), ALU.subtract).then_inc(split, 1)

            def keep(s):
                for t in range(NT):
                    cols = slice(s * HALF, (s + 1) * HALF)
                    if not normed:
                        if t == NT - 1:
                            dve.wait_ge(chunked, (s + 1) * depth + 2)
                        else:
                            dve.wait_ge(projected, s * (NT - 1) + t + 1)
                        nc.vector.tensor_tensor(x[:, t, cols], x[:, t, cols], K.ps[:, t, :], ALU.add).then_inc(kept, 1)
                        continue
                    dve.wait_ge(squared, s * NT + t + 1)
                    nc.vector.tensor_tensor(y[:, t, cols], K.ps[:, t, :], gain[:, cols], ALU.mult).then_inc(kept, 1)

            dve.sem_inc(split, 4)
            with dve.Fori(0, pairs) as i:
                for b in range(2):
                    fill(i, b, i * 2 + b)
            fill(pairs, 0, 0)
            if normed:
                dve.wait_ge(gain_landed, 16)
            else:
                dve.wait_ge(x_landed, 16)
            keep(0)
            fill(pairs, 1, 1)
            with dve.Fori(1, pairs) as i:
                for b in range(2):
                    fill(i + pairs, b, i * 2 + b)
            keep(1)
            if not normed:
                return
            nc.vector.tensor_tensor(rstd[:], ss[:, 0, :], ss[:, 1, :], ALU.add)
            dve.drain()
            nc.vector.tensor_scalar(rstd[:], rstd[:], 1.0 / D, EPS, ALU.mult, ALU.add).then_inc(meaned, 1)
            dve.wait_ge(rooted, 1)
            nc.vector.reciprocal(rstd[:], rstd[:])
            dve.wait_ge(x_landed, 16)
            dve.drain()
            with dve.Fori(0, NT) as t:
                nc.vector.scalar_tensor_tensor(x[:, t, :], y[:, t, :], rstd[:, bass.ds(t, 1)], x[:, t, :],
                                               ALU.mult, ALU.add).then_inc(added, 1)


def ffn_up(K, h_hi, h_lo, room, f):
    nc, A = K.nc, K.A
    w_up = A["ffn_w_up_2"].rearrange("o (k p) n -> p (o k) n", p=P)
    landed = [K.sem(f"u_landed{b}") for b in range(2)]
    rounded, split, projected, kept, filtered, gelued, done = (K.sem(f"u_{n}") for n in
        ("rounded", "split", "projected", "kept", "filtered", "gelued", "done"))
    with ExitStack() as scope, nc.Block() as block:
        w_end, g_end = 2 * KT * P, 2 * KT * P + 2 * (2 + S)
        w = room[:, 0:w_end].rearrange("p (u k n) -> p u k n", u=2, k=KT)
        g = room[:, w_end:g_end].rearrange("p (b n) -> p b n", b=2)
        c = room[:, g_end:g_end + 2 * S].rearrange("p (b n) -> p b n", b=2)
        w_hi = K.sb(scope, "u_w_hi", [P, 2, KT, P], F32R)
        w_lo = K.sb(scope, "u_w_lo", [P, 2, KT, P], F32R)
        taps = K.vec("ffn_conv_w_2", 0, 3 * FFT).rearrange("p (w j) -> p w j", j=FFT)
        bias = K.vec("ffn_conv_b_2", 0, FFT)

        def banks(b, up):
            return K.ps[:, 4 * b + 2 * up:4 * b + 2 * up + 2, :].rearrange("p c n -> p (c n)")

        @block.sync
        def _(sp):
            for up in range(2):
                sp.dma_start(w[:, up], w_up[:, :, up * DFF:up * DFF + P]).then_inc(landed[up], 16)
            with sp.Fori(1, FFT) as j:
                for up in range(2):
                    off = sp.snap(j * P + up * DFF)
                    sp.wait_ge(split, j * 2 + (up - 1))
                    sp.dma_start(w[:, up], w_up[:, :, bass.ds(off, P)]).then_inc(landed[up], 16)

        @block.tensor
        def _(pe):
            with pe.Fori(0, FFT // 2) as i:
                for b in range(2):
                    for up in range(2):
                        pe.wait_ge(split, i * 4 + (2 * b + up + 1))
                        pe.wait_ge(done, i * 2 + (b + 1))
                        for h in range(2):
                            bank, tokens = K.ps[:, 4 * b + 2 * up + h, :], slice(h * HALF, (h + 1) * HALF)
                            for k in range(KT):
                                nc.tensor.matmul(bank, w_hi[:, up, k, :], h_hi[:, k, tokens], start=(k == 0), stop=False)
                                nc.tensor.matmul(bank, w_hi[:, up, k, :], h_lo[:, k, tokens], start=False, stop=False)
                                mm = nc.tensor.matmul(bank, w_lo[:, up, k, :], h_hi[:, k, tokens], start=False, stop=(k == KT - 1))
                        mm.then_inc(projected, 1)

        @block.scalar
        def _(act):
            def fill(j, up):
                act.wait_ge(landed[up], j * 16 + 16)
                nc.scalar.activation(w_hi[:, up], w[:, up], ACT.Copy).then_inc(rounded, 1)

            def step(j, b, more):
                act.wait_ge(projected, j * 2 + 1)
                act.wait_ge(done, j + 1)
                nc.scalar.activation(g[:, b, 2:2 + S], banks(b, 0), ACT.Copy).then_inc(kept, 1)
                if more:
                    fill(j + 1, 0)
                    act.wait_ge(projected, j * 2 + 2)
                    fill(j + 1, 1)
                act.wait_ge(filtered, j + 1)
                nc.scalar.activation(c[:, b, :], c[:, b, :], ACT.Gelu_apprx_tanh).then_inc(gelued, 1)

            for up in range(2):
                fill(0, up)
            with act.Fori(0, FFT // 2 - 1) as i:
                for b in range(2):
                    step(i * 2 + b, b, True)
            step(FFT - 2, 0, True)
            step(FFT - 1, 1, False)

        @block.vector
        def _(dve):
            def fill(n, up):
                dve.wait_ge(rounded, n + 1)
                nc.vector.tensor_tensor(w_lo[:, up], w[:, up], w_hi[:, up].bitcast(F32), ALU.subtract).then_inc(split, 1)

            def step(j, b, more):
                tap = lambda v: taps[:, v, bass.ds(j, 1)]
                dve.wait_ge(kept, j + 1)
                nc.vector.tensor_scalar(c[:, b, :], g[:, b, 0:S], tap(0), bias[:, bass.ds(j, 1)], ALU.mult, ALU.add)
                dve.drain()
                nc.vector.scalar_tensor_tensor(c[:, b, :], g[:, b, 1:1 + S], tap(1), c[:, b, :], ALU.mult, ALU.add)
                dve.drain()
                nc.vector.scalar_tensor_tensor(c[:, b, :], g[:, b, 2:2 + S], tap(2), c[:, b, :], ALU.mult, ALU.add) \
                    .then_inc(filtered, 1)
                if more:
                    fill(j * 2 + 2, 0)
                    fill(j * 2 + 3, 1)
                dve.wait_ge(projected, j * 2 + 2)
                dve.wait_ge(gelued, j + 1)
                nc.vector.tensor_tensor(f[:, j, :], c[:, b, :], banks(b, 1), ALU.mult).then_inc(done, 1)

            nc.vector.memset(g[:, :, 0:2], 0.0).then_inc(done, 2)
            for up in range(2):
                fill(up, up)
            with dve.Fori(0, FFT // 2 - 1) as i:
                for b in range(2):
                    step(i * 2 + b, b, True)
            step(FFT - 2, 0, True)
            step(FFT - 1, 1, False)


def prepare_mixers(K, Z, R):
    nc, A = K.nc, K.A
    CAP, DK = 15.0, 32
    filtered, silued, saved = (K.sem(f"q_{n}") for n in ("filtered", "silued", "saved"))
    const_landed = K.sem("q_const_landed")
    landed, biased, capped, decayed, logged, summed, turned, rows_saved, spread, revealed, spread_kept = (K.sem(f"q_{n}") for n in
        ("landed", "biased", "capped", "decayed", "logged", "summed", "turned", "rows_saved", "spread", "revealed", "spread_kept"))
    with ExitStack() as scope, nc.Block() as block:
        sb = lambda name, shape: K.sb(scope, f"q_{name}", shape)
        bias = sb("bias", [4, 3])
        bias15 = sb("bias15", [4, 2])
        t = sb("t", [4, 2, S])
        x = sb("x", [4, S])
        u = sb("u", [4, 2, S])
        rel = sb("rel", [32, 4])
        band = sb("band", [4, 3 * P])
        raw, gates = Z["mlstm"], Z["gates"]
        mqk, total, keys = Z["mlstm_qk"], Z["total"], Z["keys"]
        least = keys[:, 1, :]

        @block.sync
        def _(sp):
            sp.dma_start(K.tables["mixer_consts"][:], A["mixer_consts"]).then_inc(const_landed, 16)
            for j, name in enumerate(("mlstm_b_i_2", "mlstm_b_f_2", "fox_b_f_2")):
                sp.dma_start(bias[:, j:j + 1], A[name].rearrange("o h -> h o")).then_inc(landed, 16)
            sp.dma_start(rel[:], A["rel_bias_2"]).then_inc(landed, 16)
            sp.dma_start(R["swa_q"].rearrange("(j p) t -> p j t", p=P), Z["swa_q"][:]).then_inc(saved, 16)
            for r in range(2):
                sp.dma_start(R["swa_k"].rearrange("(g r p) t -> g r p t", g=2, r=2)[:, r],
                             Z["swa_k"][:, 0, :]).then_inc(saved, 16)
            sp.wait_ge(spread_kept, 1)
            sp.dma_start(R["band"], band[:]).then_inc(revealed, 16)
            sp.wait_ge(revealed, 16)
            tile = bass.AP(R["band"].tensor, 0, [[1, P], [3 * P, 4], [1, 2 * P]])
            sp.dma_start(K.window_bias[:], tile).then_inc(saved, 16)
            sp.dma_start(K.sinks[:], A["swa_sinks_2"].to_broadcast([P, 4])).then_inc(saved, 16)
            sp.wait_ge(saved, 16 * 5)

        @block.tensor
        def _(pe):
            pe.wait_ge(landed, 64)
            pe.wait_ge(const_landed, 16)
            nc.tensor.matmul(K.ps[0:4, 0, 0:3 * P], rel[:], K.const("bucket")[0:32, :], start=True, stop=True).then_inc(spread, 1)
            pe.wait_ge(summed, 1)
            for i in range(NT):
                mm = nc.tensor.transpose(K.ps[:, 1, 4 * i:4 * i + 4], keys[:, 0, i * P:(i + 1) * P], K.const("ident")[0:4, 0:4])
            mm.then_inc(turned, 1)

        @block.vector
        def _(dve):
            ts, tt, stt = nc.vector.tensor_scalar, nc.vector.tensor_tensor, nc.vector.scalar_tensor_tensor
            dve.wait_ge(landed, 64)
            ts(bias15[:], bias[:, 0:2], 1.0 / CAP, None, ALU.mult).then_inc(biased, 1)
            ts(x[:], gates[:, 2, :], bias[:, 2:3], None, ALU.add)
            dve.drain()
            ts(least, x[:], 0.0, None, ALU.min)
            stt(u[:, 1, :], x[:], -1.0, x[:], ALU.mult, ALU.max).then_inc(biased, 1)
            for c in range(2):
                out = mqk[:, c, :]
                ts(out, raw[:, c, 0:S], K.vec("mlstm_conv_w_2", c), None, ALU.mult)
                for w in range(1, 4):
                    dve.drain()
                    last = stt(out, raw[:, c, w:w + S], K.vec("mlstm_conv_w_2", 2 * w + c), out, ALU.mult, ALU.add)
                last.then_inc(filtered, 1)
            dve.wait_ge(spread, 1)
            tt(band[:], K.ps[0:4, 0, 0:3 * P], K.const("outside")[0:4, :], ALU.add).then_inc(spread_kept, 1)
            dve.wait_ge(silued, 2)
            ts(mqk[:, 0, :], mqk[:, 0, :], DK ** -0.5, None, ALU.mult)
            dve.wait_ge(logged, 1)
            ts(u[:, 0, :], u[:, 0, :], -1.0, None, ALU.mult)
            tt(u[:, 1, :], least, u[:, 1, :], ALU.subtract)
            dve.drain()
            for c in range(2):
                nc.vector.tensor_tensor_scan(total[:, c, :], K.const("ones")[0:4, 0:1].to_broadcast([4, S]), u[:, c, :], 0.0, ALU.mult, ALU.add)
            dve.drain()
            stt(keys[:, 0, :], t[:, 0, :], CAP, total[:, 0, :], ALU.mult, ALU.subtract)
            ts(keys[:, 1, :], total[:, 1, :], -1.0, None, ALU.mult)
            dve.drain()
            dve.sem_inc(summed, 1)
            dve.wait_ge(turned, 1)
            nc.vector.tensor_copy(K.mlstm_keys[:], K.ps[:, 1, 0:4 * NT])

        @block.scalar
        def _(act):
            act.wait_ge(biased, 2)
            for c in range(2):
                nc.scalar.activation(t[:, c, :], gates[:, c, :], ACT.Tanh, scale=1.0 / CAP, bias=bias15[:, c:c + 1])
            act.drain()
            nc.scalar.activation(u[:, 0, :], t[:, 1, :], ACT.Exp, scale=-CAP)
            nc.scalar.activation(u[:, 1, :], u[:, 1, :], ACT.Exp, scale=-1.0)
            act.drain()
            nc.scalar.activation(u[:], u[:], ACT.Ln, bias=1.0).then_inc(logged, 1)
            for c in range(2):
                act.wait_ge(filtered, c + 1)
                nc.scalar.activation(mqk[:, c, :], mqk[:, c, :], ACT.Silu, bias=K.vec("mlstm_conv_b_2", c)).then_inc(silued, 1)


def window_attention(K, tag, q_rows, k_rows, v, v_col, o, o_col):
    nc = K.nc
    dk, DV, N = HD, 64, 2 * NT
    loaded = [K.sem(f"{tag}_loaded{x}") for x in range(2)]
    scored, peaked, exped, rated, turned, turned_kept, weighed, stored = (K.sem(f"{tag}_{n}") for n in
        ("scored", "peaked", "exped", "rated", "turned", "turned_kept", "weighed", "stored"))
    begun = K.sem(f"{tag}_begun")
    with ExitStack() as scope, nc.Block() as block:
        qh = K.sb(scope, f"{tag}_q", [dk, 2, S])
        kh = K.sb(scope, f"{tag}_k", [dk, 2, S])
        p = K.sb(scope, f"{tag}_p", [P, 2, 2 * P])
        pT = K.sb(scope, f"{tag}_pT", [P, 2, 2 * P])
        low = K.sb(scope, f"{tag}_low", [P, 2])
        mass = K.sb(scope, f"{tag}_mass", [P, 2])
        drop = K.sb(scope, f"{tag}_drop", [P, 2])
        share = K.sb(scope, f"{tag}_share", [P, 2])

        def place(n):
            t = n % NT
            return n // NT, t, max(t - 1, 0), min(t + 1, 2) * P, n % 2

        def score_bank(n):
            return K.ps[:, n % 2, 0:place(n)[3]]

        def turn_bank(n):
            return K.ps[:, 2 + n % 2, 0:place(n)[3]]

        def out_bank(n):
            return K.ps[:, 4 + n % 2, 0:DV]

        @block.sync
        def _(sp):
            with sp.Fori(0, 2) as i:
                for x in range(2):
                    row = sp.snap((i * 2 + x) * dk)
                    sp.wait_ge(weighed, i * N + (NT * x + 1))
                    sp.dma_start(qh[:, x, :], q_rows[bass.ds(row, dk), :]).then_inc(loaded[x], 16)
                    sp.dma_start(kh[:, x, :], k_rows[bass.ds(row, dk), :]).then_inc(loaded[x], 16)

        @block.tensor
        def _(pe):
            pe.sem_inc(weighed, NT + 1)
            pe.sem_inc(turned, 2)
            with pe.Fori(0, 2) as i:
                def scores(n):
                    x, t, first, width, _ = place(n)
                    if t == 0:
                        pe.wait_ge(loaded[x], i * 32 + 32)
                    pe.wait_ge(exped, i * N + (n + 1))
                    nc.tensor.matmul(score_bank(n), qh[:, x, t * P:(t + 1) * P], kh[:, x, first * P:(t + 1) * P], start=True, stop=False)
                    nc.tensor.matmul(score_bank(n), K.const("flip"), K.window_bias[:, i * 2 + x, 2 * P - width:2 * P],
                                     start=False, stop=True).then_inc(scored, 1)

                def turn_weights(n):
                    s = place(n)[4]
                    pe.wait_ge(exped, i * N + (n + 3))
                    pe.wait_ge(turned_kept, i * N + (n + 1))
                    for j in range(place(n)[3] // P):
                        mm = nc.tensor.transpose(turn_bank(n)[:, j * P:(j + 1) * P], p[:, s, j * P:(j + 1) * P], K.const("ident"))
                    mm.then_inc(turned, 1)

                def weigh(n):
                    x, t, first, width, s = place(n)
                    pe.wait_ge(turned_kept, i * N + (n + 3))
                    pe.wait_ge(stored, i * N + (n + 1))
                    pe.sem_inc(begun, 1)
                    for j in range(width // P):
                        mm = nc.tensor.matmul(out_bank(n), pT[:, s, j * P:(j + 1) * P],
                                              v[:, first + j, bass.ds(i * (2 * DV) + (x * DV + v_col), DV)],
                                              start=(j == 0), stop=(j == width // P - 1))
                    mm.then_inc(weighed, 1)

                scores(0)
                for n in range(N):
                    if n + 1 < N:
                        scores(n + 1)
                    turn_weights(n)
                    if n > 0:
                        weigh(n - 1)
                weigh(N - 1)

        @block.vector
        def _(dve):
            with dve.Fori(0, 2) as i:
                def peaks(n):
                    x, s = place(n)[0], place(n)[4]
                    dve.wait_ge(scored, i * N + (n + 1))
                    nc.vector.tensor_reduce(low[:, s:s + 1], score_bank(n), AX, ALU.max)
                    dve.drain()
                    nc.vector.tensor_scalar(low[:, s:s + 1], low[:, s:s + 1], K.sinks[:, bass.ds(i * 2 + x, 1)], -1.0,
                                            ALU.max, ALU.mult).then_inc(peaked, 1)

                def rate(n):
                    s = place(n)[4]
                    dve.wait_ge(exped, i * N + (n + 3))
                    dve.wait_ge(stored, i * N + (n + 1))
                    nc.vector.tensor_tensor(mass[:, s:s + 1], mass[:, s:s + 1], drop[:, s:s + 1], ALU.add)
                    dve.drain()
                    nc.vector.reciprocal(share[:, s:s + 1], mass[:, s:s + 1]).then_inc(rated, 1)

                peaks(0)
                for n in range(N):
                    if n + 1 < N:
                        peaks(n + 1)
                    rate(n)

        @block.scalar
        def _(act):
            act.sem_inc(exped, 2)
            act.sem_inc(turned_kept, 2)
            act.sem_inc(stored, 2)
            act.sem_inc(begun, 1)
            with act.Fori(0, 2) as i:
                def exps(n):
                    x, s, width = place(n)[0], place(n)[4], place(n)[3]
                    act.wait_ge(peaked, i * N + (n + 1))
                    act.wait_ge(turned, i * N + (n + 1))
                    if n > 1:
                        act.wait_ge(rated, i * N + (n - 1))
                    act.sem_inc(begun, 1)
                    nc.scalar.activation(drop[:, s:s + 1], K.sinks[:, bass.ds(i * 2 + x, 1)], ACT.Exp, bias=low[:, s:s + 1])
                    nc.scalar.activation(p[:, s, 0:width], score_bank(n), ACT.Exp, bias=low[:, s:s + 1],
                                         accum_out=mass[:, s:s + 1]).then_inc(exped, 1)

                def keep_turned(n):
                    act.wait_ge(turned, i * N + (n + 3))
                    nc.scalar.activation(pT[:, place(n)[4], 0:place(n)[3]], turn_bank(n), ACT.Copy).then_inc(turned_kept, 1)

                def finish(n):
                    x, t, _, _, s = place(n)
                    act.wait_ge(rated, i * N + (n + 1))
                    act.wait_ge(weighed, i * N + (n + NT + 2))
                    act.sem_inc(begun, 1)
                    nc.scalar.activation(o[:, t, bass.ds(i * (2 * DV) + (x * DV + o_col), DV)], out_bank(n), ACT.Copy,
                                         scale=share[:, s:s + 1]).then_inc(stored, 1)

                exps(0)
                for n in range(N):
                    if n + 1 < N:
                        exps(n + 1)
                    keep_turned(n)
                    if n > 0:
                        finish(n - 1)
                finish(N - 1)


def mlstm_attention(K, tag, R, values, v_col, o, o_col):
    nc = K.nc
    HM, DK, DV = 4, 32, 64
    NC = len(CHUNKS)
    loads = 16 * 9
    loaded = [K.sem(f"{tag}_loaded{b}") for b in range(2)]
    filled, staged, scored, exped, mixed, weighed, stored, fetching, begun = (K.sem(f"{tag}_{n}") for n in
        ("filled", "staged", "scored", "exped", "mixed", "weighed", "stored", "fetching", "begun"))
    with ExitStack() as scope, nc.Block() as block:
        q = K.sb(scope, f"{tag}_q", [P, 2, S], F32R)
        k = K.sb(scope, f"{tag}_k", [P, 2, S], F32R)
        rise = K.sb(scope, f"{tag}_rise", [2, 2, S], F32R)
        ones = K.sb(scope, f"{tag}_ones", [2, P], F32R)
        w = K.sb(scope, f"{tag}_w", [P, 2, HALF])
        weights = [K.sb(scope, f"{tag}_weights{h}", [P, 4 * (h + 1), HALF]) for h in range(2)]
        vs = K.sb(scope, f"{tag}_v", [P, 2, NT, DV + 1])
        share = K.sb(scope, f"{tag}_share", [P, 2])
        size = K.sb(scope, f"{tag}_size", [P, 2])

        @block.gpsimd
        def _(pool):
            pool.wait_ge(filled, 1)
            with pool.Fori(0, HM // 2) as i:
                for x in range(2):
                    row, line = pool.snap((i * 2 + x) * DK), pool.snap(i * 2 + x)
                    pool.wait_ge(weighed, i * 16 + (8 * x + 8))
                    pool.sem_inc(fetching, 1)
                    for n, (q_part, k_part) in enumerate((("hi", "hi"), ("lo", "hi"), ("hi", "lo"), ("lo", "lo"))):
                        rows = slice(n * DK, (n + 1) * DK)
                        pool.dma_start(q[rows, x, :], R[f"q_{q_part}"][bass.ds(row, DK), :]).then_inc(loaded[x], 16)
                        pool.dma_start(k[rows, x, :], R[f"k_{k_part}"][bass.ds(row, DK), :]).then_inc(loaded[x], 16)
                    pool.dma_start(rise[:, x, :], R["rise"][bass.ds(line, 1)].rearrange("o c s -> (o c) s")).then_inc(loaded[x], 16)
                    nc.gpsimd.tensor_copy(vs[:, x, :, 0:DV], values[:, :, bass.ds((i * 2 + x) * DV + v_col, DV)]).then_inc(staged, 1)

        @block.tensor
        def _(pe):
            mm = nc.tensor.matmul
            pe.sem_inc(weighed, 16)
            pe.wait_ge(filled, 1)
            with pe.Fori(0, HM // 2) as i:
                for x in range(2):
                    pe.wait_ge(loaded[x], i * loads + loads)
                    for c, (half, j, q0, n) in enumerate(CHUNKS):
                        pe.wait_ge(mixed, i * (2 * NC) + (NC * x + c + 1))
                        keys = slice(j * P, (j + 1) * P)
                        crossing = q0 == j * P
                        decay = K.ps[:, 2 + c % 2, 0:n]
                        mm(K.ps[:, c % 2, 0:n], k[:, x, keys], q[:, x, q0:q0 + n], start=True, stop=True)
                        last = mm(decay, ones[:], rise[:, x, q0:q0 + n], start=True, stop=not crossing)
                        if crossing:
                            last = mm(decay[:, 0:P], K.ident_r[:], K.causal_t_r[:], start=False, stop=True)
                        last.then_inc(scored, 1)
                    pe.wait_ge(staged, i * 2 + (x + 1))
                    for t in range(NT):
                        half = t // 4
                        c = CHUNKS.index((half, t, t * P, (half + 1) * HALF - t * P))
                        pe.wait_ge(mixed, i * (2 * NC) + (NC * x + c + 3))
                        pe.wait_ge(stored, i * 16 + (8 * x + t + 1))
                        for j in range(t + 1):
                            last = mm(K.ps[:, 6 + t % 2, 0:DV + 1], weights[half][:, j, (t - 4 * half) * P:(t - 4 * half + 1) * P],
                                      vs[:, x, j, :], start=(j == 0), stop=(j == t))
                        last.then_inc(weighed, 1)

        @block.scalar
        def _(act):
            with act.Fori(0, HM // 2) as i:
                for x in range(2):
                    for c, (half, j, q0, n) in enumerate(CHUNKS):
                        act.wait_ge(scored, i * (2 * NC) + (NC * x + c + 1))
                        act.sem_inc(begun, 1)
                        nc.scalar.activation(w[:, c % 2, 0:n], K.ps[:, 2 + c % 2, 0:n], ACT.Exp,
                                             bias=K.mlstm_keys[:, bass.ds(i * 2 + (4 * j + x), 1)]).then_inc(exped, 1)

        @block.vector
        def _(dve):
            nc.vector.memset(vs[:, :, :, DV:DV + 1], 1.0)
            nc.vector.tensor_copy(ones[:], K.const("ones")[0:2, :])
            dve.drain()
            dve.sem_inc(filled, 1)
            dve.sem_inc(mixed, 2)
            dve.sem_inc(stored, 2)
            with dve.Fori(0, HM // 2) as i:
                for x in range(2):
                    for c, (half, j, q0, n) in enumerate(CHUNKS):
                        dve.wait_ge(exped, i * (2 * NC) + (NC * x + c + 1))
                        nc.vector.tensor_tensor(weights[half][:, j, HALF - n:HALF], w[:, c % 2, 0:n], K.ps[:, c % 2, 0:n],
                                                ALU.mult).then_inc(mixed, 1)
                    for t in range(NT):
                        part, whole = share[:, t % 2:t % 2 + 1], size[:, t % 2:t % 2 + 1]
                        dve.wait_ge(weighed, i * 16 + (8 * x + t + 17))
                        nc.vector.tensor_copy(part, K.ps[:, 6 + t % 2, DV:DV + 1])
                        dve.drain()
                        nc.vector.scalar_tensor_tensor(whole, part, -1.0, part, ALU.mult, ALU.max)
                        dve.drain()
                        nc.vector.tensor_scalar(whole, whole, 1.0, None, ALU.max)
                        dve.drain()
                        nc.vector.reciprocal(part, whole)
                        dve.drain()
                        nc.vector.tensor_scalar(o[:, t, bass.ds((i * 2 + x) * DV + o_col, DV)], K.ps[:, 6 + t % 2, 0:DV], part, None,
                                                ALU.mult).then_inc(stored, 1)
            dve.drain()


def mixer_columns(Z):
    SCALE = HD ** -0.5
    ml_v, ml_o, ml_i, ml_f = ML0 + RW, ML0 + 2 * RW, ML0 + 3 * RW, ML0 + 3 * RW + 4
    sw_k, sw_v = SW0 + RW, SW0 + RW + P
    fx_k, fx_v, fx_f = FX0 + RW, FX0 + 2 * RW, FX0 + 3 * RW

    def tiles(name, col, count, lead=0, scale=1.0, func=ACT.Copy):
        return [([(col + j * P, P, 0)], lambda h, j=j: Z[name][:, j, lead + h * HALF:lead + (h + 1) * HALF], scale, func, None)
                for j in range(count)]

    units = (tiles("rwkv", 0, 8, lead=1) + tiles("mlstm", ML0, 2, lead=3) + tiles("mlstm_o", ml_o, 2, func=ACT.Sigmoid)
             + tiles("fox_q", FX0, 2, scale=SCALE) + tiles("fox_k", fx_k, 2) + tiles("swa_q", SW0, 2, scale=SCALE)
             + tiles("swa_k", sw_k, 1) + [([(ml_i, 4, 0), (ml_f, 4, 32), (fx_f, 4, 64)], None, None, None, None)])
    slabs = [([(ml_v, RW, 0), (fx_v, RW, RW)], lambda t: Z["values"][:, t, 0:2 * RW]),
             ([(sw_v + HD * (h // 2), HD, HD * h) for h in range(4)], lambda t: Z["values"][:, t, 2 * RW:3 * RW])]
    return units, slabs


def rwkv_gates(K, z, zm, W):
    nc, A = K.nc, K.A
    loaded, mixed, squashed, projected, gated, squares, rooted, summed, cumulated, exped = (K.sem(f"rg_{n}") for n in
        ("loaded", "mixed", "squashed", "projected", "gated", "squares", "rooted", "summed", "cumulated", "exped"))
    spare = [z[:, 2 * j:2 * j + 2, 1:S + 1] for j in range(4)]
    lw, c, a, tmp = spare
    r, k, v = zm[:, 0:2, :], zm[:, 2:4, :], zm[:, 4:6, :]
    kk, b = W["kk"], W["b"]

    def banks(n):
        return K.ps[:, n:n + 4, :].rearrange("p (j h) n -> p j (h n)", j=2)

    with ExitStack() as scope, nc.Block() as block:
        up = K.sb(scope, "rg_up", [P, RW])
        g_up = K.sb(scope, "rg_g_up", [P, RW])
        within = K.sb(scope, "rg_within", [P, S])

        @block.sync
        def _(sp):
            sp.dma_start(up[0:64, :], A["rwkv_w_up_2"].rearrange("o k n -> (o k) n")).then_inc(loaded, 16)
            sp.dma_start(up[64:P, :], A["rwkv_a_up_2"].rearrange("o k n -> (o k) n")).then_inc(loaded, 16)
            sp.dma_start(g_up[:], A["rwkv_g_up_2"].rearrange("o k n -> (o k) n")).then_inc(loaded, 16)

        @block.tensor
        def _(pe):
            pe.wait_ge(loaded, 48)
            pe.wait_ge(squashed, 2)
            for base, rows in ((0, slice(0, 64)), (4, slice(64, P))):
                for j in range(2):
                    for h in range(2):
                        mm = nc.tensor.matmul(K.ps[:, base + 2 * j + h, :], up[rows, j * P:(j + 1) * P],
                                              zm[rows, 6, h * HALF:(h + 1) * HALF], start=True, stop=True)
                mm.then_inc(projected, 1)
            pe.wait_ge(gated, 2)
            for j in range(2):
                for h in range(2):
                    mm = nc.tensor.matmul(K.ps[:, 2 * j + h, :], g_up[:, j * P:(j + 1) * P],
                                          zm[:, 7, h * HALF:(h + 1) * HALF], start=True, stop=True)
            mm.then_inc(projected, 1)
            for n, (base, free) in enumerate(((4, 4), (0, 6))):
                pe.wait_ge(squares, n + 1)
                pe.wait_ge(gated, free)
                for j in range(2):
                    for h in range(2):
                        mm = nc.tensor.matmul(K.ps[:, base + 2 * j + h, :], K.const("pair"),
                                              tmp[:, j, h * HALF:(h + 1) * HALF], start=True, stop=True)
                mm.then_inc(summed, 1)

        @block.vector
        def _(dve):
            ts, tt, stt = nc.vector.tensor_scalar, nc.vector.tensor_tensor, nc.vector.scalar_tensor_tensor
            for tiles in (range(6, 8), range(6)):
                span = slice(tiles.start, tiles.stop)
                tt(zm[:, span, :], z[:, span, 0:S], z[:, span, 1:S + 1], ALU.subtract)
                dve.drain()
                for j in tiles:
                    stt(zm[:, j, :], zm[:, j, :], K.vec("rwkv_mu_2", j), z[:, j, 1:S + 1], ALU.mult, ALU.add).then_inc(mixed, 1)
            dve.drain()
            for j in range(2):
                ts(kk[:, j, :], k[:, j, :], K.vec("rwkv_k_k_2", j), None, ALU.mult)
            nc.vector.memset(within[:], 1.0)
            dve.drain()
            nc.vector.memset(within[:].rearrange("p (c n) -> p c n", n=CHUNK)[:, :, 0:1], 0.0)
            tt(tmp, kk[:], kk[:], ALU.mult).then_inc(squares, 1)
            dve.wait_ge(gated, 2)
            ts(lw, lw, -math.exp(-0.5), None, ALU.mult)
            dve.drain()
            for j in range(2):
                nc.vector.tensor_tensor_scan(c[:, j, :], within[:], lw[:, j, :], 0.0, ALU.mult, ALU.add)
            dve.drain()
            tt(lw, c, lw, ALU.subtract).then_inc(cumulated, 1)
            dve.wait_ge(rooted, 1)
            ts(tmp, tmp, 1e-12, None, ALU.max)
            dve.drain()
            nc.vector.reciprocal(tmp, tmp)
            dve.drain()
            tt(kk[:], kk[:], tmp, ALU.mult)
            dve.drain()
            dve.wait_ge(gated, 4)
            for j in range(2):
                ts(tmp[:, j, :], a[:, j, :], -1.0, K.vec("rwkv_k_a_2", j), ALU.add, ALU.mult)
            dve.drain()
            stt(k, tmp, 1.0, k, ALU.add, ALU.mult)
            dve.drain()
            for j in range(2):
                bonus = stt(tmp[:, j, :], r[:, j, :], K.vec("rwkv_r_k_2", j), k[:, j, :], ALU.mult, ALU.mult)
            bonus.then_inc(squares, 1)
            tt(a, kk[:], a, ALU.mult)
            dve.wait_ge(summed, 2)
            tt(W["bonus"][:], banks(0), v, ALU.mult)
            dve.wait_ge(exped, 3)
            dve.drain()
            tt(b[:], a, tmp, ALU.mult)
            tt(kk[:], kk[:], lw, ALU.mult)
            tt(k, k, tmp, ALU.mult)
            tt(r, r, c, ALU.mult)
            for half in range(2):
                nc.vector.tensor_copy(W["whole"][:].rearrange("p (j e) n -> p e j n", e=2)[:, half],
                                      c[64 * half:64 * half + 64, :, CHUNK - 1::CHUNK])

        @block.scalar
        def _(act):
            act.wait_ge(mixed, 2)
            nc.scalar.activation(zm[0:64, 6, :], zm[0:64, 6, :], ACT.Tanh).then_inc(squashed, 1)
            nc.scalar.activation(zm[:, 7, :], zm[:, 7, :], ACT.Sigmoid).then_inc(squashed, 1)
            act.wait_ge(mixed, 8)
            for n, (out, name) in enumerate(((lw, "rwkv_w0_2"), (a, "rwkv_a0_2"))):
                act.wait_ge(projected, n + 1)
                for j in range(2):
                    nc.scalar.activation(out[:, j, :], banks(4 * n)[:, j, :], ACT.Sigmoid, bias=K.vec(name, j)).then_inc(gated, 1)
            act.wait_ge(projected, 3)
            for j in range(2):
                nc.scalar.activation(W["g"][:, j, :], banks(0)[:, j, :], ACT.Copy).then_inc(gated, 1)
            act.wait_ge(summed, 1)
            nc.scalar.activation(tmp, banks(4), ACT.Sqrt).then_inc(rooted, 1)
            act.wait_ge(cumulated, 1)
            nc.scalar.activation(lw, lw, ACT.Exp).then_inc(exped, 1)
            act.wait_ge(summed, 2)
            nc.scalar.activation(tmp, c, ACT.Exp, scale=-1.0).then_inc(exped, 1)
            act.drain()
            nc.scalar.activation(c, c, ACT.Exp).then_inc(exped, 1)


def rwkv_solve(K, W, solve, scratch):
    nc = K.nc
    H = 4
    staged, shifted, scored, kept, cut, m_saved, m_loaded, solved, t_saved, cleared, t_loaded = (K.sem(f"rm_{n}") for n in
        ("staged", "shifted", "scored", "kept", "cut", "m_saved", "m_loaded", "solved", "t_saved", "cleared", "t_loaded"))
    with ExitStack() as scope, nc.Block() as block:
        ks = K.sb(scope, "rm_kk", [64, 2, H, P])
        bs = K.sb(scope, "rm_b", [64, 2, H, P])
        masked = K.sb(scope, "rm_masked", [P, H, P])
        minus = K.sb(scope, "rm_minus", [P, NT, H, CHUNK])
        rows = K.sb(scope, "rm_rows", [P, CHUNK, CHUNK])
        prod = K.sb(scope, "rm_prod", [P, CHUNK, CHUNK])
        inv = K.sb(scope, "rm_inv", [P, CHUNK, CHUNK])

        @block.gpsimd
        def _(pool):
            with pool.Fori(0, NT // 2) as i:
                for x in range(2):
                    pool.wait_ge(scored, i * 2 + (x + 1))
                    for dst, src in ((ks, W["kk"]), (bs, W["b"])):
                        nc.gpsimd.tensor_copy(dst[:, x, 0::2, :], src[0:64, :, bass.ds((i * 2 + x) * P, P)]).then_inc(staged, 1)

        @block.tensor
        def _(pe):
            pe.sem_inc(scored, 2)
            with pe.Fori(0, NT // 2) as i:
                for x in range(2):
                    pe.wait_ge(staged, i * 4 + 2 * (x + 1))
                    pe.wait_ge(shifted, i * 4 + 2 * (x + 1))
                    pe.wait_ge(kept, i * 2 + (x + 1))
                    for h in range(H):
                        mm = nc.tensor.matmul(K.ps[:, x, h * P:(h + 1) * P], ks[:, x, h, :], bs[:, x, h, :], start=True, stop=True)
                    mm.then_inc(scored, 1)

        @block.vector
        def _(dve):
            dve.sem_inc(kept, 2)
            nc.vector.memset(solve[:], 0.0).then_inc(cleared, 1)
            below = K.const("chunk_below").unsqueeze(1).to_broadcast([P, H, P])
            with dve.Fori(0, NT // 2) as i:
                for x in range(2):
                    dve.wait_ge(scored, i * 2 + (x + 1))
                    for dst, src in ((ks, W["kk"]), (bs, W["b"])):
                        nc.vector.tensor_copy(dst[:, x, 1::2, :], src[64:P, :, bass.ds((i * 2 + x) * P, P)]).then_inc(shifted, 1)
                for x in range(2):
                    dve.wait_ge(scored, i * 2 + (x + 3))
                    nc.vector.scalar_tensor_tensor(masked[:], K.ps[:, x, :].rearrange("p (h n) -> p h n", h=H), -1.0, below,
                                                   ALU.mult, ALU.mult).then_inc(kept, 1)
                    dve.drain()
                    nc.vector.tensor_reduce(minus[:, i * 2 + x], masked[:].rearrange("p h (c s) -> p h s c", s=CHUNK), AX, ALU.add)
                    dve.drain()
            dve.sem_inc(cut, 1)
            nc.vector.memset(inv[:], 0.0)
            dve.drain()
            nc.vector.memset(inv[:].rearrange("p u t -> p (u t)")[:, 0::CHUNK + 1], 1.0)
            dve.wait_ge(m_loaded, 16)
            for t in range(1, CHUNK):
                dve.drain()
                nc.vector.tensor_tensor(prod[:, 0:t, 0:t], rows[:, t, 0:t].unsqueeze(1).to_broadcast([P, t, t]),
                                        inv[:, 0:t, 0:t], ALU.mult)
                dve.drain()
                nc.vector.tensor_reduce(inv[:, 0:t, t], prod[:, 0:t, 0:t], AX, ALU.add)
            dve.drain()
            dve.sem_inc(solved, 1)

        @block.sync
        def _(sp):
            def pieces(ap):
                return ap.rearrange("(i c h) t s -> i c t h s", i=NT, h=H)

            sp.wait_ge(cut, 1)
            for i in range(NT):
                for q in range(4):
                    sp.dma_start(pieces(scratch["minus"])[i, q], minus[q * CHUNK:(q + 1) * CHUNK, i]).then_inc(m_saved, 16)
            sp.wait_ge(m_saved, 16 * 4 * NT)
            sp.dma_start(rows[:], scratch["minus"]).then_inc(m_loaded, 16)
            sp.wait_ge(solved, 1)
            sp.dma_start(scratch["inverse"], inv[:]).then_inc(t_saved, 16)
            sp.wait_ge(cleared, 1)
            sp.wait_ge(t_saved, 16)
            for i in range(NT):
                for q in range(4):
                    sp.dma_start(solve[q * CHUNK:(q + 1) * CHUNK, H * i:H * i + H, q * CHUNK:(q + 1) * CHUNK],
                                 pieces(scratch["inverse"])[i, q]).then_inc(t_loaded, 16)
            sp.wait_ge(t_loaded, 16 * 4 * NT)


def rwkv_chunks(K, zm, W, solve, y):
    nc = K.nc
    H, N = 4, 64
    (staged, shifted, turned, tokens_kept, scored, masked, crossed, x_kept, solved, uw_kept, moved, queried, h_kept, g_kept, q_kept,
     stepped, s_kept, y_ready, y_kept, tiles_begun, steps_begun, summed, own_kept) = (K.sem(f"rs_{n}") for n in
        ("staged", "shifted", "turned", "tokens_kept", "scored", "masked", "crossed", "x_kept", "solved", "uw_kept", "moved", "queried",
         "h_kept", "g_kept", "q_kept", "stepped", "s_kept", "y_ready", "y_kept", "tiles_begun", "steps_begun",
         "summed", "own_kept"))
    with ExitStack() as scope, nc.Block() as block:
        sb = lambda name, shape: K.sb(scope, f"rs_{name}", shape)
        feat = sb("feat", [N, 5, H, P])
        inv = sb("inv", [P, H, P])
        bk = sb("bk", [P, 2, H, N])
        vt = sb("vt", [P, H, N])
        xk = sb("xk", [P, H, 2 * N])
        uw = sb("uw", [P, H, 2 * N])
        m2, n1, n2 = sb("m2", [P, H, P]), sb("n1", [P, H, P]), sb("n2", [P, H, P])
        grow = sb("grow", [N, 4, H, N])
        add = sb("add", [N, 4, H, N])
        q = sb("q", [N, H, P])
        own = sb("own", [N, H, P])
        state = sb("state", [N, 2, H, N])
        sources = (W["b"], zm[:, 2:4, :], zm[:, 4:6, :], W["kk"], zm[:, 0:2, :])
        COPIES = len(sources)

        def heads(bank, n):
            return K.ps[:, bank, 0:H * n].rearrange("p (h n) -> p h n", h=H)

        def chunk_rows(g):
            return slice(g * CHUNK, (g + 1) * CHUNK)

        @block.gpsimd
        def _(pool):
            with pool.Fori(0, NT) as i:
                pool.wait_ge(y_ready, i + 1)
                for s, src in enumerate(sources):
                    nc.gpsimd.tensor_copy(feat[:, s, 0::2, :], src[0:64, :, bass.ds(i * P, P)]).then_inc(staged, 1)
                nc.gpsimd.tensor_copy(inv[:], solve[:, bass.ds(i * H, H), :]).then_inc(staged, 1)

        @block.tensor
        def _(pe):
            mm = nc.tensor.matmul
            pe.sem_inc(y_ready, 1)
            b, k, v, kk, r = (feat[:, s] for s in range(5))
            with pe.Fori(0, NT) as i:
                pe.wait_ge(staged, i * (COPIES + 1) + (COPIES + 1))
                pe.wait_ge(shifted, i * COPIES + COPIES)
                pe.sem_inc(tiles_begun, 1)
                for n, src in enumerate((b, k, v, kk)):
                    for h in range(H):
                        last = nc.tensor.transpose(K.ps[:, n // 2, (n % 2) * RW + h * N:(n % 2) * RW + (h + 1) * N],
                                                   src[:, h, :], K.const("ident")[0:N, 0:N])
                last.then_inc(turned, 1)
                for n, (left, right) in enumerate(((k, kk), (b, r), (k, r))):
                    for h in range(H):
                        last = mm(heads(2 + n, P)[:, h], left[:, h, :], right[:, h, :], start=True, stop=True)
                    last.then_inc(scored, 1)
                pe.wait_ge(masked, i * 3 + 1)
                pe.wait_ge(tokens_kept, i * 3 + 3)
                pe.wait_ge(y_kept, i * 2 + 2)
                for h in range(H):
                    last = mm(heads(5, N)[:, h], m2[:, h, :], vt[:, h, :], start=True, stop=True)
                last.then_inc(crossed, 1)
                pe.wait_ge(x_kept, i + 1)
                for h in range(H):
                    last = mm(heads(6, 2 * N)[:, h], inv[:, h, :], xk[:, h, :], start=True, stop=True)
                last.then_inc(solved, 1)
                pe.wait_ge(masked, i * 3 + 3)
                pe.wait_ge(uw_kept, i + 1)
                for h in range(H):
                    last = mm(heads(4, P)[0:N, h], uw[:, h, N:2 * N], n1[:, h, :], start=True, stop=True)
                last.then_inc(queried, 1)
                for g in range(4):
                    for h in range(H):
                        last = mm(heads(g, N)[0:N, h], uw[chunk_rows(g), h, N:2 * N], bk[chunk_rows(g), 0, h, :], start=True, stop=True)
                for g in range(4):
                    for h in range(H):
                        out = K.ps[0:N, g, RW + h * N:RW + (h + 1) * N]
                        mm(out, bk[chunk_rows(g), 0, h, :], uw[chunk_rows(g), h, 0:N], start=True, stop=False)
                        last = mm(out, bk[chunk_rows(g), 1, h, :], vt[chunk_rows(g), h, :], start=False, stop=True)
                last.then_inc(moved, 1)
                for h in range(H):
                    mm(heads(5, P)[0:N, h], vt[:, h, :], n2[:, h, :], start=True, stop=False)
                    last = mm(heads(5, P)[0:N, h], uw[:, h, 0:N], n1[:, h, :], start=False, stop=True)
                last.then_inc(summed, 1)
                pe.wait_ge(q_kept, i + 1)
                pe.wait_ge(g_kept, i + 1)
                pe.wait_ge(h_kept, i + 1)
                for g in range(4):
                    pe.wait_ge(s_kept, i * 4 + (g + 1))
                    pe.sem_inc(steps_begun, 1)
                    for h in range(H):
                        mm(heads(7, N)[0:N, h], grow[:, g, h, :], state[:, g % 2, h, :], start=True, stop=False)
                        last = mm(heads(7, N)[0:N, h], K.const("ident")[0:N, 0:N], add[:, g, h, :], start=False, stop=True)
                    last.then_inc(stepped, 1)
                    for h in range(H):
                        last = mm(heads(6, P)[0:N, h, chunk_rows(g)], state[:, g % 2, h, :], q[:, h, chunk_rows(g)],
                                  start=True, stop=True)
                last.then_inc(y_ready, 1)

        @block.scalar
        def _(act):
            with act.Fori(0, NT) as i:
                act.wait_ge(turned, i + 1)
                nc.scalar.activation(bk[:], K.ps[:, 0, :].rearrange("p (s h n) -> p s h n", s=2, h=H), ACT.Copy).then_inc(tokens_kept, 1)
                nc.scalar.activation(vt[:], K.ps[:, 1, 0:RW].rearrange("p (h n) -> p h n", h=H), ACT.Copy).then_inc(tokens_kept, 1)
                nc.scalar.activation(xk[:, :, N:2 * N], K.ps[:, 1, RW:2 * RW].rearrange("p (h n) -> p h n", h=H),
                                     ACT.Copy).then_inc(tokens_kept, 1)
                act.wait_ge(crossed, i + 1)
                nc.scalar.activation(xk[:, :, 0:N], heads(5, N), ACT.Copy).then_inc(x_kept, 1)
                act.wait_ge(solved, i + 1)
                nc.scalar.activation(uw[:], heads(6, 2 * N), ACT.Copy, scale=-1.0).then_inc(uw_kept, 1)
                act.wait_ge(summed, i + 1)
                nc.scalar.activation(own[:], heads(5, P)[0:N], ACT.Copy).then_inc(own_kept, 1)

        @block.vector
        def _(dve):
            tt = nc.vector.tensor_tensor
            dve.sem_inc(y_kept, 2)
            nc.vector.memset(state[:, 0], 0.0).then_inc(s_kept, 1)
            above = K.const("chunk_above").unsqueeze(1).to_broadcast([P, H, P])
            upto = K.const("chunk_upto").unsqueeze(1).to_broadcast([P, H, P])
            with dve.Fori(0, NT) as i:
                dve.wait_ge(y_ready, i + 1)
                for s, src in enumerate(sources):
                    nc.vector.tensor_copy(feat[:, s, 1::2, :], src[64:P, :, bass.ds(i * P, P)]).then_inc(shifted, 1)
                for n, (dst, mask) in enumerate(((m2, above), (n1, upto), (n2, upto))):
                    dve.wait_ge(scored, i * 3 + (n + 1))
                    tt(dst[:], heads(2 + n, P), mask, ALU.mult).then_inc(masked, 1)
                dve.wait_ge(queried, i + 1)
                tt(q[:], heads(4, P)[0:N], feat[:, 4], ALU.add).then_inc(q_kept, 1)
                dve.wait_ge(moved, i + 1)
                tt(grow[:], K.ps[0:N, 0:4, 0:RW].rearrange("p g (h n) -> p g h n", h=H),
                   K.const("ident")[0:N, 0:N].unsqueeze(1).unsqueeze(1).to_broadcast([N, 4, H, N]), ALU.add).then_inc(g_kept, 1)
                nc.vector.tensor_copy(add[:], K.ps[0:N, 0:4, RW:2 * RW].rearrange("p g (h n) -> p g h n", h=H)).then_inc(h_kept, 1)
                for g in range(4):
                    dve.wait_ge(stepped, i * 4 + (g + 1))
                    tt(state[:, (g + 1) % 2], heads(7, N)[0:N],
                       W["whole"][:, :, bass.ds(i * 4 + g, 1)].to_broadcast([N, H, N]), ALU.mult).then_inc(s_kept, 1)
                dve.wait_ge(own_kept, i + 1)
                dve.wait_ge(y_ready, i + 2)
                for half in range(2):
                    tt(y[64 * half:64 * half + 64, :, bass.ds(i * P, P)], own[:, half::2, :], heads(6, P)[0:N, half::2],
                       ALU.add).then_inc(y_kept, 1)


def rwkv_finish(K, y, W, out):
    nc = K.nc
    eps = 64e-5
    summed, centred, squared, meaned, rooted = (K.sem(f"rf_{n}") for n in ("summed", "centred", "squared", "meaned", "rooted"))
    with ExitStack() as scope, nc.Block() as block:
        sq = K.sb(scope, "rf_sq", [P, 2, S])
        var = K.sb(scope, "rf_var", [P, 2, S])

        def banks(n):
            return K.ps[:, n:n + 4, :].rearrange("p (j h) n -> p j (h n)", j=2)

        @block.tensor
        def _(pe):
            for n, src in enumerate((y, sq)):
                if n:
                    pe.wait_ge(squared, 1)
                for j in range(2):
                    for h in range(2):
                        mm = nc.tensor.matmul(K.ps[:, 4 * n + 2 * j + h, :], K.const("pair"), src[:, j, h * HALF:(h + 1) * HALF],
                                              start=True, stop=True)
                mm.then_inc(summed, 1)

        @block.vector
        def _(dve):
            stt = nc.vector.scalar_tensor_tensor
            dve.wait_ge(summed, 1)
            stt(y[:], banks(0), -1.0 / 64, y[:], ALU.mult, ALU.add).then_inc(centred, 1)
            dve.wait_ge(summed, 2)
            nc.vector.tensor_scalar(var[:], banks(4), 1.0 / 64, eps, ALU.mult, ALU.add).then_inc(meaned, 1)
            dve.wait_ge(rooted, 1)
            nc.vector.reciprocal(var[:], var[:])
            dve.drain()
            nc.vector.tensor_tensor(y[:], y[:], var[:], ALU.mult)
            dve.drain()
            for j in range(2):
                nc.vector.tensor_scalar(y[:, j, :], y[:, j, :], K.vec("rwkv_ln_w_2", j), K.vec("rwkv_ln_b_2", j), ALU.mult, ALU.add)
            dve.drain()
            nc.vector.tensor_tensor(y[:], y[:], W["bonus"][:], ALU.add)
            dve.drain()
            nc.vector.tensor_tensor(out, y[:], W["g"][:], ALU.mult)

        @block.scalar
        def _(act):
            act.wait_ge(centred, 1)
            nc.scalar.activation(sq[:], y[:], ACT.Square).then_inc(squared, 1)
            act.wait_ge(meaned, 1)
            nc.scalar.activation(var[:], var[:], ACT.Sqrt).then_inc(rooted, 1)


def rwkv(K, z, yT):
    scratch = {n: K.dram(f"rwkv_{n}", (P, CHUNK, CHUNK)) for n in ("minus", "inverse")}
    with ExitStack() as scope:
        wide = lambda name: K.sb(scope, f"rwkv_{name}", [P, 2, S])
        W = {name: wide(name) for name in ("kk", "b", "g", "bonus")}
        W["whole"] = K.sb(scope, "rwkv_whole", [64, 4, S // CHUNK])
        zm = K.sb(scope, "rwkv_zm", [P, 8, S])
        solve = K.sb(scope, "rwkv_solve", [P, 4 * NT, P])
        rwkv_gates(K, z, zm, W)
        rwkv_solve(K, W, solve, scratch)
        y = zm[:, 6:8, :]
        rwkv_chunks(K, zm, W, solve, y)
        rwkv_finish(K, y, W, yT[:, 0:2, :])


def first_block(K, x):
    x_dram = K.A["x"].rearrange("o s d -> (o s) d")
    rows, results = K.dram("expert_rows", (S, D)), K.dram("expert_results", (ROWS, D))
    table = K.dram("expert_table", (ROWS, 1), I32)
    flat = x[:].rearrange("p t d -> p (t d)")
    with ExitStack() as right, ExitStack() as scope:
        h_hi, h_lo = (K.sb(right, f"h1_{part}", [P, KT, S], F32R, side="right") for part in ("hi", "lo"))
        conv = K.sb(scope, "conv", [P, CT, S])
        nothing, cleared = K.sb(scope, "nothing", [P, 256]), K.sem("e_cleared")
        with ExitStack() as inner:
            whole = K.sb(inner, "n1_whole", [P, 2 * D])
            norm_and_turn(K, "n1", x, K.vec("attn_norm_g", 0, KT), h_hi, h_lo, whole[:], src=x_dram)
        with ExitStack() as inner:
            qkv = K.sb(inner, "qkv", [P, NT, 3 * HALF])
            project_and_convolve(K, h_hi, h_lo, conv, qkv, flat)
            clear_results(K, results, nothing, cleared)
            conv_norm(K, conv)
            qkT = x
            group_norm_and_turn(K, "qk", qkv[:, :, 0:2 * HALF], 4 * HEADS, K.qk_gain[:], qkT[:])
            o = qkv[:, :, 0:HALF]
            R = {f"{r}_{part}": K.dram(f"{r}_{part}", (HALF, S)) for r in "qk" for part in ("hi", "lo")}
            part_rows(K, "dp", [(qkT[:, j, :], *(R[f"{r}_{part}"][(j % HEADS) * P:(j % HEADS + 1) * P] for part in ("hi", "lo")))
                                for j in range(2 * HEADS) for r in ("q" if j < HEADS else "k")])
            soft_attention(K, "da", 2 * HEADS, R, qkv, 2 * HALF, VD, o, 0, HD ** -0.5, decay=False, paired=True, room=flat)
            oT = K.sb(right, "oT", [P, HEADS, S], side="right")
            group_norm_and_turn(K, "on", o, HEADS, K.head_gain[:], oT[:])
        merged = K.sb(scope, "merged", [P, KT, S])
        merge_branches(K, h_hi, h_lo, conv, oT, merged)
        project_and_add(K, "wo", merged, KT, K.A["w_out"], None, x, None, src=x_dram, out=None)
    with ExitStack() as scope:
        logits = K.sb(scope, "logits", [P, NT, GROUPS + EXPERTS])
        weights = K.sb(scope, "weights", [P, NT, 2])
        dest = K.sb(scope, "dest", [P, 2 * NT], I32)
        expert_of_block = K.sb(scope, "expert_of_block", [P, BLOCKS + 1], I32)
        pairs = K.sb(scope, "pairs", [P, 1], I32)
        norm_and_route(K, x, rows, logits)
        with ExitStack() as inner:
            experts = ExpertWeights(K, inner)
            choose_experts(K, logits, weights, dest, expert_of_block, pairs, table, experts)
            run_experts(K, rows, table, expert_of_block, pairs, results, experts, cleared)
        combine_experts(K, x, weights, dest, results)


def mixers(K, h_hi, h_lo, h_scope, y_scope, table_scope, z):
    nc = K.nc
    both = ("hi", "lo")
    window = {name: K.dram(name, (n, S)) for name, n in (("swa_q", RW), ("swa_k", RW))}
    window["band"] = K.dram("window_band", (4, 3 * P))
    fox = {f"{r}_{part}": K.dram(f"fox_{r}_{part}", (RW, S)) for r in "qk" for part in both}
    mlstm = {f"{r}_{part}": K.dram(f"mlstm_{r}_{part}", (P, S)) for r in "qk" for part in both}
    fox["decay"], mlstm["rise"] = K.dram("fox_decay", (4, 2, S)), K.dram("mlstm_rise", (4, 2, S))
    with ExitStack() as scope:
        sb = lambda name, shape: K.sb(scope, name, shape)
        Z = {"rwkv": z, "mlstm_o": sb("mlstm_o", [P, 2, S]), "values": sb("values", [P, NT, 3 * RW])}
        with ExitStack() as inner:
            for name, tiles in (("fox_q", 2), ("fox_k", 2), ("swa_q", 2), ("swa_k", 1)):
                Z[name] = K.sb(inner, f"z_{name}", [P, tiles, S])
            Z["mlstm"] = K.sb(inner, "z_mlstm", [P, 2, 3 + S])
            Z["gates"] = K.sb(inner, "z_gates", [4, 3, S])
            with nc.Block() as block:

                @block.vector
                def _(dve):
                    nc.vector.memset(z[:, :, 0:1], 0.0)
                    nc.vector.memset(Z["mlstm"][:, :, 0:3], 0.0)

            units, slabs = mixer_columns(Z)
            project_columns(K, "z", K.A["w_in_2"], h_hi, h_lo, units, slabs, gates=Z["gates"])
            h_scope.close()
            yT = K.sb(y_scope, "yT", [P, KT, S], side="right")
            K.tables["mixer_consts"] = K.sb(table_scope, "mixer_table", [P, K.A["mixer_consts"].shape[1]], side="right")
            K.window_bias, K.sinks = (K.sb(scope, name, shape, side="right")
                                      for name, shape in (("window_bias", [P, 4, 2 * P]), ("sinks", [P, 4])))
            K.mlstm_keys = K.sb(scope, "mlstm_keys", [P, 4 * NT], side="right")
            Z["mlstm_qk"] = K.sb(inner, "z_mlstm_qk", [P, 2, S])
            Z["total"], Z["keys"] = K.sb(inner, "z_total", [4, 2, S]), K.sb(inner, "z_keys", [4, 2, S])
            prepare_mixers(K, Z, window)
            part_rows(K, "mp", [(Z[f"fox_{r}"][:, j, :], *(fox[f"{r}_{part}"][j * P:(j + 1) * P] for part in both))
                                for r in "qk" for j in range(2)]
                      + [(Z["mlstm_qk"][:, j, :], *(mlstm[f"{r}_{part}"] for part in both)) for j, r in enumerate("qk")]
                      + [(Z["keys"][:, 1, :], fox["decay"][:, 0], fox["decay"][:, 1]),
                         (Z["total"][:, 0, :], mlstm["rise"][:, 0], mlstm["rise"][:, 1])])
        o = sb("o_soft", [P, NT, 2 * RW])
        o_mlstm = sb("o_mlstm", [P, NT, RW])
        values = Z["values"]
        soft_attention(K, "fx", 4, fox, values, RW, HD, o, RW, 1.0, decay=True, paired=False)
        window_attention(K, "sw", window["swa_q"], window["swa_k"], values, 2 * RW, o, 0)
        mlstm_attention(K, "ml", mlstm, values, 0, o_mlstm, 0)
        turn(K, "tm", o, yT[:, 4:8, :])
        group_norm_and_turn(K, "mn", o_mlstm[:], 4, K.vec("mlstm_norm_2", 0, 2), yT[:, 2:4, :], gate=Z["mlstm_o"][:])
    K.recycle()
    rwkv(K, z, yT)
    return yT


def build(nc, A, out):
    with ExitStack() as ctx:
        K = Kernel(nc, A, out, ctx)
        load_vectors(K)
        x_kept, x_mixed = K.dram("x_kept", (S, D)), K.dram("x_mixed", (S, D))
        h_scope, y_scope = ctx.enter_context(ExitStack()), ctx.enter_context(ExitStack())
        with ExitStack() as scope:
            x = K.sb(scope, "x_first", [P, NT, D])
            first_block(K, x)
            K.recycle()
            h_hi, h_lo = (K.sb(h_scope, f"h2_{part}", [P, KT, S], F32R, side="right") for part in ("hi", "lo"))
            whole = K.sb(scope, "n3_whole", [P, 2 * D])
            norm_and_turn(K, "n3", x, K.vec("norm_mix_pre_2", 0, KT), h_hi, h_lo, whole[:], keep=x_kept)
        with ExitStack() as scope:
            z = K.sb(scope, "z_rwkv", [P, 8, 1 + S])
            yT = mixers(K, h_hi, h_lo, h_scope, y_scope, scope, z)
        with ExitStack() as scope:
            f = K.sb(scope, "f", [P, FFT, S])
            x, y = f[:, 0:NT, :], f[:, NT:2 * NT, :]
            project_and_add(K, "o2", yT, KT, A["w_out_2"], A["norm_mix_post_2"], x, y, src=x_kept, out=x_mixed)
            with ExitStack() as inner:
                h_hi, h_lo = (K.sb(inner, f"h3_{part}", [P, KT, S], F32R) for part in ("hi", "lo"))
                norm_and_turn(K, "n4", x, K.vec("norm_ffn_pre_2", 0, KT), h_hi, h_lo,
                              y[:, 0:2, :].rearrange("p t d -> p (t d)"))
                ffn_up(K, h_hi, h_lo, yT[:].rearrange("p k n -> p (k n)"), f)
            x = K.sb(scope, "x_last", [P, NT, D])
            project_and_add(K, "fd", f, FFT, A["ffn_w_down_2"], A["norm_ffn_post_2"], x, yT, src=x_mixed, out=out)


_INS = ["x", "attn_norm_g", "w_in", "conv_dw_w", "conv_dw_b", "conv_ln_g", "conv_ln_b", "w_conv_out", "q_norm_g", "k_norm_g",
        "lambda_q1", "lambda_k1", "lambda_q2", "lambda_k2", "subln_g", "w_attn_out", "w_out", "ffn_norm_g", "w_router_group",
        "b_router_group", "w_router_expert", "b_router_expert", "w_gate_e", "w_up_e", "w_down_e", "w_in_2", "w_out_2",
        "norm_mix_pre_2", "norm_mix_post_2", "norm_ffn_pre_2", "norm_ffn_post_2", "rwkv_mu_2", "rwkv_w0_2", "rwkv_w_up_2",
        "rwkv_a0_2", "rwkv_a_up_2", "rwkv_g_up_2", "rwkv_k_k_2", "rwkv_k_a_2", "rwkv_r_k_2", "rwkv_ln_w_2", "rwkv_ln_b_2",
        "mlstm_conv_w_2", "mlstm_conv_b_2", "mlstm_b_i_2", "mlstm_b_f_2", "mlstm_norm_2", "swa_sinks_2", "fox_b_f_2", "rel_bias_2",
        "ffn_w_up_2", "ffn_conv_w_2", "ffn_conv_b_2", "ffn_w_down_2"]


def kernel(**inputs):
    import concourse.bacc as bacc
    from concourse.bass_utils import run_bass_kernel_spmd

    nc = bacc.Bacc("TRN2", target_bir_lowering=False, num_devices=1)
    arrays, A = {}, {}
    given = {name: np.ascontiguousarray(inputs[name]) for name in _INS}
    given.update(shape_constants()[0])
    for name, a in given.items():
        arrays[f"in_{name}_dram"] = a
        A[name] = nc.dram_tensor(f"in_{name}_dram", a.shape, mybir.dt.from_np(a.dtype), kind="ExternalInput").ap()
    out = nc.dram_tensor("out_0_dram", (1, S, D), F32, kind="ExternalOutput").ap()
    build(nc, A, out.rearrange("o s d -> (o s) d"))
    r = run_bass_kernel_spmd(nc, [arrays], core_ids=[0])
    return r.results[0]["out_0_dram"]
```

```python
import math
from contextlib import ExitStack

import numpy as np

import concourse.bass as bass
from concourse import mybir

F32 = mybir.dt.float32
F32R = mybir.dt.float32r
I32 = mybir.dt.int32
U32 = mybir.dt.uint32
ACT = mybir.ActivationFunctionType
ALU = mybir.AluOpType
AX = mybir.AxisListType.X

P = 128
S = 1024
D = 1024
NT = S // P
KT = D // P
HALF = 512
EPS = 1e-6
NEG = -1e30

CONV_CH, TAPS = 512, 31
CT = CONV_CH // P
HEADS, HD, VD = 4, 64, 128
LAM_INIT = 0.8 - 0.6 * math.exp(0.0)
GROUPS, EPG = 4, 8
EXPERTS = GROUPS * EPG
DE = 512
FT = DE // P
ROWS = 2 * S + EXPERTS * P
BLOCKS = ROWS // P
COL_QKV, COL_GATE = 1024, 2560

RW = 256
CHUNK = 32
ML0, SW0, FX0, N_IN = 1024, 1800, 2312, 3084
WINDOW = 128
DFF = 2816
FFT = DFF // P


def shape_constants():
    p, j = np.arange(P)[:, None], np.arange(P)[None, :]
    same = (p // CHUNK) == (j // CHUNK)
    parts = {
        "ident": p == j,
        "flip": p == P - 1 - j,
        "ones": np.ones((P, P)),
        "pair": (p // 64) == (j // 64),
        "before": p < j,
        "causal": np.where(j <= p, 0.0, NEG),
        "causal_t": np.where(p <= j, 0.0, NEG),
        "chunk_below": same & (j < p),
        "chunk_above": same & (p < j),
        "chunk_upto": same & (p <= j),
        "block_start": np.broadcast_to(np.arange(BLOCKS) * P, (P, BLOCKS)),
        "rank4": np.broadcast_to(np.arange(GROUPS, 0, -1), (P, GROUPS)),
        "rank8": np.broadcast_to(np.arange(EPG, 0, -1), (P, EPG)),
        "token": np.arange(NT)[None, :] * P + p,
    }
    dist = 255 - np.arange(3 * P)
    d = np.maximum(np.clip(dist, 0, WINDOW - 1), 1).astype(np.float32)
    large = 16 + (np.log(d / 16) / math.log(128 / 16) * 16).astype(np.int32)
    bucket = np.where(np.clip(dist, 0, WINDOW - 1) < 16, np.clip(dist, 0, WINDOW - 1), np.minimum(large, 31))
    inside = (dist >= 0) & (dist < WINDOW)
    onehot = np.zeros((P, 3 * P))
    onehot[:32] = (np.arange(32)[:, None] == bucket[None, :]) & inside[None, :]
    parts["bucket"] = onehot
    parts["outside"] = np.broadcast_to(np.where(inside, 0.0, NEG), (P, 3 * P))
    for_mixers = ("flip", "pair", "chunk_below", "chunk_above", "chunk_upto", "bucket", "outside")
    tables, places = {}, {}
    for table, names in (("shape_consts", [n for n in parts if n not in for_mixers]), ("mixer_consts", for_mixers)):
        off = 0
        for name in names:
            places[name] = (table, off, off + parts[name].shape[1])
            off += parts[name].shape[1]
        tables[table] = np.ascontiguousarray(
            np.concatenate([np.broadcast_to(parts[n], (P, parts[n].shape[1])).astype(np.float32) for n in names], 1))
    return tables, places


CONST_PLACES = shape_constants()[1]

VECTORS = [
    ("conv_dw_w", TAPS * CT),
    ("attn_norm_g", KT), ("ffn_norm_g", KT), ("norm_mix_pre_2", KT), ("norm_ffn_pre_2", KT),
    ("conv_dw_b", CT), ("conv_ln_g", CT), ("conv_ln_b", CT), ("subln_g", 1), ("q_norm_g", 1), ("k_norm_g", 1),
    ("rwkv_mu_2", 8), ("rwkv_w0_2", 2), ("rwkv_a0_2", 2), ("rwkv_k_k_2", 2), ("rwkv_k_a_2", 2), ("rwkv_r_k_2", 2),
    ("rwkv_ln_w_2", 2), ("rwkv_ln_b_2", 2), ("mlstm_conv_w_2", 8), ("mlstm_conv_b_2", 2), ("mlstm_norm_2", 2),
    ("ffn_conv_w_2", 3 * FFT), ("ffn_conv_b_2", FFT),
]


def vector_places():
    places, tile, row = {}, 0, 0
    for name, n in VECTORS:
        if row + n > P:
            tile, row = tile + 1, 0
        places[name] = (tile, row, n)
        row += n
    return places, tile + 1


class Kernel:

    def __init__(self, nc, A, out, ctx):
        self.nc, self.A, self.out, self.ctx = nc, A, out, ctx
        self.ps = ctx.enter_context(nc.psum_tensor("banks", [P, 8, HALF], F32))
        self.sems = []
        self.tables = {}

    def place_vectors(self):
        self.tables["shape_consts"] = self.sb(self.ctx, "consts", [P, self.A["shape_consts"].shape[1]])
        self.vplaces, tiles = vector_places()
        self.vectors = self.sb(self.ctx, "vectors", [P, tiles * P])
        self.row_squares = self.sb(self.ctx, "row_squares", [P, NT])
        self.lam = self.sb(self.ctx, "minus_lambda", [P, 1])
        self.qk_gain = self.sb(self.ctx, "qk_gain", [P, 2 * HEADS])
        self.head_gain = self.sb(self.ctx, "head_gain", [P, HEADS])
        self.ident_r, self.causal_r, self.causal_t_r = (self.sb(self.ctx, f"{name}_r", [P, P], F32R) for name in ("ident", "causal", "causal_t"))

    def sem(self, name):
        self.sems.append(self.nc.alloc_semaphore(name))
        return self.sems[-1]

    def recycle(self):
        self.nc.clear_and_free_semaphores(self.sems)
        self.nc.all_engine_barrier()
        self.sems = []

    def sb(self, scope, name, shape, dt=F32, side=None):
        return scope.enter_context(self.nc.sbuf_tensor(name, shape, dt, side=side))

    def dram(self, name, shape, dt=F32):
        return self.nc.dram_tensor(name, shape, dt).ap()

    def const(self, name):
        table, a, b = CONST_PLACES[name]
        return self.tables[table][:, a:b]

    def vec(self, name, j=0, n=1):
        tile, row, _ = self.vplaces[name]
        return self.vectors[:, tile * P + row + j:tile * P + row + j + n]


def rows_of(ap):
    return ap.rearrange("o (r p) -> (o r) p", p=P)


def load_vectors(K, x, x_dram):
    nc, A = K.nc, K.A
    tiles = vector_places()[1]
    x_landed = [K.sem(f"x_landed{h}") for h in range(2)]
    zeroed, landed, const_landed = K.sem("rows_zeroed"), K.sem("rows_landed"), K.sem("const_landed")
    turned, lam_landed, lam_dot, lam_exp = K.sem("rows_turned"), K.sem("lam_landed"), K.sem("lam_dot"), K.sem("lam_exp")
    loads = 0
    with ExitStack() as scope, nc.Block() as block:
        rows = K.sb(scope, "vector_rows", [P, tiles, P])
        lam4 = K.sb(scope, "lam_vectors", [P, 4, HD])
        prod = K.sb(scope, "lam_products", [P, 2, HD])
        dots = K.sb(scope, "lam_dots", [P, 2])
        exps = K.sb(scope, "lam_exps", [P, 2])
        sources = []
        for name, n in VECTORS:
            tile, row, _ = K.vplaces[name]
            src = A[name]
            if name in ("q_norm_g", "k_norm_g"):
                sources += [(rows[row:row + 1, tile, 0:HD], src), (rows[row:row + 1, tile, HD:P], src)]
            elif len(src.shape) == 3 and name != "rwkv_r_k_2":
                sources.append((rows[row:row + n, tile, :], src.rearrange("o w (r p) -> (o w r) p", p=P)))
            elif name == "rwkv_r_k_2":
                sources.append((rows[row:row + n, tile, :], src.rearrange("o (r g) n -> (o r) (g n)", g=2)))
            else:
                sources.append((rows[row:row + n, tile, :], rows_of(src)))

        @block.sync
        def _(sp):
            sp.dma_start(K.tables["shape_consts"][:], A["shape_consts"]).then_inc(const_landed, 16)
            for j, name in enumerate(("lambda_q1", "lambda_q2", "lambda_k1", "lambda_k2")):
                sp.dma_start(lam4[:, j, :], A[name].to_broadcast([P, HD])).then_inc(lam_landed, 16)
            sp.wait_ge(zeroed, 1)
            for dst, src in sources:
                sp.dma_start(dst, src).then_inc(landed, 16)

        @block.tensor
        def _(pe):
            pe.wait_ge(const_landed, 16)
            pe.wait_ge(landed, 16 * len(sources))
            for t in range(tiles):
                mm = nc.tensor.transpose(K.ps[:, 0, t * P:(t + 1) * P], rows[:, t, :], K.const("ident"))
            mm.then_inc(turned, 1)

        @block.vector
        def _(dve):
            nc.vector.memset(rows[:], 0.0).then_inc(zeroed, 1)
            dve.wait_ge(lam_landed, 64)
            nc.vector.tensor_tensor(prod[:], lam4[:, 0:2, :], lam4[:, 2:4, :], ALU.mult)
            dve.drain()
            nc.vector.tensor_reduce(dots[:], prod[:], AX, ALU.add).then_inc(lam_dot, 1)
            dve.wait_ge(lam_exp, 1)
            nc.vector.tensor_scalar(K.lam[:], exps[:, 1:2], exps[:, 0:1], -LAM_INIT, ALU.subtract, ALU.add)
            dve.wait_ge(turned, 1)
            nc.vector.tensor_copy(K.vectors[:], K.ps[:, 0, 0:tiles * P])
            dve.drain()
            for h in range(HEADS):
                nc.vector.tensor_copy(K.qk_gain[:, h:h + 1], K.vec("q_norm_g"))
                nc.vector.tensor_copy(K.qk_gain[:, HEADS + h:HEADS + h + 1], K.vec("k_norm_g"))
                nc.vector.tensor_scalar(K.head_gain[:, h:h + 1], K.vec("subln_g"), 1.0 - LAM_INIT, None, ALU.mult)

        @block.scalar
        def _(act):
            for h in range(2):
                half = slice(h * NT // 2, (h + 1) * NT // 2)
                act.dma_start(x[:, half, :], x_dram.rearrange("(t p) d -> p t d", p=P)[:, half, :]).then_inc(x_landed[h], 16)
            act.wait_ge(const_landed, 16)
            for dst, name in ((K.ident_r, "ident"), (K.causal_r, "causal"), (K.causal_t_r, "causal_t")):
                nc.scalar.activation(dst[:], K.const(name), ACT.Copy)
            act.wait_ge(lam_dot, 1)
            nc.scalar.activation(exps[:], dots[:], ACT.Exp).then_inc(lam_exp, 1)
    return x_landed


def norm_and_turn(K, tag, x, gain, hi, lo, room, landed=None, keep=None):
    nc = K.nc
    squared, meaned, rooted, rated, begun = (K.sem(f"{tag}_{n}") for n in ("squared", "meaned", "rooted", "rated", "begun"))
    scaled, turned, gained, rounded = (K.sem(f"{tag}_{n}") for n in ("scaled", "turned", "gained", "rounded"))
    with ExitStack() as scope, nc.Block() as block:
        junk = None if landed is None else K.sb(scope, f"{tag}_junk", [P, D])
        ss = K.row_squares
        rstd = K.sb(scope, f"{tag}_rstd", [P, NT])
        xn = K.sb(scope, f"{tag}_xn", [P, 2, D])
        whole = room.rearrange("p (b k n) -> p b k n", b=2, k=KT)

        if keep is not None:
            x_kept = K.sem(f"{tag}_x_kept")

            @block.sync
            def _(sp):
                sp.dma_start(keep.rearrange("(t p) d -> p t d", p=P), x[:]).then_inc(x_kept, 16)
                sp.wait_ge(x_kept, 16)

        @block.scalar
        def _(act):
            if landed is not None:
                for h in range(2):
                    act.wait_ge(landed[h], 16)
                    with act.Fori(4 * h, 4 * h + 4) as t:
                        nc.scalar.activation(junk[:], x[:, t, :], ACT.Square, accum_out=ss[:, bass.ds(t, 1)])
                        act.drain()
            act.sem_inc(squared, 1)
            act.wait_ge(meaned, 1)
            nc.scalar.activation(rstd[:], ss[:], ACT.Sqrt).then_inc(rooted, 1)
            act.wait_ge(rated, 1)

            def scale(t, b):
                act.wait_ge(turned, t + 1)
                act.sem_inc(begun, 1)
                nc.scalar.activation(xn[:, b, :], x[:, t, :], ACT.Copy, scale=rstd[:, bass.ds(t, 1)]).then_inc(scaled, 1)

            def round_off(t, b):
                act.wait_ge(gained, t + 3)
                act.sem_inc(begun, 1)
                nc.scalar.activation(hi[:, :, bass.ds(t * P, P)], whole[:, b], ACT.Copy).then_inc(rounded, 1)

            for b in range(2):
                scale(b, b)
            with act.Fori(0, NT // 2 - 1) as i:
                for b in range(2):
                    round_off(i * 2 + b, b)
                    scale(i * 2 + (b + 2), b)
            for b in range(2):
                round_off(NT - 2 + b, b)

        @block.vector
        def _(dve):
            def times_gain(t, b):
                dve.wait_ge(turned, t + 3)
                nc.vector.tensor_tensor(whole[:, b], K.ps[:, 2 * b:2 * b + 2, :].rearrange("p c (k n) -> p (c k) n", n=P),
                                        gain.unsqueeze(2).to_broadcast([P, KT, P]), ALU.mult).then_inc(gained, 1)

            def rest(t, b):
                tokens = bass.ds(t * P, P)
                dve.wait_ge(rounded, t + 1)
                nc.vector.tensor_tensor(lo[:, :, tokens], whole[:, b], hi[:, :, tokens].bitcast(F32), ALU.subtract)
                dve.drain()

            dve.sem_inc(gained, 2)
            dve.wait_ge(squared, 1)
            nc.vector.tensor_scalar(ss[:], ss[:], 1.0 / D, EPS, ALU.mult, ALU.add).then_inc(meaned, 1)
            dve.wait_ge(rooted, 1)
            nc.vector.reciprocal(rstd[:], rstd[:]).then_inc(rated, 1)
            times_gain(0, 0)
            with dve.Fori(0, NT // 2 - 1) as i:
                for b in range(2):
                    times_gain(i * 2 + (b + 1), 1 - b)
                    rest(i * 2 + b, b)
            times_gain(NT - 1, 1)
            for b in range(2):
                rest(NT - 2 + b, b)

        @block.tensor
        def _(pe):
            pe.sem_inc(turned, 2)
            with pe.Fori(0, NT // 2) as i:
                for b in range(2):
                    pe.wait_ge(scaled, i * 2 + (b + 1))
                    pe.wait_ge(gained, i * 2 + (b + 1))
                    for k in range(KT):
                        mm = nc.tensor.transpose(K.ps[:, 2 * b + k // 4, (k % 4) * P:(k % 4 + 1) * P],
                                                 xn[:, b, k * P:(k + 1) * P], K.const("ident"))
                    mm.then_inc(turned, 1)


def project_columns(K, tag, weight, h_hi, h_lo, units, slabs, gates=None, vector=None):
    nc = K.nc
    U, C = len(units), KT * len(slabs)
    w_in = weight.rearrange("o (k p) n -> p (o k) n", p=P)
    widths = [max(at + n for _, n, at in pieces) for pieces, _ in slabs]
    landed = [K.sem(f"{tag}_landed{b}") for b in range(2)]
    rounded, split, projected, chunked, kept, gates_kept = (K.sem(f"{tag}_{n}") for n in
        ("rounded", "split", "projected", "chunked", "kept", "gates_kept"))
    with ExitStack() as scope, nc.Block() as block:
        w = K.sb(scope, f"{tag}_w", [P, 2, KT * P])
        w_hi = K.sb(scope, f"{tag}_w_hi", [P, 2, KT * P], F32R)
        w_lo = K.sb(scope, f"{tag}_w_lo", [P, 2, KT * P], F32R)
        sizes = [KT * P] * U + [m for m in widths for _ in range(KT)]
        pieces_of = [pieces for pieces, *_ in units] + [pieces for pieces, _ in slabs for _ in range(KT)]

        @block.sync
        def _(sp):
            for n, pieces in enumerate(pieces_of):
                if n >= 2:
                    sp.wait_ge(split, n - 1)
                for col, m, at in pieces:
                    if n < U:
                        sp.dma_start(w[:, n % 2].rearrange("p (k n) -> p k n", k=KT)[:, :, at:at + m], w_in[:, :, col:col + m],
                                     allow_slow_non_contiguous=True).then_inc(landed[n % 2], 16)
                    else:
                        sp.dma_start(w[:, n % 2, at:at + m], w_in[:, (n - U) % KT, col:col + m]).then_inc(landed[n % 2], 16)

        @block.tensor
        def _(pe):
            mm = nc.tensor.matmul
            with pe.Fori(0, U // 2) as i:
                for b in range(2):
                    pe.wait_ge(split, i * 2 + (b + 1))
                    for h in range(2):
                        pe.wait_ge(kept, i * 4 + (2 * b + h + 1))
                        bank, tokens = K.ps[:, 2 * b + h, :], slice(h * HALF, (h + 1) * HALF)
                        for k in range(KT):
                            cols = slice(k * P, (k + 1) * P)
                            mm(bank, w_hi[:, b, cols], h_hi[:, k, tokens], start=(k == 0), stop=False)
                            mm(bank, w_hi[:, b, cols], h_lo[:, k, tokens], start=False, stop=False)
                            last = mm(bank, w_lo[:, b, cols], h_hi[:, k, tokens], start=False, stop=(k == KT - 1))
                        last.then_inc(projected, 1)
            done = 2 * U + 4 - (2 if gates else 0)
            if gates:
                pe.wait_ge(gates_kept, 2)
            for s, m in enumerate(widths):
                for k in range(KT):
                    n = U + s * KT + k
                    pe.wait_ge(split, n + 1)
                    for t in range(NT):
                        if k == 0:
                            pe.wait_ge(kept, done if s == 0 else done + (s - 1) * NT + t + 1)
                        bank, tokens, b = K.ps[:, t, 0:m], slice(t * P, (t + 1) * P), n % 2
                        mm(bank, h_hi[:, k, tokens], w_hi[:, b, 0:m], start=(k == 0), stop=False)
                        mm(bank, h_hi[:, k, tokens], w_lo[:, b, 0:m], start=False, stop=False)
                        last = mm(bank, h_lo[:, k, tokens], w_hi[:, b, 0:m], start=False, stop=(k == KT - 1))
                        if t == NT - 1:
                            last.then_inc(chunked, 1)
                        elif k == KT - 1:
                            last.then_inc(projected, 1)

        @block.scalar
        def _(act):
            act.sem_inc(kept, 4)
            loads = [0, 0]

            def fill(n):
                if n >= U + C:
                    return
                loads[n % 2] += 16 * len(pieces_of[n])
                act.wait_ge(landed[n % 2], loads[n % 2])
                nc.scalar.activation(w_hi[:, n % 2, 0:sizes[n]], w[:, n % 2, 0:sizes[n]], ACT.Copy).then_inc(rounded, 1)

            fill(0)
            fill(1)
            for u, (_, out, scale, func, wait) in enumerate(units):
                if wait is not None:
                    act.wait_ge(*wait)
                for h in range(2):
                    act.wait_ge(projected, 2 * u + h + 1)
                    if not (gates and u == U - 1):
                        nc.scalar.activation(out(h), K.ps[:, 2 * (u % 2) + h, :], func, scale=scale).then_inc(kept, 1)
                fill(u + 2)
            for s, (_, out) in enumerate(slabs):
                for k in range(KT):
                    n = s * KT + k
                    if k < KT - 1:
                        act.wait_ge(chunked, n + 1)
                        fill(U + n + 2)
                for t in range(NT):
                    if t < NT - 1:
                        act.wait_ge(projected, 2 * U + s * (NT - 1) + t + 1)
                    else:
                        act.wait_ge(chunked, (s + 1) * KT)
                    nc.scalar.activation(out(t), K.ps[:, t, 0:widths[s]], ACT.Copy).then_inc(kept, 1)
                fill(U + s * KT + KT + 1)

        @block.gpsimd
        def _(pool):
            for n, m in enumerate(sizes):
                pool.wait_ge(rounded, n + 1)
                nc.gpsimd.tensor_tensor(w_lo[:, n % 2, 0:m], w[:, n % 2, 0:m], w_hi[:, n % 2, 0:m].bitcast(F32), ALU.subtract) \
                    .then_inc(split, 1)

        @block.vector
        def _(dve):
            if gates:
                for h in range(2):
                    dve.wait_ge(projected, 2 * (U - 1) + h + 1)
                    for g in range(3):
                        copy = nc.vector.tensor_copy(gates[:, g, h * HALF:(h + 1) * HALF], K.ps[32 * g:32 * g + 4, 2 * ((U - 1) % 2) + h, :])
                    copy.then_inc(gates_kept, 1)
            if vector is not None:
                vector(dve, kept)


def project_and_convolve(K, h_hi, h_lo, conv, qkv, room):
    nc = K.nc
    PAD = TAPS - 1
    gated = K.sem("p_gated")
    y_end = CT * (PAD + S)
    y = room[:, 0:y_end].rearrange("p (c n) -> p c n", c=CT)
    gate = room[:, y_end:y_end + 2 * S].rearrange("p (b n) -> p b n", b=2)

    def tokens(tile, lead=0):
        return lambda h: tile[:, lead + h * HALF:lead + (h + 1) * HALF]

    units = []
    for c in range(CT):
        units.append(([(c * P, P, 0)], tokens(y[:, c, :], PAD), 1.0, ACT.Copy, None))
        units.append(([(CONV_CH + c * P, P, 0)], tokens(gate[:, c % 2, :]), 1.0, ACT.Sigmoid,
                      (gated, c - 1) if c >= 2 else None))
    slabs = [([(COL_QKV + s * HALF, HALF, 0)], lambda t, s=s: qkv[:, t, s * HALF:(s + 1) * HALF]) for s in range(3)]

    def convolve(dve, kept):
        nc.vector.memset(y[:, :, 0:PAD], 0.0)
        for c in range(CT):
            dve.wait_ge(kept, 4 * c + 8)
            nc.vector.tensor_tensor(y[:, c, PAD:PAD + S], y[:, c, PAD:PAD + S], gate[:, c % 2, :], ALU.mult).then_inc(gated, 1)
            dve.drain()
            tap = lambda j: K.vec("conv_dw_w", j * CT + c)
            nc.vector.tensor_scalar(conv[:, c, :], y[:, c, 0:S], tap(0), K.vec("conv_dw_b", c), ALU.mult, ALU.add)
            for j in range(1, TAPS):
                dve.drain()
                nc.vector.scalar_tensor_tensor(conv[:, c, :], y[:, c, j:j + S], tap(j), conv[:, c, :], ALU.mult, ALU.add)
        dve.drain()

    project_columns(K, "p", K.A["w_in"], h_hi, h_lo, units, slabs, vector=convolve)


def conv_norm(K, conv):
    nc = K.nc
    summed, centred, squared, varied, rooted, ready = (K.sem(f"cn_{n}") for n in
        ("summed", "centred", "squared", "varied", "rooted", "ready"))
    whitened = K.sem("cn_whitened")
    with ExitStack() as scope, nc.Block() as block:
        sq = K.sb(scope, "cn_sq", [P, CT, S])
        rstd = K.sb(scope, "cn_rstd", [P, S])

        def halves(bank):
            return K.ps[:, bank:bank + 2, :].rearrange("p b n -> p (b n)")

        @block.tensor
        def _(pe):
            for h in range(2):
                for c in range(CT):
                    mm = nc.tensor.matmul(K.ps[:, h, :], K.const("ones"), conv[:, c, h * HALF:(h + 1) * HALF],
                                          start=(c == 0), stop=(c == CT - 1))
            mm.then_inc(summed, 1)
            for h in range(2):
                for c in range(CT):
                    pe.wait_ge(squared, c + 1)
                    mm = nc.tensor.matmul(K.ps[:, 2 + h, :], K.const("ones"), sq[:, c, h * HALF:(h + 1) * HALF],
                                          start=(c == 0), stop=(c == CT - 1))
            mm.then_inc(varied, 1)

        @block.vector
        def _(dve):
            dve.wait_ge(summed, 1)
            for c in range(CT):
                nc.vector.scalar_tensor_tensor(conv[:, c, :], halves(0), -1.0 / CONV_CH, conv[:, c, :],
                                               ALU.mult, ALU.add).then_inc(centred, 1)
            dve.wait_ge(varied, 1)
            nc.vector.tensor_scalar(rstd[:], halves(2), 1.0 / CONV_CH, EPS, ALU.mult, ALU.add).then_inc(ready, 1)
            dve.wait_ge(rooted, 1)
            nc.vector.reciprocal(rstd[:], rstd[:])
            dve.drain()
            for c in range(CT):
                nc.vector.tensor_tensor(conv[:, c, :], conv[:, c, :], rstd[:], ALU.mult).then_inc(whitened, 1)

        @block.scalar
        def _(act):
            for c in range(CT):
                act.wait_ge(centred, c + 1)
                nc.scalar.activation(sq[:, c, :], conv[:, c, :], ACT.Square).then_inc(squared, 1)
            act.wait_ge(ready, 1)
            nc.scalar.activation(rstd[:], rstd[:], ACT.Sqrt).then_inc(rooted, 1)
            for c in range(CT):
                act.wait_ge(whitened, c + 1)
                nc.scalar.activation(conv[:, c, :], conv[:, c, :], ACT.Silu,
                                     scale=K.vec("conv_ln_g", c), bias=K.vec("conv_ln_b", c))


def group_norm_and_turn(K, tag, src, groups, gain, dst, gate=None):
    nc = K.nc
    width = src.shape[2]
    size, tiles = width // groups, width // P
    squared, summed, meaned, rooted, scaled, turned, kept = (K.sem(f"{tag}_{n}") for n in
        ("squared", "summed", "meaned", "rooted", "scaled", "turned", "kept"))
    with ExitStack() as scope, nc.Block() as block:
        sq = K.sb(scope, f"{tag}_sq", [P, 2, width])
        ss = K.sb(scope, f"{tag}_ss", [P, NT, groups])
        rstd = K.sb(scope, f"{tag}_rstd", [P, NT, groups])
        xn = K.sb(scope, f"{tag}_xn", [P, 2, width])

        @block.scalar
        def _(act):
            with act.Fori(0, NT // 2) as i:
                for b in range(2):
                    act.wait_ge(summed, i * 2 + (b + 1))
                    nc.scalar.activation(sq[:, b, :], src[:, i * 2 + b, :], ACT.Square).then_inc(squared, 1)
            act.wait_ge(meaned, 1)
            nc.scalar.activation(rstd[:], ss[:], ACT.Sqrt).then_inc(rooted, 1)

        @block.vector
        def _(dve):
            dve.sem_inc(kept, 2)
            dve.sem_inc(summed, 2)
            with dve.Fori(0, NT // 2) as i:
                for b in range(2):
                    dve.wait_ge(squared, i * 2 + (b + 1))
                    nc.vector.tensor_reduce(ss[:, i * 2 + b, :], sq[:, b, :].rearrange("p (g n) -> p g n", g=groups),
                                            AX, ALU.add).then_inc(summed, 1)
            dve.drain()
            nc.vector.tensor_scalar(ss[:], ss[:], 1.0 / size, EPS, ALU.mult, ALU.add).then_inc(meaned, 1)
            dve.wait_ge(rooted, 1)
            nc.vector.reciprocal(rstd[:], rstd[:])
            dve.drain()

            def scale(t, b):
                dve.wait_ge(turned, t + 1)
                nc.vector.tensor_tensor(
                    xn[:, b, :].rearrange("p (g n) -> p g n", g=groups),
                    src[:, bass.ds(t, 1), :].rearrange("p o (g n) -> p (o g) n", g=groups),
                    rstd[:, bass.ds(t, 1), :].rearrange("p o g -> p (o g)").unsqueeze(2).to_broadcast([P, groups, size]),
                    ALU.mult).then_inc(scaled, 1)

            def times_gain(t, b):
                dve.wait_ge(turned, t + 3)
                nc.vector.tensor_tensor(
                    dst[:, :, bass.ds(t * P, P)],
                    K.ps[:, 2 * b:2 * b + 2, :].rearrange("p c (k n) -> p (c k) n", n=P)[:, 0:tiles, :],
                    gain.unsqueeze(2).to_broadcast([P, tiles, P]), ALU.mult).then_inc(kept, 1)

            for b in range(2):
                scale(b, b)
            with dve.Fori(0, NT // 2 - 1) as i:
                for b in range(2):
                    times_gain(i * 2 + b, b)
                    scale(i * 2 + (b + 2), b)
            for b in range(2):
                times_gain(NT - 2 + b, b)
            if gate is not None:
                dve.drain()
                nc.vector.tensor_tensor(dst, dst, gate, ALU.mult)

        @block.tensor
        def _(pe):
            pe.sem_inc(turned, 2)
            with pe.Fori(0, NT // 2) as i:
                for b in range(2):
                    pe.wait_ge(scaled, i * 2 + (b + 1))
                    pe.wait_ge(kept, i * 2 + (b + 1))
                    for k in range(tiles):
                        mm = nc.tensor.transpose(K.ps[:, 2 * b + k // 4, (k % 4) * P:(k % 4 + 1) * P],
                                                 xn[:, b, k * P:(k + 1) * P], K.const("ident"))
                    mm.then_inc(turned, 1)


def part_rows(K, tag, jobs, slots=None):
    nc = K.nc
    rounded, split = K.sem(f"{tag}_rounded"), K.sem(f"{tag}_split")
    with ExitStack() as scope, nc.Block() as block:
        hi, lo = slots or (K.sb(scope, f"{tag}_{part}", [P, 2, S], F32R) for part in ("hi", "lo"))
        count = hi.shape[1]
        stored = [K.sem(f"{tag}_stored{b}") for b in range(count)]

        @block.scalar
        def _(act):
            for n, (src, _, _) in enumerate(jobs):
                if n >= count:
                    act.wait_ge(stored[n % count], 32 * (n // count))
                nc.scalar.activation(hi[0:src.shape[0], n % count, :], src, ACT.Copy).then_inc(rounded, 1)

        @block.vector
        def _(dve):
            for n, (src, _, _) in enumerate(jobs):
                m = src.shape[0]
                dve.wait_ge(rounded, n + 1)
                nc.vector.tensor_tensor(lo[0:m, n % count, :], src, hi[0:m, n % count, :].bitcast(F32), ALU.subtract).then_inc(split, 1)

        @block.sync
        def _(sp):
            for n, (src, to_hi, to_lo) in enumerate(jobs):
                sp.wait_ge(split, n + 1)
                sp.dma_start(to_hi, hi[0:src.shape[0], n % count, :].bitcast(F32)).then_inc(stored[n % count], 16)
                sp.dma_start(to_lo, lo[0:src.shape[0], n % count, :].bitcast(F32)).then_inc(stored[n % count], 16)
            for b in range(count):
                sp.wait_ge(stored[b], 32 * len(range(b, len(jobs), count)))


CHUNKS = [(half, j, max(half * HALF, j * P), (half + 1) * HALF - max(half * HALF, j * P))
          for half in range(2) for j in range(4 * (half + 1))]


def soft_attention(K, tag, maps, R, values, v_col, dv, o, o_col, scale, decay, paired, room=None):
    nc = K.nc
    MAX_ROW, EXTRA = 96, 64
    ROWS_2 = MAX_ROW + 1
    seen = EXTRA + (2 if decay else 0)
    loaded = [K.sem(f"{tag}_loaded{b}") for b in range(2)]
    filled, staged, scored, peaked, lowered, m_turned, m_kept, t_scored, exped, weighed, stored, begun, fetching = (K.sem(f"{tag}_{n}") for n in
        ("filled", "staged", "scored", "peaked", "lowered", "m_turned", "m_kept", "t_scored", "exped", "weighed", "stored", "begun", "fetching"))
    loads = 16 * (7 if decay else 6)
    NC = len(CHUNKS)
    with ExitStack() as scope, nc.Block() as block:
        q1 = K.sb(scope, f"{tag}_q1", [P, 2, S], F32R)
        k1 = K.sb(scope, f"{tag}_k1", [P, 2, S], F32R)
        q2 = K.sb(scope, f"{tag}_q2", [P, 2, S], F32R)
        k2 = K.sb(scope, f"{tag}_k2", [P, 2, S], F32R)
        if room is None:
            room = K.sb(scope, f"{tag}_weights", [P, 12 * HALF])[:]
        weights = [room[:, 4 * h * HALF:(4 + 8 * h) * HALF].rearrange("p (j n) -> p j n", n=HALF) for h in range(2)]
        vs = K.sb(scope, f"{tag}_v", [P, 1 if paired else 2, NT, dv + 1])
        peak = K.sb(scope, f"{tag}_peak", [P, 2, NT])
        low = K.sb(scope, f"{tag}_low", [P, 2, NT], F32R)
        share = K.sb(scope, f"{tag}_share", [P, 2])

        def head(i, x):
            return i if paired else i * 2 + x

        def score_bank(t):
            return K.ps[:, 2 * (t % 2):2 * (t % 2) + 2, :].rearrange("p b n -> p (b n)")

        @block.gpsimd
        def _(pool):
            def load(i, x):
                row = pool.snap((i * 2 + x) * HD)
                line = pool.snap(i * 2 + x)
                pool.wait_ge(t_scored, i * (2 * NC) + (NC * x + NC))
                pool.sem_inc(fetching, 1)
                for dst, name in ((q1[0:HD], "q_hi"), (q1[HD:P], "q_lo"), (k1[0:HD], "k_hi"), (k1[HD:P], "k_hi"),
                                  (q2[0:HD], "q_hi"), (k2[0:HD], "k_lo")):
                    pool.dma_start(dst[:, x, :], R[name][bass.ds(row, HD), :]).then_inc(loaded[x], 16)
                if decay:
                    pool.dma_start(k2[EXTRA:EXTRA + 2, x, :], R["decay"][bass.ds(line, 1)].rearrange("o c s -> (o c) s")) \
                        .then_inc(loaded[x], 16)

            pool.wait_ge(filled, 1)
            with pool.Fori(0, maps // 2) as i:
                for x in range(2):
                    load(i, x)
                for x in range(1 if paired else 2):
                    pool.wait_ge(weighed, i * 16 + (16 if paired else 8 * x + 8))
                    nc.gpsimd.tensor_copy(vs[:, x, :, 0:dv], values[:, :, bass.ds(head(i, x) * dv + v_col, dv)]).then_inc(staged, 1)

        @block.tensor
        def _(pe):
            mm = nc.tensor.matmul
            pe.sem_inc(weighed, 16)
            pe.sem_inc(t_scored, 2 * NC)

            def scores(i, x, tiles):
                if tiles.start == 0:
                    pe.wait_ge(loaded[x], i * loads + loads)
                for t in tiles:
                    pe.wait_ge(peaked, i * 16 + (8 * x + t + 1))
                    pe.sem_inc(begun, 1)
                    n, queries = (t + 1) * P, slice(t * P, (t + 1) * P)
                    for b in range(0, n, HALF):
                        keys = slice(b, min(b + HALF, n))
                        mm(score_bank(t)[:, keys], q1[:, x, queries], k1[:, x, keys], start=True, stop=False)
                        mm(score_bank(t)[:, keys], q2[0:seen, x, queries], k2[0:seen, x, keys], start=False, stop=(keys.stop < n))
                    mm(score_bank(t)[:, n - P:n], K.ident_r[:], K.causal_r[:], start=False, stop=True).then_inc(scored, 1)

            def maxima(i, x):
                pe.wait_ge(lowered, i * 2 + (x + 1))
                pe.sem_inc(begun, 1)
                for t in range(NT):
                    last = mm(score_bank(0)[0:1, t * P:(t + 1) * P], low[:, x, t:t + 1], K.ident_r[:], start=True, stop=True)
                last.then_inc(m_turned, 1)

            def turned_scores(i, x, chunks):
                for c in chunks:
                    _, j, q0, n = CHUNKS[c]
                    if c == 0:
                        pe.wait_ge(m_kept, i * 2 + (x + 1))
                    pe.wait_ge(exped, i * (2 * NC) + (NC * x + c + 1))
                    bank, keys = K.ps[:, 4 + c % 2, 0:n], slice(j * P, (j + 1) * P)
                    crossing = q0 == j * P
                    mm(bank, k1[:, x, keys], q1[:, x, q0:q0 + n], start=True, stop=False)
                    last = mm(bank, k2[0:ROWS_2, x, keys], q2[0:ROWS_2, x, q0:q0 + n], start=False, stop=not crossing)
                    if crossing:
                        last = mm(bank[:, 0:P], K.ident_r[:], K.causal_t_r[:], start=False, stop=True)
                    last.then_inc(t_scored, 1)

            def weigh(i, x, tiles):
                for t in tiles:
                    half = t // 4
                    if t == 0 and not (paired and x):
                        pe.wait_ge(staged, i + 1 if paired else i * 2 + (x + 1))
                    c = CHUNKS.index((half, t, t * P, (half + 1) * HALF - t * P))
                    pe.wait_ge(exped, i * (2 * NC) + (NC * x + c + 3))
                    pe.wait_ge(stored, i * 16 + (8 * x + t + 1))
                    for j in range(t + 1):
                        last = mm(K.ps[:, 6 + t % 2, 0:dv + 1], weights[half][:, j, (t - 4 * half) * P:(t - 4 * half + 1) * P],
                                  vs[:, 0 if paired else x, j, :], start=(j == 0), stop=(j == t))
                    last.then_inc(weighed, 1)

            def step(i, x, more):
                ahead = (i, 1) if x == 0 else (i + 1, 0)
                turned_scores(i, x, range(4))
                if more:
                    scores(*ahead, range(4))
                weigh(i, x, range(2))
                if more:
                    scores(*ahead, range(4, NT))
                turned_scores(i, x, range(4, 8))
                weigh(i, x, (2, 3))
                turned_scores(i, x, range(8, NC))
                if more:
                    maxima(*ahead)
                weigh(i, x, range(4, NT))

            scores(0, 0, range(NT))
            maxima(0, 0)
            with pe.Fori(0, maps // 2 - 1) as i:
                for x in range(2):
                    step(i, x, True)
            step(maps // 2 - 1, 0, True)
            step(maps // 2 - 1, 1, False)

        @block.scalar
        def _(act):
            act.sem_inc(exped, 2)
            with act.Fori(0, maps // 2) as i:
                for x in range(2):
                    for c, (half, j, q0, n) in enumerate(CHUNKS):
                        act.wait_ge(t_scored, i * (2 * NC) + (NC * x + c + 2 * NC + 1))
                        nc.scalar.activation(weights[half][:, j, HALF - n:HALF], K.ps[:, 4 + c % 2, 0:n], ACT.Exp, scale=scale) \
                            .then_inc(exped, 1)

        @block.vector
        def _(dve):
            for dst, first, end, value in ((q2, EXTRA, MAX_ROW, 1.0), (k2, EXTRA, MAX_ROW, 0.0), (k2, MAX_ROW, ROWS_2, 1.0)):
                ones = K.const("ones")[first:end, 0:1].unsqueeze(2).to_broadcast([end - first, 2, S])
                nc.vector.tensor_scalar(dst[first:end], ones, value, None, ALU.mult)
            nc.vector.memset(vs[:, :, :, dv:dv + 1], 1.0)
            dve.drain()
            dve.sem_inc(filled, 1)
            dve.sem_inc(peaked, 2)
            dve.sem_inc(stored, 2)

            def peaks(i, x, tiles):
                for t in tiles:
                    dve.wait_ge(scored, i * 16 + (8 * x + t + 1))
                    nc.vector.tensor_reduce(peak[:, x, t:t + 1], score_bank(t)[:, 0:(t + 1) * P], AX, ALU.max).then_inc(peaked, 1)
                if tiles.stop == NT:
                    dve.drain()
                    nc.vector.tensor_scalar(low[:, x, :], peak[:, x, :], -1.0, None, ALU.mult).then_inc(lowered, 1)

            def keep_maxima(i, x):
                dve.wait_ge(m_turned, i * 2 + (x + 1))
                nc.vector.tensor_copy(q2[MAX_ROW:ROWS_2, x, :], score_bank(0)[0:1, :]).then_inc(m_kept, 1)

            def finish(i, x, tiles):
                for t in tiles:
                    y, part = K.ps[:, 6 + t % 2, 0:dv], share[:, t % 2:t % 2 + 1]
                    place = o[:, t, bass.ds(head(i, x) * dv + o_col, dv)]
                    dve.wait_ge(weighed, i * 16 + (8 * x + t + 17))
                    nc.vector.reciprocal(part, K.ps[:, 6 + t % 2, dv:dv + 1])
                    dve.drain()
                    if paired and x:
                        nc.vector.tensor_scalar(part, part, K.lam[:], None, ALU.mult)
                        dve.drain()
                        nc.vector.scalar_tensor_tensor(place, y, part, place, ALU.mult, ALU.add).then_inc(stored, 1)
                    else:
                        nc.vector.tensor_scalar(place, y, part, None, ALU.mult).then_inc(stored, 1)

            def step(i, x, more):
                ahead = (i, 1) if x == 0 else (i + 1, 0)
                if more:
                    peaks(*ahead, range(4))
                finish(i, x, range(2))
                if more:
                    peaks(*ahead, range(4, NT))
                finish(i, x, range(2, 4))
                if more:
                    keep_maxima(*ahead)
                finish(i, x, range(4, NT))

            peaks(0, 0, range(NT))
            keep_maxima(0, 0)
            with dve.Fori(0, maps // 2 - 1) as i:
                for x in range(2):
                    step(i, x, True)
            step(maps // 2 - 1, 0, True)
            step(maps // 2 - 1, 1, False)
            dve.drain()


def merge_branches(K, h_hi, h_lo, conv, oT, merged):
    nc, A = K.nc, K.A
    w_in = A["w_in"].rearrange("o (k p) n -> p (o k) n", p=P)
    branches = [(A["w_conv_out"].rearrange("o (k p) n -> p (o k) n", p=P), conv, 0, CT),
                (A["w_attn_out"].rearrange("o (k p) n -> p (o k) n", p=P), oT, CT, HEADS)]
    landed = [K.sem(f"m_landed{b}") for b in range(2)]
    b_landed = [K.sem(f"m_b_landed{b}") for b in range(2)]
    rounded, split, projected, gate_done, opened, joined = (K.sem(f"m_{n}") for n in
        ("rounded", "split", "projected", "gate_done", "opened", "joined"))
    tiles = D // P
    with ExitStack() as scope, nc.Block() as block:
        w = K.sb(scope, "m_w", [P, 2, KT, P])
        w_hi = K.sb(scope, "m_w_hi", [P, 2, KT, P], F32R)
        w_lo = K.sb(scope, "m_w_lo", [P, 2, KT, P], F32R)
        wb = K.sb(scope, "m_wb", [P, 2, CT + HEADS, P])
        gates = K.sb(scope, "m_gates", [P, 2, 2, HALF])

        @block.sync
        def _(sp):
            for c in range(tiles):
                for g in range(2):
                    if c:
                        sp.wait_ge(split, 2 * c + g - 1)
                    col = COL_GATE + g * D + c * P
                    sp.dma_start(w[:, g], w_in[:, :, col:col + P]).then_inc(landed[g], 16)
                if c >= 2:
                    sp.wait_ge(projected, 2 * (c - 1))
                for src, _, k0, kn in branches:
                    sp.dma_start(wb[:, c % 2, k0:k0 + kn], src[:, :, c * P:(c + 1) * P]).then_inc(b_landed[c % 2], 16)

        @block.tensor
        def _(pe):
            mm = nc.tensor.matmul
            with pe.Fori(0, tiles // 2) as i:
                for b in range(2):
                    for g in range(2):
                        pe.wait_ge(split, i * 4 + (2 * b + g + 1))
                        for h in range(2):
                            if g == 0:
                                pe.wait_ge(joined, i * 4 + (2 * b + h + 1))
                            bank, tokens = K.ps[:, 4 * h + g, :], slice(h * HALF, (h + 1) * HALF)
                            for k in range(KT):
                                mm(bank, w_hi[:, g, k, :], h_hi[:, k, tokens], start=(k == 0), stop=False)
                                mm(bank, w_hi[:, g, k, :], h_lo[:, k, tokens], start=False, stop=False)
                                last = mm(bank, w_lo[:, g, k, :], h_hi[:, k, tokens], start=False, stop=(k == KT - 1))
                        last.then_inc(gate_done, 1)
                    pe.wait_ge(b_landed[b], i * 32 + 32)
                    for h in range(2):
                        for n, (_, src, k0, kn) in enumerate(branches):
                            for k in range(kn):
                                last = mm(K.ps[:, 4 * h + 2 + n, :], wb[:, b, k0 + k, :], src[:, k, h * HALF:(h + 1) * HALF],
                                          start=(k == 0), stop=(k == kn - 1))
                        last.then_inc(projected, 1)

        @block.scalar
        def _(act):
            def fill(c, g):
                act.wait_ge(landed[g], c * 16 + 16)
                nc.scalar.activation(w_hi[:, g], w[:, g], ACT.Copy).then_inc(rounded, 1)

            def step(c, more):
                for g in range(2):
                    if more:
                        act.wait_ge(gate_done, c * 2 + (g + 1))
                        fill(c + 1, g)
                for h in range(2):
                    act.wait_ge(joined, c * 2 + (h + 1))
                    act.wait_ge(projected, c * 2 + (h + 1))
                    nc.scalar.activation(gates[:, h], K.ps[:, 4 * h:4 * h + 2, :], ACT.Sigmoid).then_inc(opened, 1)

            for g in range(2):
                fill(0, g)
            with act.Fori(0, tiles - 1) as c:
                step(c, True)
            step(tiles - 1, False)

        @block.vector
        def _(dve):
            def fill(n, g):
                dve.wait_ge(rounded, n + 1)
                nc.vector.tensor_tensor(w_lo[:, g], w[:, g], w_hi[:, g].bitcast(F32), ALU.subtract).then_inc(split, 1)

            def step(c, more):
                for g in range(2):
                    if more:
                        fill(c * 2 + (g + 2), g)
                for h in range(2):
                    dve.wait_ge(opened, c * 2 + (h + 1))
                    nc.vector.tensor_tensor(gates[:, h], gates[:, h], K.ps[:, 4 * h + 2:4 * h + 4, :], ALU.mult)
                    dve.drain()
                    nc.vector.tensor_tensor(merged[:, c, h * HALF:(h + 1) * HALF], gates[:, h, 0, :], gates[:, h, 1, :],
                                            ALU.add).then_inc(joined, 1)

            dve.sem_inc(joined, 2)
            for g in range(2):
                fill(g, g)
            with dve.Fori(0, tiles - 1) as c:
                step(c, True)
            step(tiles - 1, False)


def norm_and_route(K, x, rows, logits):
    nc, A = K.nc, K.A
    NL = GROUPS + EXPERTS
    meaned, rooted, scaled, turned, kept, routed, biased = (K.sem(f"r_{n}") for n in
        ("meaned", "rooted", "scaled", "turned", "kept", "routed", "biased"))
    landed = K.sem("r_landed")
    stored = [K.sem(f"r_stored{b}") for b in range(2)]
    with ExitStack() as scope, nc.Block() as block:
        gain = K.sb(scope, "r_gain", [P, D])
        wr = K.sb(scope, "r_w", [P, KT, NL])
        bias = K.sb(scope, "r_bias", [P, NL])
        ss = K.row_squares
        h2 = K.sb(scope, "r_h2", [P, 2, D])
        h2T = K.sb(scope, "r_h2T", [P, 2, KT, P])

        @block.sync
        def _(sp):
            sp.dma_start(gain[:], A["ffn_norm_g"].to_broadcast([P, D])).then_inc(landed, 16)
            sp.dma_start(wr[:, :, 0:GROUPS], A["w_router_group"].rearrange("o (k p) n -> p (o k) n", p=P)).then_inc(landed, 16)
            sp.dma_start(wr[:, :, GROUPS:NL], A["w_router_expert"].rearrange("o (k p) n -> p (o k) n", p=P)).then_inc(landed, 16)
            sp.dma_start(bias[:, 0:GROUPS], A["b_router_group"].to_broadcast([P, GROUPS])).then_inc(landed, 16)
            sp.dma_start(bias[:, GROUPS:NL], A["b_router_expert"].to_broadcast([P, EXPERTS])).then_inc(landed, 16)
            for t in range(NT):
                sp.wait_ge(scaled, t + 1)
                sp.dma_start(rows[t * P:(t + 1) * P, :], h2[:, t % 2, :]).then_inc(stored[t % 2], 16)
            for b in range(2):
                sp.wait_ge(stored[b], 16 * (NT // 2 + 1))

        @block.scalar
        def _(act):
            act.sem_inc(kept, 2)
            act.wait_ge(meaned, 1)
            nc.scalar.activation(ss[:], ss[:], ACT.Sqrt).then_inc(rooted, 1)
            with act.Fori(0, NT // 2) as i:
                for b in range(2):
                    act.wait_ge(turned, i * 2 + (b + 3))
                    act.wait_ge(routed, i * 2 + (b + 1))
                    nc.scalar.activation(h2T[:, b], K.ps[:, 2 * b:2 * b + 2, :].rearrange("p c (k n) -> p (c k) n", n=P),
                                         ACT.Copy).then_inc(kept, 1)

        @block.vector
        def _(dve):
            dve.sem_inc(stored[0], 16)
            dve.sem_inc(stored[1], 16)
            dve.sem_inc(biased, 2)
            nc.vector.tensor_scalar(ss[:], ss[:], 1.0 / D, EPS, ALU.mult, ALU.add).then_inc(meaned, 1)
            dve.wait_ge(rooted, 1)
            nc.vector.reciprocal(ss[:], ss[:])
            dve.drain()
            dve.wait_ge(landed, 80)

            def scale(t, b, stores):
                dve.wait_ge(turned, t + 1)
                dve.wait_ge(stored[b], stores)
                nc.vector.scalar_tensor_tensor(h2[:, b, :], x[:, t, :], ss[:, bass.ds(t, 1)], gain[:], ALU.mult, ALU.mult) \
                    .then_inc(scaled, 1)

            def add_bias(t, b):
                dve.wait_ge(routed, t + 3)
                nc.vector.tensor_tensor(logits[:, t, :], K.ps[:, 4 + b, 0:NL], bias[:], ALU.add).then_inc(biased, 1)

            for b in range(2):
                scale(b, b, 16)
            with dve.Fori(0, NT // 2 - 1) as i:
                for b in range(2):
                    scale(i * 2 + (b + 2), b, i * 16 + 32)
                    add_bias(i * 2 + b, b)
            for b in range(2):
                add_bias(NT - 2 + b, b)

        @block.tensor
        def _(pe):
            pe.sem_inc(turned, 2)
            pe.sem_inc(routed, 2)
            pe.wait_ge(landed, 80)

            def turn_rows(t, b):
                pe.wait_ge(scaled, t + 1)
                pe.wait_ge(kept, t + 1)
                for k in range(KT):
                    mm = nc.tensor.transpose(K.ps[:, 2 * b + k // 4, (k % 4) * P:(k % 4 + 1) * P],
                                             h2[:, b, k * P:(k + 1) * P], K.const("ident"))
                mm.then_inc(turned, 1)

            def route(t, b):
                pe.wait_ge(kept, t + 3)
                pe.wait_ge(biased, t + 1)
                for k in range(KT):
                    mm = nc.tensor.matmul(K.ps[:, 4 + b, 0:NL], h2T[:, b, k, :], wr[:, k, :], start=(k == 0), stop=(k == KT - 1))
                mm.then_inc(routed, 1)

            turn_rows(0, 0)
            with pe.Fori(0, NT // 2 - 1) as i:
                for b in range(2):
                    turn_rows(i * 2 + (b + 1), 1 - b)
                    route(i * 2 + b, b)
            turn_rows(NT - 1, 1)
            for b in range(2):
                route(NT - 2 + b, b)


class ExpertWeights:

    def __init__(self, K, scope):
        sb = lambda name, shape: K.sb(scope, f"e_{name}", [P, 2, *shape])
        self.K, self.gate, self.up, self.down = K, sb("wg", [KT, DE]), sb("wu", [KT, DE]), sb("wd", [FT, D])
        self.gate_landed, self.up_landed, self.down_landed = (
            [K.sem(f"e_{n}_landed{b}") for b in range(2)] for n in ("gate", "up", "down"))

    def load(self, sp, expert_of_block, n, b, opened=None, closed=None):
        def part(dst, name, landed):
            sp.dma_start(dst[:, b], self.K.A[name][0][bass.ds(e, 1)].rearrange("e (k p) n -> p (e k) n", p=P)).then_inc(landed[b], 16)

        e = sp.value_load(expert_of_block[0:1, bass.ds(n, 1)], min_val=0, max_val=EXPERTS - 1)
        if opened is not None:
            sp.wait_ge(*opened)
        part(self.gate, "w_gate_e", self.gate_landed)
        part(self.up, "w_up_e", self.up_landed)
        if closed is not None:
            sp.wait_ge(*closed)
        part(self.down, "w_down_e", self.down_landed)


def clear_results(K, results, nothing, cleared):
    nc = K.nc
    sure = 2 * S // P
    zeroed = K.sem("e_zeroed")
    with nc.Block() as block:

        @block.vector
        def _(dve):
            nc.vector.memset(nothing[:], 0.0).then_inc(zeroed, 1)

        @block.sync
        def _(sp):
            sp.wait_ge(zeroed, 1)
            width = nothing.shape[1]
            sp.dma_start(results[sure * P:ROWS].rearrange("(p b) (c d) -> p (b c) d", p=P, d=width),
                         nothing[:].unsqueeze(1).to_broadcast([P, (BLOCKS - sure) * D // width, width])).then_inc(cleared, 16)


def choose_experts(K, logits, weights, dest, expert_of_block, pairs, table, experts):
    nc = K.nc
    owned = K.sem("c_owned")
    exped, peaked, chosen, counted, placed, zeroed, cleared, scattered = (K.sem(f"c_{n}") for n in
        ("exped", "peaked", "chosen", "counted", "placed", "zeroed", "cleared", "scattered"))
    with ExitStack() as scope, nc.Block() as block:
        sb = lambda name, shape, dt=F32: K.sb(scope, f"c_{name}", shape, dt)
        gpeak, gexp, gmass = sb("gpeak", [P, NT]), sb("gexp", [P, NT, GROUPS]), sb("gmass", [P, NT])
        ghot, g_pick = sb("ghot", [P, NT, GROUPS]), sb("g_pick", [P, NT])
        mine, part = sb("mine", [P, NT, EPG]), sb("part", [P, NT, EPG])
        top = sb("top", [P, 2, NT])
        hot = sb("hot", [P, 2, NT, EPG])
        hot32 = sb("hot32", [P, 2, NT, EXPERTS])
        both = sb("both", [P, NT, EXPERTS])
        gap, share = sb("gap", [P, NT]), sb("share", [P, NT])
        count_i, padded = sb("count_i", [P, EXPERTS], I32), sb("padded", [P, EXPERTS])
        ends, begins, ones = sb("ends", [P, EXPERTS]), sb("begins", [P, EXPERTS]), sb("ones", [P, EXPERTS])
        place, dest_f = sb("place", [P, NT, EXPERTS]), sb("dest_f", [P, NT, 2])
        behind, owner = sb("behind", [P, BLOCKS, EXPERTS]), sb("owner", [P, BLOCKS])
        tokens, zeros = sb("tokens", [P, NT], I32), sb("zeros", [P, BLOCKS], I32)

        def wide(ap, n):
            return ap.unsqueeze(2).to_broadcast([P, ap.shape[1], n])

        def rows(ap):
            return ap.unsqueeze(1).to_broadcast([P, NT, ap.shape[1]])

        @block.vector
        def _(dve):
            tt, ts = nc.vector.tensor_tensor, nc.vector.tensor_scalar

            def first_of(equal, rank, pick, out):
                tt(equal, equal, rows(rank), ALU.mult)
                dve.drain()
                nc.vector.tensor_reduce(pick, equal, AX, ALU.max)
                dve.drain()
                tt(out, rows(rank), wide(pick, rank.shape[1]), ALU.is_equal)
                dve.drain()

            nc.vector.memset(zeros[:], 0).then_inc(zeroed, 1)
            nc.vector.memset(ones[:], 1.0)
            nc.vector.tensor_copy(tokens[:], K.const("token"))
            g = logits[:, :, 0:GROUPS]
            nc.vector.tensor_reduce(gpeak[:], g, AX, ALU.max)
            dve.drain()
            tt(gexp[:], g, wide(gpeak[:], GROUPS), ALU.subtract).then_inc(peaked, 1)
            tt(ghot[:], g, wide(gpeak[:], GROUPS), ALU.is_equal)
            dve.drain()
            first_of(ghot[:], K.const("rank4"), g_pick[:], ghot[:])
            for j in range(GROUPS):
                e = logits[:, :, GROUPS + j * EPG:GROUPS + (j + 1) * EPG]
                tt(part[:] if j else mine[:], e, wide(ghot[:, :, j], EPG), ALU.mult)
                dve.drain()
                if j:
                    tt(mine[:], mine[:], part[:], ALU.add)
                    dve.drain()
            for c in range(2):
                nc.vector.tensor_reduce(top[:, c, :], mine[:], AX, ALU.max)
                dve.drain()
                tt(part[:], mine[:], wide(top[:, c, :], EPG), ALU.is_equal)
                dve.drain()
                first_of(part[:], K.const("rank8"), g_pick[:], hot[:, c])
                if c == 0:
                    nc.vector.scalar_tensor_tensor(mine[:], hot[:, 0], 4 * NEG, mine[:], ALU.mult, ALU.add)
                    dve.drain()
            for c in range(2):
                for j in range(GROUPS):
                    tt(hot32[:, c, :, j * EPG:(j + 1) * EPG], hot[:, c], wide(ghot[:, :, j], EPG), ALU.mult)
            dve.drain()
            tt(both[:], hot32[:, 0], hot32[:, 1], ALU.add).then_inc(chosen, 1)
            tt(gap[:], top[:, 1, :], top[:, 0, :], ALU.subtract).then_inc(peaked, 1)
            dve.wait_ge(exped, 2)
            nc.vector.tensor_reduce(gmass[:], gexp[:], AX, ALU.add)
            ts(share[:], gap[:], 1.0, None, ALU.add)
            dve.drain()
            tt(share[:], share[:], gmass[:], ALU.mult)
            dve.drain()
            nc.vector.reciprocal(share[:], share[:])
            dve.drain()
            nc.vector.tensor_copy(weights[:, :, 0], share[:])
            tt(weights[:, :, 1], share[:], gap[:], ALU.mult)
            dve.wait_ge(counted, 1)
            ts(count_i[:], K.ps[:, 0, NT * EXPERTS:(NT + 1) * EXPERTS], float(P - 1), None, ALU.add)
            dve.drain()
            ts(count_i[:], count_i[:], 7, 7, ALU.logical_shift_right, ALU.logical_shift_left)
            dve.drain()
            nc.vector.tensor_copy(padded[:], count_i[:])
            dve.drain()
            nc.vector.tensor_tensor_scan(ends[:], ones[:], padded[:], 0.0, ALU.mult, ALU.add)
            dve.drain()
            tt(begins[:], ends[:], padded[:], ALU.subtract)
            dve.drain()
            tt(place[:], K.ps[:, 0, 0:NT * EXPERTS].rearrange("p (t e) -> p t e", e=EXPERTS), rows(begins[:]), ALU.add)
            dve.drain()
            for c in range(2):
                tt(both[:], place[:], hot32[:, c], ALU.mult)
                dve.drain()
                nc.vector.tensor_reduce(dest_f[:, :, c], both[:], AX, ALU.add)
                dve.drain()
            nc.vector.tensor_copy(dest[:], dest_f[:].rearrange("p t c -> p (t c)")).then_inc(placed, 1)
            tt(behind[:], ends[:].unsqueeze(1).to_broadcast([P, BLOCKS, EXPERTS]), wide(K.const("block_start"), EXPERTS),
               ALU.is_le)
            dve.drain()
            nc.vector.tensor_reduce(owner[:], behind[:], AX, ALU.add)
            dve.drain()
            nc.vector.tensor_copy(count_i[:, 0:1], ends[:, EXPERTS - 1:EXPERTS])
            dve.drain()
            ts(pairs[:], count_i[:, 0:1], 2 * P - 1, None, ALU.add)
            dve.drain()
            ts(pairs[:], pairs[:], 8, None, ALU.logical_shift_right)
            ts(expert_of_block[:, 0:BLOCKS], owner[:], float(EXPERTS - 1), None, ALU.min).then_inc(owned, 1)

        @block.sync
        def _(sp):
            sp.wait_ge(owned, 1)
            experts.load(sp, expert_of_block, 0, 0)

        @block.scalar
        def _(act):
            act.wait_ge(peaked, 1)
            nc.scalar.activation(gexp[:], gexp[:], ACT.Exp).then_inc(exped, 1)
            act.wait_ge(peaked, 2)
            nc.scalar.activation(gap[:], gap[:], ACT.Exp).then_inc(exped, 1)

        @block.tensor
        def _(pe):
            pe.wait_ge(chosen, 1)
            nc.tensor.matmul(K.ps[:, 0, 0:NT * EXPERTS], K.const("before"), both[:].rearrange("p t e -> p (t e)"),
                             start=True, stop=False, skip_group_check=True)
            for j in range(NT):
                mm = nc.tensor.matmul(K.ps[:, 0, (j + 1) * EXPERTS:(NT + 1) * EXPERTS].rearrange("p (t e) -> p t e", e=EXPERTS),
                                      K.const("ones"), both[:, j, :].unsqueeze(1).to_broadcast([P, NT - j, EXPERTS]),
                                      start=False, stop=(j == NT - 1), skip_group_check=True)
            mm.then_inc(counted, 1)

        @block.gpsimd
        def _(pool):
            pool.wait_ge(zeroed, 1)
            pool.dma_start(table.rearrange("(p b) o -> p (b o)", p=P), zeros[:]).then_inc(cleared, 16)
            pool.wait_ge(cleared, 16)
            pool.wait_ge(placed, 1)
            for t in range(NT):
                for c in range(2):
                    pool.indirect_dma_start(table, bass.IndirectOffsetOnAxis(ap=dest[:, 2 * t + c:2 * t + c + 1], axis=0),
                                            tokens[:, t:t + 1], None).then_inc(scattered, 16)
            pool.wait_ge(scattered, 16 * 2 * NT)


def run_experts(K, rows, table, expert_of_block, pairs, results, experts, cleared):
    nc, A = K.nc, K.A
    gathered = [K.sem(f"e_gathered{b}") for b in range(2)]
    wg, wu, wd = experts.gate, experts.up, experts.down
    stored = [K.sem(f"e_stored{b}") for b in range(2)]
    padded, fetching, ended, gate_made, mid_rounded, w_rounded, w_split = (K.sem(f"e_{n}") for n in
        ("padded", "fetching", "ended", "gate_made", "mid_rounded", "w_rounded", "w_split"))
    listed, picked, turned, x_kept, opened, silued, gated, mid_turned, mid_kept, closed, y_kept = (K.sem(f"e_{n}") for n in
        ("listed", "picked", "turned", "x_kept", "opened", "silued", "gated", "mid_turned", "mid_kept", "closed", "y_kept"))
    with ExitStack() as scope, nc.Block() as block:
        index = K.sb(scope, "e_index", [P, BLOCKS + 1], I32)
        pick = K.sb(scope, "e_pick", [P, 2, 1], I32)
        xb = K.sb(scope, "e_x", [P, 2, D])
        xT = K.sb(scope, "e_xT", [P, 2, KT, P])
        sg = K.sb(scope, "e_sg", [P, DE])
        mid = K.sb(scope, "e_mid", [P, DE])
        midT_hi, midT_lo = (K.sb(scope, f"e_midT_{part}", [P, FT, P], F32R) for part in ("hi", "lo"))
        wd_hi, wd_lo = (K.sb(scope, f"e_wd_{part}", [P, FT, D], F32R) for part in ("hi", "lo"))
        y = K.sb(scope, "e_y", [P, 2, D])
        x_banks = K.ps[:, 0:2, :].rearrange("p c (k n) -> p (c k) n", n=P)
        g_bank, u_bank, mid_bank = K.ps[:, 2, :], K.ps[:, 3, :], K.ps[:, 4, :]
        y_banks = K.ps[:, 6:8, :].rearrange("p c n -> p (c n)")

        @block.gpsimd
        def _(pool):
            pool.wait_ge(listed, 16)
            pool.wait_ge(padded, 1)

            def gather(n, b):
                pool.wait_ge(turned, n + 1)
                nc.gpsimd.tensor_copy(pick[:, b, :], index[:, bass.ds(n, 1)]).then_inc(picked, 1)
                pool.wait_ge(picked, n + 1)
                pool.sem_inc(fetching, 1)
                pool.indirect_dma_start(xb[:, b, :], None, rows, bass.IndirectOffsetOnAxis(ap=pick[:, b, :], axis=0)) \
                    .then_inc(gathered[b], 16)

            gather(0, 0)
            used = pool.value_load(pairs[0:1, 0:1], min_val=1, max_val=BLOCKS // 2)
            with pool.Fori(0, BLOCKS // 2) as i:
                with pool.If(i < used):
                    for b in range(2):
                        gather(i * 2 + (b + 1), 1 - b)

        @block.sync
        def _(sp):
            used = sp.value_load(pairs[0:1, 0:1], min_val=1, max_val=BLOCKS // 2)
            sp.wait_ge(gathered[0], 16)
            with sp.Fori(0, BLOCKS // 2) as i:
                with sp.If(i < used):
                    experts.load(sp, expert_of_block, i * 2 + 1, 1, (opened, i * 2 + 2), (closed, i * 2 + 2))
                with sp.If(i + 1 < used):
                    experts.load(sp, expert_of_block, i * 2 + 2, 0, (opened, i * 2 + 3), (closed, i * 2 + 3))

        @block.tensor
        def _(pe):
            pe.sem_inc(turned, 2)
            pe.sem_inc(opened, 2)
            pe.sem_inc(closed, 2)

            def y_bank(h):
                return K.ps[:, 6 + h, :]

            def half_of(h):
                return slice(h * HALF, (h + 1) * HALF)

            def turn_x(b, tiles):
                for k in tiles:
                    mm = nc.tensor.transpose(x_banks[:, k, :], xb[:, b, k * P:(k + 1) * P], K.const("ident"))
                return mm

            pe.wait_ge(gathered[0], 16)
            turn_x(0, range(KT)).then_inc(turned, 1)
            used = pe.value_load(pairs[0:1, 0:1], min_val=1, max_val=BLOCKS // 2)
            with pe.Fori(0, BLOCKS // 2) as i:
                with pe.If(i < used):
                    for b in range(2):
                        n = i * 2 + b
                        pe.wait_ge(x_kept, n + 1)
                        pe.wait_ge(gated, n + 1)
                        for w, bank, landed, made in ((wg, g_bank, experts.gate_landed, gate_made), (wu, u_bank, experts.up_landed, opened)):
                            pe.wait_ge(landed[b], i * 16 + 16)
                            for k in range(KT):
                                mm = nc.tensor.matmul(bank, xT[:, b, k, :], w[:, b, k, :], start=(k == 0), stop=(k == KT - 1))
                            mm.then_inc(made, 1)
                        pe.wait_ge(gathered[1 - b], i * 16 + 16 * (b + 1))
                        turn_x(1 - b, range(3))
                        pe.wait_ge(gated, n + 2)
                        pe.wait_ge(mid_kept, n + 1)
                        for k in range(FT):
                            mm = nc.tensor.transpose(mid_bank[:, k * P:(k + 1) * P], mid[:, k * P:(k + 1) * P], K.const("ident"))
                        mm.then_inc(mid_turned, 1)
                        turn_x(1 - b, range(3, KT)).then_inc(turned, 1)
                        pe.wait_ge(mid_rounded, n + 1)
                        pe.wait_ge(y_kept, n + 1)
                        for k in range(FT):
                            pe.wait_ge(w_split, i * (2 * FT) + (FT * b + k + 1))
                            for h in range(2):
                                nc.tensor.matmul(y_bank(h), midT_hi[:, k, :], wd_hi[:, k, half_of(h)], start=(k == 0), stop=False)
                                nc.tensor.matmul(y_bank(h), midT_hi[:, k, :], wd_lo[:, k, half_of(h)], start=False, stop=False)
                            if k == 0:
                                pe.wait_ge(mid_kept, n + 2)
                            for h in range(2):
                                mm = nc.tensor.matmul(y_bank(h), midT_lo[:, k, :], wd_hi[:, k, half_of(h)], start=False, stop=(k == FT - 1))
                        mm.then_inc(closed, 1)

        @block.scalar
        def _(act):
            act.dma_start(index[:, 0:BLOCKS], table.rearrange("(b p) o -> p (b o)", p=P),
                          allow_slow_non_contiguous=True).then_inc(listed, 16)

            def keep_x(n, b):
                act.wait_ge(turned, n + 3)
                nc.scalar.activation(xT[:, b], x_banks, ACT.Copy).then_inc(x_kept, 1)

            keep_x(0, 0)
            act.wait_ge(cleared, 16)
            used = act.value_load(pairs[0:1, 0:1], min_val=1, max_val=BLOCKS // 2)
            with act.Fori(0, BLOCKS // 2) as i:
                with act.If(i < used):
                    for b in range(2):
                        n = i * 2 + b
                        act.wait_ge(experts.down_landed[b], i * 16 + 16)
                        act.wait_ge(closed, n + 2)
                        for k in range(FT):
                            nc.scalar.activation(wd_hi[:, k, :], wd[:, b, k, :], ACT.Copy).then_inc(w_rounded, 1)
                        act.wait_ge(gate_made, n + 1)
                        act.wait_ge(gated, n + 1)
                        nc.scalar.activation(sg[:], g_bank, ACT.Silu).then_inc(silued, 1)
                        act.wait_ge(mid_turned, n + 1)
                        nc.scalar.activation(midT_hi[:].rearrange("p k n -> p (k n)"), mid_bank, ACT.Copy).then_inc(mid_rounded, 1)
                        keep_x(n + 1, 1 - b)
                        act.wait_ge(y_kept, n + 2)
                        act.dma_start(results[bass.ds(n * P, P), :], y[:, b, :]).then_inc(stored[b], 16)
            for b in range(2):
                act.wait_ge(stored[b], used * 16 + 16)
                act.sem_inc(ended, 1)

        @block.vector
        def _(dve):
            nc.vector.memset(index[:, BLOCKS:BLOCKS + 1], 0).then_inc(padded, 1)
            dve.sem_inc(gated, 1)
            dve.sem_inc(mid_kept, 1)
            dve.sem_inc(y_kept, 1)
            dve.sem_inc(stored[0], 16)
            dve.sem_inc(stored[1], 16)
            used = dve.value_load(pairs[0:1, 0:1], min_val=1, max_val=BLOCKS // 2)
            with dve.Fori(0, BLOCKS // 2) as i:
                with dve.If(i < used):
                    for b in range(2):
                        n = i * 2 + b
                        for k in range(FT):
                            dve.wait_ge(w_rounded, i * (2 * FT) + (FT * b + k + 1))
                            nc.vector.tensor_tensor(wd_lo[:, k, :], wd[:, b, k, :], wd_hi[:, k, :].bitcast(F32), ALU.subtract) \
                                .then_inc(w_split, 1)
                        dve.wait_ge(silued, n + 1)
                        dve.wait_ge(opened, n + 3)
                        nc.vector.tensor_tensor(mid[:], sg[:], u_bank, ALU.mult).then_inc(gated, 1)
                        dve.wait_ge(mid_rounded, n + 1)
                        nc.vector.tensor_tensor(midT_lo[:].rearrange("p k n -> p (k n)"), mid_bank,
                                                midT_hi[:].rearrange("p k n -> p (k n)").bitcast(F32), ALU.subtract).then_inc(mid_kept, 1)
                        dve.wait_ge(closed, n + 3)
                        dve.wait_ge(stored[b], i * 16 + 16)
                        nc.vector.tensor_copy(y[:, b, :], y_banks).then_inc(y_kept, 1)


def combine_experts(K, x, weights, dest, results):
    nc = K.nc
    gathered = [K.sem(f"a_gathered{t}") for t in range(NT // 2)]
    added = K.sem("a_added")
    with ExitStack() as scope, nc.Block() as block:
        y = K.sb(scope, "a_y", [P, NT, 2, D])
        junk = K.sb(scope, "a_junk", [P, D])

        @block.scalar
        def _(act):
            square_rows(K, "a", act, x, junk, added, 0)

        @block.gpsimd
        def _(pool):
            for t in range(NT):
                for c in range(2):
                    pool.indirect_dma_start(y[:, t, c, :], None, results,
                                            bass.IndirectOffsetOnAxis(ap=dest[:, 2 * t + c:2 * t + c + 1], axis=0)) \
                        .then_inc(gathered[t // 2], 16)

        @block.vector
        def _(dve):
            for t in range(NT):
                dve.wait_ge(gathered[t // 2], 64)
                for c in range(2):
                    last = nc.vector.scalar_tensor_tensor(x[:, t, :], y[:, t, c, :], weights[:, t, c:c + 1], x[:, t, :],
                                                          ALU.mult, ALU.add)
                    if c == 0:
                        dve.drain()
                last.then_inc(added, 1)


def turn(K, tag, src, dst):
    nc = K.nc
    tiles = src.shape[2] // P
    turned, kept, staged = K.sem(f"{tag}_turned"), K.sem(f"{tag}_kept"), K.sem(f"{tag}_staged")
    with ExitStack() as scope, nc.Block() as block:
        stage = K.sb(scope, f"{tag}_stage", [P, 2, src.shape[2]])

        @block.vector
        def _(dve):
            with dve.Fori(0, NT // 2) as i:
                for b in range(2):
                    dve.wait_ge(turned, i * 2 + (b + 1))
                    nc.vector.tensor_copy(stage[:, b, :], src[:, i * 2 + b, :]).then_inc(staged, 1)

        @block.tensor
        def _(pe):
            pe.sem_inc(turned, 2)
            with pe.Fori(0, NT // 2) as i:
                for b in range(2):
                    pe.wait_ge(staged, i * 2 + (b + 1))
                    pe.wait_ge(kept, i * 2 + (b + 1))
                    for k in range(tiles):
                        mm = nc.tensor.transpose(K.ps[:, b, k * P:(k + 1) * P], stage[:, b, k * P:(k + 1) * P],
                                                 K.const("ident"))
                    mm.then_inc(turned, 1)

        @block.scalar
        def _(act):
            act.sem_inc(kept, 2)
            with act.Fori(0, NT // 2) as i:
                for b in range(2):
                    act.wait_ge(turned, i * 2 + (b + 3))
                    nc.scalar.activation(dst[:, :, bass.ds((i * 2 + b) * P, P)],
                                         K.ps[:, b, 0:tiles * P].rearrange("p (k n) -> p k n", n=P), ACT.Copy) \
                        .then_inc(kept, 1)


def square_rows(K, tag, act, x, junk, added, before):
    begun = K.sem(f"{tag}_squaring")
    with act.Fori(0, NT) as t:
        act.wait_ge(added, t + (before + 1))
        act.sem_inc(begun, 1)
        K.nc.scalar.activation(junk[:], x[:, t, :], ACT.Square, accum_out=K.row_squares[:, bass.ds(t, 1)])
        act.drain()


def project_and_add(K, tag, srcT, depth, weight, gain_row, x, y, src, out, squares=False):
    nc = K.nc
    landed = [K.sem(f"{tag}_landed{b}") for b in range(2)]
    gain_landed, x_landed, stored = K.sem(f"{tag}_gain_landed"), K.sem(f"{tag}_x_landed"), K.sem(f"{tag}_stored")
    rounded, split, chunked, projected, squared, kept, meaned, rooted, added = (K.sem(f"{tag}_{n}") for n in
        ("rounded", "split", "chunked", "projected", "squared", "kept", "meaned", "rooted", "added"))
    with ExitStack() as scope, nc.Block() as block:
        w = K.sb(scope, f"{tag}_w", [P, 2, HALF])
        w_hi = K.sb(scope, f"{tag}_w_hi", [P, 2, HALF], F32R)
        w_lo = K.sb(scope, f"{tag}_w_lo", [P, 2, HALF], F32R)
        s_hi = K.sb(scope, f"{tag}_s_hi", [P, 2, S], F32R)
        s_lo = K.sb(scope, f"{tag}_s_lo", [P, 2, S], F32R)
        normed = gain_row is not None
        gain = K.sb(scope, f"{tag}_gain", [P, D]) if normed else None
        junk = K.sb(scope, f"{tag}_junk", [P, D]) if normed or squares else None
        ss = K.sb(scope, f"{tag}_ss", [P, 2, NT])
        rstd = K.sb(scope, f"{tag}_rstd", [P, NT])
        pairs = depth // 2

        @block.sync
        def _(sp):
            def load(q, b, s, c):
                row = sp.snap(c * P)
                sp.wait_ge(split, q * 4 + (2 * b + 1))
                sp.dma_start(w[:, b, :], weight[0][bass.ds(row, P), s * HALF:(s + 1) * HALF]).then_inc(landed[b], 16)

            for s in range(2):
                with sp.Fori(0, pairs) as i:
                    for b in range(2):
                        load(i + s * pairs, b, s, i * 2 + b)
                if s == 0 and normed:
                    sp.dma_start(gain[:], gain_row.to_broadcast([P, D])).then_inc(gain_landed, 16)
                if s == 0:
                    sp.dma_start(x[:], src.rearrange("(t p) d -> p t d", p=P)).then_inc(x_landed, 16)
            if out is not None:
                for t in range(NT):
                    sp.wait_ge(added, t + 1)
                    sp.dma_start(out[t * P:(t + 1) * P, :], x[:, t, :]).then_inc(stored, 16)
                sp.wait_ge(stored, 16 * NT)

        @block.tensor
        def _(pe):
            def chunk(q, b, s, first=False, last=False):
                pe.wait_ge(split, q * 4 + (2 * b + 6))
                for t in range(NT):
                    if first and s:
                        pe.wait_ge(kept, t + 1)
                    tokens = slice(t * P, (t + 1) * P)
                    nc.tensor.matmul(K.ps[:, t, :], s_hi[:, b, tokens], w_hi[:, b, :], start=first, stop=False)
                    nc.tensor.matmul(K.ps[:, t, :], s_hi[:, b, tokens], w_lo[:, b, :], start=False, stop=False)
                    mm = nc.tensor.matmul(K.ps[:, t, :], s_lo[:, b, tokens], w_hi[:, b, :], start=False, stop=last)
                    if t == NT - 1:
                        mm.then_inc(chunked, 1)
                    elif last:
                        mm.then_inc(projected, 1)

            pe.sem_inc(chunked, 2)
            for s in range(2):
                chunk(s * pairs, 0, s, first=True)
                chunk(s * pairs, 1, s)
                with pe.Fori(1 + s * pairs, pairs - 1 + s * pairs) as q:
                    for b in range(2):
                        chunk(q, b, s)
                chunk(pairs - 1 + s * pairs, 0, s)
                chunk(pairs - 1 + s * pairs, 1, s, last=True)

        @block.scalar
        def _(act):
            def fill(q, b, c):
                act.wait_ge(landed[b], q * 16 + 16)
                act.wait_ge(chunked, q * 2 + (b + 1))
                nc.scalar.activation(w_hi[:, b, :], w[:, b, :], ACT.Copy).then_inc(rounded, 1)
                nc.scalar.activation(s_hi[:, b, :], srcT[:, c, :], ACT.Copy).then_inc(rounded, 1)

            def half_squares(s):
                for t in range(NT):
                    if t == NT - 1:
                        act.wait_ge(chunked, (s + 1) * depth + 2)
                    else:
                        act.wait_ge(projected, s * (NT - 1) + t + 1)
                    act.drain()
                    nc.scalar.activation(junk[:, 0:HALF], K.ps[:, t, :], ACT.Square, accum_out=ss[:, s, t:t + 1]).then_inc(squared, 1)

            with act.Fori(0, pairs) as i:
                for b in range(2):
                    fill(i, b, i * 2 + b)
            fill(pairs, 0, 0)
            if normed:
                half_squares(0)
            fill(pairs, 1, 1)
            with act.Fori(1, pairs) as i:
                for b in range(2):
                    fill(i + pairs, b, i * 2 + b)
            if normed:
                half_squares(1)
                act.wait_ge(meaned, 1)
                nc.scalar.activation(rstd[:], rstd[:], ACT.Sqrt).then_inc(rooted, 1)
            if squares:
                act.drain()
                square_rows(K, tag, act, x, junk, *((added, 0) if normed else (kept, NT)))

        @block.vector
        def _(dve):
            def fill(q, b, c):
                dve.wait_ge(rounded, q * 4 + (2 * b + 1))
                nc.vector.tensor_tensor(w_lo[:, b, :], w[:, b, :], w_hi[:, b, :].bitcast(F32), ALU.subtract).then_inc(split, 1)
                dve.wait_ge(rounded, q * 4 + (2 * b + 2))
                nc.vector.tensor_tensor(s_lo[:, b, :], srcT[:, c, :], s_hi[:, b, :].bitcast(F32), ALU.subtract).then_inc(split, 1)

            def keep(s):
                for t in range(NT):
                    cols = slice(s * HALF, (s + 1) * HALF)
                    if not normed:
                        if t == NT - 1:
                            dve.wait_ge(chunked, (s + 1) * depth + 2)
                        else:
                            dve.wait_ge(projected, s * (NT - 1) + t + 1)
                        nc.vector.tensor_tensor(x[:, t, cols], x[:, t, cols], K.ps[:, t, :], ALU.add).then_inc(kept, 1)
                        continue
                    dve.wait_ge(squared, s * NT + t + 1)
                    nc.vector.tensor_tensor(y[:, t, cols], K.ps[:, t, :], gain[:, cols], ALU.mult).then_inc(kept, 1)

            dve.sem_inc(split, 4)
            with dve.Fori(0, pairs) as i:
                for b in range(2):
                    fill(i, b, i * 2 + b)
            fill(pairs, 0, 0)
            if normed:
                dve.wait_ge(gain_landed, 16)
            else:
                dve.wait_ge(x_landed, 16)
            keep(0)
            fill(pairs, 1, 1)
            with dve.Fori(1, pairs) as i:
                for b in range(2):
                    fill(i + pairs, b, i * 2 + b)
            keep(1)
            if not normed:
                return
            nc.vector.tensor_tensor(rstd[:], ss[:, 0, :], ss[:, 1, :], ALU.add)
            dve.drain()
            nc.vector.tensor_scalar(rstd[:], rstd[:], 1.0 / D, EPS, ALU.mult, ALU.add).then_inc(meaned, 1)
            dve.wait_ge(rooted, 1)
            nc.vector.reciprocal(rstd[:], rstd[:])
            dve.wait_ge(x_landed, 16)
            dve.drain()
            with dve.Fori(0, NT) as t:
                nc.vector.scalar_tensor_tensor(x[:, t, :], y[:, t, :], rstd[:, bass.ds(t, 1)], x[:, t, :],
                                               ALU.mult, ALU.add).then_inc(added, 1)


def ffn_up(K, h_hi, h_lo, room, f):
    nc, A = K.nc, K.A
    w_up = A["ffn_w_up_2"].rearrange("o (k p) n -> p (o k) n", p=P)
    landed = [K.sem(f"u_landed{b}") for b in range(2)]
    rounded, split, projected, kept, filtered, gelued, done = (K.sem(f"u_{n}") for n in
        ("rounded", "split", "projected", "kept", "filtered", "gelued", "done"))
    with ExitStack() as scope, nc.Block() as block:
        w_end, g_end = 2 * KT * P, 2 * KT * P + 2 * (2 + S)
        w = room[:, 0:w_end].rearrange("p (u k n) -> p u k n", u=2, k=KT)
        g = room[:, w_end:g_end].rearrange("p (b n) -> p b n", b=2)
        c = room[:, g_end:g_end + 2 * S].rearrange("p (b n) -> p b n", b=2)
        w_hi = K.sb(scope, "u_w_hi", [P, 2, KT, P], F32R)
        w_lo = K.sb(scope, "u_w_lo", [P, 2, KT, P], F32R)
        taps = K.vec("ffn_conv_w_2", 0, 3 * FFT).rearrange("p (w j) -> p w j", j=FFT)
        bias = K.vec("ffn_conv_b_2", 0, FFT)

        def banks(b, up):
            return K.ps[:, 4 * b + 2 * up:4 * b + 2 * up + 2, :].rearrange("p c n -> p (c n)")

        @block.sync
        def _(sp):
            for up in range(2):
                sp.dma_start(w[:, up], w_up[:, :, up * DFF:up * DFF + P]).then_inc(landed[up], 16)
            with sp.Fori(1, FFT) as j:
                for up in range(2):
                    off = sp.snap(j * P + up * DFF)
                    sp.wait_ge(split, j * 2 + (up - 1))
                    sp.dma_start(w[:, up], w_up[:, :, bass.ds(off, P)]).then_inc(landed[up], 16)

        @block.tensor
        def _(pe):
            with pe.Fori(0, FFT // 2) as i:
                for b in range(2):
                    for up in range(2):
                        pe.wait_ge(split, i * 4 + (2 * b + up + 1))
                        pe.wait_ge(done, i * 2 + (b + 1))
                        for h in range(2):
                            bank, tokens = K.ps[:, 4 * b + 2 * up + h, :], slice(h * HALF, (h + 1) * HALF)
                            for k in range(KT):
                                nc.tensor.matmul(bank, w_hi[:, up, k, :], h_hi[:, k, tokens], start=(k == 0), stop=False)
                                nc.tensor.matmul(bank, w_hi[:, up, k, :], h_lo[:, k, tokens], start=False, stop=False)
                                mm = nc.tensor.matmul(bank, w_lo[:, up, k, :], h_hi[:, k, tokens], start=False, stop=(k == KT - 1))
                        mm.then_inc(projected, 1)

        @block.scalar
        def _(act):
            def fill(j, up):
                act.wait_ge(landed[up], j * 16 + 16)
                nc.scalar.activation(w_hi[:, up], w[:, up], ACT.Copy).then_inc(rounded, 1)

            def step(j, b, more):
                act.wait_ge(projected, j * 2 + 1)
                act.wait_ge(done, j + 1)
                nc.scalar.activation(g[:, b, 2:2 + S], banks(b, 0), ACT.Copy).then_inc(kept, 1)
                if more:
                    fill(j + 1, 0)
                    act.wait_ge(projected, j * 2 + 2)
                    fill(j + 1, 1)
                act.wait_ge(filtered, j + 1)
                nc.scalar.activation(c[:, b, :], c[:, b, :], ACT.Gelu_apprx_tanh).then_inc(gelued, 1)

            for up in range(2):
                fill(0, up)
            with act.Fori(0, FFT // 2 - 1) as i:
                for b in range(2):
                    step(i * 2 + b, b, True)
            step(FFT - 2, 0, True)
            step(FFT - 1, 1, False)

        @block.vector
        def _(dve):
            def fill(n, up):
                dve.wait_ge(rounded, n + 1)
                nc.vector.tensor_tensor(w_lo[:, up], w[:, up], w_hi[:, up].bitcast(F32), ALU.subtract).then_inc(split, 1)

            def step(j, b, more):
                tap = lambda v: taps[:, v, bass.ds(j, 1)]
                dve.wait_ge(kept, j + 1)
                nc.vector.tensor_scalar(c[:, b, :], g[:, b, 0:S], tap(0), bias[:, bass.ds(j, 1)], ALU.mult, ALU.add)
                dve.drain()
                nc.vector.scalar_tensor_tensor(c[:, b, :], g[:, b, 1:1 + S], tap(1), c[:, b, :], ALU.mult, ALU.add)
                dve.drain()
                nc.vector.scalar_tensor_tensor(c[:, b, :], g[:, b, 2:2 + S], tap(2), c[:, b, :], ALU.mult, ALU.add) \
                    .then_inc(filtered, 1)
                if more:
                    fill(j * 2 + 2, 0)
                    fill(j * 2 + 3, 1)
                dve.wait_ge(projected, j * 2 + 2)
                dve.wait_ge(gelued, j + 1)
                nc.vector.tensor_tensor(f[:, j, :], c[:, b, :], banks(b, 1), ALU.mult).then_inc(done, 1)

            nc.vector.memset(g[:, :, 0:2], 0.0).then_inc(done, 2)
            for up in range(2):
                fill(up, up)
            with dve.Fori(0, FFT // 2 - 1) as i:
                for b in range(2):
                    step(i * 2 + b, b, True)
            step(FFT - 2, 0, True)
            step(FFT - 1, 1, False)


def prepare_mixers(K, Z, R):
    nc, A = K.nc, K.A
    CAP, DK = 15.0, 32
    filtered, silued, saved = (K.sem(f"q_{n}") for n in ("filtered", "silued", "saved"))
    const_landed = K.sem("q_const_landed")
    landed, biased, logged, summed, turned, spread, revealed, spread_kept = (K.sem(f"q_{n}") for n in
        ("landed", "biased", "logged", "summed", "turned", "spread", "revealed", "spread_kept"))
    with ExitStack() as scope, nc.Block() as block:
        sb = lambda name, shape: K.sb(scope, f"q_{name}", shape)
        bias = sb("bias", [4, 3])
        bias15 = sb("bias15", [4, 2])
        t = sb("t", [4, 2, S])
        x = sb("x", [4, S])
        u = sb("u", [4, 2, S])
        rel = sb("rel", [32, 4])
        band = sb("band", [4, 3 * P])
        raw, gates = Z["mlstm"], Z["gates"]
        mqk, total, keys = Z["mlstm_qk"], Z["total"], Z["keys"]
        least = keys[:, 1, :]

        @block.sync
        def _(sp):
            sp.dma_start(K.tables["mixer_consts"][:], A["mixer_consts"]).then_inc(const_landed, 16)
            for j, name in enumerate(("mlstm_b_i_2", "mlstm_b_f_2", "fox_b_f_2")):
                sp.dma_start(bias[:, j:j + 1], A[name].rearrange("o h -> h o")).then_inc(landed, 16)
            sp.dma_start(rel[:], A["rel_bias_2"]).then_inc(landed, 16)
            sp.dma_start(R["swa_q"].rearrange("(j p) t -> p j t", p=P), Z["swa_q"][:]).then_inc(saved, 16)
            for r in range(2):
                sp.dma_start(R["swa_k"].rearrange("(g r p) t -> g r p t", g=2, r=2)[:, r],
                             Z["swa_k"][:, 0, :]).then_inc(saved, 16)
            sp.wait_ge(spread_kept, 1)
            sp.dma_start(R["band"], band[:]).then_inc(revealed, 16)
            sp.wait_ge(revealed, 16)
            tile = bass.AP(R["band"].tensor, 0, [[1, P], [3 * P, 4], [1, 2 * P]])
            sp.dma_start(K.window_bias[:], tile).then_inc(saved, 16)
            sp.dma_start(K.sinks[:], A["swa_sinks_2"].to_broadcast([P, 4])).then_inc(saved, 16)
            sp.wait_ge(saved, 16 * 5)

        @block.tensor
        def _(pe):
            pe.wait_ge(landed, 64)
            pe.wait_ge(const_landed, 16)
            nc.tensor.matmul(K.ps[0:4, 0, 0:3 * P], rel[:], K.const("bucket")[0:32, :], start=True, stop=True).then_inc(spread, 1)
            pe.wait_ge(summed, 1)
            for i in range(NT):
                mm = nc.tensor.transpose(K.ps[:, 1, 4 * i:4 * i + 4], keys[:, 0, i * P:(i + 1) * P], K.const("ident")[0:4, 0:4])
            mm.then_inc(turned, 1)

        @block.vector
        def _(dve):
            ts, tt, stt = nc.vector.tensor_scalar, nc.vector.tensor_tensor, nc.vector.scalar_tensor_tensor
            dve.wait_ge(landed, 64)
            ts(bias15[:], bias[:, 0:2], 1.0 / CAP, None, ALU.mult).then_inc(biased, 1)
            ts(x[:], gates[:, 2, :], bias[:, 2:3], None, ALU.add)
            dve.drain()
            ts(least, x[:], 0.0, None, ALU.min)
            stt(u[:, 1, :], x[:], -1.0, x[:], ALU.mult, ALU.max).then_inc(biased, 1)
            for c in range(2):
                out = mqk[:, c, :]
                ts(out, raw[:, c, 0:S], K.vec("mlstm_conv_w_2", c), None, ALU.mult)
                for w in range(1, 4):
                    dve.drain()
                    last = stt(out, raw[:, c, w:w + S], K.vec("mlstm_conv_w_2", 2 * w + c), out, ALU.mult, ALU.add)
                last.then_inc(filtered, 1)
            dve.wait_ge(spread, 1)
            tt(band[:], K.ps[0:4, 0, 0:3 * P], K.const("outside")[0:4, :], ALU.add).then_inc(spread_kept, 1)
            dve.wait_ge(silued, 2)
            ts(mqk[:, 0, :], mqk[:, 0, :], DK ** -0.5, None, ALU.mult)
            dve.wait_ge(logged, 1)
            ts(u[:, 0, :], u[:, 0, :], -1.0, None, ALU.mult)
            tt(u[:, 1, :], least, u[:, 1, :], ALU.subtract)
            dve.drain()
            for c in range(2):
                nc.vector.tensor_tensor_scan(total[:, c, :], K.const("ones")[0:4, 0:1].to_broadcast([4, S]), u[:, c, :], 0.0, ALU.mult, ALU.add)
            dve.drain()
            stt(keys[:, 0, :], t[:, 0, :], CAP, total[:, 0, :], ALU.mult, ALU.subtract)
            ts(keys[:, 1, :], total[:, 1, :], -1.0, None, ALU.mult)
            dve.drain()
            dve.sem_inc(summed, 1)
            dve.wait_ge(turned, 1)
            nc.vector.tensor_copy(K.mlstm_keys[:], K.ps[:, 1, 0:4 * NT])

        @block.scalar
        def _(act):
            act.wait_ge(biased, 2)
            for c in range(2):
                nc.scalar.activation(t[:, c, :], gates[:, c, :], ACT.Tanh, scale=1.0 / CAP, bias=bias15[:, c:c + 1])
            act.drain()
            nc.scalar.activation(u[:, 0, :], t[:, 1, :], ACT.Exp, scale=-CAP)
            nc.scalar.activation(u[:, 1, :], u[:, 1, :], ACT.Exp, scale=-1.0)
            act.drain()
            nc.scalar.activation(u[:], u[:], ACT.Ln, bias=1.0).then_inc(logged, 1)
            for c in range(2):
                act.wait_ge(filtered, c + 1)
                nc.scalar.activation(mqk[:, c, :], mqk[:, c, :], ACT.Silu, bias=K.vec("mlstm_conv_b_2", c)).then_inc(silued, 1)


def window_attention(K, tag, q_rows, k_rows, v, v_col, o, o_col):
    nc = K.nc
    dk, DV, N = HD, 64, 2 * NT
    loaded = [K.sem(f"{tag}_loaded{x}") for x in range(2)]
    scored, peaked, exped, rated, turned, turned_kept, weighed, stored = (K.sem(f"{tag}_{n}") for n in
        ("scored", "peaked", "exped", "rated", "turned", "turned_kept", "weighed", "stored"))
    begun = K.sem(f"{tag}_begun")
    with ExitStack() as scope, nc.Block() as block:
        qh = K.sb(scope, f"{tag}_q", [dk, 2, S])
        kh = K.sb(scope, f"{tag}_k", [dk, 2, S])
        p = K.sb(scope, f"{tag}_p", [P, 2, 2 * P])
        pT = K.sb(scope, f"{tag}_pT", [P, 2, 2 * P])
        low = K.sb(scope, f"{tag}_low", [P, 2])
        mass = K.sb(scope, f"{tag}_mass", [P, 2])
        drop = K.sb(scope, f"{tag}_drop", [P, 2])
        share = K.sb(scope, f"{tag}_share", [P, 2])

        def place(n):
            t = n % NT
            return n // NT, t, max(t - 1, 0), min(t + 1, 2) * P, n % 2

        def score_bank(n):
            return K.ps[:, n % 2, 0:place(n)[3]]

        def turn_bank(n):
            return K.ps[:, 2 + n % 2, 0:place(n)[3]]

        def out_bank(n):
            return K.ps[:, 4 + n % 2, 0:DV]

        @block.sync
        def _(sp):
            with sp.Fori(0, 2) as i:
                for x in range(2):
                    row = sp.snap((i * 2 + x) * dk)
                    sp.wait_ge(weighed, i * N + (NT * x + 1))
                    sp.dma_start(qh[:, x, :], q_rows[bass.ds(row, dk), :]).then_inc(loaded[x], 16)
                    sp.dma_start(kh[:, x, :], k_rows[bass.ds(row, dk), :]).then_inc(loaded[x], 16)

        @block.tensor
        def _(pe):
            pe.sem_inc(weighed, NT + 1)
            pe.sem_inc(turned, 2)
            with pe.Fori(0, 2) as i:
                def scores(n):
                    x, t, first, width, _ = place(n)
                    if t == 0:
                        pe.wait_ge(loaded[x], i * 32 + 32)
                    pe.wait_ge(exped, i * N + (n + 1))
                    nc.tensor.matmul(score_bank(n), qh[:, x, t * P:(t + 1) * P], kh[:, x, first * P:(t + 1) * P], start=True, stop=False)
                    nc.tensor.matmul(score_bank(n), K.const("flip"), K.window_bias[:, i * 2 + x, 2 * P - width:2 * P],
                                     start=False, stop=True).then_inc(scored, 1)

                def turn_weights(n):
                    s = place(n)[4]
                    pe.wait_ge(exped, i * N + (n + 3))
                    pe.wait_ge(turned_kept, i * N + (n + 1))
                    for j in range(place(n)[3] // P):
                        mm = nc.tensor.transpose(turn_bank(n)[:, j * P:(j + 1) * P], p[:, s, j * P:(j + 1) * P], K.const("ident"))
                    mm.then_inc(turned, 1)

                def weigh(n):
                    x, t, first, width, s = place(n)
                    pe.wait_ge(turned_kept, i * N + (n + 3))
                    pe.wait_ge(stored, i * N + (n + 1))
                    pe.sem_inc(begun, 1)
                    for j in range(width // P):
                        mm = nc.tensor.matmul(out_bank(n), pT[:, s, j * P:(j + 1) * P],
                                              v[:, first + j, bass.ds(i * (2 * DV) + (x * DV + v_col), DV)],
                                              start=(j == 0), stop=(j == width // P - 1))
                    mm.then_inc(weighed, 1)

                scores(0)
                for n in range(N):
                    if n + 1 < N:
                        scores(n + 1)
                    turn_weights(n)
                    if n > 0:
                        weigh(n - 1)
                weigh(N - 1)

        @block.vector
        def _(dve):
            with dve.Fori(0, 2) as i:
                def peaks(n):
                    x, s = place(n)[0], place(n)[4]
                    dve.wait_ge(scored, i * N + (n + 1))
                    nc.vector.tensor_reduce(low[:, s:s + 1], score_bank(n), AX, ALU.max)
                    dve.drain()
                    nc.vector.tensor_scalar(low[:, s:s + 1], low[:, s:s + 1], K.sinks[:, bass.ds(i * 2 + x, 1)], -1.0,
                                            ALU.max, ALU.mult).then_inc(peaked, 1)

                def rate(n):
                    s = place(n)[4]
                    dve.wait_ge(exped, i * N + (n + 3))
                    dve.wait_ge(stored, i * N + (n + 1))
                    nc.vector.tensor_tensor(mass[:, s:s + 1], mass[:, s:s + 1], drop[:, s:s + 1], ALU.add)
                    dve.drain()
                    nc.vector.reciprocal(share[:, s:s + 1], mass[:, s:s + 1]).then_inc(rated, 1)

                peaks(0)
                for n in range(N):
                    if n + 1 < N:
                        peaks(n + 1)
                    rate(n)

        @block.scalar
        def _(act):
            act.sem_inc(exped, 2)
            act.sem_inc(turned_kept, 2)
            act.sem_inc(stored, 2)
            act.sem_inc(begun, 1)
            with act.Fori(0, 2) as i:
                def exps(n):
                    x, s, width = place(n)[0], place(n)[4], place(n)[3]
                    act.wait_ge(peaked, i * N + (n + 1))
                    act.wait_ge(turned, i * N + (n + 1))
                    if n > 1:
                        act.wait_ge(rated, i * N + (n - 1))
                    act.sem_inc(begun, 1)
                    nc.scalar.activation(drop[:, s:s + 1], K.sinks[:, bass.ds(i * 2 + x, 1)], ACT.Exp, bias=low[:, s:s + 1])
                    nc.scalar.activation(p[:, s, 0:width], score_bank(n), ACT.Exp, bias=low[:, s:s + 1],
                                         accum_out=mass[:, s:s + 1]).then_inc(exped, 1)

                def keep_turned(n):
                    act.wait_ge(turned, i * N + (n + 3))
                    nc.scalar.activation(pT[:, place(n)[4], 0:place(n)[3]], turn_bank(n), ACT.Copy).then_inc(turned_kept, 1)

                def finish(n):
                    x, t, _, _, s = place(n)
                    act.wait_ge(rated, i * N + (n + 1))
                    act.wait_ge(weighed, i * N + (n + NT + 2))
                    act.sem_inc(begun, 1)
                    nc.scalar.activation(o[:, t, bass.ds(i * (2 * DV) + (x * DV + o_col), DV)], out_bank(n), ACT.Copy,
                                         scale=share[:, s:s + 1]).then_inc(stored, 1)

                exps(0)
                for n in range(N):
                    if n + 1 < N:
                        exps(n + 1)
                    keep_turned(n)
                    if n > 0:
                        finish(n - 1)
                finish(N - 1)


def mlstm_attention(K, tag, R, values, v_col, o, o_col):
    nc = K.nc
    HM, DK, DV = 4, 32, 64
    NC = len(CHUNKS)
    loads = 16 * 9
    loaded = [K.sem(f"{tag}_loaded{b}") for b in range(2)]
    filled, staged, scored, exped, mixed, weighed, rated, stored, fetching, begun = (K.sem(f"{tag}_{n}") for n in
        ("filled", "staged", "scored", "exped", "mixed", "weighed", "rated", "stored", "fetching", "begun"))

    def score_bank(c, n):
        return K.ps[:, c % 3, 0:n]

    def decay_bank(c, n):
        return K.ps[:, 3 + c % 3, 0:n]

    def chunks_of(half):
        return [(c, j, q0, n) for c, (part, j, q0, n) in enumerate(CHUNKS) if part == half]

    def each_head(eng, step):
        with eng.Fori(0, HM // 2 - 1) as i:
            for x in range(2):
                step(i, x, True)
        step(HM // 2 - 1, 0, True)
        step(HM // 2 - 1, 1, False)

    def following(i, x):
        return (i, 1) if x == 0 else (i + 1, 0)

    with ExitStack() as scope, nc.Block() as block:
        q = K.sb(scope, f"{tag}_q", [P, 2, S], F32R)
        k = K.sb(scope, f"{tag}_k", [P, 2, S], F32R)
        rise = K.sb(scope, f"{tag}_rise", [2, 2, S], F32R)
        ones = K.sb(scope, f"{tag}_ones", [2, P], F32R)
        w = K.sb(scope, f"{tag}_w", [P, 3, HALF])
        weights = [K.sb(scope, f"{tag}_weights{h}", [P, 4 * (h + 1), HALF]) for h in range(2)]
        vs = K.sb(scope, f"{tag}_v", [P, 2, NT, DV + 1])
        share = K.sb(scope, f"{tag}_share", [P, 2])
        size = K.sb(scope, f"{tag}_size", [P, 2])

        @block.gpsimd
        def _(pool):
            pool.wait_ge(filled, 1)
            with pool.Fori(0, HM // 2) as i:
                for x in range(2):
                    row, line = pool.snap((i * 2 + x) * DK), pool.snap(i * 2 + x)
                    pool.wait_ge(scored, i * (2 * NC) + (NC * x + NC))
                    pool.sem_inc(fetching, 1)
                    for n, (q_part, k_part) in enumerate((("hi", "hi"), ("lo", "hi"), ("hi", "lo"), ("lo", "lo"))):
                        rows = slice(n * DK, (n + 1) * DK)
                        pool.dma_start(q[rows, x, :], R[f"q_{q_part}"][bass.ds(row, DK), :]).then_inc(loaded[x], 16)
                        pool.dma_start(k[rows, x, :], R[f"k_{k_part}"][bass.ds(row, DK), :]).then_inc(loaded[x], 16)
                    pool.dma_start(rise[:, x, :], R["rise"][bass.ds(line, 1)].rearrange("o c s -> (o c) s")).then_inc(loaded[x], 16)
                    pool.wait_ge(weighed, i * 16 + (8 * x + 8))
                    nc.gpsimd.tensor_copy(vs[:, x, :, 0:DV], values[:, :, bass.ds((i * 2 + x) * DV + v_col, DV)]).then_inc(staged, 1)

        @block.tensor
        def _(pe):
            mm = nc.tensor.matmul
            pe.sem_inc(weighed, 16)
            pe.sem_inc(scored, 2 * NC)
            pe.wait_ge(filled, 1)

            def scores(i, x, half):
                if half == 0:
                    pe.wait_ge(loaded[x], i * loads + loads)
                for c, j, q0, n in chunks_of(half):
                    pe.wait_ge(mixed, i * (2 * NC) + (NC * x + c + 1))
                    keys = slice(j * P, (j + 1) * P)
                    crossing = q0 == j * P
                    mm(score_bank(c, n), k[:, x, keys], q[:, x, q0:q0 + n], start=True, stop=True)
                    last = mm(decay_bank(c, n), ones[:], rise[:, x, q0:q0 + n], start=True, stop=not crossing)
                    if crossing:
                        last = mm(decay_bank(c, P), K.ident_r[:], K.causal_t_r[:], start=False, stop=True)
                    last.then_inc(scored, 1)

            def weigh(i, x, half):
                if half == 0:
                    pe.wait_ge(staged, i * 2 + (x + 1))
                for t in range(4 * half, 4 * half + 4):
                    c = CHUNKS.index((half, t, t * P, (half + 1) * HALF - t * P))
                    pe.wait_ge(mixed, i * (2 * NC) + (NC * x + c + 4))
                    pe.wait_ge(stored, i * 16 + (8 * x + t + 1))
                    for j in range(t + 1):
                        last = mm(K.ps[:, 6 + t % 2, 0:DV + 1], weights[half][:, j, (t - 4 * half) * P:(t - 4 * half + 1) * P],
                                  vs[:, x, j, :], start=(j == 0), stop=(j == t))
                    last.then_inc(weighed, 1)

            def step(i, x, more):
                scores(i, x, 1)
                weigh(i, x, 0)
                if more:
                    scores(*following(i, x), 0)
                weigh(i, x, 1)

            scores(0, 0, 0)
            each_head(pe, step)

        @block.scalar
        def _(act):
            act.sem_inc(stored, 2)

            def exps(i, x, half):
                for c, j, q0, n in chunks_of(half):
                    act.wait_ge(scored, i * (2 * NC) + (NC * x + c + 2 * NC + 1))
                    act.sem_inc(begun, 1)
                    nc.scalar.activation(w[:, c % 3, 0:n], decay_bank(c, n), ACT.Exp,
                                         bias=K.mlstm_keys[:, bass.ds(i * 2 + (4 * j + x), 1)]).then_inc(exped, 1)

            def finish(i, x, half):
                for t in range(4 * half, 4 * half + 4):
                    act.wait_ge(rated, i * 16 + (8 * x + t + 1))
                    act.sem_inc(begun, 1)
                    nc.scalar.activation(o[:, t, bass.ds((i * 2 + x) * DV + o_col, DV)], K.ps[:, 6 + t % 2, 0:DV], ACT.Copy,
                                         scale=share[:, t % 2:t % 2 + 1]).then_inc(stored, 1)

            def step(i, x, more):
                exps(i, x, 1)
                finish(i, x, 0)
                if more:
                    exps(*following(i, x), 0)
                finish(i, x, 1)

            exps(0, 0, 0)
            each_head(act, step)

        @block.vector
        def _(dve):
            nc.vector.memset(vs[:, :, :, DV:DV + 1], 1.0)
            nc.vector.tensor_copy(ones[:], K.const("ones")[0:2, :])
            dve.drain()
            dve.sem_inc(filled, 1)
            dve.sem_inc(mixed, 3)

            def mix(i, x, half):
                for c, j, q0, n in chunks_of(half):
                    dve.wait_ge(exped, i * (2 * NC) + (NC * x + c + 1))
                    nc.vector.tensor_tensor(weights[half][:, j, HALF - n:HALF], w[:, c % 3, 0:n], score_bank(c, n),
                                            ALU.mult).then_inc(mixed, 1)

            def rate(i, x, half):
                for t in range(4 * half, 4 * half + 4):
                    total, floor = K.ps[:, 6 + t % 2, DV:DV + 1], size[:, t % 2:t % 2 + 1]
                    dve.wait_ge(weighed, i * 16 + (8 * x + t + 17))
                    dve.wait_ge(stored, i * 16 + (8 * x + t + 1))
                    nc.vector.tensor_scalar(floor, total, -1.0, 1.0, ALU.mult, ALU.max)
                    dve.drain()
                    nc.vector.tensor_tensor(floor, total, floor, ALU.max)
                    dve.drain()
                    nc.vector.reciprocal(share[:, t % 2:t % 2 + 1], floor).then_inc(rated, 1)

            def step(i, x, more):
                mix(i, x, 1)
                rate(i, x, 0)
                if more:
                    mix(*following(i, x), 0)
                rate(i, x, 1)

            mix(0, 0, 0)
            each_head(dve, step)


def mixer_columns(Z):
    SCALE = HD ** -0.5
    ml_v, ml_o, ml_i, ml_f = ML0 + RW, ML0 + 2 * RW, ML0 + 3 * RW, ML0 + 3 * RW + 4
    sw_k, sw_v = SW0 + RW, SW0 + RW + P
    fx_k, fx_v, fx_f = FX0 + RW, FX0 + 2 * RW, FX0 + 3 * RW

    def tiles(name, col, count, lead=0, scale=1.0, func=ACT.Copy):
        return [([(col + j * P, P, 0)], lambda h, j=j: Z[name][:, j, lead + h * HALF:lead + (h + 1) * HALF], scale, func, None)
                for j in range(count)]

    units = (tiles("rwkv", 0, 8, lead=1) + tiles("mlstm", ML0, 2, lead=3) + tiles("mlstm_o", ml_o, 2, func=ACT.Sigmoid)
             + tiles("fox_q", FX0, 2, scale=SCALE) + tiles("fox_k", fx_k, 2) + tiles("swa_q", SW0, 2, scale=SCALE)
             + tiles("swa_k", sw_k, 1) + [([(ml_i, 4, 0), (ml_f, 4, 32), (fx_f, 4, 64)], None, None, None, None)])
    slabs = [([(ml_v, RW, 0), (fx_v, RW, RW)], lambda t: Z["values"][:, t, 0:2 * RW]),
             ([(sw_v + HD * (h // 2), HD, HD * h) for h in range(4)], lambda t: Z["values"][:, t, 2 * RW:3 * RW])]
    return units, slabs


def rwkv_gates(K, z, zm, W):
    nc, A = K.nc, K.A
    loaded, mixed, squashed, projected, gated, squares, rooted, summed, cumulated, exped = (K.sem(f"rg_{n}") for n in
        ("loaded", "mixed", "squashed", "projected", "gated", "squares", "rooted", "summed", "cumulated", "exped"))
    spare = [z[:, 2 * j:2 * j + 2, 1:S + 1] for j in range(4)]
    lw, c, a, tmp = spare
    r, k, v = zm[:, 0:2, :], zm[:, 2:4, :], zm[:, 4:6, :]
    kk, b = W["kk"], W["b"]

    def banks(n):
        return K.ps[:, n:n + 4, :].rearrange("p (j h) n -> p j (h n)", j=2)

    with ExitStack() as scope, nc.Block() as block:
        up = K.sb(scope, "rg_up", [P, RW])
        g_up = K.sb(scope, "rg_g_up", [P, RW])
        within = K.sb(scope, "rg_within", [P, S])

        @block.sync
        def _(sp):
            sp.dma_start(up[0:64, :], A["rwkv_w_up_2"].rearrange("o k n -> (o k) n")).then_inc(loaded, 16)
            sp.dma_start(up[64:P, :], A["rwkv_a_up_2"].rearrange("o k n -> (o k) n")).then_inc(loaded, 16)
            sp.dma_start(g_up[:], A["rwkv_g_up_2"].rearrange("o k n -> (o k) n")).then_inc(loaded, 16)

        @block.tensor
        def _(pe):
            pe.wait_ge(loaded, 48)
            pe.wait_ge(squashed, 2)
            for base, rows in ((0, slice(0, 64)), (4, slice(64, P))):
                for j in range(2):
                    for h in range(2):
                        mm = nc.tensor.matmul(K.ps[:, base + 2 * j + h, :], up[rows, j * P:(j + 1) * P],
                                              zm[rows, 6, h * HALF:(h + 1) * HALF], start=True, stop=True)
                mm.then_inc(projected, 1)
            pe.wait_ge(gated, 2)
            for j in range(2):
                for h in range(2):
                    mm = nc.tensor.matmul(K.ps[:, 2 * j + h, :], g_up[:, j * P:(j + 1) * P],
                                          zm[:, 7, h * HALF:(h + 1) * HALF], start=True, stop=True)
            mm.then_inc(projected, 1)
            for n, (base, free) in enumerate(((4, 4), (0, 6))):
                pe.wait_ge(squares, n + 1)
                pe.wait_ge(gated, free)
                for j in range(2):
                    for h in range(2):
                        mm = nc.tensor.matmul(K.ps[:, base + 2 * j + h, :], K.const("pair"),
                                              tmp[:, j, h * HALF:(h + 1) * HALF], start=True, stop=True)
                mm.then_inc(summed, 1)

        @block.vector
        def _(dve):
            ts, tt, stt = nc.vector.tensor_scalar, nc.vector.tensor_tensor, nc.vector.scalar_tensor_tensor
            for tiles in (range(6, 8), range(6)):
                span = slice(tiles.start, tiles.stop)
                tt(zm[:, span, :], z[:, span, 0:S], z[:, span, 1:S + 1], ALU.subtract)
                dve.drain()
                for j in tiles:
                    stt(zm[:, j, :], zm[:, j, :], K.vec("rwkv_mu_2", j), z[:, j, 1:S + 1], ALU.mult, ALU.add).then_inc(mixed, 1)
            dve.drain()
            for j in range(2):
                ts(kk[:, j, :], k[:, j, :], K.vec("rwkv_k_k_2", j), None, ALU.mult)
            nc.vector.memset(within[:], 1.0)
            dve.drain()
            nc.vector.memset(within[:].rearrange("p (c n) -> p c n", n=CHUNK)[:, :, 0:1], 0.0)
            tt(tmp, kk[:], kk[:], ALU.mult).then_inc(squares, 1)
            dve.wait_ge(gated, 2)
            ts(lw, lw, -math.exp(-0.5), None, ALU.mult)
            dve.drain()
            for j in range(2):
                nc.vector.tensor_tensor_scan(c[:, j, :], within[:], lw[:, j, :], 0.0, ALU.mult, ALU.add)
            dve.drain()
            tt(lw, c, lw, ALU.subtract).then_inc(cumulated, 1)
            dve.wait_ge(rooted, 1)
            ts(tmp, tmp, 1e-12, None, ALU.max)
            dve.drain()
            nc.vector.reciprocal(tmp, tmp)
            dve.drain()
            tt(kk[:], kk[:], tmp, ALU.mult)
            dve.drain()
            dve.wait_ge(gated, 4)
            for j in range(2):
                ts(tmp[:, j, :], a[:, j, :], -1.0, K.vec("rwkv_k_a_2", j), ALU.add, ALU.mult)
            dve.drain()
            stt(k, tmp, 1.0, k, ALU.add, ALU.mult)
            dve.drain()
            for j in range(2):
                bonus = stt(tmp[:, j, :], r[:, j, :], K.vec("rwkv_r_k_2", j), k[:, j, :], ALU.mult, ALU.mult)
            bonus.then_inc(squares, 1)
            tt(a, kk[:], a, ALU.mult)
            dve.wait_ge(summed, 2)
            tt(W["bonus"][:], banks(0), v, ALU.mult)
            dve.wait_ge(exped, 3)
            dve.drain()
            tt(b[:], a, tmp, ALU.mult)
            tt(kk[:], kk[:], lw, ALU.mult)
            tt(k, k, tmp, ALU.mult)
            tt(r, r, c, ALU.mult)
            for half in range(2):
                nc.vector.tensor_copy(W["whole"][:].rearrange("p (j e) n -> p e j n", e=2)[:, half],
                                      c[64 * half:64 * half + 64, :, CHUNK - 1::CHUNK])

        @block.scalar
        def _(act):
            act.wait_ge(mixed, 2)
            nc.scalar.activation(zm[0:64, 6, :], zm[0:64, 6, :], ACT.Tanh).then_inc(squashed, 1)
            nc.scalar.activation(zm[:, 7, :], zm[:, 7, :], ACT.Sigmoid).then_inc(squashed, 1)
            act.wait_ge(mixed, 8)
            for n, (out, name) in enumerate(((lw, "rwkv_w0_2"), (a, "rwkv_a0_2"))):
                act.wait_ge(projected, n + 1)
                for j in range(2):
                    nc.scalar.activation(out[:, j, :], banks(4 * n)[:, j, :], ACT.Sigmoid, bias=K.vec(name, j)).then_inc(gated, 1)
            act.wait_ge(projected, 3)
            for j in range(2):
                nc.scalar.activation(W["g"][:, j, :], banks(0)[:, j, :], ACT.Copy).then_inc(gated, 1)
            act.wait_ge(summed, 1)
            nc.scalar.activation(tmp, banks(4), ACT.Sqrt).then_inc(rooted, 1)
            act.wait_ge(cumulated, 1)
            nc.scalar.activation(lw, lw, ACT.Exp).then_inc(exped, 1)
            act.wait_ge(summed, 2)
            nc.scalar.activation(tmp, c, ACT.Exp, scale=-1.0).then_inc(exped, 1)
            act.drain()
            nc.scalar.activation(c, c, ACT.Exp).then_inc(exped, 1)


def rwkv_solve(K, W, solve, scratch):
    nc = K.nc
    H = 4
    begun, staged, shifted, scored, kept, cut, m_saved, m_loaded, solved, t_saved, cleared, t_loaded = (K.sem(f"rm_{n}") for n in
        ("begun", "staged", "shifted", "scored", "kept", "cut", "m_saved", "m_loaded", "solved", "t_saved", "cleared", "t_loaded"))
    with ExitStack() as scope, nc.Block() as block:
        ks = K.sb(scope, "rm_kk", [64, 2, H, P])
        bs = K.sb(scope, "rm_b", [64, 2, H, P])
        masked = K.sb(scope, "rm_masked", [P, 2, H, P])
        minus = K.sb(scope, "rm_minus", [P, NT, H, CHUNK])
        rows = K.sb(scope, "rm_rows", [P, CHUNK, CHUNK])
        prod = K.sb(scope, "rm_prod", [P, CHUNK, CHUNK])
        inv = K.sb(scope, "rm_inv", [P, CHUNK, CHUNK])

        @block.gpsimd
        def _(pool):
            with pool.Fori(0, NT // 2) as i:
                for x in range(2):
                    pool.wait_ge(scored, i * 2 + (x + 1))
                    for dst, src in ((ks, W["kk"]), (bs, W["b"])):
                        nc.gpsimd.tensor_copy(dst[:, x, 0::2, :], src[0:64, :, bass.ds((i * 2 + x) * P, P)]).then_inc(staged, 1)

        @block.tensor
        def _(pe):
            pe.sem_inc(scored, 2)
            with pe.Fori(0, NT // 2) as i:
                for x in range(2):
                    pe.wait_ge(staged, i * 4 + 2 * (x + 1))
                    pe.wait_ge(shifted, i * 4 + 2 * (x + 1))
                    pe.wait_ge(kept, i * 2 + (x + 1))
                    for h in range(H):
                        mm = nc.tensor.matmul(K.ps[:, x, h * P:(h + 1) * P], ks[:, x, h, :], bs[:, x, h, :], start=True, stop=True)
                    mm.then_inc(scored, 1)

        @block.vector
        def _(dve):
            dve.sem_inc(kept, 2)
            below = K.const("chunk_below").unsqueeze(1).to_broadcast([P, H, P])

            def shift(t, x):
                dve.wait_ge(scored, t + 1)
                dve.sem_inc(begun, 1)
                for dst, src in ((ks, W["kk"]), (bs, W["b"])):
                    nc.vector.tensor_copy(dst[:, x, 1::2, :], src[64:P, :, bass.ds(t * P, P)]).then_inc(shifted, 1)

            def cut_out(t, x):
                dve.wait_ge(scored, t + 3)
                nc.vector.scalar_tensor_tensor(masked[:, x], K.ps[:, x, :].rearrange("p (h n) -> p h n", h=H), -1.0, below,
                                               ALU.mult, ALU.mult).then_inc(kept, 1)
                dve.drain()
                nc.vector.tensor_reduce(minus[:, t], masked[:, x].rearrange("p h (c s) -> p h s c", s=CHUNK), AX, ALU.add)

            for x in range(2):
                shift(x, x)
            with dve.Fori(0, NT // 2 - 1) as i:
                for x in range(2):
                    cut_out(i * 2 + x, x)
                    shift(i * 2 + (x + 2), x)
            for x in range(2):
                cut_out(NT - 2 + x, x)
            dve.drain()
            dve.sem_inc(cut, 1)
            nc.vector.memset(solve[:], 0.0).then_inc(cleared, 1)
            nc.vector.memset(inv[:], 0.0)
            dve.drain()
            nc.vector.memset(inv[:].rearrange("p u t -> p (u t)")[:, 0::CHUNK + 1], 1.0)
            dve.wait_ge(m_loaded, 16)
            for t in range(1, CHUNK):
                dve.drain()
                nc.vector.tensor_tensor(prod[:, 0:t, 0:t], rows[:, t, 0:t].unsqueeze(1).to_broadcast([P, t, t]),
                                        inv[:, 0:t, 0:t], ALU.mult)
                dve.drain()
                nc.vector.tensor_reduce(inv[:, 0:t, t], prod[:, 0:t, 0:t], AX, ALU.add)
            dve.drain()
            dve.sem_inc(solved, 1)

        @block.sync
        def _(sp):
            def pieces(ap):
                return ap.rearrange("(c u) t s -> c t u s", c=4)

            sp.wait_ge(cut, 1)
            for q in range(4):
                sp.dma_start(pieces(scratch["minus"])[q], minus[q * CHUNK:(q + 1) * CHUNK].rearrange("t i h s -> t (i h) s")) \
                    .then_inc(m_saved, 16)
            sp.wait_ge(m_saved, 16 * 4)
            sp.dma_start(rows[:], scratch["minus"]).then_inc(m_loaded, 16)
            sp.wait_ge(solved, 1)
            sp.dma_start(scratch["inverse"], inv[:]).then_inc(t_saved, 16)
            sp.wait_ge(cleared, 1)
            sp.wait_ge(t_saved, 16)
            for q in range(4):
                sp.dma_start(solve[q * CHUNK:(q + 1) * CHUNK, :, q * CHUNK:(q + 1) * CHUNK], pieces(scratch["inverse"])[q]) \
                    .then_inc(t_loaded, 16)
            sp.wait_ge(t_loaded, 16 * 4)


def rwkv_chunks(K, zm, W, solve, y, room):
    nc = K.nc
    H, N = 4, 64
    (staged, shifted, turned, tokens_kept, scored, masked, crossed, x_kept, solved, uw_kept, moved, queried, h_kept, g_kept, q_kept,
     stepped, s_kept, y_ready, y_kept, begun, summed, own_kept) = (K.sem(f"rs_{n}") for n in
        ("staged", "shifted", "turned", "tokens_kept", "scored", "masked", "crossed", "x_kept", "solved", "uw_kept", "moved", "queried",
         "h_kept", "g_kept", "q_kept", "stepped", "s_kept", "y_ready", "y_kept", "begun", "summed", "own_kept"))
    with ExitStack() as scope, nc.Block() as block:
        sb = lambda name, shape: K.sb(scope, f"rs_{name}", shape)
        feat = [room[0:N, 5 * H * P * x:5 * H * P * (x + 1)].rearrange("p (s h n) -> p s h n", s=5, h=H)
                for x in range(2)]
        inv = [sb(f"inv{x}", [P, H, P]) for x in range(2)]
        bk = sb("bk", [P, 2, H, N])
        vt = sb("vt", [P, H, N])
        xk = sb("xk", [P, H, 2 * N])
        uw = sb("uw", [P, H, 2 * N])
        m2, n1, n2 = sb("m2", [P, H, P]), sb("n1", [P, H, P]), sb("n2", [P, H, P])
        grow = [sb(f"grow{x}", [N, 4, H, N]) for x in range(2)]
        add = [sb(f"add{x}", [N, 4, H, N]) for x in range(2)]
        q = [sb(f"q{x}", [N, H, P]) for x in range(2)]
        own = [sb(f"own{x}", [N, H, P]) for x in range(2)]
        state = sb("state", [N, 2, H, N])
        sources = (W["b"], zm[:, 2:4, :], zm[:, 4:6, :], W["kk"], zm[:, 0:2, :])
        COPIES = len(sources)

        def heads(bank, n):
            return K.ps[:, bank, 0:H * n].rearrange("p (h n) -> p h n", h=H)

        def chunk_rows(g):
            return slice(g * CHUNK, (g + 1) * CHUNK)

        def each_tile(eng, step):
            step(0, 0, False, True)
            with eng.Fori(0, NT // 2 - 1) as i:
                for x in range(2):
                    step(i * 2 + (x + 1), 1 - x, True, True)
            step(NT - 1, 1, True, False)

        @block.gpsimd
        def _(pool):
            with pool.Fori(0, NT // 2) as i:
                for x in range(2):
                    t = i * 2 + x
                    pool.wait_ge(summed, t + 1)
                    pool.wait_ge(q_kept, t + 1)
                    pool.sem_inc(begun, 1)
                    for s, src in enumerate(sources):
                        nc.gpsimd.tensor_copy(feat[x][:, s, 0::2, :], src[0:64, :, bass.ds(t * P, P)]).then_inc(staged, 1)
                    nc.gpsimd.tensor_copy(inv[x][:], solve[:, bass.ds(t * H, H), :]).then_inc(staged, 1)

        @block.tensor
        def _(pe):
            mm = nc.tensor.matmul
            pe.sem_inc(summed, 2)

            def by_token(t, x):
                b, k, v, kk, r = (feat[x][:, s] for s in range(5))
                pe.wait_ge(staged, t * (COPIES + 1) + (COPIES + 1))
                pe.wait_ge(shifted, t * COPIES + COPIES)
                pe.wait_ge(g_kept, t + 1)
                pe.wait_ge(h_kept, t + 1)
                pe.sem_inc(begun, 1)
                for n, src in enumerate((b, k, v, kk)):
                    for h in range(H):
                        last = nc.tensor.transpose(K.ps[:, n // 2, (n % 2) * RW + h * N:(n % 2) * RW + (h + 1) * N],
                                                   src[:, h, :], K.const("ident")[0:N, 0:N])
                last.then_inc(turned, 1)
                pe.wait_ge(q_kept, t + 2)
                pe.sem_inc(begun, 1)
                for n, (left, right) in enumerate(((k, kk), (b, r), (k, r))):
                    for h in range(H):
                        last = mm(heads(2 + n, P)[:, h], left[:, h, :], right[:, h, :], start=True, stop=True)
                    last.then_inc(scored, 1)

            def cross(t, x):
                pe.wait_ge(masked, t * 3 + 1)
                pe.wait_ge(tokens_kept, t * 3 + 3)
                pe.wait_ge(own_kept, t + 1)
                for h in range(H):
                    last = mm(heads(5, N)[:, h], m2[:, h, :], vt[:, h, :], start=True, stop=True)
                last.then_inc(crossed, 1)

            def solve_chunks(t, x):
                pe.wait_ge(x_kept, t + 1)
                for h in range(H):
                    last = mm(heads(1, 2 * N)[:, h], inv[x][:, h, :], xk[:, h, :], start=True, stop=True)
                last.then_inc(solved, 1)

            def move(t, x):
                pe.wait_ge(masked, t * 3 + 3)
                pe.wait_ge(uw_kept, t + 1)
                for h in range(H):
                    last = mm(heads(4, P)[0:N, h], uw[:, h, N:2 * N], n1[:, h, :], start=True, stop=True)
                last.then_inc(queried, 1)
                for g in range(4):
                    for h in range(H):
                        last = mm(heads(g, N)[0:N, h], uw[chunk_rows(g), h, N:2 * N], bk[chunk_rows(g), 0, h, :], start=True, stop=True)
                for g in range(4):
                    for h in range(H):
                        out = K.ps[0:N, g, RW + h * N:RW + (h + 1) * N]
                        mm(out, bk[chunk_rows(g), 0, h, :], uw[chunk_rows(g), h, 0:N], start=True, stop=False)
                        last = mm(out, bk[chunk_rows(g), 1, h, :], vt[chunk_rows(g), h, :], start=False, stop=True)
                last.then_inc(moved, 1)

            def sum_own(t, x):
                for h in range(H):
                    mm(heads(5, P)[0:N, h], vt[:, h, :], n2[:, h, :], start=True, stop=False)
                    last = mm(heads(5, P)[0:N, h], uw[:, h, 0:N], n1[:, h, :], start=False, stop=True)
                last.then_inc(summed, 1)

            def state_step(t, x, g):
                if g == 0:
                    pe.wait_ge(q_kept, t + 3)
                    pe.wait_ge(g_kept, t + 2)
                    pe.wait_ge(h_kept, t + 2)
                    pe.wait_ge(y_kept, t * 2 + 2)
                pe.wait_ge(s_kept, t * 4 + (g + 1))
                pe.sem_inc(begun, 1)
                for h in range(H):
                    mm(heads(7, N)[0:N, h], grow[x][:, g, h, :], state[:, g % 2, h, :], start=True, stop=False)
                    last = mm(heads(7, N)[0:N, h], K.const("ident")[0:N, 0:N], add[x][:, g, h, :], start=False, stop=True)
                last.then_inc(stepped, 1)
                for h in range(H):
                    last = mm(heads(6, P)[0:N, h, chunk_rows(g)], state[:, g % 2, h, :], q[x][:, h, chunk_rows(g)],
                              start=True, stop=True)
                if g == 3:
                    last.then_inc(y_ready, 1)

            def step(t, x, before, _):
                for g, prepare in enumerate((by_token, cross, solve_chunks, move)):
                    prepare(t, x)
                    if before:
                        state_step(t - 1, 1 - x, g)
                sum_own(t, x)

            each_tile(pe, step)
            for g in range(4):
                state_step(NT - 1, 1, g)

        @block.scalar
        def _(act):
            act.sem_inc(own_kept, 1)

            def step(t, x, _, __):
                act.wait_ge(turned, t + 1)
                nc.scalar.activation(bk[:], K.ps[:, 0, :].rearrange("p (s h n) -> p s h n", s=2, h=H), ACT.Copy).then_inc(tokens_kept, 1)
                nc.scalar.activation(vt[:], K.ps[:, 1, 0:RW].rearrange("p (h n) -> p h n", h=H), ACT.Copy).then_inc(tokens_kept, 1)
                nc.scalar.activation(xk[:, :, N:2 * N], K.ps[:, 1, RW:2 * RW].rearrange("p (h n) -> p h n", h=H),
                                     ACT.Copy).then_inc(tokens_kept, 1)
                act.wait_ge(crossed, t + 1)
                nc.scalar.activation(xk[:, :, 0:N], heads(5, N), ACT.Copy).then_inc(x_kept, 1)
                act.wait_ge(solved, t + 1)
                nc.scalar.activation(uw[:], heads(1, 2 * N), ACT.Copy, scale=-1.0).then_inc(uw_kept, 1)
                act.wait_ge(summed, t + 3)
                nc.scalar.activation(own[x][:], heads(5, P)[0:N], ACT.Copy).then_inc(own_kept, 1)

            each_tile(act, step)

        @block.vector
        def _(dve):
            tt = nc.vector.tensor_tensor
            dve.sem_inc(y_kept, 2)
            dve.sem_inc(q_kept, 2)
            dve.sem_inc(g_kept, 1)
            dve.sem_inc(h_kept, 1)
            nc.vector.memset(state[:, 0], 0.0).then_inc(s_kept, 1)
            above = K.const("chunk_above").unsqueeze(1).to_broadcast([P, H, P])
            upto = K.const("chunk_upto").unsqueeze(1).to_broadcast([P, H, P])

            def shift(t, x):
                dve.wait_ge(summed, t + 1)
                dve.sem_inc(begun, 1)
                for s, src in enumerate(sources):
                    nc.vector.tensor_copy(feat[x][:, s, 1::2, :], src[64:P, :, bass.ds(t * P, P)]).then_inc(shifted, 1)

            def keep_state(t, g):
                dve.wait_ge(stepped, t * 4 + (g + 1))
                dve.sem_inc(begun, 1)
                tt(state[:, (g + 1) % 2], heads(7, N)[0:N],
                   W["whole"][:, :, bass.ds(t * 4 + g, 1)].to_broadcast([N, H, N]), ALU.mult).then_inc(s_kept, 1)

            def finish(t, x):
                dve.wait_ge(own_kept, t + 2)
                dve.wait_ge(y_ready, t + 1)
                dve.sem_inc(begun, 1)
                for half in range(2):
                    tt(y[64 * half:64 * half + 64, :, bass.ds(t * P, P)], own[x][:, half::2, :], heads(6, P)[0:N, half::2],
                       ALU.add).then_inc(y_kept, 1)

            def step(t, x, before, after):
                for n, (dst, mask) in enumerate(((m2, above), (n1, upto), (n2, upto))):
                    dve.wait_ge(scored, t * 3 + (n + 1))
                    tt(dst[:], heads(2 + n, P), mask, ALU.mult).then_inc(masked, 1)
                if before:
                    for g in range(3):
                        keep_state(t - 1, g)
                if after:
                    shift(t + 1, 1 - x)
                dve.wait_ge(queried, t + 1)
                tt(q[x][:], heads(4, P)[0:N], feat[x][:, 4], ALU.add).then_inc(q_kept, 1)
                dve.wait_ge(moved, t + 1)
                tt(grow[x][:], K.ps[0:N, 0:4, 0:RW].rearrange("p g (h n) -> p g h n", h=H),
                   K.const("ident")[0:N, 0:N].unsqueeze(1).unsqueeze(1).to_broadcast([N, 4, H, N]), ALU.add).then_inc(g_kept, 1)
                nc.vector.tensor_copy(add[x][:], K.ps[0:N, 0:4, RW:2 * RW].rearrange("p g (h n) -> p g h n", h=H)).then_inc(h_kept, 1)
                if before:
                    keep_state(t - 1, 3)
                    finish(t - 1, 1 - x)

            shift(0, 0)
            each_tile(dve, step)
            for g in range(4):
                keep_state(NT - 1, g)
            finish(NT - 1, 1)


def rwkv_finish(K, y, W, out):
    nc = K.nc
    eps = 64e-5
    summed, centred, squared, meaned, rooted = (K.sem(f"rf_{n}") for n in ("summed", "centred", "squared", "meaned", "rooted"))
    with ExitStack() as scope, nc.Block() as block:
        sq = K.sb(scope, "rf_sq", [P, 2, S])
        var = K.sb(scope, "rf_var", [P, 2, S])

        def banks(n):
            return K.ps[:, n:n + 4, :].rearrange("p (j h) n -> p j (h n)", j=2)

        @block.tensor
        def _(pe):
            for n, src in enumerate((y, sq)):
                if n:
                    pe.wait_ge(squared, 1)
                for j in range(2):
                    for h in range(2):
                        mm = nc.tensor.matmul(K.ps[:, 4 * n + 2 * j + h, :], K.const("pair"), src[:, j, h * HALF:(h + 1) * HALF],
                                              start=True, stop=True)
                mm.then_inc(summed, 1)

        @block.vector
        def _(dve):
            stt = nc.vector.scalar_tensor_tensor
            dve.wait_ge(summed, 1)
            stt(y[:], banks(0), -1.0 / 64, y[:], ALU.mult, ALU.add).then_inc(centred, 1)
            dve.wait_ge(summed, 2)
            nc.vector.tensor_scalar(var[:], banks(4), 1.0 / 64, eps, ALU.mult, ALU.add).then_inc(meaned, 1)
            dve.wait_ge(rooted, 1)
            nc.vector.reciprocal(var[:], var[:])
            dve.drain()
            nc.vector.tensor_tensor(y[:], y[:], var[:], ALU.mult)
            dve.drain()
            for j in range(2):
                nc.vector.tensor_scalar(y[:, j, :], y[:, j, :], K.vec("rwkv_ln_w_2", j), K.vec("rwkv_ln_b_2", j), ALU.mult, ALU.add)
            dve.drain()
            nc.vector.tensor_tensor(y[:], y[:], W["bonus"][:], ALU.add)
            dve.drain()
            nc.vector.tensor_tensor(out, y[:], W["g"][:], ALU.mult)

        @block.scalar
        def _(act):
            act.wait_ge(centred, 1)
            nc.scalar.activation(sq[:], y[:], ACT.Square).then_inc(squared, 1)
            act.wait_ge(meaned, 1)
            nc.scalar.activation(var[:], var[:], ACT.Sqrt).then_inc(rooted, 1)


def rwkv(K, z, yT):
    scratch = {n: K.dram(f"rwkv_{n}", (P, CHUNK, CHUNK)) for n in ("minus", "inverse")}
    with ExitStack() as scope:
        wide = lambda name: K.sb(scope, f"rwkv_{name}", [P, 2, S])
        W = {name: wide(name) for name in ("kk", "b", "g", "bonus")}
        W["whole"] = K.sb(scope, "rwkv_whole", [64, 4, S // CHUNK])
        zm = K.sb(scope, "rwkv_zm", [P, 8, S])
        solve = K.sb(scope, "rwkv_solve", [P, 4 * NT, P])
        rwkv_gates(K, z, zm, W)
        rwkv_solve(K, W, solve, scratch)
        y = zm[:, 6:8, :]
        rwkv_chunks(K, zm, W, solve, y, z[:].rearrange("p j s -> p (j s)"))
        rwkv_finish(K, y, W, yT[:, 0:2, :])


def first_block(K, x, x_landed):
    x_dram = K.A["x"].rearrange("o s d -> (o s) d")
    rows, results = K.dram("expert_rows", (S, D)), K.dram("expert_results", (ROWS, D))
    table = K.dram("expert_table", (ROWS, 1), I32)
    flat = x[:].rearrange("p t d -> p (t d)")
    with ExitStack() as right, ExitStack() as scope:
        h_hi, h_lo = (K.sb(right, f"h1_{part}", [P, KT, S], F32R, side="right") for part in ("hi", "lo"))
        conv = K.sb(scope, "conv", [P, CT, S])
        nothing, cleared = K.sb(scope, "nothing", [P, 256]), K.sem("e_cleared")
        with ExitStack() as inner:
            whole = K.sb(inner, "n1_whole", [P, 2 * D])
            norm_and_turn(K, "n1", x, K.vec("attn_norm_g", 0, KT), h_hi, h_lo, whole[:], landed=x_landed)
        with ExitStack() as inner:
            qkv = K.sb(inner, "qkv", [P, NT, 3 * HALF])
            project_and_convolve(K, h_hi, h_lo, conv, qkv, flat)
            clear_results(K, results, nothing, cleared)
            conv_norm(K, conv)
            qkT = x
            group_norm_and_turn(K, "qk", qkv[:, :, 0:2 * HALF], 4 * HEADS, K.qk_gain[:], qkT[:])
            o = qkv[:, :, 0:HALF]
            R = {f"{r}_{part}": K.dram(f"{r}_{part}", (HALF, S)) for r in "qk" for part in ("hi", "lo")}
            part_rows(K, "dp", [(qkT[:, j, :], *(R[f"{r}_{part}"][(j % HEADS) * P:(j % HEADS + 1) * P] for part in ("hi", "lo")))
                                for j in range(2 * HEADS) for r in ("q" if j < HEADS else "k")])
            soft_attention(K, "da", 2 * HEADS, R, qkv, 2 * HALF, VD, o, 0, HD ** -0.5, decay=False, paired=True, room=flat)
            oT = K.sb(right, "oT", [P, HEADS, S], side="right")
            group_norm_and_turn(K, "on", o, HEADS, K.head_gain[:], oT[:])
        merged = K.sb(scope, "merged", [P, KT, S])
        merge_branches(K, h_hi, h_lo, conv, oT, merged)
        project_and_add(K, "wo", merged, KT, K.A["w_out"], None, x, None, src=x_dram, out=None, squares=True)
    with ExitStack() as scope:
        logits = K.sb(scope, "logits", [P, NT, GROUPS + EXPERTS])
        weights = K.sb(scope, "weights", [P, NT, 2])
        dest = K.sb(scope, "dest", [P, 2 * NT], I32)
        expert_of_block = K.sb(scope, "expert_of_block", [P, BLOCKS + 1], I32)
        pairs = K.sb(scope, "pairs", [P, 1], I32)
        norm_and_route(K, x, rows, logits)
        with ExitStack() as inner:
            experts = ExpertWeights(K, inner)
            choose_experts(K, logits, weights, dest, expert_of_block, pairs, table, experts)
            run_experts(K, rows, table, expert_of_block, pairs, results, experts, cleared)
        combine_experts(K, x, weights, dest, results)


def mixers(K, h_hi, h_lo, h_scope, y_scope, table_scope, z):
    nc = K.nc
    both = ("hi", "lo")
    window = {name: K.dram(name, (n, S)) for name, n in (("swa_q", RW), ("swa_k", RW))}
    window["band"] = K.dram("window_band", (4, 3 * P))
    fox = {f"{r}_{part}": K.dram(f"fox_{r}_{part}", (RW, S)) for r in "qk" for part in both}
    mlstm = {f"{r}_{part}": K.dram(f"mlstm_{r}_{part}", (P, S)) for r in "qk" for part in both}
    fox["decay"], mlstm["rise"] = K.dram("fox_decay", (4, 2, S)), K.dram("mlstm_rise", (4, 2, S))
    with ExitStack() as scope:
        sb = lambda name, shape: K.sb(scope, name, shape)
        Z = {"rwkv": z, "mlstm_o": sb("mlstm_o", [P, 2, S]), "values": sb("values", [P, NT, 3 * RW])}
        with ExitStack() as inner:
            for name, tiles in (("fox_q", 2), ("fox_k", 2), ("swa_q", 2), ("swa_k", 1)):
                Z[name] = K.sb(inner, f"z_{name}", [P, tiles, S])
            Z["mlstm"] = K.sb(inner, "z_mlstm", [P, 2, 3 + S])
            Z["gates"] = K.sb(inner, "z_gates", [4, 3, S])
            with nc.Block() as block:

                @block.vector
                def _(dve):
                    nc.vector.memset(z[:, :, 0:1], 0.0)
                    nc.vector.memset(Z["mlstm"][:, :, 0:3], 0.0)

            units, slabs = mixer_columns(Z)
            project_columns(K, "z", K.A["w_in_2"], h_hi, h_lo, units, slabs, gates=Z["gates"])
            h_scope.close()
            yT = K.sb(y_scope, "yT", [P, KT, S], side="right")
            K.tables["mixer_consts"] = K.sb(table_scope, "mixer_table", [P, K.A["mixer_consts"].shape[1]], side="right")
            K.window_bias, K.sinks = (K.sb(scope, name, shape, side="right")
                                      for name, shape in (("window_bias", [P, 4, 2 * P]), ("sinks", [P, 4])))
            K.mlstm_keys = K.sb(scope, "mlstm_keys", [P, 4 * NT], side="right")
            Z["mlstm_qk"] = K.sb(inner, "z_mlstm_qk", [P, 2, S])
            Z["total"], Z["keys"] = K.sb(inner, "z_total", [4, 2, S]), K.sb(inner, "z_keys", [4, 2, S])
            prepare_mixers(K, Z, window)
            part_rows(K, "mp", [(Z[f"fox_{r}"][:, j, :], *(fox[f"{r}_{part}"][j * P:(j + 1) * P] for part in both))
                                for r in "qk" for j in range(2)]
                      + [(Z["mlstm_qk"][:, j, :], *(mlstm[f"{r}_{part}"] for part in both)) for j, r in enumerate("qk")]
                      + [(Z["keys"][:, 1, :], fox["decay"][:, 0], fox["decay"][:, 1]),
                         (Z["total"][:, 0, :], mlstm["rise"][:, 0], mlstm["rise"][:, 1])],
                      [yT[:, 4 * n:4 * n + 4, :].bitcast(F32R) for n in range(2)])
        o = sb("o_soft", [P, NT, 2 * RW])
        o_mlstm = sb("o_mlstm", [P, NT, RW])
        values = Z["values"]
        soft_attention(K, "fx", 4, fox, values, RW, HD, o, RW, 1.0, decay=True, paired=False)
        window_attention(K, "sw", window["swa_q"], window["swa_k"], values, 2 * RW, o, 0)
        mlstm_attention(K, "ml", mlstm, values, 0, o_mlstm, 0)
        turn(K, "tm", o, yT[:, 4:8, :])
        group_norm_and_turn(K, "mn", o_mlstm[:], 4, K.vec("mlstm_norm_2", 0, 2), yT[:, 2:4, :], gate=Z["mlstm_o"][:])
    K.recycle()
    rwkv(K, z, yT)
    return yT


def build(nc, A, out):
    with ExitStack() as ctx:
        K = Kernel(nc, A, out, ctx)
        K.place_vectors()
        x_kept, x_mixed = K.dram("x_kept", (S, D)), K.dram("x_mixed", (S, D))
        h_scope, y_scope = ctx.enter_context(ExitStack()), ctx.enter_context(ExitStack())
        with ExitStack() as scope:
            x = K.sb(scope, "x_first", [P, NT, D])
            x_landed = load_vectors(K, x, A["x"].rearrange("o s d -> (o s) d"))
            first_block(K, x, x_landed)
            K.recycle()
            h_hi, h_lo = (K.sb(h_scope, f"h2_{part}", [P, KT, S], F32R, side="right") for part in ("hi", "lo"))
            whole = K.sb(scope, "n3_whole", [P, 2 * D])
            norm_and_turn(K, "n3", x, K.vec("norm_mix_pre_2", 0, KT), h_hi, h_lo, whole[:], keep=x_kept)
        with ExitStack() as scope:
            z = K.sb(scope, "z_rwkv", [P, 8, 1 + S])
            yT = mixers(K, h_hi, h_lo, h_scope, y_scope, scope, z)
        with ExitStack() as scope:
            f = K.sb(scope, "f", [P, FFT, S])
            x, y = f[:, 0:NT, :], f[:, NT:2 * NT, :]
            project_and_add(K, "o2", yT, KT, A["w_out_2"], A["norm_mix_post_2"], x, y, src=x_kept, out=x_mixed, squares=True)
            with ExitStack() as inner:
                h_hi, h_lo = (K.sb(inner, f"h3_{part}", [P, KT, S], F32R) for part in ("hi", "lo"))
                norm_and_turn(K, "n4", x, K.vec("norm_ffn_pre_2", 0, KT), h_hi, h_lo,
                              y[:, 0:2, :].rearrange("p t d -> p (t d)"))
                ffn_up(K, h_hi, h_lo, yT[:].rearrange("p k n -> p (k n)"), f)
            x = K.sb(scope, "x_last", [P, NT, D])
            project_and_add(K, "fd", f, FFT, A["ffn_w_down_2"], A["norm_ffn_post_2"], x, yT, src=x_mixed, out=out)


_INS = ["x", "attn_norm_g", "w_in", "conv_dw_w", "conv_dw_b", "conv_ln_g", "conv_ln_b", "w_conv_out", "q_norm_g", "k_norm_g",
        "lambda_q1", "lambda_k1", "lambda_q2", "lambda_k2", "subln_g", "w_attn_out", "w_out", "ffn_norm_g", "w_router_group",
        "b_router_group", "w_router_expert", "b_router_expert", "w_gate_e", "w_up_e", "w_down_e", "w_in_2", "w_out_2",
        "norm_mix_pre_2", "norm_mix_post_2", "norm_ffn_pre_2", "norm_ffn_post_2", "rwkv_mu_2", "rwkv_w0_2", "rwkv_w_up_2",
        "rwkv_a0_2", "rwkv_a_up_2", "rwkv_g_up_2", "rwkv_k_k_2", "rwkv_k_a_2", "rwkv_r_k_2", "rwkv_ln_w_2", "rwkv_ln_b_2",
        "mlstm_conv_w_2", "mlstm_conv_b_2", "mlstm_b_i_2", "mlstm_b_f_2", "mlstm_norm_2", "swa_sinks_2", "fox_b_f_2", "rel_bias_2",
        "ffn_w_up_2", "ffn_conv_w_2", "ffn_conv_b_2", "ffn_w_down_2"]


def kernel(**inputs):
    import concourse.bacc as bacc
    from concourse.bass_utils import run_bass_kernel_spmd

    nc = bacc.Bacc("TRN2", target_bir_lowering=False, num_devices=1)
    arrays, A = {}, {}
    given = {name: np.ascontiguousarray(inputs[name]) for name in _INS}
    given.update(shape_constants()[0])
    for name, a in given.items():
        arrays[f"in_{name}_dram"] = a
        A[name] = nc.dram_tensor(f"in_{name}_dram", a.shape, mybir.dt.from_np(a.dtype), kind="ExternalInput").ap()
    out = nc.dram_tensor("out_0_dram", (1, S, D), F32, kind="ExternalOutput").ap()
    build(nc, A, out.rearrange("o s d -> (o s) d"))
    r = run_bass_kernel_spmd(nc, [arrays], core_ids=[0])
    return r.results[0]["out_0_dram"]
```
